# Optimizing a Trainium2 kernel written in Bass

```python
import jax, jax.numpy as jnp
from jax import lax
import numpy as np
import math

D_MODEL = 1024
BATCH = 1
SEQ = 1024
DEPTH = 1

D_MIX = 2 * D_MODEL
D_A = D_MIX // 2
D_B = D_MIX - D_A
A_GROUPS = 8
A_GROUP_DIM = D_A // A_GROUPS
A_CHUNK = 128
B_HEADS = 4
B_DK = D_B // 2 // B_HEADS
B_DV = D_B // B_HEADS
B_GATE_RANK = 16
B_GATE_TAU = 16.0
B_CHUNK = 64
D_IN = 3 * D_A + 2 * B_HEADS * B_DK + 2 * D_B + B_GATE_RANK
EPS = 1e-6


def rmsnorm(x, g):
    xf = x.astype(jnp.float32)
    y = xf * lax.rsqrt(jnp.mean(xf * xf, axis=-1, keepdims=True) + EPS)
    return (y * g.astype(jnp.float32)).astype(x.dtype)

def layernorm(x, g, b):
    xf = x.astype(jnp.float32)
    mu = jnp.mean(xf, axis=-1, keepdims=True)
    xc = xf - mu
    y = xc * lax.rsqrt(jnp.mean(xc * xc, axis=-1, keepdims=True) + EPS)
    return (y * g.astype(jnp.float32) + b.astype(jnp.float32)).astype(x.dtype)

def chunked_sgu(u, v, ln_g, ln_b, w_s, b_s):
    bsz, s = u.shape[:2]
    n = s // A_CHUNK
    vn = layernorm(v, ln_g, ln_b).reshape(bsz, n, A_CHUNK, A_GROUPS, A_GROUP_DIM)
    causal = jnp.tril(jnp.ones((A_CHUNK, A_CHUNK), dtype=bool))
    w = jnp.where(causal[None], w_s, jnp.zeros_like(w_s))
    sp = jnp.einsum('gts,bnsgc->bntgc', w, vn) + b_s.T[None, None, :, :, None]
    return u * sp.reshape(bsz, s, D_A).astype(u.dtype)

def gla_chunked(q, k, v, log_a):
    bsz, s = q.shape[:2]
    n = s // B_CHUNK
    f32 = jnp.float32

    def blk(t, d):
        return t.astype(f32).reshape(bsz, n, B_CHUNK, B_HEADS, d).transpose(0, 3, 1, 2, 4)

    q = blk(q, B_DK) * (B_DK ** -0.5)
    k = blk(k, B_DK)
    v = blk(v, B_DV)
    b = jnp.cumsum(blk(log_a, B_DK), axis=3)
    b_last = b[:, :, :, -1:, :]
    b_ref = b[:, :, :, B_CHUNK // 2 - 1:B_CHUNK // 2, :]

    qe = q * jnp.exp(b - b_ref)
    ke = k * jnp.exp(b_ref - b)
    scores = jnp.einsum('bhncd,bhnsd->bhncs', qe, ke)
    causal = jnp.tril(jnp.ones((B_CHUNK, B_CHUNK), dtype=bool))
    scores = jnp.where(causal, scores, 0.0)
    o_intra = jnp.einsum('bhncs,bhnsv->bhncv', scores, v)

    chunk_kv = jnp.einsum('bhncd,bhncv->bhndv', k * jnp.exp(b_last - b), v)
    decay = jnp.exp(b_last[:, :, :, 0, :])

    def step(state, inp):
        dec, kv = inp
        return dec[..., None] * state + kv, state

    s0 = jnp.zeros((bsz, B_HEADS, B_DK, B_DV), f32)
    _, s_prev = lax.scan(step, s0, (decay.transpose(2, 0, 1, 3), chunk_kv.transpose(2, 0, 1, 3, 4)))
    s_prev = s_prev.transpose(1, 2, 0, 3, 4)
    o_inter = jnp.einsum('bhncd,bhndv->bhncv', q * jnp.exp(b), s_prev)

    o = o_intra + o_inter
    return o.transpose(0, 2, 3, 1, 4).reshape(bsz, s, B_HEADS, B_DV)

def hybrid_layer(x, pre_g, w_in, w_a2, b_a2, a_ln_g, a_ln_b, a_w_s, a_b_s, b_norm_g, w_out, post_g):
    bsz, s, _ = x.shape
    h = rmsnorm(x, pre_g)
    z = jnp.einsum('bsd,de->bse', h, w_in)
    sizes = [D_A, D_A, D_A, B_HEADS * B_DK, B_HEADS * B_DK, D_B, D_B, B_GATE_RANK]
    cuts = np.cumsum(sizes)[:-1].tolist()
    a_u, a_v, a_gate, b_q, b_k, b_v, b_gate, b_lr = jnp.split(z, cuts, axis=-1)

    a_out = chunked_sgu(jax.nn.gelu(a_u, approximate=False), jax.nn.gelu(a_v, approximate=False),
                        a_ln_g, a_ln_b, a_w_s, a_b_s)
    a_out = a_out * jax.nn.silu(a_gate)

    gate_logit = jnp.einsum('bsr,re->bse', b_lr.astype(jnp.float32), w_a2.astype(jnp.float32)) + b_a2.astype(jnp.float32)
    log_a = jax.nn.log_sigmoid(gate_logit) / B_GATE_TAU
    o = gla_chunked(b_q.reshape(bsz, s, B_HEADS, B_DK), b_k.reshape(bsz, s, B_HEADS, B_DK),
                    b_v.reshape(bsz, s, B_HEADS, B_DV), log_a.reshape(bsz, s, B_HEADS, B_DK))
    o = rmsnorm(o, b_norm_g.reshape(B_HEADS, B_DV)).reshape(bsz, s, D_B).astype(x.dtype)
    b_out = o * jax.nn.silu(b_gate)

    mixed = jnp.concatenate([a_out, b_out], axis=-1)
    y = jnp.einsum('bse,ed->bsd', mixed, w_out)
    return x + rmsnorm(y, post_g)

def first_inputs(seed: int = 0) -> dict:
    key = jax.random.key(seed)
    ks = jax.random.split(key, 13)
    f32 = jnp.float32
    nrm = lambda k, shp, sc: jax.random.normal(k, shp, f32) * sc
    return {
        "x": jax.random.normal(ks[0], (BATCH, SEQ, D_MODEL), f32),
        "pre_norm_g": 1.0 + nrm(ks[1], (DEPTH, D_MODEL), 0.02),
        "w_in": nrm(ks[2], (DEPTH, D_MODEL, D_IN), D_MODEL ** -0.5),
        "w_a2": nrm(ks[3], (DEPTH, B_GATE_RANK, B_HEADS * B_DK), B_GATE_RANK ** -0.5),
        "b_a2": nrm(ks[4], (DEPTH, B_HEADS * B_DK), 0.1),
        "a_ln_g": 1.0 + nrm(ks[5], (DEPTH, D_A), 0.02),
        "a_ln_b": nrm(ks[6], (DEPTH, D_A), 0.02),
        "a_w_s": nrm(ks[7], (DEPTH, A_GROUPS, A_CHUNK, A_CHUNK), A_CHUNK ** -0.5),
        "a_b_s": 1.0 + nrm(ks[8], (DEPTH, A_GROUPS, A_CHUNK), 0.02),
        "b_norm_g": 1.0 + nrm(ks[9], (DEPTH, D_B), 0.02),
        "w_out": nrm(ks[10], (DEPTH, D_MIX, D_MODEL), D_MIX ** -0.5),
        "post_norm_g": 1.0 + nrm(ks[11], (DEPTH, D_MODEL), 0.02),
    }

def first_block(x, pre_norm_g, w_in, w_a2, b_a2, a_ln_g, a_ln_b, a_w_s, a_b_s, b_norm_g, w_out, post_norm_g):
    for l in range(DEPTH):
        x = hybrid_layer(x, pre_norm_g[l], w_in[l], w_a2[l], b_a2[l], a_ln_g[l], a_ln_b[l],
                         a_w_s[l], a_b_s[l], b_norm_g[l], w_out[l], post_norm_g[l])
    return x


_first_inputs = first_inputs


def first_inputs(seed=0):
    import zlib

    import numpy as np

    out = dict(_first_inputs(seed))
    spreads = {}
    factors = {}
    for name, (base, spread) in spreads.items():
        noise = np.random.default_rng([zlib.crc32(name.encode()), seed]).standard_normal(out[name].shape)
        drawn = base * np.exp(spread * noise) if base else spread * noise
        out[name] = __import__('jax').numpy.asarray(drawn.astype(out[name].dtype))
    for name, factor in factors.items():
        out[name] = (out[name] * factor).astype(out[name].dtype)
    return out


_narrow_inputs = first_inputs


def first_inputs(seed=0):

    out = dict(_narrow_inputs(seed))
    wider = {'a_ln_g': 12.0, 'a_ln_b': 12.0, 'a_b_s': 9.49, 'b_norm_g': 5.78, 'post_norm_g': 4.5}
    for name, times in wider.items():
        mean = out[name].mean()
        out[name] = (mean + times * (out[name] - mean)).astype(out[name].dtype)
    return out


D_PLE = 256
M_HEADS = 4
M_HEAD_DIM = 128
M_WIDTH = M_HEADS * M_HEAD_DIM
M_CONV = 5
M_CHUNK = 64
N_GATE = 4 * M_HEADS
A_HEADS = 8
A_KV_HEADS = 2
A_HEAD_DIM = 64
A_WIDTH = A_HEADS * A_HEAD_DIM
A_KV_WIDTH = A_KV_HEADS * A_HEAD_DIM
A_GROUP = A_HEADS // A_KV_HEADS
WINDOW = 128
A_BLOCK = 128
MIX_WIDTH = M_WIDTH + A_WIDTH
IN_WIDTH = 4 * M_WIDTH + N_GATE + A_WIDTH + 2 * A_KV_WIDTH
D_FF = ((-(-8 * D_MODEL // 3) + 255) // 256) * 256
ALPHA = (2 * DEPTH) ** 0.25
BETA = (8 * DEPTH) ** -0.25
LN_EPS = 1e-5
MH_EPS = 1e-6


def _layer_norm(x, g, b):
    xf = x.astype(jnp.float32)
    mu = xf.mean(-1, keepdims=True)
    var = jnp.mean(jnp.square(xf - mu), -1, keepdims=True)
    return ((xf - mu) * lax.rsqrt(var + LN_EPS) * g + b).astype(x.dtype)

def _centred_dwconv(x, w, b):
    pad = w.shape[0] // 2
    y = lax.conv_general_dilated(x, w[:, None, :], window_strides=(1,), padding=[(pad, pad)],
                                 dimension_numbers=("NWC", "WIO", "NWC"),
                                 feature_group_count=x.shape[-1])
    return y + b

def _mlstm_scan(q, k, v, i_pre, log_f):
    B, H, S, dh = q.shape
    L = M_CHUNK
    nc = S // L

    def chunks(t):
        return jnp.moveaxis(t.reshape(B, H, nc, L, *t.shape[3:]), 2, 0)

    lower = jnp.tril(jnp.ones((L, L), dtype=bool))

    def step(carry, xs):
        C, n, m = carry
        qc, kc, vc, ic, fc = xs
        b = jnp.cumsum(fc, axis=-1)
        dmat = b[..., :, None] - b[..., None, :] + ic[..., None, :]
        dmat = jnp.where(lower, dmat, -jnp.inf)
        inter = b + m[..., None]
        m_t = jnp.maximum(dmat.max(-1), inter)
        w_intra = jnp.exp(dmat - m_t[..., None])
        w_inter = jnp.exp(inter - m_t)
        s = jnp.einsum('bhtd,bhsd->bhts', qc, kc) * w_intra
        num = jnp.einsum('bhts,bhse->bhte', s, vc) + w_inter[..., None] * jnp.einsum('bhed,bhtd->bhte', C, qc)
        den = s.sum(-1) + w_inter * jnp.einsum('bhd,bhtd->bht', n, qc)
        h = num / jnp.maximum(jnp.abs(den), jnp.exp(-m_t))[..., None]
        g = b[..., -1]
        a = g[..., None] - b + ic
        m_new = jnp.maximum(g + m, a.max(-1))
        decay = jnp.exp(g + m - m_new)
        wa = jnp.exp(a - m_new[..., None])
        C = decay[..., None, None] * C + jnp.einsum('bhs,bhse,bhsd->bhed', wa, vc, kc)
        n = decay[..., None] * n + jnp.einsum('bhs,bhsd->bhd', wa, kc)
        return (C, n, m_new), h

    init = (jnp.zeros((B, H, dh, dh), jnp.float32), jnp.zeros((B, H, dh), jnp.float32),
            jnp.zeros((B, H), jnp.float32))
    _, h = lax.scan(step, init, (chunks(q), chunks(k), chunks(v), chunks(i_pre), chunks(log_f)))
    return jnp.moveaxis(h, 0, 2).reshape(B, H, S, dh)

def _mlstm_group(qk, v, o, gates, b_gate, conv_w, conv_b, norm_g):
    B, S, _ = v.shape
    qk = jax.nn.silu(_centred_dwconv(qk, conv_w, conv_b))
    q, k = jnp.split(qk, 2, axis=-1)

    def to_heads(t):
        return t.reshape(B, S, M_HEADS, M_HEAD_DIM).transpose(0, 2, 1, 3).astype(jnp.float32)

    q, k, vh = to_heads(q), to_heads(k) * (M_HEAD_DIM ** -0.5), to_heads(v)
    g = (gates + b_gate).astype(jnp.float32).reshape(B, S, 4, M_HEADS).transpose(2, 0, 3, 1)
    h_fwd = _mlstm_scan(q, k, vh, g[0], jax.nn.log_sigmoid(g[2]))

    def flip(t):
        return jnp.flip(t, axis=2)

    h_bwd = flip(_mlstm_scan(flip(q), flip(k), flip(vh), flip(g[1]), flip(jax.nn.log_sigmoid(g[3]))))
    h = h_fwd + h_bwd
    mu = h.mean(-1, keepdims=True)
    var = jnp.mean(jnp.square(h - mu), -1, keepdims=True)
    h = ((h - mu) * lax.rsqrt(var + MH_EPS)).transpose(0, 2, 1, 3).reshape(B, S, M_WIDTH)
    return (h * norm_g * jax.nn.sigmoid(o.astype(jnp.float32))).astype(v.dtype)

def _window_gqa(q, k, v, sink):
    B, S, _ = q.shape
    nb = S // A_BLOCK
    qb = q.reshape(B, nb, A_BLOCK, A_KV_HEADS, A_GROUP, A_HEAD_DIM)

    def band(t):
        t = t.reshape(B, nb, A_BLOCK, A_KV_HEADS, A_HEAD_DIM)
        t = jnp.pad(t, ((0, 0), (1, 1), (0, 0), (0, 0), (0, 0)))
        return jnp.concatenate([t[:, :-2], t[:, 1:-1], t[:, 2:]], axis=2)

    kb, vb = band(k), band(v)
    s = jnp.einsum('bnqhgd,bnkhd->bnhgqk', qb, kb).astype(jnp.float32) * (A_HEAD_DIM ** -0.5)
    blk = jnp.arange(nb)[:, None]
    qpos = blk * A_BLOCK + jnp.arange(A_BLOCK)[None]
    kpos = (blk - 1) * A_BLOCK + jnp.arange(3 * A_BLOCK)[None]
    rel = jnp.abs(kpos[:, None, :] - qpos[:, :, None])
    valid = (rel <= WINDOW) & (kpos[:, None, :] >= 0) & (kpos[:, None, :] < S)
    slopes = jnp.exp2(-8.0 * jnp.arange(1, A_HEADS + 1, dtype=jnp.float32) / A_HEADS)
    bias = -slopes.reshape(A_KV_HEADS, A_GROUP)[None, :, :, None, None] * rel[:, None, None].astype(jnp.float32)
    s = jnp.where(valid[:, None, None], s + bias, -jnp.inf)
    sk = sink.astype(jnp.float32).reshape(A_KV_HEADS, A_GROUP)[None, None, :, :, None, None]
    mx = jnp.maximum(s.max(-1, keepdims=True), sk)
    e = jnp.exp(s - mx)
    prob = e / (e.sum(-1, keepdims=True) + jnp.exp(sk - mx))
    out = jnp.einsum('bnhgqk,bnkhd->bnqhgd', prob.astype(v.dtype), vb)
    return out.reshape(B, S, A_WIDTH)

def _hybrid_layer(x, p_i, w_in, b_gate, conv_w, conv_b, mlstm_norm_g, attn_sink, w_out,
                  ln1_g, ln1_b, w_ffn_in, w_ffn_out, ln2_g, ln2_b, w_ple_gate, w_ple_proj):
    u = x @ w_in
    cuts = np.cumsum([2 * M_WIDTH, M_WIDTH, M_WIDTH, N_GATE, A_WIDTH, A_KV_WIDTH]).tolist()
    m_qk, m_v, m_o, m_gates, a_q, a_k, a_v = jnp.split(u, cuts, axis=-1)
    h_m = _mlstm_group(m_qk, m_v, m_o, m_gates, b_gate, conv_w, conv_b, mlstm_norm_g)
    h_a = _window_gqa(a_q, a_k, a_v, attn_sink)
    mix = jnp.concatenate([h_m, h_a], axis=-1) @ w_out
    x = _layer_norm(ALPHA * x + mix, ln1_g, ln1_b)
    gate_ff, up_ff = jnp.split(x @ w_ffn_in, 2, axis=-1)
    ffn = (jax.nn.silu(gate_ff) * up_ff) @ w_ffn_out
    ple = jax.nn.sigmoid(x @ w_ple_gate) * (p_i @ w_ple_proj)
    return _layer_norm(ALPHA * x + ffn + ple, ln2_g, ln2_b)

def second_inputs(seed: int = 0) -> dict:
    key = jax.random.key(seed)
    ks = jax.random.split(key, 20)
    nrm = lambda k, shape: jax.random.normal(k, shape, jnp.float32)
    col_scale = np.ones((IN_WIDTH,), np.float32)
    col_scale[3 * M_WIDTH - M_WIDTH:3 * M_WIDTH] = BETA
    av0 = 4 * M_WIDTH + N_GATE + A_WIDTH + A_KV_WIDTH
    col_scale[av0:av0 + A_KV_WIDTH] = BETA
    w_in = nrm(ks[2], (DEPTH, D_MODEL, IN_WIDTH)) * (D_MODEL ** -0.5) * jnp.asarray(col_scale)
    f_lin = jnp.linspace(3.0, 6.0, M_HEADS, dtype=jnp.float32)
    b_gate = jnp.concatenate([0.1 * nrm(ks[3], (DEPTH, 2 * M_HEADS)),
                              jnp.concatenate([f_lin, f_lin])[None] + 0.1 * nrm(ks[4], (DEPTH, 2 * M_HEADS))], axis=-1)
    return {
        "x": nrm(ks[0], (BATCH, SEQ, D_MODEL)),
        "p": nrm(ks[1], (DEPTH, BATCH, SEQ, D_PLE)),
        "w_in": w_in,
        "b_gate": b_gate,
        "conv_w": nrm(ks[5], (DEPTH, M_CONV, 2 * M_WIDTH)) * (M_CONV ** -0.5),
        "conv_b": 0.01 * nrm(ks[6], (DEPTH, 2 * M_WIDTH)),
        "mlstm_norm_g": 1.0 + 0.01 * nrm(ks[7], (DEPTH, M_WIDTH)),
        "attn_sink": 0.5 * nrm(ks[8], (DEPTH, A_HEADS)),
        "w_out": nrm(ks[9], (DEPTH, MIX_WIDTH, D_MODEL)) * (MIX_WIDTH ** -0.5) * BETA,
        "ln1_g": 1.0 + 0.01 * nrm(ks[10], (DEPTH, D_MODEL)),
        "ln1_b": 0.01 * nrm(ks[11], (DEPTH, D_MODEL)),
        "w_ffn_in": nrm(ks[12], (DEPTH, D_MODEL, 2 * D_FF)) * (D_MODEL ** -0.5) * BETA,
        "w_ffn_out": nrm(ks[13], (DEPTH, D_FF, D_MODEL)) * (D_FF ** -0.5) * BETA,
        "ln2_g": 1.0 + 0.01 * nrm(ks[14], (DEPTH, D_MODEL)),
        "ln2_b": 0.01 * nrm(ks[15], (DEPTH, D_MODEL)),
        "w_ple_gate": nrm(ks[16], (DEPTH, D_MODEL, D_MODEL)) * (D_MODEL ** -0.5),
        "w_ple_proj": nrm(ks[17], (DEPTH, D_PLE, D_MODEL)) * (D_PLE ** -0.5) * BETA,
    }

def second_block(x, p, w_in, b_gate, conv_w, conv_b, mlstm_norm_g, attn_sink, w_out,
              ln1_g, ln1_b, w_ffn_in, w_ffn_out, ln2_g, ln2_b, w_ple_gate, w_ple_proj):
    h = x
    for i in range(DEPTH):
        h = _hybrid_layer(h, p[i], w_in[i], b_gate[i], conv_w[i], conv_b[i], mlstm_norm_g[i],
                          attn_sink[i], w_out[i], ln1_g[i], ln1_b[i], w_ffn_in[i], w_ffn_out[i],
                          ln2_g[i], ln2_b[i], w_ple_gate[i], w_ple_proj[i])
    return h


_first_inputs_2 = second_inputs


def second_inputs(seed=0):
    import zlib

    import numpy as np

    out = dict(_first_inputs_2(seed))
    spreads = {}
    factors = {'conv_b': 8.0,
     'mlstm_norm_g': 8.0,
     'attn_sink': 8.0,
     'ln1_g': 5.994,
     'ln1_b': 5.808,
     'ln2_g': 5.753,
     'ln2_b': 5.727}
    for name, (base, spread) in spreads.items():
        noise = np.random.default_rng([zlib.crc32(name.encode()), seed]).standard_normal(out[name].shape)
        drawn = base * np.exp(spread * noise) if base else spread * noise
        out[name] = __import__('jax').numpy.asarray(drawn.astype(out[name].dtype))
    for name, factor in factors.items():
        out[name] = (out[name] * factor).astype(out[name].dtype)
    return out


_narrow_inputs_2 = second_inputs


def second_inputs(seed=0):

    out = dict(_narrow_inputs_2(seed))
    wider = {'mlstm_norm_g': 6.4,
     'attn_sink': 7.66,
     'ln1_g': 5.68,
     'ln1_b': 5.66,
     'ln2_g': 6.5,
     'ln2_b': 6.47}
    for name, times in wider.items():
        mean = out[name].mean()
        out[name] = (mean + times * (out[name] - mean)).astype(out[name].dtype)
    return out


GRID_W = 64
D_MIX_3 = D_MODEL
GDN_WIDTH = D_MIX_3 // 2
NA_WIDTH = D_MIX_3 - GDN_WIDTH
GDN_HEAD_DIM = 128
GDN_HEADS = GDN_WIDTH // GDN_HEAD_DIM
NA_HEAD_DIM = 64
NA_HEADS = NA_WIDTH // NA_HEAD_DIM
CONV_WIDTH = 5
GDN_CHUNK = 64
GDN_CONV_CH = 3 * GDN_WIDTH
NA_WIN_R = 8
NA_WIN_C = 16
NA_QBLK_C = 16
NA_KSPAN_C = NA_QBLK_C + NA_WIN_C
D_FF_3 = 4 * D_MODEL
DEEPNORM_ALPHA = (2 * DEPTH) ** 0.25
DEEPNORM_BETA = (8 * DEPTH) ** -0.25
RMS_EPS = 1e-6
SPLIT_POINTS = (3 * GDN_WIDTH, 4 * GDN_WIDTH, 4 * GDN_WIDTH + 2 * GDN_HEADS, 4 * GDN_WIDTH + 4 * GDN_HEADS)
D_IN_3 = 4 * GDN_WIDTH + 4 * GDN_HEADS + 3 * NA_WIDTH


def layer_norm(x, g, b):
    xf = x.astype(jnp.float32)
    mu = jnp.mean(xf, axis=-1, keepdims=True)
    var = jnp.mean(jnp.square(xf - mu), axis=-1, keepdims=True)
    y = (xf - mu) * lax.rsqrt(var + LN_EPS)
    return (y * g + b).astype(x.dtype)

def rms_norm(x, g):
    xf = x.astype(jnp.float32)
    y = xf * lax.rsqrt(jnp.mean(jnp.square(xf), axis=-1, keepdims=True) + RMS_EPS)
    return y * g

def l2_normalize(x):
    xf = x.astype(jnp.float32)
    return xf * lax.rsqrt(jnp.sum(jnp.square(xf), axis=-1, keepdims=True) + RMS_EPS)

def short_conv(x, w):
    pad = CONV_WIDTH // 2
    T = x.shape[1]
    xp = jnp.pad(x, ((0, 0), (pad, pad), (0, 0)))
    return sum(xp[:, i:i + T] * w[i] for i in range(CONV_WIDTH))

def gated_delta_chunked(q, k, v, g, beta):
    out_dtype = v.dtype
    B, T, H, dk = q.shape
    dv = v.shape[-1]
    C = GDN_CHUNK
    N = T // C
    f32 = jnp.float32

    def chunk(t):
        t = t.astype(f32).reshape((B, N, C, H) + t.shape[3:])
        return jnp.moveaxis(t, 3, 1)

    q = chunk(q) * (dk ** -0.5)
    k = chunk(k)
    v = chunk(v)
    g = chunk(g)
    beta = chunk(beta)
    gc = jnp.cumsum(g, axis=-1)
    lower = jnp.tril(jnp.ones((C, C), dtype=bool))
    strict = jnp.tril(jnp.ones((C, C), dtype=bool), -1)
    gamma = jnp.exp(jnp.where(lower, gc[..., :, None] - gc[..., None, :], -jnp.inf))
    kb = k * beta[..., None]
    a_mat = jnp.where(strict, jnp.einsum('bhncd,bhnsd->bhncs', kb, k) * gamma, 0.0)
    t_mat = a_mat + jnp.eye(C, dtype=f32)
    u = lax.linalg.triangular_solve(t_mat, v * beta[..., None], left_side=True, lower=True, unit_diagonal=True)
    w = lax.linalg.triangular_solve(t_mat, kb * jnp.exp(gc)[..., None], left_side=True, lower=True, unit_diagonal=True)
    qk = jnp.einsum('bhncd,bhnsd->bhncs', q, k) * gamma
    q_dec = q * jnp.exp(gc)[..., None]
    k_dec = k * jnp.exp(gc[..., -1:] - gc)[..., None]
    g_last = jnp.exp(gc[..., -1])
    xs = tuple(jnp.moveaxis(t, 2, 0) for t in (q_dec, k_dec, u, w, qk, g_last))

    def step(S, inp):
        qd, kd, u_n, w_n, qk_n, gl = inp
        v_new = u_n - jnp.einsum('bhck,bhkv->bhcv', w_n, S)
        o = jnp.einsum('bhck,bhkv->bhcv', qd, S) + jnp.einsum('bhcs,bhsv->bhcv', qk_n, v_new)
        S = S * gl[..., None, None] + jnp.einsum('bhck,bhcv->bhkv', kd, v_new)
        return S, o

    S0 = jnp.zeros((B, H, dk, dv), f32)
    _, o = lax.scan(step, S0, xs)
    o = jnp.transpose(o, (1, 0, 3, 2, 4)).reshape(B, T, H, dv)
    return o.astype(out_dtype)

def gdn_mixer(h_qkv, h_z, h_a, h_b, conv_w, a_log, dt_bias, norm_g):
    B, T, _ = h_qkv.shape
    qkv = jax.nn.silu(short_conv(h_qkv, conv_w))
    q, k, v = jnp.split(qkv, 3, axis=-1)
    q = l2_normalize(q.reshape(B, T, GDN_HEADS, GDN_HEAD_DIM))
    k = l2_normalize(k.reshape(B, T, GDN_HEADS, GDN_HEAD_DIM))
    v = v.reshape(B, T, GDN_HEADS, GDN_HEAD_DIM)
    a = h_a.astype(jnp.float32).reshape(B, T, 2, GDN_HEADS)
    b = h_b.astype(jnp.float32).reshape(B, T, 2, GDN_HEADS)
    g = -jnp.exp(a_log.astype(jnp.float32)) * jax.nn.softplus(a + dt_bias.astype(jnp.float32))
    beta = jax.nn.sigmoid(b)
    q2 = jnp.concatenate([q, q[:, ::-1]], axis=0)
    k2 = jnp.concatenate([k, k[:, ::-1]], axis=0)
    v2 = jnp.concatenate([v, v[:, ::-1]], axis=0)
    g2 = jnp.concatenate([g[:, :, 0], g[:, ::-1, 1]], axis=0)
    beta2 = jnp.concatenate([beta[:, :, 0], beta[:, ::-1, 1]], axis=0)
    o2 = gated_delta_chunked(q2, k2, v2, g2, beta2)
    o = o2[:B].astype(jnp.float32) + o2[B:, ::-1].astype(jnp.float32)
    z = h_z.reshape(B, T, GDN_HEADS, GDN_HEAD_DIM).astype(jnp.float32)
    o = rms_norm(o, norm_g) * jax.nn.silu(z)
    return o.reshape(B, T, GDN_WIDTH).astype(h_qkv.dtype)

def _na_column_tables():
    n_blk = GRID_W // NA_QBLK_C
    j = np.arange(n_blk)
    span_start = np.clip(j * NA_QBLK_C - NA_WIN_C // 2, 0, GRID_W - NA_KSPAN_C)
    key_cols = span_start[:, None] + np.arange(NA_KSPAN_C)[None, :]
    q_cols = j[:, None] * NA_QBLK_C + np.arange(NA_QBLK_C)[None, :]
    win_start = np.clip(q_cols - NA_WIN_C // 2, 0, GRID_W - NA_WIN_C)
    kc = key_cols[:, None, :]
    in_win = (kc >= win_start[:, :, None]) & (kc < win_start[:, :, None] + NA_WIN_C)
    rel_idx = np.clip(kc - q_cols[:, :, None] + NA_WIN_C - 1, 0, 2 * NA_WIN_C - 2)
    return key_cols, in_win, rel_idx

def neighborhood_attention(q, k, v, rpb):
    B, T, H, d = q.shape
    rows = T // GRID_W
    kr = min(NA_WIN_R, rows)
    n_blk = GRID_W // NA_QBLK_C
    key_cols, in_win, rel_idx = _na_column_tables()
    qg = q.reshape(B, rows, n_blk, NA_QBLK_C, H, d)
    kg = k.reshape(B, rows, GRID_W, H, d)
    vg = v.reshape(B, rows, GRID_W, H, d)
    scale = d ** -0.5
    mask = jnp.asarray(in_win)[None, None, :, :, None, :]
    rpb_cols = rpb.astype(jnp.float32)[:, :, rel_idx]

    def one_row(r):
        r0 = jnp.clip(r - kr // 2, 0, rows - kr)
        k_band = lax.dynamic_slice_in_dim(kg, r0, kr, axis=1)[:, :, key_cols]
        v_band = lax.dynamic_slice_in_dim(vg, r0, kr, axis=1)[:, :, key_cols]
        q_row = lax.dynamic_index_in_dim(qg, r, axis=1, keepdims=False)
        s = jnp.einsum('bjqhd,brjkhd->bhjqrk', q_row, k_band).astype(jnp.float32) * scale
        dr = r0 + jnp.arange(kr) - r + NA_WIN_R - 1
        bias = jnp.take(rpb_cols, dr, axis=1)
        s = s + jnp.transpose(bias, (0, 2, 3, 1, 4))[None]
        s = jnp.where(mask, s, -jnp.inf)
        p = jax.nn.softmax(s.reshape(s.shape[:4] + (kr * NA_KSPAN_C,)), axis=-1).reshape(s.shape)
        o = jnp.einsum('bhjqrk,brjkhd->bjqhd', p.astype(v.dtype), v_band)
        return o.reshape(B, GRID_W, H, d)

    out = lax.map(one_row, jnp.arange(rows))
    return jnp.transpose(out, (1, 0, 2, 3, 4)).reshape(B, T, H, d)

def third_inputs(seed: int = 0) -> dict:
    key = jax.random.key(seed)
    ks = jax.random.split(key, 20)
    f32 = jnp.float32

    def nrm(k, shape, scale):
        return jax.random.normal(k, shape, f32) * scale

    x = nrm(ks[0], (BATCH, SEQ, D_MODEL), 1.0)
    ln_in_g = 1.0 + nrm(ks[1], (D_MODEL,), 0.02)
    ln_in_b = nrm(ks[2], (D_MODEL,), 0.02)
    w_in = nrm(ks[3], (DEPTH, D_MODEL, D_IN_3), D_MODEL ** -0.5)
    conv_w = nrm(ks[4], (DEPTH, CONV_WIDTH, GDN_CONV_CH), CONV_WIDTH ** -0.5)
    a_log = jnp.log(jax.random.uniform(ks[5], (DEPTH, 2, GDN_HEADS), f32, 1.0, 16.0))
    dt = jnp.exp(jax.random.uniform(ks[6], (DEPTH, 2, GDN_HEADS), f32, math.log(1e-3), math.log(1e-1)))
    dt_bias = dt + jnp.log(-jnp.expm1(-dt))
    gdn_norm_g = 1.0 + nrm(ks[7], (DEPTH, GDN_HEAD_DIM), 0.02)
    rpb = nrm(ks[8], (DEPTH, NA_HEADS, 2 * NA_WIN_R - 1, 2 * NA_WIN_C - 1), 0.1)
    na_norm_g = 1.0 + nrm(ks[9], (DEPTH, NA_HEAD_DIM), 0.02)
    w_out = nrm(ks[10], (DEPTH, D_MIX_3, D_MODEL), D_MIX_3 ** -0.5 * DEEPNORM_BETA)
    ln1_g = 1.0 + nrm(ks[11], (DEPTH, D_MODEL), 0.02)
    ln1_b = nrm(ks[12], (DEPTH, D_MODEL), 0.02)
    w1 = nrm(ks[13], (DEPTH, D_MODEL, D_FF_3), D_MODEL ** -0.5)
    b1 = nrm(ks[14], (DEPTH, D_FF_3), 0.01)
    w2 = nrm(ks[15], (DEPTH, D_FF_3, D_MODEL), D_FF_3 ** -0.5 * DEEPNORM_BETA)
    b2 = nrm(ks[16], (DEPTH, D_MODEL), 0.01)
    ln2_g = 1.0 + nrm(ks[17], (DEPTH, D_MODEL), 0.02)
    ln2_b = nrm(ks[18], (DEPTH, D_MODEL), 0.02)
    return {"x": x, "ln_in_g": ln_in_g, "ln_in_b": ln_in_b, "w_in": w_in, "conv_w": conv_w,
            "a_log": a_log, "dt_bias": dt_bias, "gdn_norm_g": gdn_norm_g, "rpb": rpb,
            "na_norm_g": na_norm_g, "w_out": w_out, "ln1_g": ln1_g, "ln1_b": ln1_b,
            "w1": w1, "b1": b1, "w2": w2, "b2": b2, "ln2_g": ln2_g, "ln2_b": ln2_b}

def third_block(x, ln_in_g, ln_in_b, w_in, conv_w, a_log, dt_bias, gdn_norm_g, rpb,
              na_norm_g, w_out, ln1_g, ln1_b, w1, b1, w2, b2, ln2_g, ln2_b):
    B, T, _ = x.shape
    x = layer_norm(x, ln_in_g, ln_in_b)
    for l in range(DEPTH):
        h = jnp.einsum('btd,de->bte', x, w_in[l])
        h_qkv, h_z, h_a, h_b, h_na = jnp.split(h, SPLIT_POINTS, axis=-1)
        o_gdn = gdn_mixer(h_qkv, h_z, h_a, h_b, conv_w[l], a_log[l], dt_bias[l], gdn_norm_g[l])
        q_na, k_na, v_na = (t.reshape(B, T, NA_HEADS, NA_HEAD_DIM) for t in jnp.split(h_na, 3, axis=-1))
        o_na = neighborhood_attention(q_na, k_na, v_na, rpb[l])
        o_na = rms_norm(o_na, na_norm_g[l]).reshape(B, T, NA_WIDTH).astype(x.dtype)
        mix = jnp.einsum('bte,ed->btd', jnp.concatenate([o_gdn, o_na], axis=-1), w_out[l])
        x = layer_norm(DEEPNORM_ALPHA * x + mix, ln1_g[l], ln1_b[l])
        ff = jnp.square(jax.nn.relu(jnp.einsum('btd,df->btf', x, w1[l]) + b1[l]))
        ff = jnp.einsum('btf,fd->btd', ff, w2[l]) + b2[l]
        x = layer_norm(DEEPNORM_ALPHA * x + ff, ln2_g[l], ln2_b[l])
    return x


_first_inputs_3 = third_inputs


def third_inputs(seed=0):
    import zlib

    import numpy as np

    out = dict(_first_inputs_3(seed))
    spreads = {}
    factors = {'gdn_norm_g': 38.333,
     'na_norm_g': 21.652,
     'ln1_g': 2.708,
     'ln1_b': 2.761,
     'b1': 8.0,
     'b2': 35.337,
     'ln2_g': 8.18,
     'ln2_b': 8.325}
    for name, (base, spread) in spreads.items():
        noise = np.random.default_rng([zlib.crc32(name.encode()), seed]).standard_normal(out[name].shape)
        drawn = base * np.exp(spread * noise) if base else spread * noise
        out[name] = __import__('jax').numpy.asarray(drawn.astype(out[name].dtype))
    for name, factor in factors.items():
        out[name] = (out[name] * factor).astype(out[name].dtype)
    return out


_narrow_inputs_3 = third_inputs


def third_inputs(seed=0):

    out = dict(_narrow_inputs_3(seed))
    wider = {'gdn_norm_g': 3.81, 'na_norm_g': 3.75, 'ln2_g': 3.21, 'ln2_b': 3.21}
    for name, times in wider.items():
        mean = out[name].mean()
        out[name] = (mean + times * (out[name] - mean)).astype(out[name].dtype)
    return out


def setup_inputs(seed=0):
    out = dict(first_inputs(seed))
    for name, value in second_inputs(seed + 1).items():
        if name != "x":
            out[name + "_2"] = value
    for name, value in third_inputs(seed + 2).items():
        if name != "x":
            out[name + "_3"] = value
    return out


def reference(
    x, pre_norm_g, w_in, w_a2, b_a2, a_ln_g, a_ln_b, a_w_s, a_b_s, b_norm_g, w_out, post_norm_g,
    p_2, w_in_2, b_gate_2, conv_w_2, conv_b_2, mlstm_norm_g_2, attn_sink_2, w_out_2, ln1_g_2,
    ln1_b_2, w_ffn_in_2, w_ffn_out_2, ln2_g_2, ln2_b_2, w_ple_gate_2, w_ple_proj_2, ln_in_g_3,
    ln_in_b_3, w_in_3, conv_w_3, a_log_3, dt_bias_3, gdn_norm_g_3, rpb_3, na_norm_g_3, w_out_3,
    ln1_g_3, ln1_b_3, w1_3, b1_3, w2_3, b2_3, ln2_g_3, ln2_b_3,
):
    x = first_block(
        x, pre_norm_g, w_in, w_a2, b_a2, a_ln_g, a_ln_b, a_w_s, a_b_s, b_norm_g, w_out,
        post_norm_g,
    )
    x = second_block(
        x, p_2, w_in_2, b_gate_2, conv_w_2, conv_b_2, mlstm_norm_g_2, attn_sink_2, w_out_2,
        ln1_g_2, ln1_b_2, w_ffn_in_2, w_ffn_out_2, ln2_g_2, ln2_b_2, w_ple_gate_2, w_ple_proj_2,
    )
    return third_block(
        x, ln_in_g_3, ln_in_b_3, w_in_3, conv_w_3, a_log_3, dt_bias_3, gdn_norm_g_3, rpb_3,
        na_norm_g_3, w_out_3, ln1_g_3, ln1_b_3, w1_3, b1_3, w2_3, b2_3, ln2_g_3, ln2_b_3,
    )


_drawn_inputs = setup_inputs


def setup_inputs(seed=0):
    import zlib

    import numpy as np

    out = dict(_drawn_inputs(seed))
    spreads = {}
    factors = {}
    for name, (base, spread) in spreads.items():
        noise = np.random.default_rng([zlib.crc32(name.encode()), seed]).standard_normal(out[name].shape)
        drawn = base * np.exp(spread * noise) if base else spread * noise
        out[name] = __import__('jax').numpy.asarray(drawn.astype(out[name].dtype))
    for name, factor in factors.items():
        out[name] = (out[name] * factor).astype(out[name].dtype)
    return out
```

```python
from contextlib import ExitStack

import concourse.bass as bass
from concourse import mybir

P = 128
S = 1024
HALF = 512
DT = 8
F32 = mybir.dt.float32
ACT = mybir.ActivationFunctionType
ALU = mybir.AluOpType
AX_X = mybir.AxisListType.X
ALPHA = 2.0 ** 0.25
BIG = 1.0e30


class Phase:

    def __init__(self, nc, name):
        self.nc, self.name, self.stack, self.sems = nc, name, ExitStack(), []

    def __enter__(self):
        self.stack.__enter__()
        return self

    def __exit__(self, *what):
        for sem in self.sems:
            self.nc.sync.sem_clear(sem)
        return self.stack.__exit__(*what)

    def sb(self, name, shape, dt=F32):
        return self.stack.enter_context(self.nc.sbuf_tensor(f"{self.name}_{name}", shape, dt))

    def ps(self, name, shape, dt=F32):
        return self.stack.enter_context(self.nc.psum_tensor(f"{self.name}_{name}", shape, dt))

    def sem(self, name):
        self.sems.append(self.stack.enter_context(self.nc.semaphore(f"{self.name}_{name}")))
        return self.sems[-1]


def load_phase(nc, name, pairs):
    with Phase(nc, name) as ph:
        landed = [ph.sem(f"landed{i}") for i in range(len(pairs))]
        with nc.Block() as block:

            @block.sync
            def _(sp):
                for i, (dst, src) in enumerate(pairs):
                    sp.dma_start(dst, src).then_inc(landed[i], 16)
                for i in range(len(pairs)):
                    sp.wait_ge(landed[i], 16)


def project_rows(nc, name, w, KT, rhs, NB, act=None, dve=None, kp=P, m=P):
    with Phase(nc, name) as ph:
        wt = [ph.sb(f"w{i}", [kp, KT, m]) for i in range(2)]
        tmp = [ph.sb(f"tmp{i}", [m, S]) for i in range(2)]
        acc = [ph.ps(f"acc{i}", [m, S]) for i in range(2)]
        w_landed = [ph.sem(f"w_landed{i}") for i in range(2)]
        acc_ready = ph.sem("acc_ready")
        act_done = ph.sem("act_done")
        taken = ph.sem("taken")
        blocks2, odd = NB // 2, NB % 2
        last_reader_is_dve = dve is not None

        with nc.Block() as block:

            @block.sync
            def _(sp):
                def load(n, i):
                    sp.dma_start(wt[i][:], w[n].rearrange("k (t m) -> k t m", t=KT)).then_inc(w_landed[i], 16)

                load(0, 0)
                if NB > 1:
                    load(1, 1)
                if blocks2 > 1:
                    with sp.Fori(1, blocks2) as j:
                        for i in range(2):
                            sp.wait_ge(acc_ready, 2 * j - 1 + i)
                            load(2 * j + i, i)
                if odd and NB > 1:
                    sp.wait_ge(acc_ready, NB - 2)
                    load(NB - 1, 0)

            @block.tensor
            def _(pe):
                def product(n, i, round_):
                    pe.wait_ge(w_landed[i], 16 * round_ + 16)
                    pe.wait_ge(taken, n + 1)
                    for k in range(KT):
                        for half in range(2):
                            cols = slice(half * HALF, (half + 1) * HALF)
                            last = nc.tensor.matmul(acc[i][:, cols], wt[i][:, k, :], rhs(k)[:, cols],
                                                    start=(k == 0), stop=(k == KT - 1))
                    last.then_inc(acc_ready, 1)

                if blocks2:
                    with pe.Fori(0, blocks2) as j:
                        for i in range(2):
                            product(2 * j + i, i, j)
                if odd:
                    product(NB - 1, 0, blocks2)

            if act is not None:
                @block.scalar
                def _(se):
                    if not last_reader_is_dve:
                        se.sem_inc(taken, 2)

                    def take(n, i):
                        se.wait_ge(acc_ready, n + 1)
                        if last_reader_is_dve:
                            se.wait_ge(taken, n + 1)
                        act(n, acc[i], tmp[i], i).then_inc(act_done if last_reader_is_dve else taken, 1)

                    if blocks2:
                        with se.Fori(0, blocks2) as j:
                            for i in range(2):
                                take(2 * j + i, i)
                    if odd:
                        take(NB - 1, 0)

            if last_reader_is_dve:
                @block.vector
                def _(ve):
                    ve.sem_inc(taken, 2)

                    def take(n, i):
                        ve.wait_ge(act_done if act is not None else acc_ready, n + 1)
                        last = dve(n, acc[i], tmp[i], i)
                        if last is None:
                            ve.drain().then_inc(taken, 1)
                        else:
                            last.then_inc(taken, 1)

                    if blocks2:
                        with ve.Fori(0, blocks2) as j:
                            for i in range(2):
                                take(2 * j + i, i)
                    if odd:
                        take(NB - 1, 0)


def project_tokens(nc, name, w, N, src, act):
    with Phase(nc, name) as ph:
        wt = ph.sb("w", [P, DT, N])
        stage = [ph.sb(f"stage{i}", [P, DT, P]) for i in range(2)]
        acc = [ph.ps(f"acc{i}", [P, N]) for i in range(2)]
        w_landed = [ph.sem(f"w_landed{k}") for k in range(DT)]
        staged = ph.sem("staged")
        acc_ready = ph.sem("acc_ready")
        taken = ph.sem("taken")
        w3 = w.rearrange("p (t n) -> p t n", t=DT)

        with nc.Block() as block:

            @block.sync
            def _(sp):
                for k in range(DT):
                    sp.dma_start(wt[:, k, :], w3[:, k, :]).then_inc(w_landed[k], 16)

            @block.gpsimd
            def _(pool):
                for i in range(2):
                    nc.gpsimd.tensor_copy(stage[i][:], src[:, :, i * P:(i + 1) * P]).then_inc(staged, 1)
                with pool.Fori(1, DT // 2) as j:
                    for i in range(2):
                        pool.wait_ge(acc_ready, 2 * j - 1 + i)
                        nc.gpsimd.tensor_copy(stage[i][:], tile_of(src, 2 * j + i)).then_inc(staged, 1)

            @block.tensor
            def _(pe):
                for k in range(DT):
                    pe.wait_ge(w_landed[k], 16)
                with pe.Fori(0, DT // 2) as j:
                    for i in range(2):
                        pe.wait_ge(staged, 2 * j + i + 1)
                        pe.wait_ge(taken, 2 * j + i + 1)
                        last = tile_product(nc, acc[i], stage[i], wt, N)
                        last.then_inc(acc_ready, 1)

            @block.scalar
            def _(se):
                se.sem_inc(taken, 2)
                with se.Fori(0, DT // 2) as j:
                    for i in range(2):
                        se.wait_ge(acc_ready, 2 * j + i + 1)
                        act(2 * j + i, acc[i]).then_inc(taken, 1)


def tile_of(src, n):
    return src[:].rearrange("p t (n c) -> p t n c", c=P)[:, :, n, :]


def tile_product(nc, acc, stage, wt, N):
    for k in range(DT):
        for a in range(0, N, HALF):
            cols = slice(a, min(a + HALF, N))
            last = nc.tensor.matmul(acc[:, cols], stage[:, k, :], wt[:, k, cols], start=(k == 0), stop=(k == DT - 1))
    return last


def norm_rows(nc, name, x, out, ones, g, b=None, centre=False, eps=1e-5, add=None):
    D = DT * P
    with Phase(nc, name) as ph:
        sq = [ph.sb(f"sq{i}", [P, S]) for i in range(2)]
        rstd = ph.sb("rstd", [P, S])
        addt = [ph.sb(f"add{i}", [P, S]) for i in range(2)] if add is not None else None
        total = ph.ps("total", [P, S])
        total_sq = ph.ps("total_sq", [P, S])
        summed = ph.sem("summed")
        centred = ph.sem("centred")
        squared = ph.sem("squared")
        sq_used = ph.sem("sq_used")
        std_ready = ph.sem("std_ready")
        scaled = ph.sem("scaled")
        add_landed = [ph.sem(f"add_landed{i}") for i in range(2)]
        added = ph.sem("added")
        with nc.Block() as block:

            @block.tensor
            def _(pe):
                if centre:
                    for k in range(DT):
                        for half in range(2):
                            cols = slice(half * HALF, (half + 1) * HALF)
                            last = nc.tensor.matmul(total[:, cols], ones, x[:, k, cols], start=(k == 0), stop=(k == DT - 1))
                    last.then_inc(summed, 1)
                for k in range(DT):
                    pe.wait_ge(squared, k + 1)
                    for half in range(2):
                        cols = slice(half * HALF, (half + 1) * HALF)
                        last = nc.tensor.matmul(total_sq[:, cols], ones, sq[k % 2][:, cols], start=(k == 0), stop=(k == DT - 1))
                    last.then_inc(sq_used, 1)

            @block.scalar
            def _(se):
                for k in range(DT):
                    if centre:
                        se.wait_ge(centred, k + 1)
                    if k >= 2:
                        se.wait_ge(sq_used, k - 1)
                    nc.scalar.activation(sq[k % 2][:], x[:, k, :], ACT.Square).then_inc(squared, 1)
                se.wait_ge(sq_used, DT)
                nc.scalar.activation(rstd[:], total_sq[:], ACT.Sqrt, scale=1.0 / D, bias=eps).then_inc(std_ready, 1)
                if b is not None:
                    for k in range(DT):
                        se.wait_ge(scaled, k + 1)
                        nc.scalar.activation(out[:, k, :], out[:, k, :], ACT.Identity, bias=b[:, k:k + 1])

            if add is not None:
                @block.sync
                def _(sp):
                    for k in range(DT):
                        if k >= 2:
                            sp.wait_ge(added, k - 1)
                        sp.dma_start(addt[k % 2][:], add.rearrange("p (t s) -> p t s", t=DT)[:, k, :]).then_inc(add_landed[k % 2], 16)

            @block.vector
            def _(ve):
                if centre:
                    ve.wait_ge(summed, 1)
                    for k in range(DT):
                        nc.vector.scalar_tensor_tensor(out=x[:, k, :], in0=total[:], scalar=-1.0 / D, in1=x[:, k, :],
                                                       op0=ALU.mult, op1=ALU.add).then_inc(centred, 1)
                ve.wait_ge(std_ready, 1)
                nc.vector.reciprocal(rstd[:], rstd[:])
                ve.drain()
                for k in range(DT):
                    nc.vector.scalar_tensor_tensor(out=out[:, k, :], in0=x[:, k, :], scalar=g[:, k:k + 1], in1=rstd[:],
                                                   op0=ALU.mult, op1=ALU.mult).then_inc(scaled, 1)
                    if add is not None:
                        ve.wait_ge(scaled, k + 1)
                        ve.wait_ge(add_landed[k % 2], 16 * (k // 2) + 16)
                        nc.vector.tensor_tensor(out[:, k, :], out[:, k, :], addt[k % 2][:], ALU.add).then_inc(added, 1)

GLA_H, GLA_DK, GLA_DV, GLA_C = 4, 128, 256, 64


def gated_linear_attention(nc, consts, cols, logits, qk, v, out):
    NCH = S // GLA_C
    qscale = GLA_DK ** -0.5
    with Phase(nc, "gla") as ph:
        low = ph.sb("low", [P, S])
        bc = ph.sb("bc", [P, S])
        kd = ph.sb("kd", [P, S])
        ke = ph.sb("ke", [P, S])
        qe = ph.sb("qe", [P, S])
        qb = ph.sb("qb", [P, S])
        soft, dref, dlast = qb, ke, kd
        decay = ph.sb("decay", [P, NCH])
        kdt = ph.sb("kdt", [P, DT, P])
        vh = ph.sb("vh", [P, DT, GLA_DV])
        state = ph.sb("state", [P, NCH + 1, GLA_DV])
        probs = ph.sb("probs", [P, 2, P])
        junk = low[:, 0:GLA_DV]
        ss = ph.sb("ss", [P, 2])
        rstd = ph.sb("rstd", [P, 2])
        on = low[:, 2 * GLA_DV:4 * GLA_DV].rearrange("p (a c) -> p a c", a=2)
        turned = ph.ps("turned", [P, S])
        sc = [turned[:, 0:P], turned[:, HALF:HALF + P]]
        kv = [ph.ps(f"kv{i}", [P, HALF]) for i in range(2)]
        o = [ph.ps(f"o{i}", [P, HALF]) for i in range(2)]
        ot = [ph.ps(f"ot{i}", [P, 4, P]) for i in range(2)]
        soft_ready = ph.sem("soft_ready")
        cum_ready = ph.sem("cum_ready")
        exp_ready = ph.sem("exp_ready")
        derived = ph.sem("derived")
        turned_ready = ph.sem("turned_ready")
        kdt_ready = ph.sem("kdt_ready")
        v_staged = ph.sem("v_staged")
        head_free = ph.sem("head_free")
        kv_ready = ph.sem("kv_ready")
        state_done = ph.sem("state_done")
        sc_ready = ph.sem("sc_ready")
        masked = ph.sem("masked")
        o_ready = ph.sem("o_ready")
        std_ready = ph.sem("std_ready")
        on_done = ph.sem("on_done")
        ot_ready = ph.sem("ot_ready")
        ot_done = ph.sem("ot_done")
        ident, mask, resets = consts["ident"], consts["gla_mask"], consts["reset64"]
        ba, bg = cols["b_a2"], cols["b_norm_g"]

        def tile(x, p):
            return x[:, p * P:(p + 1) * P]

        with nc.Block() as block:

            @block.scalar
            def _(se):
                with se.Fori(0, GLA_H) as h:
                    se.wait_ge(head_free, h + 1)
                    nc.scalar.activation(soft[:], logits[:, h, :], ACT.Abs, bias=ba[:, bass.ds(h, 1)])
                    se.drain()
                    nc.scalar.activation(soft[:], soft[:], ACT.Exp, scale=-1.0)
                    se.drain()
                    nc.scalar.activation(soft[:], soft[:], ACT.Ln, bias=1.0).then_inc(soft_ready, 1)
                    se.wait_ge(cum_ready, h + 1)
                    for dst, src, scale in ((kd, dlast, 1.0), (qe, dref, 1.0), (ke, dref, -1.0), (qb, bc, 1.0)):
                        nc.scalar.activation(dst[:], src[:], ACT.Exp, scale=scale / 16.0).then_inc(exp_ready, 1)
                    last_b = bc[:].rearrange("p (n c) -> p n c", c=GLA_C)[:, :, GLA_C - 1]
                    nc.scalar.activation(decay[:], last_b, ACT.Exp, scale=1.0 / 16.0).then_inc(exp_ready, 1)
                    se.wait_ge(turned_ready, h + 1)
                    nc.scalar.activation(kdt[:].rearrange("p t c -> p (t c)"), turned[:], ACT.Copy).then_inc(kdt_ready, 1)
                    for p in range(DT + 1):
                        if p < DT:
                            se.wait_ge(o_ready, DT * h + p + 1)
                            nc.scalar.activation(junk, o[p % 2][:, 0:GLA_DV], ACT.Square, scale=GLA_DV ** -0.5,
                                                 accum_out=ss[:, p % 2:p % 2 + 1])
                            se.drain()
                            nc.scalar.activation(rstd[:, p % 2:p % 2 + 1], ss[:, p % 2:p % 2 + 1], ACT.Sqrt,
                                                 bias=1e-6).then_inc(std_ready, 1)
                        if p >= 1:
                            q = p - 1
                            se.wait_ge(ot_ready, DT * h + q + 1)
                            for i in range(2):
                                last = nc.scalar.activation(out[:, 2 * h + i, q * P:(q + 1) * P], ot[q % 2][:, i, :],
                                                            ACT.Copy, scale=bg[:, bass.ds(2 * h + i, 1)])
                            last.then_inc(ot_done, 1)

            @block.vector
            def _(ve):
                nc.vector.memset(state[:, 0, :], 0.0)
                with ve.Fori(0, GLA_H) as h:
                    ve.wait_ge(head_free, h + 1)
                    nc.vector.tensor_scalar(low[:], logits[:, h, :], ba[:, bass.ds(h, 1)], 0.0, ALU.add, ALU.min)
                    ve.drain()
                    ve.wait_ge(soft_ready, h + 1)
                    nc.vector.tensor_tensor(low[:], low[:], soft[:], ALU.subtract)
                    ve.drain()
                    nc.vector.tensor_tensor_scan(bc[:], resets, low[:], 0.0, ALU.mult, ALU.add)
                    ve.drain()
                    b3 = bc[:].rearrange("p (n c) -> p n c", c=GLA_C)
                    nc.vector.tensor_tensor(dref[:].rearrange("p (n c) -> p n c", c=GLA_C), b3,
                                            b3[:, :, GLA_C // 2 - 1:GLA_C // 2].broadcast_to([P, NCH, GLA_C]), ALU.subtract)
                    nc.vector.tensor_tensor(dlast[:].rearrange("p (n c) -> p n c", c=GLA_C),
                                            b3[:, :, GLA_C - 1:GLA_C].broadcast_to([P, NCH, GLA_C]), b3,
                                            ALU.subtract).then_inc(cum_ready, 1)
                    for i, (dst, of_q) in enumerate(((kd, 0), (qe, 1), (ke, 0), (qb, 1))):
                        ve.wait_ge(exp_ready, 5 * h + i + 1)
                        nc.vector.scalar_tensor_tensor(out=dst[:], in0=qk[:, (h if of_q else h + GLA_H), :],
                                                       scalar=(qscale if of_q else 1.0), in1=dst[:],
                                                       op0=ALU.mult, op1=ALU.mult).then_inc(derived, 1)
                    ve.wait_ge(exp_ready, 5 * h + 5)
                    for p in range(DT + 1):
                        if p < DT:
                            ve.wait_ge(kv_ready, DT * h + p + 1)
                            for c in (2 * p, 2 * p + 1):
                                if c:
                                    ve.wait_ge(state_done, NCH * h + c)
                                nc.vector.scalar_tensor_tensor(out=state[:, c + 1, :], in0=state[:, c, :],
                                                               scalar=decay[:, c:c + 1], in1=kv[c % 2][:, 0:GLA_DV],
                                                               op0=ALU.mult, op1=ALU.add).then_inc(state_done, 1)
                            ve.wait_ge(sc_ready, DT * h + p + 1)
                            if p >= 2:
                                ve.wait_ge(o_ready, DT * h + p - 1)
                            nc.vector.scalar_tensor_tensor(out=probs[:, p % 2, :], in0=sc[p % 2], scalar=3.0e38,
                                                           in1=mask, op0=ALU.min, op1=ALU.mult).then_inc(masked, 1)
                        if p >= 1:
                            q = p - 1
                            ve.wait_ge(std_ready, DT * h + q + 1)
                            nc.vector.reciprocal(rstd[:, q % 2:q % 2 + 1], rstd[:, q % 2:q % 2 + 1])
                            ve.drain()
                            if q >= 2:
                                ve.wait_ge(ot_ready, DT * h + q - 1)
                            nc.vector.tensor_scalar(on[:, q % 2, :], o[q % 2][:, 0:GLA_DV], rstd[:, q % 2:q % 2 + 1], None,
                                                    ALU.mult).then_inc(on_done, 1)

            @block.gpsimd
            def _(pool):
                with pool.Fori(0, GLA_H) as h:
                    pool.wait_ge(head_free, h + 1)
                    nc.gpsimd.tensor_copy(vh[:], v[:].rearrange("p t (h d) -> p t h d", h=GLA_H)[:, :, h, :]).then_inc(v_staged, 1)

            @block.tensor
            def _(pe):
                pe.sem_inc(head_free, 1)
                with pe.Fori(0, GLA_H) as h:
                    pe.wait_ge(derived, 4 * h + 1)
                    for p in range(DT):
                        last = nc.tensor.transpose(tile(turned, p), tile(kd, p), ident)
                    last.then_inc(turned_ready, 1)
                    pe.wait_ge(kdt_ready, h + 1)
                    pe.wait_ge(v_staged, h + 1)
                    pe.wait_ge(derived, 4 * h + 4)
                    for p in range(DT + 2):
                        if p < DT:
                            if p >= 1:
                                pe.wait_ge(state_done, NCH * h + 2 * p)
                            for c in range(2):
                                rows = slice(c * GLA_C, (c + 1) * GLA_C)
                                last = nc.tensor.matmul(kv[c][:, 0:GLA_DV], kdt[rows, p, :], vh[rows, p, :], start=True, stop=True)
                            last.then_inc(kv_ready, 1)
                            if p >= 2:
                                pe.wait_ge(masked, DT * h + p - 1)
                            nc.tensor.matmul(sc[p % 2], tile(ke, p), tile(qe, p), start=True, stop=True).then_inc(sc_ready, 1)
                        if 1 <= p <= DT:
                            q = p - 1
                            pe.wait_ge(masked, DT * h + q + 1)
                            if q >= 2:
                                pe.wait_ge(on_done, DT * h + q - 1)
                            nc.tensor.matmul(o[q % 2][:, 0:GLA_DV], probs[:, q % 2, :], vh[:, q, :], start=True, stop=False, skip_group_check=True)
                            for c in range(2):
                                if q or c:
                                    pe.wait_ge(state_done, NCH * h + 2 * q + c)
                                rows = slice(c * GLA_C, (c + 1) * GLA_C)
                                at = q * P + c * GLA_C
                                last = nc.tensor.matmul(o[q % 2][rows, 0:GLA_DV], qb[:, at:at + GLA_C], state[:, 2 * q + c, :],
                                                        start=False, stop=(c == 1), skip_group_check=True)
                            last.then_inc(o_ready, 1)
                        if p >= 2:
                            q = p - 2
                            pe.wait_ge(on_done, DT * h + q + 1)
                            if q >= 2:
                                pe.wait_ge(ot_done, DT * h + q - 1)
                            for i in range(2):
                                last = nc.tensor.transpose(ot[q % 2][:, i, :], on[:, q % 2, i * P:(i + 1) * P], ident)
                            last.then_inc(ot_ready, 1)
                    pe.drain().then_inc(head_free, 1)


def spatial_gating(nc, consts, cols, w_v, h, w_s, b_s, out):
    G = 8
    with Phase(nc, "sgu") as ph:
        wt = ph.sb("w", [P, DT, S])
        ws = ph.sb("ws", [P, G, P])
        bs = ph.sb("bs", [P, G, P])
        shift = ph.sb("shift", [P, G, P])
        stage = [ph.sb(f"stage{i}", [P, DT, P]) for i in range(2)]
        gv = [ph.sb(f"gv{i}", [P, S]) for i in range(2)]
        stats = ph.sb("stats", [P, 2, 6])
        mv = ph.sb("mv", [P, 2, 2])
        rstd = ph.sb("rstd", [P, 2])
        acc = [ph.ps(f"acc{i}", [P, S]) for i in range(2)]
        mix = [ph.ps(f"mix{i}", [P, S]) for i in range(2)]
        w_landed = [ph.sem(f"w_landed{k}") for k in range(DT)]
        ws_landed, bs_landed = ph.sem("ws_landed"), ph.sem("bs_landed")
        ws_masked = ph.sem("ws_masked")
        sums_ready = ph.sem("sums_ready")
        staged = ph.sem("staged")
        acc_ready = ph.sem("acc_ready")
        gelu_done = ph.sem("gelu_done")
        mv_ready = ph.sem("mv_ready")
        std_ready = ph.sem("std_ready")
        normed = ph.sem("normed")
        mixed = ph.sem("mixed")
        mix_taken = ph.sem("mix_taken")
        g, b = cols["a_ln_g"], cols["a_ln_b"]
        w3 = w_v.rearrange("p (t n) -> p t n", t=DT)

        with nc.Block() as block:

            @block.sync
            def _(sp):
                sp.dma_start(ws[:].rearrange("p g t -> p (g t)"), w_s).then_inc(ws_landed, 16)
                sp.dma_start(bs[:].rearrange("p g t -> p (g t)"), b_s.broadcast_to([P, G * P])).then_inc(bs_landed, 16)
                for k in range(DT):
                    sp.dma_start(wt[:, k, :], w3[:, k, :]).then_inc(w_landed[k], 16)

            @block.gpsimd
            def _(pool):
                for i in range(2):
                    nc.gpsimd.tensor_copy(stage[i][:], h[:, :, i * P:(i + 1) * P]).then_inc(staged, 1)

                with pool.Fori(1, DT // 2) as j:
                    for i in range(2):
                        pool.wait_ge(acc_ready, 2 * j - 1 + i)
                        nc.gpsimd.tensor_copy(stage[i][:], tile_of(h, 2 * j + i)).then_inc(staged, 1)

            @block.tensor
            def _(pe):
                pe.wait_ge(ws_masked, 1)
                for half in range(2):
                    last = nc.tensor.matmul(mix[0][:, half * HALF:(half + 1) * HALF], consts["ones"],
                                            ws[:].rearrange("p g t -> p (g t)")[:, half * HALF:(half + 1) * HALF],
                                            start=True, stop=True)
                last.then_inc(sums_ready, 1)
                for k in range(DT):
                    pe.wait_ge(w_landed[k], 16)

                def project(n, i, first=False):
                    pe.wait_ge(staged, n + 1)
                    if not first:
                        pe.wait_ge(gelu_done, n - 1)
                    tile_product(nc, acc[i], stage[i], wt, S).then_inc(acc_ready, 1)

                def mixing(n, i, first=False):
                    pe.wait_ge(normed, n + 1)
                    pe.wait_ge(mix_taken, n + 1 if first else n)
                    for gr in range(G):
                        last = nc.tensor.matmul(mix[i][:, gr * P:(gr + 1) * P], gv[i][:, gr * P:(gr + 1) * P], ws[:, gr, :],
                                                start=True, stop=True)
                    last.then_inc(mixed, 1)

                project(0, 0, True)
                project(1, 1, True)
                mixing(0, 0, True)
                with pe.Fori(1, DT // 2) as j:
                    project(2 * j, 0)
                    mixing(2 * j - 1, 1)
                    project(2 * j + 1, 1)
                    mixing(2 * j, 0)
                mixing(DT - 1, 1)

            @block.scalar
            def _(se):
                def gelu(n, i, first=False):
                    se.wait_ge(acc_ready, n + 1)
                    if not first:
                        se.wait_ge(mixed, n - 1)
                    nc.scalar.activation(gv[i][:], acc[i][:], ACT.Gelu).then_inc(gelu_done, 1)

                def std(n, i):
                    se.wait_ge(mv_ready, n + 1)
                    nc.scalar.activation(rstd[:, i:i + 1], mv[:, i, 1:2], ACT.Sqrt, bias=1e-6).then_inc(std_ready, 1)

                gelu(0, 0, True)
                std(0, 0)
                gelu(1, 1, True)
                std(1, 1)
                with se.Fori(1, DT // 2) as j:
                    for i in range(2):
                        gelu(2 * j + i, i)
                        std(2 * j + i, i)

            @block.vector
            def _(ve):
                ve.wait_ge(ws_landed, 16)
                nc.vector.tensor_tensor(ws[:], ws[:], consts["le3"], ALU.mult).then_inc(ws_masked, 1)
                ve.wait_ge(sums_ready, 1)
                ve.wait_ge(bs_landed, 16)
                for gr in range(G):
                    last = nc.vector.scalar_tensor_tensor(out=shift[:, gr, :], in0=mix[0][:, gr * P:(gr + 1) * P],
                                                          scalar=b[:, gr:gr + 1], in1=bs[:, gr, :], op0=ALU.mult, op1=ALU.add)
                last.then_inc(mix_taken, 1)
                ve.drain()

                def norm(n, i):
                    ve.wait_ge(gelu_done, n + 1)
                    for half in range(2):
                        nc.vector.bn_stats(stats[:, half, :], gv[i][:, half * HALF:(half + 1) * HALF])
                    ve.drain()
                    nc.vector.bn_aggr(mv[:, i, :], stats[:].rearrange("p a b -> p (a b)")).then_inc(mv_ready, 1)
                    ve.wait_ge(std_ready, n + 1)
                    nc.vector.reciprocal(rstd[:, i:i + 1], rstd[:, i:i + 1])
                    ve.drain()
                    nc.vector.tensor_scalar(gv[i][:], gv[i][:], mv[:, i, 0:1], rstd[:, i:i + 1],
                                            ALU.subtract, ALU.mult).then_inc(normed, 1)

                def take(n, i):
                    ve.wait_ge(mixed, n + 1)
                    for gr in range(G):
                        last = nc.vector.scalar_tensor_tensor(
                            out=out[:].rearrange("p t (n c) -> p t n c", c=P)[:, gr, n, :], in0=mix[i][:, gr * P:(gr + 1) * P],
                            scalar=g[:, gr:gr + 1], in1=shift[:, gr, :], op0=ALU.mult, op1=ALU.add)
                    last.then_inc(mix_taken, 1)

                norm(0, 0)
                with ve.Fori(0, DT // 2 - 1) as j:
                    norm(2 * j + 1, 1)
                    take(2 * j, 0)
                    norm(2 * j + 2, 0)
                    take(2 * j + 1, 1)
                norm(DT - 1, 1)
                take(DT - 2, 0)
                take(DT - 1, 1)


def first_block(nc, d, consts, cols, x):
    with Phase(nc, "b1") as ph:
        h = ph.sb("h", [P, DT, S])
        attn = ph.sb("attn", [P, DT, S])
        ones = consts["ones"]
        resets = ph.sb("reset64", [P, S])
        consts = dict(consts, reset64=resets[:])
        load_phase(nc, "b1_x", [(x[:, :, :], d["xT"].rearrange("p (t s) -> p t s", t=DT)), (resets[:], d["reset64"])])
        norm_rows(nc, "b1_pre", x, h, ones, cols["pre_g"], eps=1e-6)

        def rows(k):
            return h[:, k, :]

        with Phase(nc, "b1a") as pa:
            v = x
            qk = pa.sb("qk", [P, 8, S])
            logits = pa.sb("logits", [P, 4, S])
            with Phase(nc, "b1lr") as pl:
                lr = pl.sb("lr", [16, S])
                project_rows(nc, "b1_lr", d["w_lr"], DT, rows, 1, m=16,
                             act=lambda n, acc, tmp, i: nc.scalar.activation(lr[:], acc[:], ACT.Copy))
                project_rows(nc, "b1_log", d["w_a2"], 1, lambda k: lr[:], 4, kp=16,
                             act=lambda n, acc, tmp, i: nc.scalar.activation(logits[:, n, :], acc[:], ACT.Copy))
            project_rows(nc, "b1_qk", d["w_qk"], DT, rows, 8,
                         act=lambda n, acc, tmp, i: nc.scalar.activation(qk[:, n, :], acc[:], ACT.Copy))
            project_tokens(nc, "b1_v", d["w_bv"], S, h,
                           act=lambda n, acc: nc.scalar.activation(v[:, n, :], acc[:], ACT.Copy))
            gated_linear_attention(nc, consts, cols, logits, qk, v, attn)
        with Phase(nc, "b1b") as pb:
            gate = pb.sb("gate", [P, DT, S])
            def times(dst):
                return lambda n, acc, tmp, i: nc.vector.tensor_tensor(dst[:, n, :], dst[:, n, :], tmp[:], ALU.mult)
            project_rows(nc, "b1_bgate", d["w_bgate"], DT, rows, 8,
                         act=lambda n, acc, tmp, i: nc.scalar.activation(tmp[:], acc[:], ACT.Silu), dve=times(attn))
            spatial_gating(nc, consts, cols, d["w_av"], h, d["w_sT"], d["b_s"], gate)
            project_rows(nc, "b1_au", d["w_au"], DT, rows, 8,
                         act=lambda n, acc, tmp, i: nc.scalar.activation(tmp[:], acc[:], ACT.Gelu), dve=times(gate))
            project_rows(nc, "b1_agate", d["w_agate"], DT, rows, 8,
                         act=lambda n, acc, tmp, i: nc.scalar.activation(tmp[:], acc[:], ACT.Silu), dve=times(gate))
            project_rows(nc, "b1_out", d["w_out1"], 2 * DT, lambda k: gate[:, k, :] if k < DT else attn[:, k - DT, :], 8,
                         act=lambda n, acc, tmp, i: nc.scalar.activation(h[:, n, :], acc[:], ACT.Copy))
        norm_rows(nc, "b1_post", h, x, ones, cols["post_g"], eps=1e-6, add=d["xT"])

M_H, M_DH = 4, 128
GQ_D, GQ_KV = 64, 2
D_FF2 = 2816
GATE_ROWS = 36
TAPS = 5
PAD = TAPS // 2


def conv_rows(nc, ph, w, taps_of, NB, rhs, out, finish, name):
    with Phase(nc, name) as pc:
        padded = [pc.sb(f"padded{i}", [P, S + 2 * PAD]) for i in range(2)]
        conv = [pc.sb(f"conv{i}", [P, S]) for i in range(2)]
        wt = [pc.sb(f"w{i}", [P, DT, P]) for i in range(2)]
        acc = [pc.ps(f"acc{i}", [P, S]) for i in range(2)]
        w_landed = [pc.sem(f"w_landed{i}") for i in range(2)]
        acc_ready = pc.sem("acc_ready")
        zeroed = pc.sem("zeroed")
        acc_taken = pc.sem("acc_taken")
        conv_done = pc.sem("conv_done")
        finished = pc.sem("finished")
        with nc.Block() as block:

            @block.sync
            def _(sp):
                def load(n, i):
                    sp.dma_start(wt[i][:], w[n].rearrange("k (t m) -> k t m", t=DT)).then_inc(w_landed[i], 16)

                load(0, 0)
                load(1, 1)
                with sp.Fori(1, NB // 2) as j:
                    for i in range(2):
                        sp.wait_ge(acc_ready, 2 * j - 1 + i)
                        load(2 * j + i, i)

            @block.tensor
            def _(pe):
                with pe.Fori(0, NB // 2) as j:
                    for i in range(2):
                        pe.wait_ge(w_landed[i], 16 * j + 16)
                        pe.wait_ge(acc_taken, 2 * j + i + 1)
                        for k in range(DT):
                            for half in range(2):
                                c = slice(half * HALF, (half + 1) * HALF)
                                last = nc.tensor.matmul(acc[i][:, c], wt[i][:, k, :], rhs(k)[:, c], start=(k == 0), stop=(k == DT - 1))
                        last.then_inc(acc_ready, 1)

            @block.scalar
            def _(se):
                se.sem_inc(acc_taken, 2)
                se.sem_inc(finished, 2)
                se.wait_ge(zeroed, 1)

                def copy(n, i):
                    se.wait_ge(acc_ready, n + 1)
                    se.wait_ge(conv_done, n + 1)
                    nc.scalar.activation(padded[i][:, PAD:PAD + S], acc[i][:], ACT.Copy).then_inc(acc_taken, 1)

                def end(n, i):
                    se.wait_ge(conv_done, n + 3)
                    finish(n, conv[i]).then_inc(finished, 1)

                copy(0, 0)
                with se.Fori(0, NB // 2 - 1) as j:
                    copy(2 * j + 1, 1)
                    end(2 * j, 0)
                    copy(2 * j + 2, 0)
                    end(2 * j + 1, 1)
                copy(NB - 1, 1)
                end(NB - 2, 0)
                end(NB - 1, 1)

            @block.vector
            def _(ve):
                for i in range(2):
                    nc.vector.memset(padded[i][:, 0:PAD], 0.0)
                    nc.vector.memset(padded[i][:, PAD + S:], 0.0)
                ve.drain().then_inc(zeroed, 1)
                ve.sem_inc(conv_done, 2)
                with ve.Fori(0, NB // 2) as j:
                    for i in range(2):
                        n = 2 * j + i
                        ve.wait_ge(acc_taken, n + 3)
                        ve.wait_ge(finished, n + 1)
                        nc.vector.tensor_scalar(conv[i][:], padded[i][:, 0:S], taps_of(n, 0), None, ALU.mult)
                        for tap in range(1, TAPS):
                            ve.drain()
                            last = nc.vector.scalar_tensor_tensor(out=conv[i][:], in0=padded[i][:, tap:tap + S],
                                                                  scalar=taps_of(n, tap), in1=conv[i][:], op0=ALU.mult, op1=ALU.add)
                        last.then_inc(conv_done, 1)


def mlstm_rows(nc, d, gi, gf, cols, consts, dram, col_out, name="mrow"):
    R = GATE_ROWS
    NCH = DT
    with Phase(nc, name) as ph:
        soft = ph.sb("soft", [R, S])
        lf = ph.sb("lf", [R, S])
        b = ph.sb("b", [R, S])
        m = ph.sb("m", [R, S])
        rel = ph.sb("rel", [R, S])
        quant = [ph.sb(f"quant{i}", [R, S]) for i in range(4)]
        before = ph.sb("before", [R, NCH])
        ends = ph.sb("ends", [R, 3, NCH])
        decay = ph.sb("decay", [R, NCH])
        turned = [ph.ps(f"turned{i}", [P, DT, R]) for i in range(4)]
        soft_ready, lf_ready = ph.sem("soft_ready"), ph.sem("lf_ready")
        biased = ph.sem("biased")
        args_ready = ph.sem("args_ready")
        exps_done = ph.sem("exps_done")
        turned_ready = ph.sem("turned_ready")
        stored = [ph.sem(f"stored{i}") for i in range(2)]
        bi, bf = cols["m_bi"], cols["m_bf"]
        F, B = slice(0, M_H), slice(32, 32 + M_H)

        def chunks(x):
            return x.rearrange("p (n c) -> p n c", c=P)

        with nc.Block() as block:

            @block.scalar
            def _(se):
                nc.scalar.activation(soft[:], gf[:], ACT.Abs, bias=bf[0:R, :])
                se.drain()
                nc.scalar.activation(soft[:], soft[:], ACT.Exp, scale=-1.0)
                se.drain()
                nc.scalar.activation(soft[:], soft[:], ACT.Ln, bias=1.0).then_inc(soft_ready, 1)
                se.wait_ge(args_ready, 1)
                for i in (1, 2):
                    nc.scalar.activation(quant[i][:], quant[i][:], ACT.Exp)
                nc.scalar.activation(quant[3][:], m[:], ACT.Exp, scale=-1.0)
                nc.scalar.activation(decay[:], decay[:], ACT.Exp)
                se.drain().then_inc(exps_done, 1)
                for i in range(4):
                    se.wait_ge(turned_ready, i + 1)
                    nc.scalar.activation(col_out[:, i, :, :], turned[i][:], ACT.Copy, scale=(M_DH ** -0.5 if i == 1 else 1.0))

            @block.vector
            def _(ve):
                nc.vector.tensor_scalar(gi[:], gi[:], bi[0:R, :], None, ALU.add)
                nc.vector.tensor_scalar(lf[:], gf[:], bf[0:R, :], 0.0, ALU.add, ALU.min)
                nc.vector.memset(b[:], 0.0)
                nc.vector.memset(m[:], 0.0)
                nc.vector.memset(before[:], 0.0)
                nc.vector.memset(ends[:], 0.0)
                ve.drain()
                ve.wait_ge(soft_ready, 1)
                nc.vector.tensor_tensor(lf[:], lf[:], soft[:], ALU.subtract)
                ve.drain()
                nc.vector.tensor_tensor_scan(b[F, :], consts["reset128"][F, :], lf[F, :], 0.0, ALU.mult, ALU.add)
                nc.vector.tensor_tensor_scan(b[B, ::-1], consts["reset128"][B, :], lf[B, ::-1], 0.0, ALU.mult, ALU.add)
                nc.vector.tensor_tensor_scan(m[F, :], lf[F, :], gi[F, :], 0.0, ALU.add, ALU.max)
                nc.vector.tensor_tensor_scan(m[B, ::-1], lf[B, ::-1], gi[B, ::-1], 0.0, ALU.add, ALU.max)
                ve.drain()
                b3, m3 = chunks(b[:]), chunks(m[:])
                nc.vector.tensor_copy(ends[F, 0, :], b3[F, :, P - 1])
                nc.vector.tensor_copy(ends[B, 0, :], b3[B, :, 0])
                nc.vector.tensor_copy(ends[F, 1, :], m3[F, :, P - 1])
                nc.vector.tensor_copy(ends[B, 1, :], m3[B, :, 0])
                nc.vector.tensor_copy(before[F, 1:NCH], m3[F, 0:NCH - 1, P - 1])
                nc.vector.tensor_copy(before[B, 0:NCH - 1], m3[B, 1:NCH, 0])
                nc.vector.tensor_tensor(rel[:], b[:], m[:], ALU.subtract)
                nc.vector.tensor_tensor(quant[0][:], gi[:], b[:], ALU.subtract)
                ve.drain()
                nc.vector.tensor_tensor(ends[:, 2, :], ends[:, 0, :], ends[:, 1, :], ALU.subtract)
                ve.drain()
                nc.vector.tensor_tensor(decay[:], ends[:, 2, :], before[:], ALU.add)
                nc.vector.tensor_tensor(chunks(quant[1][:]), chunks(rel[:]), before[:, :, None].broadcast_to([R, NCH, P]), ALU.add)
                nc.vector.tensor_tensor(chunks(quant[2][:]), chunks(quant[0][:]), ends[:, 2, :, None].broadcast_to([R, NCH, P]), ALU.add)
                ve.drain().then_inc(args_ready, 1)

            @block.tensor
            def _(pe):
                pe.wait_ge(exps_done, 1)
                for i in range(4):
                    for t in range(DT):
                        last = nc.tensor.transpose(turned[i][:, t, :], quant[i][:, t * P:(t + 1) * P], consts["ident"][0:R, 0:R])
                    last.then_inc(turned_ready, 1)

            @block.sync
            def _(sp):
                sp.wait_ge(exps_done, 1)
                sp.dma_start(dram["m_rel"], rel[:]).then_inc(stored[0], 16)
                sp.dma_start(dram["m_decay"], decay[:]).then_inc(stored[1], 16)
                for i in range(2):
                    sp.wait_ge(stored[i], 16)


def mlstm(nc, d, consts, cols, dram, qk, v, og, gate_cols, mix):
    NU = 2 * DT
    with Phase(nc, "mlstm") as ph:
        qs = ph.sb("qs", [P, S])
        ks = ph.sb("ks", [P, S])
        vs = ph.sb("vs", [P, DT, M_DH + 2])
        kt = ph.sb("kt", [P, DT, P])
        rel = [ph.sb(f"rel{i}", [P, S]) for i in range(2)]
        decay = ph.sb("decay", [P, 2, DT])
        wexp = ph.sb("wexp", [P, 2, P])
        probs = ph.sb("probs", [P, 2, P])
        vw = ph.sb("vw", [P, 2, M_DH + 2])
        state = ph.sb("state", [P, 2, M_DH + 2])
        den = ph.sb("den", [P, 2])
        num = ph.sb("num", [P, 2, M_DH + 2])
        hsum = ph.sb("hsum", [P, DT, P])
        stats = ph.sb("stats", [P, DT, 6])
        mv = ph.sb("mv", [P, DT, 2])
        rstd = ph.sb("rstd", [P, DT])
        tmp = ph.sb("tmp", [P, S])
        sc = [ph.ps(f"sc{i}", [P, HALF]) for i in range(2)]
        kv = ph.ps("kv", [P, HALF])
        inter = ph.ps("inter", [P, HALF])
        intra = [ph.ps(f"intra{i}", [P, HALF]) for i in range(2)]
        turned = ph.ps("turned", [P, S])
        staged = ph.sem("staged")
        rel_landed = [ph.sem(f"rel_landed{i}") for i in range(2)]
        decay_landed = [ph.sem(f"decay_landed{i}") for i in range(2)]
        head_free = ph.sem("head_free")
        kt_ps = ph.sem("kt_ps")
        kt_ready = ph.sem("kt_ready")
        warg = ph.sem("warg")
        wexp_ready = ph.sem("wexp_ready")
        vw_ready = ph.sem("vw_ready")
        sc_ready = ph.sem("sc_ready")
        probs_ready = ph.sem("probs_ready")
        kv_ready = ph.sem("kv_ready")
        inter_ready = ph.sem("inter_ready")
        intra_ready = ph.sem("intra_ready")
        state_done = ph.sem("state_done")
        num_done = ph.sem("num_done")
        mv_ready = ph.sem("mv_ready")
        std_ready = ph.sem("std_ready")
        normed = ph.sem("normed")
        h_turned = ph.sem("h_turned")
        masks = (consts["m_mask_f"], consts["m_mask_b"])
        W = M_DH + 1
        units = [(0, c) for c in range(DT)] + [(1, DT - 1 - c) for c in range(DT)]

        def gate_col(q, chunk, dr, h):
            return gate_cols[:, q, chunk, bass.ds(32 * dr + h, 1)]

        with nc.Block() as block:

            @block.sync
            def _(sp):
                with sp.Fori(0, M_H) as h:
                    sp.wait_ge(head_free, h + 1)
                    for dr in range(2):
                        sp.dma_start(rel[dr][:], dram["m_rel"][bass.ds(32 * dr + h, 1), :].broadcast_to([P, S])).then_inc(rel_landed[dr], 16)
                        sp.dma_start(decay[:, dr, :], dram["m_decay"][bass.ds(32 * dr + h, 1), :].broadcast_to([P, DT])).then_inc(decay_landed[dr], 16)

            @block.gpsimd
            def _(pool):
                with pool.Fori(0, M_H) as h:
                    pool.wait_ge(head_free, h + 1)
                    nc.gpsimd.tensor_copy(ks[:], qk[:, h + M_H, :])
                    nc.gpsimd.tensor_copy(qs[:], qk[:, h, :])
                    nc.gpsimd.tensor_copy(vs[:], v[:, :, h, :])
                    pool.drain().then_inc(staged, 1)

            @block.tensor
            def _(pe):
                with pe.Fori(0, M_H) as h:
                    pe.wait_ge(staged, h + 1)
                    for t in range(DT):
                        last = nc.tensor.transpose(turned[:, t * P:(t + 1) * P], ks[:, t * P:(t + 1) * P], consts["ident"])
                    last.then_inc(kt_ps, 1)
                    for u in range(NU + 1):
                        if u < NU:
                            dr, c = units[u]
                            tok = slice(c * P, (c + 1) * P)
                            if u >= 2:
                                pe.wait_ge(probs_ready, NU * h + u - 1)
                            nc.tensor.matmul(sc[u % 2][:, 0:P], ks[:, tok], qs[:, tok], start=True, stop=True).then_inc(sc_ready, 1)
                            if u == 0:
                                pe.wait_ge(kt_ready, h + 1)
                        if u >= 1:
                            q = u - 1
                            dr, c = units[q]
                            tok = slice(c * P, (c + 1) * P)
                            pe.wait_ge(vw_ready, NU * h + q + 1)
                            pe.wait_ge(probs_ready, NU * h + q + 1)
                            if q:
                                pe.wait_ge(state_done, NU * h + q)
                                pe.wait_ge(num_done, NU * h + q)
                            nc.tensor.matmul(inter[:, 0:W], qs[:, tok], state[:, q % 2, 0:W], start=True, stop=True).then_inc(inter_ready, 1)
                            nc.tensor.matmul(kv[:, 0:W], kt[:, c, :], vw[:, q % 2, 0:W], start=True, stop=True).then_inc(kv_ready, 1)
                            nc.tensor.matmul(intra[q % 2][:, 0:W], probs[:, q % 2, :], vs[:, c, 0:W], start=True, stop=True).then_inc(intra_ready, 1)
                    pe.wait_ge(normed, h + 1)
                    for t in range(DT):
                        last = nc.tensor.transpose(turned[:, t * P:(t + 1) * P], hsum[:, t, :], consts["ident"])
                    last.then_inc(h_turned, 1)

            @block.scalar
            def _(se):
                with se.Fori(0, M_H) as h:
                    se.wait_ge(kt_ps, h + 1)
                    nc.scalar.activation(kt[:].rearrange("p t c -> p (t c)"), turned[:], ACT.Copy).then_inc(kt_ready, 1)
                    for u in range(NU):
                        dr, c = units[u]
                        if u >= 2:
                            se.wait_ge(kv_ready, NU * h + u - 1)
                        nc.scalar.activation(vw[:, u % 2, 0:W], vs[:, c, 0:W], ACT.Copy, scale=gate_col(2, c, dr, h)).then_inc(vw_ready, 1)
                        se.wait_ge(warg, NU * h + u + 1)
                        nc.scalar.activation(wexp[:, u % 2, :], wexp[:, u % 2, :], ACT.Exp).then_inc(wexp_ready, 1)
                    se.wait_ge(mv_ready, h + 1)
                    nc.scalar.activation(rstd[:], mv[:, :, 1], ACT.Sqrt, bias=1e-6).then_inc(std_ready, 1)

            @block.vector
            def _(ve):
                ve.sem_inc(head_free, 1)
                with ve.Fori(0, M_H) as h:
                    nc.vector.memset(state[:, 0, :], 0.0)
                    for dr in range(2):
                        ve.wait_ge(rel_landed[dr], 16 * h + 16)
                        ve.wait_ge(decay_landed[dr], 16 * h + 16)

                    def argument(u):
                        dr, c = units[u]
                        nc.vector.scalar_tensor_tensor(out=wexp[:, u % 2, :], in0=rel[dr][:, c * P:(c + 1) * P],
                                                       scalar=gate_col(0, c, dr, h), in1=masks[dr],
                                                       op0=ALU.add, op1=ALU.min).then_inc(warg, 1)

                    argument(0)
                    for u in range(NU):
                        dr, c = units[u]
                        if u + 1 < NU:
                            if u >= 1:
                                ve.wait_ge(probs_ready, NU * h + u)
                            argument(u + 1)
                        ve.wait_ge(sc_ready, NU * h + u + 1)
                        ve.wait_ge(wexp_ready, NU * h + u + 1)
                        nc.vector.scalar_tensor_tensor(out=probs[:, u % 2, :], in0=sc[u % 2][:, 0:P], scalar=M_DH ** -0.5,
                                                       in1=wexp[:, u % 2, :], op0=ALU.mult, op1=ALU.mult).then_inc(probs_ready, 1)
                        ve.wait_ge(kv_ready, NU * h + u + 1)
                        if u == DT - 1:
                            nc.vector.memset(state[:, 0, :], 0.0).then_inc(state_done, 1)
                        else:
                            nc.vector.scalar_tensor_tensor(out=state[:, (u + 1) % 2, 0:W], in0=state[:, u % 2, 0:W],
                                                           scalar=decay[:, dr, c:c + 1], in1=kv[:, 0:W],
                                                           op0=ALU.mult, op1=ALU.add).then_inc(state_done, 1)
                        ve.wait_ge(inter_ready, NU * h + u + 1)
                        ve.wait_ge(intra_ready, NU * h + u + 1)
                        i = u % 2
                        nc.vector.tensor_scalar(num[:, 0, 0:W], inter[:, 0:W], gate_col(1, c, dr, h), None, ALU.mult)
                        ve.drain()
                        nc.vector.tensor_tensor(num[:, 1, 0:W], num[:, 0, 0:W], intra[i][:, 0:W], ALU.add).then_inc(num_done, 1)
                        ve.wait_ge(num_done, NU * h + u + 1)
                        nc.vector.tensor_scalar(den[:, 0:1], num[:, 1, M_DH:W], -1.0, None, ALU.mult)
                        ve.drain()
                        nc.vector.tensor_tensor(den[:, 0:1], den[:, 0:1], num[:, 1, M_DH:W], ALU.max)
                        ve.drain()
                        nc.vector.tensor_tensor(den[:, 0:1], den[:, 0:1], gate_col(3, c, dr, h), ALU.max)
                        ve.drain()
                        nc.vector.reciprocal(den[:, 1:2], den[:, 0:1])
                        ve.drain()
                        if dr == 0:
                            nc.vector.tensor_scalar(hsum[:, c, :], num[:, 1, 0:M_DH], den[:, 1:2], None, ALU.mult)
                        else:
                            nc.vector.scalar_tensor_tensor(out=hsum[:, c, :], in0=num[:, 1, 0:M_DH], scalar=den[:, 1:2],
                                                           in1=hsum[:, c, :], op0=ALU.mult, op1=ALU.add)
                    ve.drain()
                    for t in range(DT):
                        nc.vector.bn_stats(stats[:, t, :], hsum[:, t, :])
                    ve.drain()
                    for t in range(DT):
                        last = nc.vector.bn_aggr(mv[:, t, :], stats[:, t, :])
                    last.then_inc(mv_ready, 1)
                    ve.wait_ge(std_ready, h + 1)
                    nc.vector.reciprocal(rstd[:], rstd[:])
                    ve.drain()
                    for t in range(DT):
                        last = nc.vector.tensor_scalar(hsum[:, t, :], hsum[:, t, :], mv[:, t, 0:1], rstd[:, t:t + 1],
                                                       ALU.subtract, ALU.mult)
                    last.then_inc(normed, 1)
                    ve.wait_ge(h_turned, h + 1)
                    nc.vector.scalar_tensor_tensor(out=mix[:, h, :], in0=turned[:], scalar=cols["m_norm_g"][:, bass.ds(h, 1)],
                                                   in1=og[:, h, :], op0=ALU.mult, op1=ALU.mult).then_inc(head_free, 1)


def window_attention(nc, d, consts, cols, aq, ak, av, mix):
    with Phase(nc, "gqa") as ph:
        qs = [ph.sb(f"qs{i}", [P, S]) for i in range(2)]
        bias = ph.sb("bias", [P, 2, 2, 3 * P])
        sink = ph.sb("sink", [P, 8])
        s = ph.sb("s", [P, 2, 3 * P])
        e = ph.sb("e", [P, 2, 3 * P])
        et = ph.sb("et", [P, 2, 3 * P])
        small = ph.sb("small", [P, 2, 4])
        sc = [ph.ps(f"sc{i}", [P, HALF]) for i in range(2)]
        turned = [ph.ps(f"turned{i}", [P, HALF]) for i in range(2)]
        o = [ph.ps(f"o{i}", [P, HALF]) for i in range(2)]
        staged = ph.sem("staged")
        bias_landed = [ph.sem(f"bias_landed{i}") for i in range(2)]
        sink_landed = ph.sem("sink_landed")
        pair_done = ph.sem("pair_done")
        sc_ready = ph.sem("sc_ready")
        max_ready = ph.sem("max_ready")
        exp_ready = ph.sem("exp_ready")
        e_ready = ph.sem("e_ready")
        turned_ready = ph.sem("turned_ready")
        et_ready = ph.sem("et_ready")
        o_ready = ph.sem("o_ready")
        o_taken = ph.sem("o_taken")
        NU = 2 * DT
        units = [(n, j) for n in range(DT) for j in range(2)]

        def window(n):
            lo, hi = max(n - 1, 0), min(n + 2, DT)
            return lo, hi, slice((lo - n + 1) * P, (hi - n + 1) * P)

        with nc.Block() as block:

            @block.sync
            def _(sp):
                sp.dma_start(sink[:], d["a_sink"].broadcast_to([P, 8])).then_inc(sink_landed, 16)
                with sp.Fori(0, 2) as b2:
                    for i in range(2):
                        sp.wait_ge(pair_done, 2 * b2 + i + 1)
                        sp.dma_start(bias[:, i, :, :].rearrange("p j c -> p (j c)"),
                                     d["a_bias"][2 * b2 + i]).then_inc(bias_landed[i], 16)

            @block.gpsimd
            def _(pool):
                with pool.Fori(0, 2) as b2:
                    for i in range(2):
                        pool.wait_ge(pair_done, 2 * b2 + i + 1)
                        nc.gpsimd.tensor_copy(qs[i][:], aq[:, 2 * b2 + i, :]).then_inc(staged, 1)

            @block.tensor
            def _(pe):
                pe.sem_inc(pair_done, 1)
                with pe.Fori(0, 2) as b2:
                    for i in range(2):
                        b = 2 * b2 + i
                        pe.wait_ge(staged, b + 1)
                        for u in range(NU + 2):
                            if u < NU:
                                n, j = units[u]
                                lo, hi, w = window(n)
                                rows = slice(GQ_D * j, GQ_D * (j + 1))
                                if u >= 2:
                                    pe.wait_ge(max_ready, NU * b + u - 1)
                                nc.tensor.matmul(sc[u % 2][:, w], qs[i][rows, n * P:(n + 1) * P], ak[rows, lo * P:hi * P],
                                                 start=True, stop=True).then_inc(sc_ready, 1)
                            if 1 <= u <= NU:
                                n, j = units[u - 1]
                                lo, hi, w = window(n)
                                pe.wait_ge(e_ready, NU * b + u)
                                if u >= 3:
                                    pe.wait_ge(et_ready, NU * b + u - 2)
                                for t in range(hi - lo):
                                    last = nc.tensor.transpose(turned[(u - 1) % 2][:, t * P:(t + 1) * P],
                                                               e[:, (u - 1) % 2, w.start + t * P:w.start + (t + 1) * P], consts["ident"])
                                last.then_inc(turned_ready, 1)
                            if u >= 2:
                                q = u - 2
                                n, j = units[q]
                                lo, hi, w = window(n)
                                rows = slice(GQ_D * j, GQ_D * (j + 1))
                                pe.wait_ge(et_ready, NU * b + q + 1)
                                if j == 0 and n >= 2:
                                    pe.wait_ge(o_taken, DT * b + n - 1)
                                for t in range(hi - lo):
                                    last = nc.tensor.matmul(o[n % 2][rows, 0:P], av[:, lo + t, rows], et[:, q % 2, t * P:(t + 1) * P],
                                                            start=(t == 0), stop=(t == hi - lo - 1))
                                if j == 1:
                                    last.then_inc(o_ready, 1)
                        pe.drain().then_inc(pair_done, 1)

            @block.vector
            def _(ve):
                ve.wait_ge(sink_landed, 16)
                with ve.Fori(0, 2) as b2:
                    for i in range(2):
                        b = 2 * b2 + i
                        ve.wait_ge(bias_landed[i], 16 * b2 + 16)
                        for u in range(NU + 1):
                            if u < NU:
                                n, j = units[u]
                                lo, hi, w = window(n)
                                ve.wait_ge(sc_ready, NU * b + u + 1)
                                if u >= 2:
                                    ve.wait_ge(exp_ready, NU * b + u - 1)
                                sl = u % 2
                                nc.vector.scalar_tensor_tensor(out=s[:, sl, w], in0=sc[sl][:, w], scalar=GQ_D ** -0.5,
                                                               in1=bias[:, i, j, w], op0=ALU.mult, op1=ALU.add)
                                ve.drain()
                                nc.vector.tensor_reduce(small[:, sl, 0:1], s[:, sl, w], AX_X, ALU.max)
                                ve.drain()
                                nc.vector.tensor_scalar(small[:, sl, 0:1], small[:, sl, 0:1], sink[:, bass.ds(b + 4 * j, 1)], -1.0,
                                                        ALU.max, ALU.mult).then_inc(max_ready, 1)
                            if u >= 1:
                                q = u - 1
                                n, j = units[q]
                                lo, hi, w = window(n)
                                sl = q % 2
                                ve.wait_ge(exp_ready, NU * b + q + 1)
                                nc.vector.tensor_tensor(small[:, sl, 1:2], small[:, sl, 1:2], small[:, sl, 2:3], ALU.add)
                                ve.drain()
                                nc.vector.reciprocal(small[:, sl, 3:4], small[:, sl, 1:2])
                                ve.drain()
                                nc.vector.tensor_scalar(e[:, sl, w], e[:, sl, w], small[:, sl, 3:4], None, ALU.mult).then_inc(e_ready, 1)

            @block.scalar
            def _(se):
                se.wait_ge(sink_landed, 16)
                with se.Fori(0, 2) as b2:
                    for i in range(2):
                        b = 2 * b2 + i
                        for u in range(NU + 2):
                            if u < NU:
                                n, j = units[u]
                                lo, hi, w = window(n)
                                sl = u % 2
                                se.wait_ge(max_ready, NU * b + u + 1)
                                if u >= 2:
                                    se.wait_ge(turned_ready, NU * b + u - 1)
                                nc.scalar.activation(e[:, sl, w], s[:, sl, w], ACT.Exp, bias=small[:, sl, 0:1], accum_out=small[:, sl, 1:2])
                                nc.scalar.activation(small[:, sl, 2:3], sink[:, bass.ds(b + 4 * j, 1)], ACT.Exp, bias=small[:, sl, 0:1])
                                se.drain().then_inc(exp_ready, 1)
                            if u >= 1 and u <= NU:
                                q = u - 1
                                n, j = units[q]
                                lo, hi, w = window(n)
                                se.wait_ge(turned_ready, NU * b + q + 1)
                                nc.scalar.activation(et[:, q % 2, 0:(hi - lo) * P], turned[q % 2][:, 0:(hi - lo) * P], ACT.Copy).then_inc(et_ready, 1)
                            if u >= 2 and (u - 2) % 2 == 1:
                                n = (u - 2) // 2
                                se.wait_ge(o_ready, DT * b + n + 1)
                                nc.scalar.activation(mix[:, 4 + b, n * P:(n + 1) * P], o[n % 2][:, 0:P], ACT.Copy).then_inc(o_taken, 1)


def second_block(nc, d, consts, cols, x):
    def x_rows(k):
        return x[:, k, :]

    dram = {"m_rel": nc.dram_tensor("m_rel", (GATE_ROWS, S), F32, kind="Internal").ap(),
            "m_decay": nc.dram_tensor("m_decay", (GATE_ROWS, DT), F32, kind="Internal").ap()}

    def copy_to(dst, func=ACT.Copy):
        return lambda n, acc, tmp, i: nc.scalar.activation(dst[:, n, :], acc[:], func)

    with Phase(nc, "b2") as pm:
        mix = pm.sb("mix", [P, DT, S])
        with Phase(nc, "b2m") as ph:
            qk = ph.sb("qk", [P, 8, S])
            og = ph.sb("og", [P, 4, S])
            v = ph.sb("v", [P, DT, M_H, M_DH + 2])
            gate_cols = ph.sb("gate_cols", [P, 4, DT, GATE_ROWS])
            with Phase(nc, "b2g") as pg:
                gi, gf = pg.sb("gi", [GATE_ROWS, S]), pg.sb("gf", [GATE_ROWS, S])
                resets = pg.sb("resets", [P, S])
                load_phase(nc, "b2_resets", [(resets[:], d["reset128"])])
                project_rows(nc, "b2_gi", d["w_mi"], DT, x_rows, 1, m=GATE_ROWS,
                             act=lambda n, acc, tmp, i: nc.scalar.activation(gi[:], acc[:], ACT.Copy))
                project_rows(nc, "b2_gf", d["w_mf"], DT, x_rows, 1, m=GATE_ROWS,
                             act=lambda n, acc, tmp, i: nc.scalar.activation(gf[:], acc[:], ACT.Copy))
                mlstm_rows(nc, d, gi, gf, cols, dict(consts, reset128=resets[:]), dram, gate_cols)
            project_tokens(nc, "b2_v", d["w_mv"], M_H * M_DH, x,
                           act=lambda n, acc: nc.scalar.activation(v[:, n, :, 0:M_DH], acc[:].rearrange("p (h e) -> p h e", h=M_H), ACT.Copy))
            with Phase(nc, "b2one") as po:
                done = po.sem("done")
                with nc.Block() as block:

                    @block.vector
                    def _(ve):
                        nc.vector.memset(v[:, :, :, M_DH:], 1.0)
            project_rows(nc, "b2_o", d["w_mo"], DT, x_rows, 4, act=copy_to(og, ACT.Sigmoid))
            conv_rows(nc, ph, d["w_mqk"], lambda n, tap: cols["m_taps"][:, bass.ds(TAPS * n + tap, 1)], 8, x_rows, qk,
                      lambda n, conv: nc.scalar.activation(qk[:, n, :], conv[:], ACT.Silu, bias=cols["m_conv_b"][:, bass.ds(n, 1)]), "b2_conv")
            mlstm(nc, d, consts, cols, dram, qk, v, og, gate_cols, mix)
        with Phase(nc, "b2a") as ph:
            aq = ph.sb("aq", [P, 4, S])
            ak = ph.sb("ak", [P, S])
            av = ph.sb("av", [P, DT, P])
            project_rows(nc, "b2_aq", d["w_aq"], DT, x_rows, 4, act=copy_to(aq))
            project_rows(nc, "b2_ak", d["w_ak"], DT, x_rows, 1,
                         act=lambda n, acc, tmp, i: nc.scalar.activation(ak[:], acc[:], ACT.Copy))
            project_tokens(nc, "b2_av", d["w_av2"], P, x, act=lambda n, acc: nc.scalar.activation(av[:, n, :], acc[:], ACT.Copy))
            window_attention(nc, d, consts, cols, aq, ak, av, mix)
        project_rows(nc, "b2_out", d["w_out2"], DT, lambda k: mix[:, k, :], 8,
                     dve=lambda n, acc, tmp, i: nc.vector.scalar_tensor_tensor(out=x[:, n, :], in0=x[:, n, :], scalar=ALPHA, in1=acc[:],
                                                                               op0=ALU.mult, op1=ALU.add))
    norm_rows(nc, "b2_ln1", x, x, consts["ones"], cols["ln1_g2"], cols["ln1_b2"], centre=True)
    NF = D_FF2 // P
    with Phase(nc, "b2f") as ph:
        hid = ph.sb("hid", [P, NF, S])
        base = ph.sb("base", [P, DT, S])
        gated_pairs(nc, "b2_ffn", d["w_ffn"], x_rows, NF, ACT.Silu,
                    lambda n, acc, tmp: nc.vector.tensor_tensor(hid[:, n, :], acc[:], tmp[:], ALU.mult))
        with Phase(nc, "b2p") as pp:
            p_t = pp.sb("p", [P, 2, S])
            load_phase(nc, "b2_p", [(p_t[:], d["pT"].rearrange("p (t s) -> p t s", t=2))])
            project_rows(nc, "b2_plep", d["w_plep"], 2, lambda k: p_t[:, k, :], 8, act=copy_to(base))
        def add_gate(n, acc, tmp, i):
            nc.vector.tensor_tensor(base[:, n, :], base[:, n, :], tmp[:], ALU.mult)
            nc.vector.drain()
            return nc.vector.scalar_tensor_tensor(out=base[:, n, :], in0=x[:, n, :], scalar=ALPHA, in1=base[:, n, :], op0=ALU.mult, op1=ALU.add)
        project_rows(nc, "b2_pleg", d["w_pleg"], DT, x_rows, 8,
                     act=lambda n, acc, tmp, i: nc.scalar.activation(tmp[:], acc[:], ACT.Sigmoid), dve=add_gate)
        project_rows(nc, "b2_ffo", d["w_ffo"], NF, lambda k: hid[:, k, :], 8,
                     dve=lambda n, acc, tmp, i: nc.vector.tensor_tensor(x[:, n, :], base[:, n, :], acc[:], ALU.add))
    norm_rows(nc, "b2_ln2", x, x, consts["ones"], cols["ln2_g2"], cols["ln2_b2"], centre=True)


def gated_pairs(nc, name, w, rhs, NB, func, dve):
    with Phase(nc, name) as ph:
        wt = [ph.sb(f"w{i}", [P, DT, P]) for i in range(2)]
        tmp = ph.sb("tmp", [P, S])
        acc = [ph.ps(f"acc{i}", [P, S]) for i in range(2)]
        w_landed = [ph.sem(f"w_landed{i}") for i in range(2)]
        w_used = [ph.sem(f"w_used{i}") for i in range(2)]
        acc_taken = [ph.sem(f"acc_taken{i}") for i in range(2)]
        with nc.Block() as block:

            @block.sync
            def _(sp):
                def load(n, i):
                    sp.dma_start(wt[i][:], w[n].rearrange("k (t m) -> k t m", t=DT)).then_inc(w_landed[i], 16)

                load(0, 0)
                load(1, 1)
                with sp.Fori(1, NB) as j:
                    for i in range(2):
                        sp.wait_ge(w_used[i], j)
                        load(2 * j + i, i)

            @block.tensor
            def _(pe):
                with pe.Fori(0, NB) as j:
                    for i in range(2):
                        pe.wait_ge(w_landed[i], 16 * j + 16)
                        pe.wait_ge(acc_taken[i], j + 1)
                        for k in range(DT):
                            for half in range(2):
                                c = slice(half * HALF, (half + 1) * HALF)
                                last = nc.tensor.matmul(acc[i][:, c], wt[i][:, k, :], rhs(k)[:, c], start=(k == 0), stop=(k == DT - 1))
                        last.then_inc(w_used[i], 1)

            @block.scalar
            def _(se):
                se.sem_inc(acc_taken[0], 1)
                with se.Fori(0, NB) as j:
                    se.wait_ge(w_used[0], j + 1)
                    se.wait_ge(acc_taken[1], j + 1)
                    nc.scalar.activation(tmp[:], acc[0][:], func).then_inc(acc_taken[0], 1)

            @block.vector
            def _(ve):
                ve.sem_inc(acc_taken[1], 1)
                with ve.Fori(0, NB) as j:
                    ve.wait_ge(acc_taken[0], j + 2)
                    ve.wait_ge(w_used[1], j + 1)
                    dve(j, acc[1], tmp).then_inc(acc_taken[1], 1)


L2_COLUMNS = {"m_bi": 1, "m_bf": 1, "m_taps": 40, "m_conv_b": 8, "m_norm_g": 4, "ln1_g2": 8, "ln1_b2": 8, "ln2_g2": 8, "ln2_b2": 8}
L2_SQUARES = ("m_mask_f", "m_mask_b")


def gate_rows(w):
    import numpy as np
    out = np.zeros((w.shape[0], GATE_ROWS), np.float32)
    out[:, 0:4], out[:, 32:36] = w[:, 0:4], w[:, 4:8]
    return out


def gate_column(b):
    import numpy as np
    out = np.zeros((P, 1), np.float32)
    out[0:4, 0], out[32:36, 0] = b[0:4], b[4:8]
    return out


def second_arrays(a):
    import numpy as np
    w = a["w_in_2"][0]
    mqk, mv, mo, gates, aq, ak, av = np.split(w, np.cumsum([1024, 512, 512, 16, 512, 128]), axis=1)
    order = np.concatenate([np.r_[b * 64:(b + 1) * 64, (b + 4) * 64:(b + 5) * 64] for b in range(4)])
    wo = a["w_out_2"][0]
    ffn = a["w_ffn_in_2"][0]
    pair = rows_weight(ffn).reshape(2, D_FF2 // P, P, 1024).transpose(1, 0, 2, 3).reshape(-1, P, 1024)
    q, k = np.arange(P)[:, None], np.arange(3 * P)[None, :]
    rel = np.abs(k - P - q).astype(np.float32)
    slopes = 2.0 ** (-8.0 * np.arange(1, 9, dtype=np.float32) / 8)
    bias = np.where(rel[None] <= 128, -slopes[:, None, None] * rel[None], -BIG).astype(np.float32)
    bias = np.stack([bias[0:4], bias[4:8]], axis=2)
    tiles = lambda g: gate_rows(g).reshape(DT, P, GATE_ROWS).transpose(1, 0, 2).reshape(1, P, DT * GATE_ROWS)
    out = {"w_mqk": rows_weight(mqk), "w_mv": tokens_weight(mv), "w_mo": rows_weight(mo),
           "w_mi": tiles(gates[:, 0:8]), "w_mf": tiles(gates[:, 8:16]),
           "w_aq": rows_weight(aq[:, order]), "w_ak": rows_weight(ak), "w_av2": tokens_weight(av),
           "a_bias": bias.reshape(4, P, 2 * 3 * P), "a_sink": a["attn_sink_2"],
           "w_out2": rows_weight(np.concatenate([wo[0:512], wo[512:][order]])), "w_ffn": pair,
           "w_ffo": rows_weight(a["w_ffn_out_2"][0]), "w_pleg": rows_weight(a["w_ple_gate_2"][0]),
           "w_plep": rows_weight(a["w_ple_proj_2"][0]),
           "pT": a["p_2"][0, 0].T.reshape(2, P, S).transpose(1, 0, 2).reshape(P, 2 * S),
           "reset128": np.broadcast_to((np.arange(S) % P != 0).astype(np.float32), (P, S))}
    bg = a["b_gate_2"][0]
    taps = a["conv_w_2"][0].reshape(TAPS, 8, P).transpose(2, 1, 0).reshape(P, 40)
    columns = {"m_bi": gate_column(bg[0:8]), "m_bf": gate_column(bg[8:16]), "m_taps": taps,
               "m_conv_b": column(a["conv_b_2"]), "m_norm_g": column(a["mlstm_norm_g_2"]),
               "ln1_g2": column(a["ln1_g_2"]), "ln1_b2": column(a["ln1_b_2"]),
               "ln2_g2": column(a["ln2_g_2"]), "ln2_b2": column(a["ln2_b_2"])}
    i = np.arange(P)
    seen = i[:, None] <= i[None, :]
    squares = {"m_mask_f": np.where(seen, 0, -BIG).astype(np.float32), "m_mask_b": np.where(seen.T, 0, -BIG).astype(np.float32)}
    return out, columns, squares

G_H, G_D = 4, 128
LEVELS = 7
GRID, GRID_ROWS = 64, 16
WIN_R, WIN_C = 8, 16
N_D = 64
RPB_R, RPB_C = 2 * WIN_R - 1, 2 * WIN_C - 1
D_FF3 = 4096


def l2_normalise(nc, d, qkv):
    NB = 2 * G_H
    with Phase(nc, "l2n") as ph:
        pick = ph.sb("pick", [P, NB, NB])
        spread = ph.sb("spread", [NB, NB, P])
        sq = [ph.sb(f"sq{i}", [P, S]) for i in range(2)]
        rows = ph.sb("rows", [NB, S])
        total = ph.ps("total", [NB, S])
        every = [ph.ps(f"every{i}", [P, S]) for i in range(2)]
        pick_landed, spread_landed = ph.sem("pick_landed"), ph.sem("spread_landed")
        squared, summed = ph.sem("squared"), ph.sem("summed")
        std_ready, rstd_ready = ph.sem("std_ready"), ph.sem("rstd_ready")
        spread_ready, scaled = ph.sem("spread_ready"), ph.sem("scaled")
        with nc.Block() as block:

            @block.sync
            def _(sp):
                sp.dma_start(pick[:].rearrange("p a b -> p (a b)"), d["l2_pick"]).then_inc(pick_landed, 16)
                sp.dma_start(spread[:].rearrange("p a b -> p (a b)"), d["l2_spread"]).then_inc(spread_landed, 16)

            @block.scalar
            def _(se):
                for k in range(NB):
                    if k >= 2:
                        se.wait_ge(summed, k - 1)
                    nc.scalar.activation(sq[k % 2][:], qkv[:, k, :], ACT.Square).then_inc(squared, 1)
                se.wait_ge(summed, NB)
                nc.scalar.activation(rows[:], total[:], ACT.Sqrt, bias=1e-6).then_inc(std_ready, 1)

            @block.tensor
            def _(pe):
                pe.wait_ge(pick_landed, 16)
                for k in range(NB):
                    pe.wait_ge(squared, k + 1)
                    for half in range(2):
                        c = slice(half * HALF, (half + 1) * HALF)
                        last = nc.tensor.matmul(total[:, c], pick[:, k, :], sq[k % 2][:, c], start=(k == 0), stop=(k == NB - 1))
                    last.then_inc(summed, 1)
                pe.wait_ge(spread_landed, 16)
                pe.wait_ge(rstd_ready, 1)
                for k in range(NB):
                    if k >= 2:
                        pe.wait_ge(scaled, k - 1)
                    for half in range(2):
                        c = slice(half * HALF, (half + 1) * HALF)
                        last = nc.tensor.matmul(every[k % 2][:, c], spread[:, k, :], rows[:, c], start=True, stop=True)
                    last.then_inc(spread_ready, 1)

            @block.vector
            def _(ve):
                ve.wait_ge(std_ready, 1)
                nc.vector.reciprocal(rows[:], rows[:]).then_inc(rstd_ready, 1)
                for k in range(NB):
                    ve.wait_ge(spread_ready, k + 1)
                    nc.vector.scalar_tensor_tensor(out=qkv[:, k, :], in0=qkv[:, k, :], scalar=(G_D ** -0.5 if k < G_H else 1.0),
                                                   in1=every[k % 2][:], op0=ALU.mult, op1=ALU.mult).then_inc(scaled, 1)


def delta_rows(nc, ga, gb, cols, consts, dram, col_out):
    R, NCH = GATE_ROWS, DT
    with Phase(nc, "grow") as ph:
        soft = ph.sb("soft", [R, S])
        g = ph.sb("g", [R, S])
        quant = [ph.sb(f"quant{i}", [R, S]) for i in range(4)]
        ends = ph.sb("ends", [R, NCH])
        rate = ph.sb("rate", [R, 1])
        turned = [ph.ps(f"turned{i}", [P, DT, R]) for i in range(4)]
        soft_ready, rate_ready = ph.sem("soft_ready"), ph.sem("rate_ready")
        args_ready, exps_done = ph.sem("args_ready"), ph.sem("exps_done")
        turned_ready = ph.sem("turned_ready")
        stored = [ph.sem(f"stored{i}") for i in range(3)]
        F, B = slice(0, G_H), slice(32, 32 + G_H)

        def chunks(x):
            return x.rearrange("p (n c) -> p n c", c=P)

        with nc.Block() as block:

            @block.scalar
            def _(se):
                nc.scalar.activation(soft[:], ga[:], ACT.Abs, bias=cols["g_dt"][0:R, :])
                nc.scalar.activation(rate[:], cols["g_alog"][0:R, :], ACT.Exp).then_inc(rate_ready, 1)
                se.drain()
                nc.scalar.activation(soft[:], soft[:], ACT.Exp, scale=-1.0)
                se.drain()
                nc.scalar.activation(soft[:], soft[:], ACT.Ln, bias=1.0).then_inc(soft_ready, 1)
                nc.scalar.activation(quant[1][:], gb[:], ACT.Sigmoid)
                se.wait_ge(args_ready, 1)
                nc.scalar.activation(quant[2][:], quant[0][:], ACT.Exp)
                nc.scalar.activation(quant[3][:], quant[3][:], ACT.Exp)
                nc.scalar.activation(ends[:], ends[:], ACT.Exp)
                se.drain().then_inc(exps_done, 1)
                for i in range(4):
                    se.wait_ge(turned_ready, i + 1)
                    nc.scalar.activation(col_out[:, i, :, :], turned[i][:], ACT.Copy)
                nc.scalar.activation(col_out[:, 4, :, :], turned[2][:], ACT.Copy, scale=-1.0)

            @block.vector
            def _(ve):
                gc = quant[0]
                nc.vector.tensor_scalar(g[:], ga[:], cols["g_dt"][0:R, :], 0.0, ALU.add, ALU.max)
                nc.vector.memset(gc[:], 0.0)
                nc.vector.memset(ends[:], 0.0)
                ve.drain()
                ve.wait_ge(soft_ready, 1)
                nc.vector.tensor_tensor(g[:], g[:], soft[:], ALU.add)
                ve.drain()
                ve.wait_ge(rate_ready, 1)
                nc.vector.tensor_scalar(g[:], g[:], rate[:], -1.0, ALU.mult, ALU.mult)
                ve.drain()
                nc.vector.tensor_tensor_scan(gc[F, :], consts["reset128"][F, :], g[F, :], 0.0, ALU.mult, ALU.add)
                nc.vector.tensor_tensor_scan(gc[B, ::-1], consts["reset128"][B, :], g[B, ::-1], 0.0, ALU.mult, ALU.add)
                ve.drain()
                nc.vector.tensor_copy(ends[F, :], chunks(gc[:])[F, :, P - 1])
                nc.vector.tensor_copy(ends[B, :], chunks(gc[:])[B, :, 0])
                ve.drain()
                nc.vector.tensor_tensor(chunks(quant[3][:]), ends[:, :, None].broadcast_to([R, NCH, P]), chunks(gc[:]),
                                        ALU.subtract)
                ve.drain().then_inc(args_ready, 1)

            @block.tensor
            def _(pe):
                pe.wait_ge(exps_done, 1)
                for i in range(4):
                    for t in range(DT):
                        last = nc.tensor.transpose(turned[i][:, t, :], quant[i][:, t * P:(t + 1) * P], consts["ident"][0:R, 0:R])
                    last.then_inc(turned_ready, 1)

            @block.sync
            def _(sp):
                sp.wait_ge(exps_done, 1)
                for i, (name, src) in enumerate((("g_gc", quant[0]), ("g_beta", quant[1]), ("g_end", ends))):
                    sp.dma_start(dram[name], src[:]).then_inc(stored[i], 16)
                for i in range(3):
                    sp.wait_ge(stored[i], 16)


def delta_rule(nc, d, consts, cols, dram, qkv, z, gate_cols, mix):
    NG = 4
    N_INV = 2 * LEVELS * 2
    N_Z = 2 * (LEVELS - 1) * 2
    NU = 2 * DT
    with Phase(nc, "delta") as ph:
        qs, ks, vf = ph.sb("qs", [P, S]), ph.sb("ks", [P, S]), ph.sb("vf", [P, S])
        kt = ph.sb("kt", [P, DT, P])
        vt = vf[:].rearrange("p (t c) -> p t c", c=P)
        gc_row = [ph.sb(f"gc_row{i}", [P, S]) for i in range(2)]
        beta_row = [ph.sb(f"beta_row{i}", [P, S]) for i in range(2)]
        end_row = ph.sb("end_row", [P, 2, DT])
        level = ph.sb("level", [P, 2 * LEVELS, P])
        gam = [ph.sb(f"gam{i}", [P, NG, P]) for i in range(2)]
        pt = [ph.sb(f"pt{i}", [P, NG, P]) for i in range(4)]
        at = [ph.sb(f"at{i}", [P, NG, P]) for i in range(4)]
        xt = [ph.sb(f"xt{i}", [P, NG, P]) for i in range(4)]
        free = [mix[:, 4 + i, :].rearrange("p (a n c) -> p a n c", a=2, c=P) for i in range(3)]
        bt = [[free[i][:, j] for j in range(2)] for i in range(2)]
        xx = [free[2][:, i] for i in range(2)]
        r, rb, vn, vkd = (mix[:, 7, 2 * i * P:2 * (i + 1) * P].rearrange("p (a c) -> p a c", a=2) for i in range(4))
        ys = gam
        state = ph.sb("state", [P, 2, P])
        t1 = ph.sb("t1", [P, 2, P])
        osum = gc_row[0][:].rearrange("p (t c) -> p t c", c=P)
        ss = ph.sb("ss", [P, DT])
        bank = [ph.ps(f"bank{i}", [P, NG, P]) for i in range(4)]
        turned_k, turned_v = ph.ps("turned_k", [P, S]), ph.ps("turned_v", [P, S])
        zt_bank = [turned_k[:, 0:HALF].rearrange("p (n c) -> p n c", c=P), turned_k[:, HALF:S].rearrange("p (n c) -> p n c", c=P)]
        level_landed = ph.sem("level_landed")
        row_landed = [ph.sem(f"row_landed{i}") for i in range(6)]
        staged = ph.sem("staged")
        head_free = ph.sem("head_free")
        turned_ready = ph.sem("turned_ready")
        kv_ready = ph.sem("kv_ready")
        prod_ready = ph.sem("prod_ready")
        garg = ph.sem("garg")
        gam_ready = ph.sem("gam_ready")
        kk_ready = ph.sem("kk_ready")
        at_ready = ph.sem("at_ready")
        bt_ready = ph.sem("bt_ready")
        y_ready = ph.sem("y_ready")
        y_copied = ph.sem("y_copied")
        z_ready = ph.sem("z_ready")
        x_done = ph.sem("x_done")
        ks_ready = ph.sem("ks_ready")
        r_ready = ph.sem("r_ready")
        rb_ready = ph.sem("rb_ready")
        vn_ready = ph.sem("vn_ready")
        vns_ready = ph.sem("vns_ready")
        vkd_ready = ph.sem("vkd_ready")
        su_ready = ph.sem("su_ready")
        s_done = ph.sem("s_done")
        ss_ready, std_ready = ph.sem("ss_ready"), ph.sem("std_ready")
        normed, o_turned = ph.sem("normed"), ph.sem("o_turned")
        ident = consts["ident"]
        masks = (consts["m_mask_f"], consts["m_mask_b"])

        def gate_col(q, chunk, dr, h):
            return gate_cols[:, q, chunk, bass.ds(32 * dr + h, 1)]

        def tok(c):
            return slice(c * P, (c + 1) * P)

        def chunk_of(step, dr):
            return step if dr == 0 else DT - 1 - step

        inverse_steps = [(pp, l, g) for pp in range(2) for l in range(LEVELS) for g in range(2)]

        with nc.Block() as block:

            @block.sync
            def _(sp):
                sp.dma_start(level[:].rearrange("p l c -> p (l c)"), d["g_levels"]).then_inc(level_landed, 16)
                with sp.Fori(0, G_H) as h:
                    sp.wait_ge(head_free, h + 1)
                    for dr in range(2):
                        row = bass.ds(32 * dr + h, 1)
                        sp.dma_start(gc_row[dr][:], dram["g_gc"][row, :].broadcast_to([P, S])).then_inc(row_landed[3 * dr], 16)
                        sp.dma_start(beta_row[dr][:], dram["g_beta"][row, :].broadcast_to([P, S])).then_inc(row_landed[3 * dr + 1], 16)
                        sp.dma_start(end_row[:, dr, :], dram["g_end"][row, :].broadcast_to([P, DT])).then_inc(row_landed[3 * dr + 2], 16)

            @block.gpsimd
            def _(pool):
                pool.wait_ge(level_landed, 16)
                with pool.Fori(0, G_H) as h:
                    pool.wait_ge(head_free, h + 1)
                    nc.gpsimd.tensor_copy(ks[:], qkv[:, h + G_H, :])
                    nc.gpsimd.tensor_copy(vf[:], qkv[:, h + 2 * G_H, :])
                    nc.gpsimd.tensor_copy(qs[:], qkv[:, h, :])
                    pool.drain().then_inc(staged, 1)
                    for dr in range(2):
                        pool.wait_ge(row_landed[3 * dr + 1], 16 * h + 16)
                    for gi in range(4):
                        pool.wait_ge(kk_ready, 4 * h + gi + 1)
                        c0 = (gi % 2) * HALF
                        nc.gpsimd.tensor_tensor(at[gi][:].rearrange("p n c -> p (n c)"), at[gi][:].rearrange("p n c -> p (n c)"),
                                                beta_row[gi // 2][:, c0:c0 + HALF], ALU.mult).then_inc(at_ready, 1)
                    pool.wait_ge(at_ready, 4 * h + 4)
                    for n, (pp, l, g) in enumerate(inverse_steps):
                        if n >= 4:
                            pool.wait_ge(x_done, N_INV * h + n - 3)
                        mask = level[:, LEVELS * pp + l:LEVELS * pp + l + 1, :].broadcast_to([P, NG, P])
                        nc.gpsimd.tensor_tensor(bt[g][(pp * LEVELS + l) % 2], at[2 * pp + g][:], mask, ALU.mult).then_inc(bt_ready, 1)

            @block.tensor
            def _(pe):
                with pe.Fori(0, G_H) as h:
                    pe.wait_ge(staged, h + 1)
                    for t in range(DT):
                        nc.tensor.transpose(turned_k[:, tok(t)], ks[:, tok(t)], ident)
                    for t in range(DT):
                        last = nc.tensor.transpose(turned_v[:, tok(t)], vf[:, tok(t)], ident)
                    last.then_inc(turned_ready, 1)
                    for half in range(2):
                        for i in range(NG):
                            c = tok(half * NG + i)
                            nc.tensor.matmul(bank[half][:, i, :], ks[:, c], ks[:, c], start=True, stop=True)
                        for i in range(NG):
                            c = tok(half * NG + i)
                            last = nc.tensor.matmul(bank[2 + half][:, i, :], ks[:, c], qs[:, c], start=True, stop=True)
                        last.then_inc(prod_ready, 1)
                    pe.wait_ge(kv_ready, h + 1)
                    pe.wait_ge(kk_ready, 4 * h + 4)
                    zn = 0
                    for pp in range(2):
                        for l in range(LEVELS):
                            n0 = (pp * LEVELS + l) * 2
                            for g in range(2):
                                pe.wait_ge(bt_ready, N_INV * h + n0 + g + 1)
                                if l:
                                    pe.wait_ge(x_done, N_INV * h + n0 + g - 1)
                                elif pp:
                                    pe.wait_ge(y_copied, N_INV * h + n0 + g - 1)
                                for i in range(NG):
                                    last = nc.tensor.matmul(bank[g][:, i, :], bt[g][(pp * LEVELS + l) % 2][:, i, :],
                                                            xx[g][:, i, :] if l else ident, start=True, stop=True)
                                last.then_inc(y_ready, 1)
                            if l:
                                for g in range(2):
                                    pe.wait_ge(y_copied, N_INV * h + n0 + g + 1)
                                    if l < LEVELS - 1:
                                        for i in range(NG):
                                            nc.tensor.matmul(bank[2 + g][:, i, :], xt[2 * pp + g][:, i, :], ys[g][:, i, :],
                                                             start=True, stop=True)
                                    for i in range(NG):
                                        last = nc.tensor.matmul(zt_bank[g][:, i, :], ys[g][:, i, :], xt[2 * pp + g][:, i, :],
                                                                start=True, stop=True)
                                    last.then_inc(z_ready, 1)
                    pe.wait_ge(x_done, N_INV * h + N_INV)
                    for k in range(DT):
                        for dr in range(2):
                            c, m = tok(chunk_of(k, dr)), 2 * k + dr
                            if k:
                                pe.wait_ge(s_done, NU * h + m - 1)
                            nc.tensor.matmul(bank[dr][:, 0, :], ks[:, c], state[:, dr, :], start=True, stop=True)
                            nc.tensor.matmul(bank[dr][:, 1, :], qs[:, c], state[:, dr, :], start=True, stop=True).then_inc(ks_ready, 1)
                        for dr in range(2):
                            ch, m = chunk_of(k, dr), 2 * k + dr
                            pe.wait_ge(rb_ready, NU * h + m + 1)
                            nc.tensor.matmul(bank[2 + dr][:, 0, :], xt[2 * dr + ch // NG][:, ch % NG, :], rb[:, dr, :],
                                             start=True, stop=True).then_inc(vn_ready, 1)
                        for dr in range(2):
                            ch, m = chunk_of(k, dr), 2 * k + dr
                            pe.wait_ge(vns_ready, NU * h + m + 1)
                            nc.tensor.matmul(zt_bank[dr][:, 0, :], pt[2 * dr + ch // NG][:, ch % NG, :], vn[:, dr, :], start=True, stop=True)
                            pe.wait_ge(vkd_ready, NU * h + m + 1)
                            nc.tensor.matmul(zt_bank[dr][:, 1, :], kt[:, ch, :], vkd[:, dr, :], start=True, stop=True).then_inc(su_ready, 1)
                    pe.wait_ge(normed, h + 1)
                    for t in range(DT):
                        last = nc.tensor.transpose(turned_v[:, tok(t)], osum[:, t, :], ident)
                    last.then_inc(o_turned, 1)

            @block.scalar
            def _(se):
                with se.Fori(0, G_H) as h:
                    se.wait_ge(turned_ready, h + 1)
                    nc.scalar.activation(kt[:].rearrange("p t c -> p (t c)"), turned_k[:], ACT.Copy)
                    nc.scalar.activation(vf[:], turned_v[:], ACT.Copy)
                    se.drain().then_inc(kv_ready, 1)
                    for gi in range(4):
                        se.wait_ge(garg, 4 * h + gi + 1)
                        nc.scalar.activation(gam[gi % 2][:], gam[gi % 2][:], ACT.Exp).then_inc(gam_ready, 1)
                    for n in range(N_INV):
                        g = n % 2
                        se.wait_ge(y_ready, N_INV * h + n + 1)
                        if n >= 2:
                            se.wait_ge(x_done, N_INV * h + n - 1)
                        nc.scalar.activation(ys[g][:], bank[g][:], ACT.Copy).then_inc(y_copied, 1)
                    for k in range(DT):
                        for dr in range(2):
                            ch, m = chunk_of(k, dr), 2 * k + dr
                            se.wait_ge(r_ready, NU * h + m + 1)
                            nc.scalar.activation(rb[:, dr, :], r[:, dr, :], ACT.Copy, scale=gate_col(1, ch, dr, h)).then_inc(rb_ready, 1)
                        for dr in range(2):
                            ch, m = chunk_of(k, dr), 2 * k + dr
                            se.wait_ge(vns_ready, NU * h + m + 1)
                            nc.scalar.activation(vkd[:, dr, :], vn[:, dr, :], ACT.Copy, scale=gate_col(3, ch, dr, h)).then_inc(vkd_ready, 1)
                    se.wait_ge(ss_ready, h + 1)
                    nc.scalar.activation(ss[:], ss[:], ACT.Sqrt, scale=1.0 / G_D, bias=1e-6).then_inc(std_ready, 1)

            @block.vector
            def _(ve):
                ve.sem_inc(head_free, 1)
                with ve.Fori(0, G_H) as h:
                    nc.vector.memset(state[:], 0.0)
                    for dr in range(2):
                        ve.wait_ge(row_landed[3 * dr], 16 * h + 16)
                        ve.wait_ge(row_landed[3 * dr + 2], 16 * h + 16)

                    def argument(gi):
                        dr, half = gi // 2, gi % 2
                        for i in range(NG):
                            c = half * NG + i
                            last = nc.vector.scalar_tensor_tensor(out=gam[gi % 2][:, i, :], in0=gc_row[dr][:, tok(c)],
                                                                  scalar=gate_col(0, c, dr, h), in1=masks[dr],
                                                                  op0=ALU.subtract, op1=ALU.min)
                        last.then_inc(garg, 1)

                    argument(0)
                    for gi in range(4):
                        if gi < 3:
                            if gi:
                                ve.wait_ge(kk_ready, 4 * h + gi)
                            argument(gi + 1)
                        ve.wait_ge(gam_ready, 4 * h + gi + 1)
                        ve.wait_ge(prod_ready, 2 * h + gi % 2 + 1)
                        nc.vector.tensor_tensor(pt[gi][:], bank[2 + gi % 2][:], gam[gi % 2][:], ALU.mult)
                        nc.vector.tensor_tensor(at[gi][:], bank[gi % 2][:], gam[gi % 2][:], ALU.mult)
                        ve.drain().then_inc(kk_ready, 1)
                    for n, (pp, l, g) in enumerate(inverse_steps):
                        gi = 2 * pp + g
                        if l == 0:
                            ve.wait_ge(y_copied, N_INV * h + n + 1)
                            ident4 = ident[:, None, :].broadcast_to([P, NG, P])
                            nc.vector.tensor_tensor(xx[g], ident4, ys[g][:], ALU.subtract)
                            nc.vector.tensor_tensor(xt[gi][:], ident4, bt[g][(pp * LEVELS + l) % 2], ALU.subtract)
                        else:
                            ve.wait_ge(z_ready, N_Z * h + (pp * (LEVELS - 1) + l - 1) * 2 + g + 1)
                            if l < LEVELS - 1:
                                nc.vector.tensor_tensor(xx[g], xx[g], bank[2 + g][:], ALU.subtract)
                            nc.vector.tensor_tensor(xt[gi][:], xt[gi][:], zt_bank[g], ALU.subtract)
                        ve.drain().then_inc(x_done, 1)
                    for k in range(DT):
                        for dr in range(2):
                            ch, m = chunk_of(k, dr), 2 * k + dr
                            ve.wait_ge(ks_ready, NU * h + m + 1)
                            nc.vector.scalar_tensor_tensor(out=r[:, dr, :], in0=bank[dr][:, 0, :], scalar=gate_col(4, ch, dr, h),
                                                           in1=vt[:, ch, :], op0=ALU.mult, op1=ALU.add).then_inc(r_ready, 1)
                            if k < DT // 2:
                                nc.vector.tensor_scalar(t1[:, dr, :], bank[dr][:, 1, :], gate_col(2, ch, dr, h), None, ALU.mult)
                            else:
                                nc.vector.scalar_tensor_tensor(out=t1[:, dr, :], in0=bank[dr][:, 1, :], scalar=gate_col(2, ch, dr, h),
                                                               in1=osum[:, ch, :], op0=ALU.mult, op1=ALU.add)
                        for dr in range(2):
                            ve.wait_ge(vn_ready, NU * h + 2 * k + dr + 1)
                            nc.vector.tensor_copy(vn[:, dr, :], bank[2 + dr][:, 0, :]).then_inc(vns_ready, 1)
                        for dr in range(2):
                            ch, m = chunk_of(k, dr), 2 * k + dr
                            ve.wait_ge(su_ready, NU * h + m + 1)
                            nc.vector.scalar_tensor_tensor(out=state[:, dr, :], in0=state[:, dr, :], scalar=end_row[:, dr, ch:ch + 1],
                                                           in1=zt_bank[dr][:, 1, :], op0=ALU.mult, op1=ALU.add).then_inc(s_done, 1)
                            nc.vector.tensor_tensor(osum[:, ch, :], t1[:, dr, :], zt_bank[dr][:, 0, :], ALU.add)
                        ve.drain()
                    nc.vector.tensor_tensor(kt[:], osum, osum, ALU.mult)
                    ve.drain()
                    nc.vector.tensor_reduce(ss[:], kt[:], AX_X, ALU.add).then_inc(ss_ready, 1)
                    ve.wait_ge(std_ready, h + 1)
                    nc.vector.reciprocal(ss[:], ss[:])
                    ve.drain()
                    nc.vector.tensor_tensor(osum, osum, ss[:, :, None].broadcast_to([P, DT, P]), ALU.mult).then_inc(normed, 1)
                    ve.wait_ge(o_turned, h + 1)
                    nc.vector.scalar_tensor_tensor(out=mix[:, h, :], in0=turned_v[:], scalar=cols["g_norm_g"], in1=z[:, h, :],
                                                   op0=ALU.mult, op1=ALU.mult).then_inc(head_free, 1)


def neighbourhood_attention(nc, d, consts, cols, dram, nq, nk, nv, mix):
    NU = 2 * DT
    WK = WIN_R * GRID
    WE = WK + P

    def first_row(r):
        return min(max(r - WIN_R // 2, 0), GRID_ROWS - WIN_R)

    def shifted(pr):
        return first_row(2 * pr) != first_row(2 * pr + 1)

    units = [(pr, j) for pr in range(DT) for j in range(2)]
    with Phase(nc, "na") as ph:
        qs, ks = ph.sb("qs", [P, S]), ph.sb("ks", [P, S])
        vs = ph.sb("vs", [P, DT, P])
        table = ph.sb("table", [P, 2, RPB_R * GRID])
        window = ph.sb("window", [P, RPB_R * GRID])
        s = ph.sb("s", [P, 2, WK])
        e = ph.sb("e", [P, 2, WE])
        et = ph.sb("et", [P, 2, WE])
        small = ph.sb("small", [P, 2, 3])
        ob = ph.sb("ob", [P, S])
        sq = ph.sb("sq", [P, S])
        sc = [ph.ps(f"sc{i}", [P, HALF]) for i in range(2)]
        turned = [ph.ps(f"turned{i}", [P, S]) for i in range(2)]
        o = [ph.ps(f"o{i}", [P, HALF]) for i in range(2)]
        window_landed = ph.sem("window_landed")
        tables_stored = ph.sem("tables_stored")
        table_landed = [ph.sem(f"table_landed{i}") for i in range(4)]
        table_ready = ph.sem("table_ready")
        staged = ph.sem("staged")
        pair_free = ph.sem("pair_free")
        waited = ph.sem("waited")
        sc_ready = ph.sem("sc_ready")
        max_ready = ph.sem("max_ready")
        exp_ready = ph.sem("exp_ready")
        e_ready = ph.sem("e_ready")
        turned_ready = ph.sem("turned_ready")
        et_ready = ph.sem("et_ready")
        o_ready = ph.sem("o_ready")
        o_taken = ph.sem("o_taken")
        squared, summed, std_ready = ph.sem("squared"), ph.sem("summed"), ph.sem("std_ready")
        rpb = d["rpb"]
        toeplitz = bass.AP(rpb.tensor, GRID - 1, [[RPB_R * 2 * GRID, 2 * 4], [2 * GRID, RPB_R], [-1, GRID], [1, GRID]])

        with nc.Block() as block:

            @block.sync
            def _(sp):
                sp.dma_start(window[:], d["na_columns"]).then_inc(window_landed, 16)
                for head in range(8):
                    sp.dma_start(dram["n_tables"][head].rearrange("q (r c) -> r q c", c=GRID), toeplitz[head]).then_inc(tables_stored, 16)
                sp.wait_ge(tables_stored, 8 * 16)
                with sp.Fori(0, 4) as b:
                    sp.wait_ge(pair_free, b + 1)
                    for j in range(2):
                        for i in range(2):
                            sp.dma_start(table[i * GRID:(i + 1) * GRID, j, :], dram["n_tables"][2 * b + j]).then_inc(table_landed[2 * j + i], 16)

            @block.gpsimd
            def _(pool):
                with pool.Fori(0, 4) as b:
                    pool.wait_ge(pair_free, b + 1)
                    nc.gpsimd.tensor_copy(qs[:], nq[:, b, :])
                    nc.gpsimd.tensor_copy(ks[:], nk[:, b, :])
                    nc.gpsimd.tensor_copy(vs[:], nv[:].rearrange("p t (b c) -> p t b c", c=P)[:, :, b, :])
                    pool.drain().then_inc(staged, 1)

            @block.tensor
            def _(pe):
                with pe.Fori(0, 4) as b:
                    pe.wait_ge(staged, b + 1)
                    for u in range(NU + 2):
                        if u < NU:
                            pr, j = units[u]
                            rows = slice(N_D * j, N_D * (j + 1))
                            if u >= 2:
                                pe.wait_ge(max_ready, NU * b + u - 1)
                            pe.sem_inc(waited, 1)
                            for i in range(2):
                                r = 2 * pr + i
                                k0 = first_row(r) * GRID
                                last = nc.tensor.matmul(sc[j][i * GRID:(i + 1) * GRID, :], qs[rows, r * GRID:(r + 1) * GRID],
                                                        ks[rows, k0:k0 + WK], start=True, stop=True)
                            last.then_inc(sc_ready, 1)
                        if 1 <= u <= NU:
                            pr, j = units[u - 1]
                            pe.wait_ge(e_ready, NU * b + u)
                            if u >= 3:
                                pe.wait_ge(et_ready, NU * b + u - 2)
                            for t in range(5 if shifted(pr) else 4):
                                last = nc.tensor.transpose(turned[j][:, t * P:(t + 1) * P], e[:, j, t * P:(t + 1) * P], consts["ident"])
                            last.then_inc(turned_ready, 1)
                        if u >= 2:
                            pr, j = units[u - 2]
                            rows = slice(N_D * j, N_D * (j + 1))
                            tiles = 5 if shifted(pr) else 4
                            pe.wait_ge(et_ready, NU * b + u - 1)
                            if j == 0 and pr >= 2:
                                pe.wait_ge(o_taken, DT * b + pr - 1)
                            for t in range(tiles):
                                last = nc.tensor.matmul(o[pr % 2][rows, 0:P], vs[:, first_row(2 * pr) // 2 + t, rows],
                                                        et[:, j, t * P:(t + 1) * P], start=(t == 0), stop=(t == tiles - 1))
                            if j == 1:
                                last.then_inc(o_ready, 1)
                    pe.wait_ge(squared, b + 1)
                    for half in range(2):
                        c = slice(half * HALF, (half + 1) * HALF)
                        last = nc.tensor.matmul(turned[0][:, c], consts["ones64"], sq[:, c], start=True, stop=True)
                    last.then_inc(summed, 1)

            @block.vector
            def _(ve):
                ve.sem_inc(pair_free, 1)
                ve.wait_ge(window_landed, 16)
                with ve.Fori(0, 4) as b:
                    for i in range(4):
                        ve.wait_ge(table_landed[i], 16 * b + 16)
                    nc.vector.tensor_tensor(table[:], table[:], window[:, None, :].broadcast_to([P, 2, RPB_R * GRID]), ALU.min)
                    ve.drain()
                    for u in range(NU + 1):
                        if u < NU:
                            pr, j = units[u]
                            ve.wait_ge(sc_ready, NU * b + u + 1)
                            if u >= 2:
                                ve.wait_ge(exp_ready, NU * b + u - 1)
                            at = [(first_row(2 * pr + i) - 2 * pr - i + WIN_R - 1) * GRID for i in range(2)]
                            for rows, a in ([(slice(0, P), at[0])] if at[0] == at[1] else
                                            [(slice(i * GRID, (i + 1) * GRID), at[i]) for i in range(2)]):
                                nc.vector.scalar_tensor_tensor(out=s[rows, j, :], in0=sc[j][rows, :], scalar=N_D ** -0.5,
                                                               in1=table[rows, j, a:a + WK], op0=ALU.mult, op1=ALU.add)
                            ve.drain()
                            nc.vector.tensor_reduce(small[:, j, 0:1], s[:, j, :], AX_X, ALU.max, negate=True)
                            if shifted(pr) and not shifted(pr - 1):
                                ve.wait_ge(turned_ready, NU * b + u - 1)
                                nc.vector.memset(e[0:GRID, j, WK:WE], 0.0)
                                nc.vector.memset(e[GRID:P, j, 0:GRID], 0.0)
                                nc.vector.memset(e[GRID:P, j, WK + GRID:WE], 0.0)
                            ve.drain().then_inc(max_ready, 1)
                        if u >= 1:
                            pr, j = units[u - 1]
                            w = WE if shifted(pr) else WK
                            ve.wait_ge(exp_ready, NU * b + u)
                            nc.vector.reciprocal(small[:, j, 2:3], small[:, j, 1:2])
                            ve.drain()
                            nc.vector.tensor_scalar(e[:, j, 0:w], e[:, j, 0:w], small[:, j, 2:3], None, ALU.mult).then_inc(e_ready, 1)
                    ve.wait_ge(std_ready, b + 1)
                    nc.vector.reciprocal(sq[:], sq[:])
                    ve.drain()
                    nc.vector.scalar_tensor_tensor(out=mix[:, 4 + b, :], in0=ob[:], scalar=cols["n_norm_g"], in1=sq[:],
                                                   op0=ALU.mult, op1=ALU.mult).then_inc(pair_free, 1)

            @block.scalar
            def _(se):
                with se.Fori(0, 4) as b:
                    for u in range(NU + 2):
                        if u < NU:
                            pr, j = units[u]
                            se.wait_ge(max_ready, NU * b + u + 1)
                            if u >= 2:
                                se.wait_ge(turned_ready, NU * b + u - 1)
                            for i, rows in enumerate((slice(0, GRID), slice(GRID, P)) if shifted(pr) else (slice(0, P),)):
                                nc.scalar.activation(e[rows, j, i * GRID:i * GRID + WK], s[rows, j, :], ACT.Exp,
                                                     bias=small[rows, j, 0:1], accum_out=small[rows, j, 1:2])
                            se.drain().then_inc(exp_ready, 1)
                        if 1 <= u <= NU:
                            pr, j = units[u - 1]
                            w = WE if shifted(pr) else WK
                            se.wait_ge(turned_ready, NU * b + u)
                            nc.scalar.activation(et[:, j, 0:w], turned[j][:, 0:w], ACT.Copy).then_inc(et_ready, 1)
                        if u >= 2 and units[u - 2][1] == 1:
                            pr = units[u - 2][0]
                            se.wait_ge(o_ready, DT * b + pr + 1)
                            nc.scalar.activation(ob[:, pr * P:(pr + 1) * P], o[pr % 2][:, 0:P], ACT.Copy).then_inc(o_taken, 1)
                    se.drain()
                    nc.scalar.activation(sq[:], ob[:], ACT.Square).then_inc(squared, 1)
                    se.wait_ge(summed, b + 1)
                    nc.scalar.activation(sq[:], turned[0][:], ACT.Sqrt, scale=1.0 / N_D, bias=1e-6).then_inc(std_ready, 1)


def third_block(nc, d, consts, cols, x):
    def x_rows(k):
        return x[:, k, :]

    def copy_to(dst, func=ACT.Copy):
        return lambda n, acc, tmp, i: nc.scalar.activation(dst[:, n, :], acc[:], func)

    dram = {"g_gc": nc.dram_tensor("g_gc", (GATE_ROWS, S), F32, kind="Internal").ap(),
            "g_beta": nc.dram_tensor("g_beta", (GATE_ROWS, S), F32, kind="Internal").ap(),
            "g_end": nc.dram_tensor("g_end", (GATE_ROWS, DT), F32, kind="Internal").ap()}
    dram["n_tables"] = nc.dram_tensor("n_tables", (8, GRID, RPB_R * GRID), F32, kind="Internal").ap()
    norm_rows(nc, "b3_in", x, x, consts["ones"], cols["ln_in_g"], cols["ln_in_b"], centre=True)
    with Phase(nc, "b3") as pm:
        mix = pm.sb("mix", [P, DT, S])
        with Phase(nc, "b3g") as ph:
            z = ph.sb("z", [P, 4, S])
            qkv = ph.sb("qkv", [P, 12, S])
            gate_cols = ph.sb("gate_cols", [P, 5, DT, GATE_ROWS])
            with Phase(nc, "b3r") as pg:
                ga, gb = pg.sb("ga", [GATE_ROWS, S]), pg.sb("gb", [GATE_ROWS, S])
                resets = pg.sb("resets", [P, S])
                load_phase(nc, "b3_resets", [(resets[:], d["reset128_3"])])
                project_rows(nc, "b3_ga", d["w_ga"], DT, x_rows, 1, m=GATE_ROWS,
                             act=lambda n, acc, tmp, i: nc.scalar.activation(ga[:], acc[:], ACT.Copy))
                project_rows(nc, "b3_gb", d["w_gb"], DT, x_rows, 1, m=GATE_ROWS,
                             act=lambda n, acc, tmp, i: nc.scalar.activation(gb[:], acc[:], ACT.Copy))
                delta_rows(nc, ga, gb, cols, dict(consts, reset128=resets[:]), dram, gate_cols)
            project_rows(nc, "b3_z", d["w_gz"], DT, x_rows, 4, act=copy_to(z, ACT.Silu))
            conv_rows(nc, ph, d["w_gqkv"], lambda n, tap: cols["g_taps"][:, bass.ds(TAPS * n + tap, 1)], 12, x_rows, qkv,
                      lambda n, conv: nc.scalar.activation(qkv[:, n, :], conv[:], ACT.Silu), "b3_conv")
            l2_normalise(nc, d, qkv)
            delta_rule(nc, d, consts, cols, dram, qkv, z, gate_cols, mix)
        with Phase(nc, "b3n") as ph:
            nq, nk = ph.sb("nq", [P, 4, S]), ph.sb("nk", [P, 4, S])
            nv = ph.sb("nv", [P, DT, HALF])
            project_rows(nc, "b3_nq", d["w_nq"], DT, x_rows, 4, act=copy_to(nq))
            project_rows(nc, "b3_nk", d["w_nk"], DT, x_rows, 4, act=copy_to(nk))
            project_tokens(nc, "b3_nv", d["w_nv"], HALF, x, act=lambda n, acc: nc.scalar.activation(nv[:, n, :], acc[:], ACT.Copy))
            neighbourhood_attention(nc, d, consts, cols, dram, nq, nk, nv, mix)
        project_rows(nc, "b3_out", d["w_out3"], DT, lambda k: mix[:, k, :], 8,
                     dve=lambda n, acc, tmp, i: nc.vector.scalar_tensor_tensor(out=x[:, n, :], in0=x[:, n, :], scalar=ALPHA, in1=acc[:],
                                                                               op0=ALU.mult, op1=ALU.add))
    norm_rows(nc, "b3_ln1", x, x, consts["ones"], cols["ln1_g3"], cols["ln1_b3"], centre=True)
    NF = D_FF3 // P // 2
    with Phase(nc, "b3f") as ph:
        hid = ph.sb("hid", [P, NF, S])
        y = ph.sb("y", [P, DT, S])
        for half in range(2):
            b1 = cols["b1_3"][:, half * NF:(half + 1) * NF]
            project_rows(nc, f"b3_w1{half}", d["w1_3"][half * NF:(half + 1) * NF], DT, x_rows, NF,
                         act=lambda n, acc, tmp, i: nc.scalar.activation(tmp[:], acc[:], ACT.Relu, bias=b1[:, bass.ds(n, 1)]),
                         dve=lambda n, acc, tmp, i: nc.vector.tensor_tensor(hid[:, n, :], tmp[:], tmp[:], ALU.mult))
            if half == 0:
                project_rows(nc, "b3_w20", d["w2a_3"], NF, lambda k: hid[:, k, :], 8,
                             act=lambda n, acc, tmp, i: nc.scalar.activation(tmp[:], acc[:], ACT.Identity, bias=cols["b2_3"][:, bass.ds(n, 1)]),
                             dve=lambda n, acc, tmp, i: nc.vector.scalar_tensor_tensor(out=y[:, n, :], in0=x[:, n, :], scalar=ALPHA, in1=tmp[:],
                                                                                       op0=ALU.mult, op1=ALU.add))
            else:
                project_rows(nc, "b3_w21", d["w2b_3"], NF, lambda k: hid[:, k, :], 8,
                             dve=lambda n, acc, tmp, i: nc.vector.tensor_tensor(x[:, n, :], y[:, n, :], acc[:], ALU.add))
    norm_rows(nc, "b3_ln2", x, x, consts["ones"], cols["ln2_g3"], cols["ln2_b3"], centre=True)


L3_COLUMNS = {"ln_in_g": 8, "ln_in_b": 8, "g_alog": 1, "g_dt": 1, "g_taps": 60, "g_norm_g": 1, "n_norm_g": 1,
              "ln1_g3": 8, "ln1_b3": 8, "b1_3": 32, "b2_3": 8, "ln2_g3": 8, "ln2_b3": 8}
L3_SQUARES = ()


def third_arrays(a):
    import numpy as np
    w = a["w_in_3"][0]
    gqkv, gz, ga, gb, nq, nk, nv = np.split(w, np.cumsum([1536, 512, 8, 8, 512, 512]), axis=1)
    tiles = lambda g: gate_rows(g).reshape(DT, P, GATE_ROWS).transpose(1, 0, 2).reshape(1, P, DT * GATE_ROWS)
    i = np.arange(P)
    forward = np.stack([(i[:, None] >> (l + 1) == i[None, :] >> (l + 1)) & ((i[:, None] >> l) % 2 == 0) & ((i[None, :] >> l) % 2 == 1)
                        for l in range(LEVELS)])
    levels = np.concatenate([forward, forward.transpose(0, 2, 1)]).astype(np.float32).transpose(1, 0, 2).reshape(P, -1)
    eye = np.eye(8, dtype=np.float32)
    rpb = np.zeros((8, RPB_R, 2 * GRID), np.float32)
    rpb[:, :, GRID - WIN_C:GRID - WIN_C + RPB_C] = a["rpb_3"][0]
    q, k = np.arange(GRID)[:, None], np.arange(GRID)[None, :]
    start = np.clip(q - WIN_C // 2, 0, GRID - WIN_C)
    window = np.where((k >= start) & (k < start + WIN_C), BIG, -BIG).astype(np.float32)
    w2 = a["w2_3"][0]
    out = {"w_gqkv": rows_weight(gqkv), "w_gz": rows_weight(gz), "w_ga": tiles(ga), "w_gb": tiles(gb),
           "w_nq": rows_weight(nq), "w_nk": rows_weight(nk), "w_nv": tokens_weight(nv),
           "g_levels": levels, "l2_pick": np.tile(eye.reshape(1, 64), (P, 1)), "l2_spread": np.repeat(eye, P, axis=1),
           "rpb": rpb, "na_columns": np.tile(window, (2, RPB_R)), "w_out3": rows_weight(a["w_out_3"][0]),
           "w1_3": rows_weight(a["w1_3"][0]), "w2a_3": rows_weight(w2[0:2048]), "w2b_3": rows_weight(w2[2048:]),
           "reset128_3": np.broadcast_to((np.arange(S) % P != 0).astype(np.float32), (P, S))}
    columns = {"ln_in_g": column(a["ln_in_g_3"]), "ln_in_b": column(a["ln_in_b_3"]),
               "g_alog": gate_column(a["a_log_3"].reshape(8)), "g_dt": gate_column(a["dt_bias_3"].reshape(8)),
               "g_taps": a["conv_w_3"][0].reshape(TAPS, 12, P).transpose(2, 1, 0).reshape(P, 60),
               "g_norm_g": column(a["gdn_norm_g_3"]), "n_norm_g": np.tile(a["na_norm_g_3"].reshape(1, 64), (2, 1)).reshape(P, 1),
               "ln1_g3": column(a["ln1_g_3"]), "ln1_b3": column(a["ln1_b_3"]), "b1_3": column(a["b1_3"]), "b2_3": column(a["b2_3"]),
               "ln2_g3": column(a["ln2_g_3"]), "ln2_b3": column(a["ln2_b_3"])}
    return out, columns, {}

COLUMNS = {"pre_g": 8, "post_g": 8, "b_a2": 4, "b_norm_g": 8, "a_ln_g": 8, "a_ln_b": 8}
COLUMNS |= L2_COLUMNS | L3_COLUMNS
SQUARES = ("ones", "ident", "le", "gla_mask", "ones64") + tuple(L2_SQUARES) + tuple(L3_SQUARES)


def build_program(nc, d, layers=(1, 2, 3)):
    with Phase(nc, "all") as ph:
        x = ph.sb("x", [P, DT, S])
        squares = ph.sb("squares", [P, len(SQUARES), P])
        columns = ph.sb("columns", [P, sum(COLUMNS.values())])
        consts = {name: squares[:, i, :] for i, name in enumerate(SQUARES)}
        cols, at = {}, 0
        for name, n in COLUMNS.items():
            cols[name] = columns[:, at:at + n]
            at += n
        load_phase(nc, "consts", [(squares[:].rearrange("p n c -> p (n c)"), d["squares"]), (columns[:], d["columns"])])
        consts["le3"] = squares[:, SQUARES.index("le"):SQUARES.index("le") + 1, :].broadcast_to([P, 8, P])
        if 1 in layers:
            first_block(nc, d, consts, cols, x)
        else:
            load_phase(nc, "x", [(x[:, :, :], d["xT"].rearrange("p (t s) -> p t s", t=DT))])
        if 2 in layers:
            second_block(nc, d, consts, cols, x)
        if 3 in layers:
            third_block(nc, d, consts, cols, x)
        with Phase(nc, "store") as ps:
            stored = ps.sem("stored")
            with nc.Block() as block:

                @block.sync
                def _(sp):
                    sp.dma_start(d["outT"].rearrange("p (t s) -> p t s", t=DT), x[:, :, :]).then_inc(stored, 16)
                    sp.wait_ge(stored, 16)



def rows_weight(w):
    K, N = w.shape
    return w.reshape(K // P, P, N // P, P).transpose(2, 1, 0, 3).reshape(N // P, P, K)


def tokens_weight(w):
    K, N = w.shape
    return w.reshape(K // P, P, N).transpose(1, 0, 2).reshape(P, (K // P) * N)


def column(v):
    return v.reshape(-1, P).T


def causal_squares():
    import numpy as np
    i = np.arange(P)
    le = (i[:, None] <= i[None, :]).astype(np.float32)
    return {"ones": np.ones((P, P), np.float32), "ident": np.eye(P, dtype=np.float32), "le": le,
            "gla_mask": le * (i[:, None] // 64 == i[None, :] // 64),
            "ones64": (i[:, None] // 64 == i[None, :] // 64).astype(np.float32)}


def first_arrays(a):
    import numpy as np
    w = a["w_in"][0]
    cuts = np.cumsum([1024, 1024, 1024, 512, 512, 1024, 1024])
    au, av, ag, bq, bk, bv, bg, lr = np.split(w, cuts, axis=1)
    out = {"w_au": rows_weight(au), "w_agate": rows_weight(ag), "w_bgate": rows_weight(bg),
           "w_qk": rows_weight(w[:, 3072:4096]), "w_av": tokens_weight(av), "w_bv": tokens_weight(bv),
           "w_lr": lr.reshape(DT, P, 16).transpose(1, 0, 2).reshape(1, P, DT * 16),
           "w_a2": a["w_a2"][0].reshape(16, 4, P).transpose(1, 0, 2),
           "w_sT": a["a_w_s"][0].transpose(2, 0, 1).reshape(P, 8 * P),
           "b_s": a["a_b_s"].reshape(1, 8 * P), "w_out1": rows_weight(a["w_out"][0]),
           "reset64": np.broadcast_to((np.arange(S) % 64 != 0).astype(np.float32), (P, S))}
    columns = {"pre_g": column(a["pre_norm_g"]), "post_g": column(a["post_norm_g"]), "b_a2": column(a["b_a2"]),
               "b_norm_g": column(a["b_norm_g"]), "a_ln_g": column(a["a_ln_g"]), "a_ln_b": column(a["a_ln_b"])}
    return out, columns, {}


def arrays_of(a, layers=(1, 2, 3)):
    import numpy as np
    out = {"xT": a["x"][0].T.reshape(DT, P, S).transpose(1, 0, 2).reshape(P, DT * S)}
    columns, squares = {}, causal_squares()
    for n, arrays in ((1, first_arrays), (2, second_arrays), (3, third_arrays)):
        more, cols, sqs = arrays(a)
        if n in layers:
            out.update(more)
        columns.update(cols)
        squares.update(sqs)
    for name, n in COLUMNS.items():
        assert columns[name].shape == (P, n), (name, columns[name].shape)
    out["columns"] = np.concatenate([columns[name] for name in COLUMNS], axis=1)
    out["squares"] = np.concatenate([squares[name] for name in SQUARES], axis=1)
    return {name: np.ascontiguousarray(v) for name, v in out.items()}


def kernel(**inputs):
    import numpy as _np
    import concourse.bacc as _bacc
    from concourse import mybir as _mybir
    from concourse.bass_utils import run_bass_kernel_spmd as _run

    nc = _bacc.Bacc("TRN2", target_bir_lowering=False, num_devices=1)
    arrays = arrays_of({name: _np.asarray(v) for name, v in inputs.items()})
    d = {name: nc.dram_tensor(name, v.shape, _mybir.dt.from_np(v.dtype), kind="ExternalInput").ap()
         for name, v in arrays.items()}
    d["outT"] = nc.dram_tensor("outT", (P, DT * S), F32, kind="ExternalOutput").ap()
    build_program(nc, d)
    r = _run(nc, [arrays], core_ids=[0])
    got = r.results[0]["outT"].reshape(P, DT, S).transpose(2, 1, 0).reshape(1, S, DT * P)
    return _np.ascontiguousarray(got)
```

```python
import math
from contextlib import ExitStack

import concourse.bass as bass
from concourse import mybir

P = 128
S = 1024
HALF = 512
DT = 8
F32 = mybir.dt.float32
F32R = mybir.dt.float32r
ACT = mybir.ActivationFunctionType
ALU = mybir.AluOpType
AX_X = mybir.AxisListType.X
ROWS = "p (t s) -> p t s"
ALPHA = 2.0 ** 0.25
TAPS = 5
PAD = TAPS // 2
BIG = 1.0e30

PLACES = {}


class Phase:

    def __init__(self, nc, name, side="left"):
        self.nc, self.name, self.side, self.stack, self.sems = nc, name, side, ExitStack(), []

    def __enter__(self):
        self.stack.__enter__()
        return self

    def __exit__(self, *what):
        for sem in self.sems:
            self.nc.sync.sem_clear(sem)
        return self.stack.__exit__(*what)

    def sb(self, name, shape, dt=F32):
        got = self.stack.enter_context(self.nc.sbuf_tensor(f"{self.name}_{name}", shape, dt, side=self.side))
        size = 4 * math.prod(shape[1:])
        PLACES[got.name] = self.nc.sbuf_base - size if self.side == "left" else self.nc.sbuf_top
        return got

    def ps(self, name, shape, dt=F32):
        return self.stack.enter_context(self.nc.psum_tensor(f"{self.name}_{name}", shape, dt))

    def sem(self, name):
        self.sems.append(self.stack.enter_context(self.nc.semaphore(f"{self.name}_{name}")))
        return self.sems[-1]


def load_phase(nc, name, pairs):
    with Phase(nc, name) as ph:
        landed = [ph.sem(f"landed{i}") for i in range(len(pairs))]
        with nc.Block() as block:

            @block.sync
            def _(sp):
                for i, (dst, src) in enumerate(pairs):
                    sp.dma_start(dst, src).then_inc(landed[i], 16)
                for i in range(len(pairs)):
                    sp.wait_ge(landed[i], 16)


def project_rows(nc, name, w, KT, rhs, NB, act=None, dve=None, kp=P, m=P):
    with Phase(nc, name) as ph:
        wt = [ph.sb(f"w{i}", [kp, KT, m]) for i in range(2)]
        tmp = [ph.sb(f"tmp{i}", [m, S]) for i in range(2)]
        acc = [ph.ps(f"acc{i}", [m, S]) for i in range(2)]
        w_landed = [ph.sem(f"w_landed{i}") for i in range(2)]
        acc_ready = ph.sem("acc_ready")
        act_done = ph.sem("act_done")
        taken = ph.sem("taken")
        blocks2, odd = NB // 2, NB % 2
        last_reader_is_dve = dve is not None

        with nc.Block() as block:

            @block.sync
            def _(sp):
                def load(n, i):
                    sp.dma_start(wt[i][:], w[n].rearrange("k (t m) -> k t m", t=KT)).then_inc(w_landed[i], 16)

                load(0, 0)
                if NB > 1:
                    load(1, 1)
                if blocks2 > 1:
                    with sp.Fori(1, blocks2) as j:
                        for i in range(2):
                            sp.wait_ge(acc_ready, 2 * j - 1 + i)
                            load(2 * j + i, i)
                if odd and NB > 1:
                    sp.wait_ge(acc_ready, NB - 2)
                    load(NB - 1, 0)

            @block.tensor
            def _(pe):
                def product(n, i, round_):
                    pe.wait_ge(w_landed[i], 16 * round_ + 16)
                    pe.wait_ge(taken, n + 1)
                    for k in range(KT):
                        for half in range(2):
                            cols = slice(half * HALF, (half + 1) * HALF)
                            last = nc.tensor.matmul(acc[i][:, cols], wt[i][:, k, :], rhs(k)[:, cols],
                                                    start=(k == 0), stop=(k == KT - 1))
                    last.then_inc(acc_ready, 1)

                if blocks2:
                    with pe.Fori(0, blocks2) as j:
                        for i in range(2):
                            product(2 * j + i, i, j)
                if odd:
                    product(NB - 1, 0, blocks2)

            if act is not None:
                @block.scalar
                def _(se):
                    if not last_reader_is_dve:
                        se.sem_inc(taken, 2)

                    def take(n, i):
                        se.wait_ge(acc_ready, n + 1)
                        if last_reader_is_dve:
                            se.wait_ge(taken, n + 1)
                        act(n, acc[i], tmp[i], i).then_inc(act_done if last_reader_is_dve else taken, 1)

                    if blocks2:
                        with se.Fori(0, blocks2) as j:
                            for i in range(2):
                                take(2 * j + i, i)
                    if odd:
                        take(NB - 1, 0)

            if last_reader_is_dve:
                @block.vector
                def _(ve):
                    ve.sem_inc(taken, 2)

                    def take(n, i):
                        ve.wait_ge(act_done if act is not None else acc_ready, n + 1)
                        last = dve(n, acc[i], tmp[i], i)
                        if last is None:
                            ve.drain().then_inc(taken, 1)
                        else:
                            last.then_inc(taken, 1)

                    if blocks2:
                        with ve.Fori(0, blocks2) as j:
                            for i in range(2):
                                take(2 * j + i, i)
                    if odd:
                        take(NB - 1, 0)


def project_tokens(nc, name, w, N, src, act):
    with Phase(nc, name) as ph:
        wt = ph.sb("w", [P, DT, N])
        stage = [ph.sb(f"stage{i}", [P, DT, P]) for i in range(2)]
        acc = [ph.ps(f"acc{i}", [P, N]) for i in range(2)]
        w_landed = [ph.sem(f"w_landed{k}") for k in range(DT)]
        staged = ph.sem("staged")
        acc_ready = ph.sem("acc_ready")
        taken = ph.sem("taken")
        w3 = w.rearrange("p (t n) -> p t n", t=DT)

        with nc.Block() as block:

            @block.sync
            def _(sp):
                for k in range(DT):
                    sp.dma_start(wt[:, k, :], w3[:, k, :]).then_inc(w_landed[k], 16)

            @block.gpsimd
            def _(pool):
                for i in range(2):
                    nc.gpsimd.tensor_copy(stage[i][:], src[:, :, i * P:(i + 1) * P]).then_inc(staged, 1)
                with pool.Fori(1, DT // 2) as j:
                    for i in range(2):
                        pool.wait_ge(acc_ready, 2 * j - 1 + i)
                        nc.gpsimd.tensor_copy(stage[i][:], tile_of(src, 2 * j + i)).then_inc(staged, 1)

            @block.tensor
            def _(pe):
                for k in range(DT):
                    pe.wait_ge(w_landed[k], 16)
                with pe.Fori(0, DT // 2) as j:
                    for i in range(2):
                        pe.wait_ge(staged, 2 * j + i + 1)
                        pe.wait_ge(taken, 2 * j + i + 1)
                        last = tile_product(nc, acc[i], stage[i], wt, N)
                        last.then_inc(acc_ready, 1)

            @block.scalar
            def _(se):
                se.sem_inc(taken, 2)
                with se.Fori(0, DT // 2) as j:
                    for i in range(2):
                        se.wait_ge(acc_ready, 2 * j + i + 1)
                        act(2 * j + i, acc[i]).then_inc(taken, 1)


def tile_of(src, n):
    return src[:].rearrange("p t (n c) -> p t n c", c=P)[:, :, n, :]


def tile_product(nc, acc, stage, wt, N):
    for k in range(DT):
        for a in range(0, N, HALF):
            cols = slice(a, min(a + HALF, N))
            last = nc.tensor.matmul(acc[:, cols], stage[:, k, :], wt[:, k, cols], start=(k == 0), stop=(k == DT - 1))
    return last


def norm_rows(nc, name, x, out, ones, g, b=None, centre=False, eps=1e-5, add=None):
    D = DT * P
    with Phase(nc, name) as ph:
        sq = [ph.sb(f"sq{i}", [P, S]) for i in range(2)]
        rstd = ph.sb("rstd", [P, S])
        addt = [ph.sb(f"add{i}", [P, S]) for i in range(2)] if add is not None else None
        total = ph.ps("total", [P, S])
        total_sq = ph.ps("total_sq", [P, S])
        summed = ph.sem("summed")
        centred = ph.sem("centred")
        squared = ph.sem("squared")
        sq_used = ph.sem("sq_used")
        std_ready = ph.sem("std_ready")
        scaled = ph.sem("scaled")
        add_landed = [ph.sem(f"add_landed{i}") for i in range(2)]
        added = ph.sem("added")
        with nc.Block() as block:

            @block.tensor
            def _(pe):
                if centre:
                    for k in range(DT):
                        for half in range(2):
                            cols = slice(half * HALF, (half + 1) * HALF)
                            last = nc.tensor.matmul(total[:, cols], ones, x[:, k, cols], start=(k == 0), stop=(k == DT - 1))
                    last.then_inc(summed, 1)
                for k in range(DT):
                    pe.wait_ge(squared, k + 1)
                    for half in range(2):
                        cols = slice(half * HALF, (half + 1) * HALF)
                        last = nc.tensor.matmul(total_sq[:, cols], ones, sq[k % 2][:, cols], start=(k == 0), stop=(k == DT - 1))
                    last.then_inc(sq_used, 1)

            @block.scalar
            def _(se):
                for k in range(DT):
                    if centre:
                        se.wait_ge(centred, k + 1)
                    if k >= 2:
                        se.wait_ge(sq_used, k - 1)
                    nc.scalar.activation(sq[k % 2][:], x[:, k, :], ACT.Square).then_inc(squared, 1)
                se.wait_ge(sq_used, DT)
                nc.scalar.activation(rstd[:], total_sq[:], ACT.Sqrt, scale=1.0 / D, bias=eps).then_inc(std_ready, 1)
                if b is not None:
                    for k in range(DT):
                        se.wait_ge(scaled, k + 1)
                        nc.scalar.activation(out[:, k, :], out[:, k, :], ACT.Identity, bias=b[:, k:k + 1])

            if add is not None:
                @block.sync
                def _(sp):
                    for k in range(DT):
                        if k >= 2:
                            sp.wait_ge(added, k - 1)
                        sp.dma_start(addt[k % 2][:], add.rearrange("p (t s) -> p t s", t=DT)[:, k, :]).then_inc(add_landed[k % 2], 16)

            @block.vector
            def _(ve):
                if centre:
                    ve.wait_ge(summed, 1)
                    for k in range(DT):
                        nc.vector.scalar_tensor_tensor(out=x[:, k, :], in0=total[:], scalar=-1.0 / D, in1=x[:, k, :],
                                                       op0=ALU.mult, op1=ALU.add).then_inc(centred, 1)
                ve.wait_ge(std_ready, 1)
                nc.vector.reciprocal(rstd[:], rstd[:])
                ve.drain()
                for k in range(DT):
                    nc.vector.scalar_tensor_tensor(out=out[:, k, :], in0=x[:, k, :], scalar=g[:, k:k + 1], in1=rstd[:],
                                                   op0=ALU.mult, op1=ALU.mult).then_inc(scaled, 1)
                    if add is not None:
                        ve.wait_ge(scaled, k + 1)
                        ve.wait_ge(add_landed[k % 2], 16 * (k // 2) + 16)
                        nc.vector.tensor_tensor(out[:, k, :], out[:, k, :], addt[k % 2][:], ALU.add).then_inc(added, 1)


class Pair:

    def __init__(self, ph, name, KT, within=None):
        self.hi = ph.sb(f"{name}_hi", [P, KT, S], F32R)
        if within is None:
            self.lo = ph.sb(f"{name}_lo", [P, KT, S], F32R)
        else:
            self.lo = ph.nc.alloc_sbuf_tensor_at(f"{ph.name}_{name}_lo", [P, KT, S], F32R, offset=PLACES[within.name])

    def rows(self, k):
        return self.hi[:, k, :], self.lo[:, k, :]


def split_rows(nc, name, x, pair, KT=DT):
    with Phase(nc, name) as ph:
        rounded = ph.sem("rounded")
        with nc.Block() as block:

            @block.scalar
            def _(se):
                for k in range(KT):
                    nc.scalar.activation(pair.hi[:, k, :], x[:, k, :], ACT.Copy).then_inc(rounded, 1)

            @block.vector
            def _(ve):
                for k in range(KT):
                    ve.wait_ge(rounded, k + 1)
                    nc.vector.tensor_tensor(pair.lo[:, k, :], x[:, k, :], pair.hi[:, k, :], ALU.subtract)


def join_rows(nc, name, pair, x, KT=DT):
    with Phase(nc, name):
        with nc.Block() as block:

            @block.vector
            def _(ve):
                for k in range(KT // 2):
                    nc.vector.tensor_tensor(x[:, k, :], pair.hi[:, k, :], pair.lo[:, k, :], ALU.add)

            @block.gpsimd
            def _(pool):
                for k in range(KT // 2, KT):
                    nc.gpsimd.tensor_tensor(x[:, k, :], pair.hi[:, k, :], pair.lo[:, k, :], ALU.add)


def project_pair(nc, name, w, KT, rhs, NB, act=None, dve=None, late=None, resid=None, pairs=False, more=None, pads=0):
    assert NB % 2 == 0 and NB >= 4
    with Phase(nc, name) as ph:
        raw = [ph.sb(f"raw{i}", [P, KT * P]) for i in range(2)]
        wh = [ph.sb(f"wh{i}", [P, KT * P], F32R) for i in range(2)]
        wl = [ph.sb(f"wl{i}", [P, KT * P], F32R) for i in range(2)]
        tmp = [ph.sb(f"tmp{i}", [P, S + 2 * pads]) for i in range(1 if pairs else 2)] if act is not None and dve is not None else [None] * 2
        tmp = tmp * 2 if pairs else tmp
        res = [ph.sb(f"res{i}", [P, S]) for i in range(2)] if resid is not None else [None] * 2
        if more is not None:
            more(ph)
        acc = [ph.ps(f"acc{i}", [P, S]) for i in range(2)]
        w_landed = [ph.sem(f"w_landed{i}") for i in range(2)]
        res_landed = [ph.sem(f"res_landed{i}") for i in range(2)]
        hi_done = ph.sem("hi_done")
        lo_done = ph.sem("lo_done")
        acc_ready = ph.sem("acc_ready")
        act_done = ph.sem("act_done")
        taken = ph.sem("taken")
        late_done = ph.sem("late_done")
        by_dve = dve is not None
        J = NB // 2

        with nc.Block() as block:

            @block.sync
            def _(sp):
                def load(j, i):
                    sp.dma_start(raw[i][:], w[2 * j + i]).then_inc(w_landed[i], 16)

                def load_resid(j, i):
                    sp.dma_start(res[i][:], resid.rearrange(ROWS, s=S)[:, 2 * j + i, :]).then_inc(res_landed[i], 16)

                for i in range(2):
                    load(0, i)
                    if resid is not None:
                        load_resid(0, i)
                with sp.Fori(0, J - 1) as j:
                    for i in range(2):
                        sp.wait_ge(lo_done, 2 * j + i + 1)
                        load(j + 1, i)
                        if resid is not None:
                            sp.wait_ge(taken, 2 * j + i + 3)
                            load_resid(j + 1, i)

            @block.tensor
            def _(pe):
                with pe.Fori(0, J) as j:
                    for i in range(2):
                        pe.wait_ge(lo_done, 2 * j + i + 1)
                        pe.wait_ge(taken, 2 * j + i + 1)
                        for k in range(KT):
                            xh, xl = rhs(k)
                            wk = slice(k * P, (k + 1) * P)
                            for half in range(2):
                                c = slice(half * HALF, (half + 1) * HALF)
                                nc.tensor.matmul(acc[i][:, c], wh[i][:, wk], xh[:, c], start=(k == 0), stop=False)
                                nc.tensor.matmul(acc[i][:, c], wh[i][:, wk], xl[:, c], start=False, stop=False)
                                last = nc.tensor.matmul(acc[i][:, c], wl[i][:, wk], xh[:, c], start=False, stop=(k == KT - 1))
                        last.then_inc(acc_ready, 1)

            @block.scalar
            def _(se):
                if not by_dve:
                    se.sem_inc(taken, 2)
                if late is not None:
                    se.sem_inc(late_done, 2)

                def high(j, i, first=False):
                    se.wait_ge(w_landed[i], 16 * j + 16)
                    if not first:
                        se.wait_ge(acc_ready, 2 * j + i - 1)
                    nc.scalar.activation(wh[i][:], raw[i][:], ACT.Copy).then_inc(hi_done, 1)

                def take(j, i):
                    n = 2 * j + i
                    if act is None or (pairs and i):
                        return
                    se.wait_ge(acc_ready, n + 1)
                    if by_dve:
                        se.wait_ge(taken, n + 2 if pairs else n + 1)
                    act(n, j, i, acc[i], tmp[i]).then_inc(act_done if by_dve else taken, 1)

                def end(n, i):
                    se.wait_ge(taken, n + 3)
                    late(n, i).then_inc(late_done, 1)

                high(0, 0, True)
                high(0, 1, True)
                take(0, 0)
                with se.Fori(0, J - 1) as j:
                    high(j + 1, 0)
                    take(j, 1)
                    if late is not None:
                        end(2 * j, 0)
                    high(j + 1, 1)
                    take(j + 1, 0)
                    if late is not None:
                        end(2 * j + 1, 1)
                take(J - 1, 1)
                if late is not None:
                    end(NB - 2, 0)
                    end(NB - 1, 1)

            @block.vector
            def _(ve):
                if by_dve:
                    ve.sem_inc(taken, 2)
                if pads:
                    for t in tmp:
                        nc.vector.memset(t[:, 0:pads], 0.0)
                        nc.vector.memset(t[:, pads + S:], 0.0)
                    ve.drain()

                def low(j, i):
                    ve.wait_ge(hi_done, 2 * j + i + 1)
                    nc.vector.tensor_tensor(wl[i][:], raw[i][:], wh[i][:], ALU.subtract).then_inc(lo_done, 1)

                def take(j, i):
                    n = 2 * j + i
                    if not by_dve:
                        return
                    if act is None or (pairs and i):
                        ve.wait_ge(acc_ready, n + 1)
                    else:
                        ve.wait_ge(act_done, j + 1 if pairs else n + 1)
                    if resid is not None:
                        ve.wait_ge(res_landed[i], 16 * j + 16)
                    if late is not None:
                        ve.wait_ge(late_done, n + 1)
                    if pairs and i == 0:
                        ve.sem_inc(taken, 1)
                    else:
                        dve(n, j, i, acc[i], tmp[i], res[i])
                        ve.drain().then_inc(taken, 1)

                low(0, 0)
                low(0, 1)
                take(0, 0)
                with ve.Fori(0, J - 1) as j:
                    low(j + 1, 0)
                    take(j, 1)
                    low(j + 1, 1)
                    take(j + 1, 0)
                take(J - 1, 1)


def conv_pair(nc, name, w, NB, rhs, taps_of, out, bias_of=None):
    conv = []

    def more(ph):
        conv.extend(ph.sb(f"conv{i}", [P, S]) for i in range(2))

    def copy(n, j, i, acc, tmp):
        return nc.scalar.activation(tmp[:, PAD:PAD + S], acc[:], ACT.Copy)

    def convolve(n, j, i, acc, tmp, res):
        nc.vector.tensor_scalar(conv[i][:], tmp[:, 0:S], taps_of(n, 0), None, ALU.mult)
        for tap in range(1, TAPS):
            nc.vector.drain()
            nc.vector.scalar_tensor_tensor(out=conv[i][:], in0=tmp[:, tap:tap + S], scalar=taps_of(n, tap), in1=conv[i][:],
                                           op0=ALU.mult, op1=ALU.add)

    def silu(n, i):
        if bias_of is None:
            return nc.scalar.activation(out[:, n, :], conv[i][:], ACT.Silu)
        return nc.scalar.activation(out[:, n, :], conv[i][:], ACT.Silu, bias=bias_of(n))

    project_pair(nc, name, w, DT, rhs, NB, act=copy, dve=convolve, late=silu, more=more, pads=PAD)


def put_pair(nc, pair, k, x):
    nc.vector.tensor_copy(pair.hi[:, k, :], x[:])
    nc.vector.drain()
    nc.vector.tensor_tensor(pair.lo[:, k, :], x[:], pair.hi[:, k, :], ALU.subtract)


def add_residual(nc, out, pair, k, more):
    nc.vector.scalar_tensor_tensor(out=out, in0=pair.lo[:, k, :], scalar=ALPHA, in1=more, op0=ALU.mult, op1=ALU.add)
    nc.vector.drain()
    nc.vector.scalar_tensor_tensor(out=out, in0=pair.hi[:, k, :], scalar=ALPHA, in1=out, op0=ALU.mult, op1=ALU.add)


def out_projection(nc, name, w, mix, x):
    with Phase(nc, name + "p") as ph:
        pair = Pair(ph, "mix", DT, within=mix)
        split_rows(nc, name + "_split", mix, pair)
        project_pair(nc, name, w, DT, pair.rows, 8,
                     dve=lambda n, j, i, acc, tmp, res: nc.vector.scalar_tensor_tensor(
                         out=x[:, n, :], in0=x[:, n, :], scalar=ALPHA, in1=acc[:], op0=ALU.mult, op1=ALU.add))

GLA_H, GLA_DK, GLA_DV, GLA_C = 4, 128, 256, 64


def gated_linear_attention(nc, consts, cols, logits, qk, v, out):
    NCH = S // GLA_C
    qscale = GLA_DK ** -0.5
    with Phase(nc, "gla") as ph:
        low = ph.sb("low", [P, S])
        bc = ph.sb("bc", [P, S])
        kd = ph.sb("kd", [P, S])
        ke = ph.sb("ke", [P, S])
        qe = ph.sb("qe", [P, S])
        qb = ph.sb("qb", [P, S])
        soft, dref, dlast = qb, ke, kd
        decay = ph.sb("decay", [P, NCH])
        kdt = ph.sb("kdt", [P, DT, P])
        vh = ph.sb("vh", [P, DT, GLA_DV])
        state = ph.sb("state", [P, NCH + 1, GLA_DV])
        probs = ph.sb("probs", [P, 2, P])
        junk = low[:, 0:GLA_DV]
        ss = ph.sb("ss", [P, 2])
        rstd = ph.sb("rstd", [P, 2])
        on = low[:, 2 * GLA_DV:4 * GLA_DV].rearrange("p (a c) -> p a c", a=2)
        turned = ph.ps("turned", [P, S])
        sc = [turned[:, 0:P], turned[:, HALF:HALF + P]]
        kv = [ph.ps(f"kv{i}", [P, HALF]) for i in range(2)]
        o = [ph.ps(f"o{i}", [P, HALF]) for i in range(2)]
        ot = [ph.ps(f"ot{i}", [P, 4, P]) for i in range(2)]
        soft_ready = ph.sem("soft_ready")
        cum_ready = ph.sem("cum_ready")
        exp_ready = ph.sem("exp_ready")
        derived = ph.sem("derived")
        turned_ready = ph.sem("turned_ready")
        kdt_ready = ph.sem("kdt_ready")
        v_staged = ph.sem("v_staged")
        head_free = ph.sem("head_free")
        kv_ready = ph.sem("kv_ready")
        state_done = ph.sem("state_done")
        sc_ready = ph.sem("sc_ready")
        masked = ph.sem("masked")
        o_ready = ph.sem("o_ready")
        std_ready = ph.sem("std_ready")
        on_done = ph.sem("on_done")
        ot_ready = ph.sem("ot_ready")
        ot_done = ph.sem("ot_done")
        ident, mask, resets = consts["ident"], consts["gla_mask"], consts["reset64"]
        ba, bg = cols["b_a2"], cols["b_norm_g"]

        def tile(x, p):
            return x[:, p * P:(p + 1) * P]

        with nc.Block() as block:

            @block.scalar
            def _(se):
                with se.Fori(0, GLA_H) as h:
                    se.wait_ge(head_free, h + 1)
                    nc.scalar.activation(soft[:], logits[:, h, :], ACT.Abs, bias=ba[:, bass.ds(h, 1)])
                    se.drain()
                    nc.scalar.activation(soft[:], soft[:], ACT.Exp, scale=-1.0)
                    se.drain()
                    nc.scalar.activation(soft[:], soft[:], ACT.Ln, bias=1.0).then_inc(soft_ready, 1)
                    se.wait_ge(cum_ready, h + 1)
                    for dst, src, scale in ((kd, dlast, 1.0), (qe, dref, 1.0), (ke, dref, -1.0), (qb, bc, 1.0)):
                        nc.scalar.activation(dst[:], src[:], ACT.Exp, scale=scale / 16.0).then_inc(exp_ready, 1)
                    last_b = bc[:].rearrange("p (n c) -> p n c", c=GLA_C)[:, :, GLA_C - 1]
                    nc.scalar.activation(decay[:], last_b, ACT.Exp, scale=1.0 / 16.0).then_inc(exp_ready, 1)
                    se.wait_ge(turned_ready, h + 1)
                    nc.scalar.activation(kdt[:].rearrange("p t c -> p (t c)"), turned[:], ACT.Copy).then_inc(kdt_ready, 1)
                    for p in range(DT + 1):
                        if p < DT:
                            se.wait_ge(o_ready, DT * h + p + 1)
                            nc.scalar.activation(junk, o[p % 2][:, 0:GLA_DV], ACT.Square, scale=GLA_DV ** -0.5,
                                                 accum_out=ss[:, p % 2:p % 2 + 1])
                            se.drain()
                            nc.scalar.activation(rstd[:, p % 2:p % 2 + 1], ss[:, p % 2:p % 2 + 1], ACT.Sqrt,
                                                 bias=1e-6).then_inc(std_ready, 1)
                        if p >= 1:
                            q = p - 1
                            se.wait_ge(ot_ready, DT * h + q + 1)
                            for i in range(2):
                                last = nc.scalar.activation(out[:, 2 * h + i, q * P:(q + 1) * P], ot[q % 2][:, i, :],
                                                            ACT.Copy, scale=bg[:, bass.ds(2 * h + i, 1)])
                            last.then_inc(ot_done, 1)

            @block.vector
            def _(ve):
                nc.vector.memset(state[:, 0, :], 0.0)
                with ve.Fori(0, GLA_H) as h:
                    ve.wait_ge(head_free, h + 1)
                    nc.vector.tensor_scalar(low[:], logits[:, h, :], ba[:, bass.ds(h, 1)], 0.0, ALU.add, ALU.min)
                    ve.drain()
                    ve.wait_ge(soft_ready, h + 1)
                    nc.vector.tensor_tensor(low[:], low[:], soft[:], ALU.subtract)
                    ve.drain()
                    nc.vector.tensor_tensor_scan(bc[:], resets, low[:], 0.0, ALU.mult, ALU.add)
                    ve.drain()
                    b3 = bc[:].rearrange("p (n c) -> p n c", c=GLA_C)
                    nc.vector.tensor_tensor(dref[:].rearrange("p (n c) -> p n c", c=GLA_C), b3,
                                            b3[:, :, GLA_C // 2 - 1:GLA_C // 2].broadcast_to([P, NCH, GLA_C]), ALU.subtract)
                    nc.vector.tensor_tensor(dlast[:].rearrange("p (n c) -> p n c", c=GLA_C),
                                            b3[:, :, GLA_C - 1:GLA_C].broadcast_to([P, NCH, GLA_C]), b3,
                                            ALU.subtract).then_inc(cum_ready, 1)
                    for i, (dst, of_q) in enumerate(((kd, 0), (qe, 1), (ke, 0), (qb, 1))):
                        ve.wait_ge(exp_ready, 5 * h + i + 1)
                        nc.vector.scalar_tensor_tensor(out=dst[:], in0=qk[:, (h if of_q else h + GLA_H), :],
                                                       scalar=(qscale if of_q else 1.0), in1=dst[:],
                                                       op0=ALU.mult, op1=ALU.mult).then_inc(derived, 1)
                    ve.wait_ge(exp_ready, 5 * h + 5)
                    for p in range(DT + 1):
                        if p < DT:
                            ve.wait_ge(kv_ready, DT * h + p + 1)
                            for c in (2 * p, 2 * p + 1):
                                if c:
                                    ve.wait_ge(state_done, NCH * h + c)
                                nc.vector.scalar_tensor_tensor(out=state[:, c + 1, :], in0=state[:, c, :],
                                                               scalar=decay[:, c:c + 1], in1=kv[c % 2][:, 0:GLA_DV],
                                                               op0=ALU.mult, op1=ALU.add).then_inc(state_done, 1)
                            ve.wait_ge(sc_ready, DT * h + p + 1)
                            if p >= 2:
                                ve.wait_ge(o_ready, DT * h + p - 1)
                            nc.vector.scalar_tensor_tensor(out=probs[:, p % 2, :], in0=sc[p % 2], scalar=3.0e38,
                                                           in1=mask, op0=ALU.min, op1=ALU.mult).then_inc(masked, 1)
                        if p >= 1:
                            q = p - 1
                            ve.wait_ge(std_ready, DT * h + q + 1)
                            nc.vector.reciprocal(rstd[:, q % 2:q % 2 + 1], rstd[:, q % 2:q % 2 + 1])
                            ve.drain()
                            if q >= 2:
                                ve.wait_ge(ot_ready, DT * h + q - 1)
                            nc.vector.tensor_scalar(on[:, q % 2, :], o[q % 2][:, 0:GLA_DV], rstd[:, q % 2:q % 2 + 1], None,
                                                    ALU.mult).then_inc(on_done, 1)

            @block.gpsimd
            def _(pool):
                with pool.Fori(0, GLA_H) as h:
                    pool.wait_ge(head_free, h + 1)
                    nc.gpsimd.tensor_copy(vh[:], v[:].rearrange("p t (h d) -> p t h d", h=GLA_H)[:, :, h, :]).then_inc(v_staged, 1)

            @block.tensor
            def _(pe):
                pe.sem_inc(head_free, 1)
                with pe.Fori(0, GLA_H) as h:
                    pe.wait_ge(derived, 4 * h + 1)
                    for p in range(DT):
                        last = nc.tensor.transpose(tile(turned, p), tile(kd, p), ident)
                    last.then_inc(turned_ready, 1)
                    pe.wait_ge(kdt_ready, h + 1)
                    pe.wait_ge(v_staged, h + 1)
                    pe.wait_ge(derived, 4 * h + 4)
                    for p in range(DT + 2):
                        if p < DT:
                            if p >= 1:
                                pe.wait_ge(state_done, NCH * h + 2 * p)
                            for c in range(2):
                                rows = slice(c * GLA_C, (c + 1) * GLA_C)
                                last = nc.tensor.matmul(kv[c][:, 0:GLA_DV], kdt[rows, p, :], vh[rows, p, :], start=True, stop=True)
                            last.then_inc(kv_ready, 1)
                            if p >= 2:
                                pe.wait_ge(masked, DT * h + p - 1)
                            nc.tensor.matmul(sc[p % 2], tile(ke, p), tile(qe, p), start=True, stop=True).then_inc(sc_ready, 1)
                        if 1 <= p <= DT:
                            q = p - 1
                            pe.wait_ge(masked, DT * h + q + 1)
                            if q >= 2:
                                pe.wait_ge(on_done, DT * h + q - 1)
                            nc.tensor.matmul(o[q % 2][:, 0:GLA_DV], probs[:, q % 2, :], vh[:, q, :], start=True, stop=False, skip_group_check=True)
                            for c in range(2):
                                if q or c:
                                    pe.wait_ge(state_done, NCH * h + 2 * q + c)
                                rows = slice(c * GLA_C, (c + 1) * GLA_C)
                                at = q * P + c * GLA_C
                                last = nc.tensor.matmul(o[q % 2][rows, 0:GLA_DV], qb[:, at:at + GLA_C], state[:, 2 * q + c, :],
                                                        start=False, stop=(c == 1), skip_group_check=True)
                            last.then_inc(o_ready, 1)
                        if p >= 2:
                            q = p - 2
                            pe.wait_ge(on_done, DT * h + q + 1)
                            if q >= 2:
                                pe.wait_ge(ot_done, DT * h + q - 1)
                            for i in range(2):
                                last = nc.tensor.transpose(ot[q % 2][:, i, :], on[:, q % 2, i * P:(i + 1) * P], ident)
                            last.then_inc(ot_ready, 1)
                    pe.drain().then_inc(head_free, 1)


def spatial_gating(nc, consts, cols, w_v, h, w_s, b_s, out):
    G = 8
    with Phase(nc, "sgu") as ph:
        wt = ph.sb("w", [P, DT, S])
        ws = ph.sb("ws", [P, G, P])
        bs = ph.sb("bs", [P, G, P])
        shift = ph.sb("shift", [P, G, P])
        stage = [ph.sb(f"stage{i}", [P, DT, P]) for i in range(2)]
        gv = [ph.sb(f"gv{i}", [P, S]) for i in range(2)]
        stats = ph.sb("stats", [P, 2, 6])
        mv = ph.sb("mv", [P, 2, 2])
        rstd = ph.sb("rstd", [P, 2])
        acc = [ph.ps(f"acc{i}", [P, S]) for i in range(2)]
        mix = [ph.ps(f"mix{i}", [P, S]) for i in range(2)]
        w_landed = [ph.sem(f"w_landed{k}") for k in range(DT)]
        ws_landed, bs_landed = ph.sem("ws_landed"), ph.sem("bs_landed")
        ws_masked = ph.sem("ws_masked")
        sums_ready = ph.sem("sums_ready")
        staged = ph.sem("staged")
        acc_ready = ph.sem("acc_ready")
        gelu_done = ph.sem("gelu_done")
        mv_ready = ph.sem("mv_ready")
        std_ready = ph.sem("std_ready")
        normed = ph.sem("normed")
        mixed = ph.sem("mixed")
        mix_taken = ph.sem("mix_taken")
        g, b = cols["a_ln_g"], cols["a_ln_b"]
        w3 = w_v.rearrange("p (t n) -> p t n", t=DT)

        with nc.Block() as block:

            @block.sync
            def _(sp):
                sp.dma_start(ws[:].rearrange("p g t -> p (g t)"), w_s).then_inc(ws_landed, 16)
                sp.dma_start(bs[:].rearrange("p g t -> p (g t)"), b_s.broadcast_to([P, G * P])).then_inc(bs_landed, 16)
                for k in range(DT):
                    sp.dma_start(wt[:, k, :], w3[:, k, :]).then_inc(w_landed[k], 16)

            @block.gpsimd
            def _(pool):
                for i in range(2):
                    nc.gpsimd.tensor_copy(stage[i][:], h[:, :, i * P:(i + 1) * P]).then_inc(staged, 1)

                with pool.Fori(1, DT // 2) as j:
                    for i in range(2):
                        pool.wait_ge(acc_ready, 2 * j - 1 + i)
                        nc.gpsimd.tensor_copy(stage[i][:], tile_of(h, 2 * j + i)).then_inc(staged, 1)

            @block.tensor
            def _(pe):
                pe.wait_ge(ws_masked, 1)
                for half in range(2):
                    last = nc.tensor.matmul(mix[0][:, half * HALF:(half + 1) * HALF], consts["ones"],
                                            ws[:].rearrange("p g t -> p (g t)")[:, half * HALF:(half + 1) * HALF],
                                            start=True, stop=True)
                last.then_inc(sums_ready, 1)
                for k in range(DT):
                    pe.wait_ge(w_landed[k], 16)

                def project(n, i, first=False):
                    pe.wait_ge(staged, n + 1)
                    if not first:
                        pe.wait_ge(gelu_done, n - 1)
                    tile_product(nc, acc[i], stage[i], wt, S).then_inc(acc_ready, 1)

                def mixing(n, i, first=False):
                    pe.wait_ge(normed, n + 1)
                    pe.wait_ge(mix_taken, n + 1 if first else n)
                    for gr in range(G):
                        last = nc.tensor.matmul(mix[i][:, gr * P:(gr + 1) * P], gv[i][:, gr * P:(gr + 1) * P], ws[:, gr, :],
                                                start=True, stop=True)
                    last.then_inc(mixed, 1)

                project(0, 0, True)
                project(1, 1, True)
                mixing(0, 0, True)
                with pe.Fori(1, DT // 2) as j:
                    project(2 * j, 0)
                    mixing(2 * j - 1, 1)
                    project(2 * j + 1, 1)
                    mixing(2 * j, 0)
                mixing(DT - 1, 1)

            @block.scalar
            def _(se):
                def gelu(n, i, first=False):
                    se.wait_ge(acc_ready, n + 1)
                    if not first:
                        se.wait_ge(mixed, n - 1)
                    nc.scalar.activation(gv[i][:], acc[i][:], ACT.Gelu).then_inc(gelu_done, 1)

                def std(n, i):
                    se.wait_ge(mv_ready, n + 1)
                    nc.scalar.activation(rstd[:, i:i + 1], mv[:, i, 1:2], ACT.Sqrt, bias=1e-6).then_inc(std_ready, 1)

                gelu(0, 0, True)
                std(0, 0)
                gelu(1, 1, True)
                std(1, 1)
                with se.Fori(1, DT // 2) as j:
                    for i in range(2):
                        gelu(2 * j + i, i)
                        std(2 * j + i, i)

            @block.vector
            def _(ve):
                ve.wait_ge(ws_landed, 16)
                nc.vector.tensor_tensor(ws[:], ws[:], consts["le3"], ALU.mult).then_inc(ws_masked, 1)
                ve.wait_ge(sums_ready, 1)
                ve.wait_ge(bs_landed, 16)
                for gr in range(G):
                    last = nc.vector.scalar_tensor_tensor(out=shift[:, gr, :], in0=mix[0][:, gr * P:(gr + 1) * P],
                                                          scalar=b[:, gr:gr + 1], in1=bs[:, gr, :], op0=ALU.mult, op1=ALU.add)
                last.then_inc(mix_taken, 1)
                ve.drain()

                def norm(n, i):
                    ve.wait_ge(gelu_done, n + 1)
                    for half in range(2):
                        nc.vector.bn_stats(stats[:, half, :], gv[i][:, half * HALF:(half + 1) * HALF])
                    ve.drain()
                    nc.vector.bn_aggr(mv[:, i, :], stats[:].rearrange("p a b -> p (a b)")).then_inc(mv_ready, 1)
                    ve.wait_ge(std_ready, n + 1)
                    nc.vector.reciprocal(rstd[:, i:i + 1], rstd[:, i:i + 1])
                    ve.drain()
                    nc.vector.tensor_scalar(gv[i][:], gv[i][:], mv[:, i, 0:1], rstd[:, i:i + 1],
                                            ALU.subtract, ALU.mult).then_inc(normed, 1)

                def take(n, i):
                    ve.wait_ge(mixed, n + 1)
                    for gr in range(G):
                        last = nc.vector.scalar_tensor_tensor(
                            out=out[:].rearrange("p t (n c) -> p t n c", c=P)[:, gr, n, :], in0=mix[i][:, gr * P:(gr + 1) * P],
                            scalar=g[:, gr:gr + 1], in1=shift[:, gr, :], op0=ALU.mult, op1=ALU.add)
                    last.then_inc(mix_taken, 1)

                norm(0, 0)
                with ve.Fori(0, DT // 2 - 1) as j:
                    norm(2 * j + 1, 1)
                    take(2 * j, 0)
                    norm(2 * j + 2, 0)
                    take(2 * j + 1, 1)
                norm(DT - 1, 1)
                take(DT - 2, 0)
                take(DT - 1, 1)


def first_block(nc, d, consts, cols, x):
    ones = consts["ones"]
    with Phase(nc, "b1") as ph:
        attn = ph.sb("attn", [P, DT, S])
        with Phase(nc, "b1h") as ph2:
            h = ph2.sb("h", [P, DT, S])
            resets = ph2.sb("reset64", [P, S])
            load_phase(nc, "b1_x", [(x[:, :, :], d["xT"].rearrange(ROWS, t=DT)), (resets[:], d["reset64"])])
            norm_rows(nc, "b1_pre", x, h, ones, cols["pre_g"], eps=1e-6)
            with Phase(nc, "b1a") as pa:
                v = x
                qk = pa.sb("qk", [P, 8, S])
                logits = pa.sb("logits", [P, 4, S])
                with Phase(nc, "b1lr") as pl:
                    lr = pl.sb("lr", [16, S])
                    project_rows(nc, "b1_lr", d["w_lr"], DT, lambda k: h[:, k, :], 1, m=16,
                                 act=lambda n, acc, tmp, i: nc.scalar.activation(lr[:], acc[:], ACT.Copy))
                    project_rows(nc, "b1_log", d["w_a2"], 1, lambda k: lr[:], 4, kp=16,
                                 act=lambda n, acc, tmp, i: nc.scalar.activation(logits[:, n, :], acc[:], ACT.Copy))
                project_tokens(nc, "b1_v", d["w_bv"], S, h,
                               act=lambda n, acc: nc.scalar.activation(v[:, n, :], acc[:], ACT.Copy))
                project_rows(nc, "b1_qk", d["w_qk"], DT, lambda k: h[:, k, :], 8,
                             act=lambda n, acc, tmp, i: nc.scalar.activation(qk[:, n, :], acc[:], ACT.Copy))
                gated_linear_attention(nc, dict(consts, reset64=resets[:]), cols, logits, qk, v, attn)
            gate = x
            spatial_gating(nc, consts, cols, d["w_av"], h, d["w_sT"], d["b_s"], gate)
            with Phase(nc, "b1b") as pb:
                pair = Pair(pb, "h", DT)
                split_rows(nc, "b1_split", h, pair)

                def times(dst):
                    return lambda n, j, i, acc, tmp, res: nc.vector.tensor_tensor(dst[:, n, :], dst[:, n, :], tmp[:], ALU.mult)

                for name, dst, func in (("w_bgate", attn, ACT.Silu), ("w_au", gate, ACT.Gelu), ("w_agate", gate, ACT.Silu)):
                    project_pair(nc, "b1_" + name, d[name], DT, pair.rows, 8, dve=times(dst),
                                 act=lambda n, j, i, acc, tmp: nc.scalar.activation(tmp[:], acc[:], func))
        with Phase(nc, "b1c") as pc:
            y = pc.sb("y", [P, DT, S])
            pair = Pair(pc, "m", DT)
            split_rows(nc, "b1_split_a", gate, pair)
            project_pair(nc, "b1_out_a", d["w_out1a"], DT, pair.rows, 8,
                         act=lambda n, j, i, acc, tmp: nc.scalar.activation(y[:, n, :], acc[:], ACT.Copy))
            split_rows(nc, "b1_split_b", attn, pair)
            project_pair(nc, "b1_out_b", d["w_out1b"], DT, pair.rows, 8,
                         dve=lambda n, j, i, acc, tmp, res: nc.vector.tensor_tensor(y[:, n, :], y[:, n, :], acc[:], ALU.add))
            norm_rows(nc, "b1_post", y, x, ones, cols["post_g"], eps=1e-6, add=d["xT"])

M_H, M_DH = 4, 128
GQ_D, GQ_KV = 64, 2
D_FF2 = 2816
FFN_CUTS2 = (8, 8, 6)
GATE_ROWS = 36


def mlstm_rows(nc, d, gi, gf, cols, consts, dram, col_out, name="mrow"):
    R = GATE_ROWS
    NCH = DT
    with Phase(nc, name) as ph:
        soft = ph.sb("soft", [R, S])
        lf = ph.sb("lf", [R, S])
        b = ph.sb("b", [R, S])
        m = ph.sb("m", [R, S])
        rel = ph.sb("rel", [R, S])
        quant = [ph.sb(f"quant{i}", [R, S]) for i in range(4)]
        before = ph.sb("before", [R, NCH])
        ends = ph.sb("ends", [R, 3, NCH])
        decay = ph.sb("decay", [R, NCH])
        turned = [ph.ps(f"turned{i}", [P, DT, R]) for i in range(4)]
        soft_ready, lf_ready = ph.sem("soft_ready"), ph.sem("lf_ready")
        biased = ph.sem("biased")
        args_ready = ph.sem("args_ready")
        exps_done = ph.sem("exps_done")
        turned_ready = ph.sem("turned_ready")
        stored = [ph.sem(f"stored{i}") for i in range(2)]
        bi, bf = cols["m_bi"], cols["m_bf"]
        F, B = slice(0, M_H), slice(32, 32 + M_H)

        def chunks(x):
            return x.rearrange("p (n c) -> p n c", c=P)

        with nc.Block() as block:

            @block.scalar
            def _(se):
                nc.scalar.activation(soft[:], gf[:], ACT.Abs, bias=bf[0:R, :])
                se.drain()
                nc.scalar.activation(soft[:], soft[:], ACT.Exp, scale=-1.0)
                se.drain()
                nc.scalar.activation(soft[:], soft[:], ACT.Ln, bias=1.0).then_inc(soft_ready, 1)
                se.wait_ge(args_ready, 1)
                for i in (1, 2):
                    nc.scalar.activation(quant[i][:], quant[i][:], ACT.Exp)
                nc.scalar.activation(quant[3][:], m[:], ACT.Exp, scale=-1.0)
                nc.scalar.activation(decay[:], decay[:], ACT.Exp)
                se.drain().then_inc(exps_done, 1)
                for i in range(4):
                    se.wait_ge(turned_ready, i + 1)
                    nc.scalar.activation(col_out[:, i, :, :], turned[i][:], ACT.Copy, scale=(M_DH ** -0.5 if i == 1 else 1.0))

            @block.vector
            def _(ve):
                nc.vector.tensor_scalar(gi[:], gi[:], bi[0:R, :], None, ALU.add)
                nc.vector.tensor_scalar(lf[:], gf[:], bf[0:R, :], 0.0, ALU.add, ALU.min)
                nc.vector.memset(b[:], 0.0)
                nc.vector.memset(m[:], 0.0)
                nc.vector.memset(before[:], 0.0)
                nc.vector.memset(ends[:], 0.0)
                ve.drain()
                ve.wait_ge(soft_ready, 1)
                nc.vector.tensor_tensor(lf[:], lf[:], soft[:], ALU.subtract)
                ve.drain()
                nc.vector.tensor_tensor_scan(b[F, :], consts["reset128"][F, :], lf[F, :], 0.0, ALU.mult, ALU.add)
                nc.vector.tensor_tensor_scan(b[B, ::-1], consts["reset128"][B, :], lf[B, ::-1], 0.0, ALU.mult, ALU.add)
                nc.vector.tensor_tensor_scan(m[F, :], lf[F, :], gi[F, :], 0.0, ALU.add, ALU.max)
                nc.vector.tensor_tensor_scan(m[B, ::-1], lf[B, ::-1], gi[B, ::-1], 0.0, ALU.add, ALU.max)
                ve.drain()
                b3, m3 = chunks(b[:]), chunks(m[:])
                nc.vector.tensor_copy(ends[F, 0, :], b3[F, :, P - 1])
                nc.vector.tensor_copy(ends[B, 0, :], b3[B, :, 0])
                nc.vector.tensor_copy(ends[F, 1, :], m3[F, :, P - 1])
                nc.vector.tensor_copy(ends[B, 1, :], m3[B, :, 0])
                nc.vector.tensor_copy(before[F, 1:NCH], m3[F, 0:NCH - 1, P - 1])
                nc.vector.tensor_copy(before[B, 0:NCH - 1], m3[B, 1:NCH, 0])
                nc.vector.tensor_tensor(rel[:], b[:], m[:], ALU.subtract)
                nc.vector.tensor_tensor(quant[0][:], gi[:], b[:], ALU.subtract)
                ve.drain()
                nc.vector.tensor_tensor(ends[:, 2, :], ends[:, 0, :], ends[:, 1, :], ALU.subtract)
                ve.drain()
                nc.vector.tensor_tensor(decay[:], ends[:, 2, :], before[:], ALU.add)
                nc.vector.tensor_tensor(chunks(quant[1][:]), chunks(rel[:]), before[:, :, None].broadcast_to([R, NCH, P]), ALU.add)
                nc.vector.tensor_tensor(chunks(quant[2][:]), chunks(quant[0][:]), ends[:, 2, :, None].broadcast_to([R, NCH, P]), ALU.add)
                ve.drain().then_inc(args_ready, 1)

            @block.tensor
            def _(pe):
                pe.wait_ge(exps_done, 1)
                for i in range(4):
                    for t in range(DT):
                        last = nc.tensor.transpose(turned[i][:, t, :], quant[i][:, t * P:(t + 1) * P], consts["ident"][0:R, 0:R])
                    last.then_inc(turned_ready, 1)

            @block.sync
            def _(sp):
                sp.wait_ge(exps_done, 1)
                sp.dma_start(dram["m_rel"], rel[:]).then_inc(stored[0], 16)
                sp.dma_start(dram["m_decay"], decay[:]).then_inc(stored[1], 16)
                for i in range(2):
                    sp.wait_ge(stored[i], 16)


def mlstm(nc, d, consts, cols, dram, qk, v, og, gate_cols, mix):
    NU = 2 * DT
    with Phase(nc, "mlstm") as ph:
        qs = ph.sb("qs", [P, S])
        ks = ph.sb("ks", [P, S])
        vs = ph.sb("vs", [P, DT, M_DH + 2])
        kt = ph.sb("kt", [P, DT, P])
        rel = [ph.sb(f"rel{i}", [P, S]) for i in range(2)]
        decay = ph.sb("decay", [P, 2, DT])
        wexp = ph.sb("wexp", [P, 2, P])
        probs = ph.sb("probs", [P, 2, P])
        vw = ph.sb("vw", [P, 2, M_DH + 2])
        state = ph.sb("state", [P, 2, M_DH + 2])
        den = ph.sb("den", [P, 2])
        num = ph.sb("num", [P, 2, M_DH + 2])
        hsum = ph.sb("hsum", [P, DT, P])
        stats = ph.sb("stats", [P, DT, 6])
        mv = ph.sb("mv", [P, DT, 2])
        rstd = ph.sb("rstd", [P, DT])
        tmp = ph.sb("tmp", [P, S])
        sc = [ph.ps(f"sc{i}", [P, HALF]) for i in range(2)]
        kv = ph.ps("kv", [P, HALF])
        inter = ph.ps("inter", [P, HALF])
        intra = [ph.ps(f"intra{i}", [P, HALF]) for i in range(2)]
        turned = ph.ps("turned", [P, S])
        staged = ph.sem("staged")
        rel_landed = [ph.sem(f"rel_landed{i}") for i in range(2)]
        decay_landed = [ph.sem(f"decay_landed{i}") for i in range(2)]
        head_free = ph.sem("head_free")
        kt_ps = ph.sem("kt_ps")
        kt_ready = ph.sem("kt_ready")
        warg = ph.sem("warg")
        wexp_ready = ph.sem("wexp_ready")
        vw_ready = ph.sem("vw_ready")
        sc_ready = ph.sem("sc_ready")
        probs_ready = ph.sem("probs_ready")
        kv_ready = ph.sem("kv_ready")
        inter_ready = ph.sem("inter_ready")
        intra_ready = ph.sem("intra_ready")
        state_done = ph.sem("state_done")
        num_done = ph.sem("num_done")
        mv_ready = ph.sem("mv_ready")
        std_ready = ph.sem("std_ready")
        normed = ph.sem("normed")
        h_turned = ph.sem("h_turned")
        masks = (consts["m_mask_f"], consts["m_mask_b"])
        W = M_DH + 1
        units = [(0, c) for c in range(DT)] + [(1, DT - 1 - c) for c in range(DT)]

        def gate_col(q, chunk, dr, h):
            return gate_cols[:, q, chunk, bass.ds(32 * dr + h, 1)]

        with nc.Block() as block:

            @block.sync
            def _(sp):
                with sp.Fori(0, M_H) as h:
                    sp.wait_ge(head_free, h + 1)
                    for dr in range(2):
                        sp.dma_start(rel[dr][:], dram["m_rel"][bass.ds(32 * dr + h, 1), :].broadcast_to([P, S])).then_inc(rel_landed[dr], 16)
                        sp.dma_start(decay[:, dr, :], dram["m_decay"][bass.ds(32 * dr + h, 1), :].broadcast_to([P, DT])).then_inc(decay_landed[dr], 16)

            @block.gpsimd
            def _(pool):
                with pool.Fori(0, M_H) as h:
                    pool.wait_ge(head_free, h + 1)
                    nc.gpsimd.tensor_copy(ks[:], qk[:, h + M_H, :])
                    nc.gpsimd.tensor_copy(qs[:], qk[:, h, :])
                    nc.gpsimd.tensor_copy(vs[:], v[:, :, h, :])
                    pool.drain().then_inc(staged, 1)

            @block.tensor
            def _(pe):
                with pe.Fori(0, M_H) as h:
                    pe.wait_ge(staged, h + 1)
                    for t in range(DT):
                        last = nc.tensor.transpose(turned[:, t * P:(t + 1) * P], ks[:, t * P:(t + 1) * P], consts["ident"])
                    last.then_inc(kt_ps, 1)
                    for u in range(NU + 1):
                        if u < NU:
                            dr, c = units[u]
                            tok = slice(c * P, (c + 1) * P)
                            if u >= 2:
                                pe.wait_ge(probs_ready, NU * h + u - 1)
                            nc.tensor.matmul(sc[u % 2][:, 0:P], ks[:, tok], qs[:, tok], start=True, stop=True).then_inc(sc_ready, 1)
                            if u == 0:
                                pe.wait_ge(kt_ready, h + 1)
                        if u >= 1:
                            q = u - 1
                            dr, c = units[q]
                            tok = slice(c * P, (c + 1) * P)
                            pe.wait_ge(vw_ready, NU * h + q + 1)
                            pe.wait_ge(probs_ready, NU * h + q + 1)
                            if q:
                                pe.wait_ge(state_done, NU * h + q)
                                pe.wait_ge(num_done, NU * h + q)
                            nc.tensor.matmul(inter[:, 0:W], qs[:, tok], state[:, q % 2, 0:W], start=True, stop=True).then_inc(inter_ready, 1)
                            nc.tensor.matmul(kv[:, 0:W], kt[:, c, :], vw[:, q % 2, 0:W], start=True, stop=True).then_inc(kv_ready, 1)
                            nc.tensor.matmul(intra[q % 2][:, 0:W], probs[:, q % 2, :], vs[:, c, 0:W], start=True, stop=True).then_inc(intra_ready, 1)
                    pe.wait_ge(normed, h + 1)
                    for t in range(DT):
                        last = nc.tensor.transpose(turned[:, t * P:(t + 1) * P], hsum[:, t, :], consts["ident"])
                    last.then_inc(h_turned, 1)

            @block.scalar
            def _(se):
                with se.Fori(0, M_H) as h:
                    se.wait_ge(kt_ps, h + 1)
                    nc.scalar.activation(kt[:].rearrange("p t c -> p (t c)"), turned[:], ACT.Copy).then_inc(kt_ready, 1)
                    for u in range(NU):
                        dr, c = units[u]
                        if u >= 2:
                            se.wait_ge(kv_ready, NU * h + u - 1)
                        nc.scalar.activation(vw[:, u % 2, 0:W], vs[:, c, 0:W], ACT.Copy, scale=gate_col(2, c, dr, h)).then_inc(vw_ready, 1)
                        se.wait_ge(warg, NU * h + u + 1)
                        nc.scalar.activation(wexp[:, u % 2, :], wexp[:, u % 2, :], ACT.Exp).then_inc(wexp_ready, 1)
                    se.wait_ge(mv_ready, h + 1)
                    nc.scalar.activation(rstd[:], mv[:, :, 1], ACT.Sqrt, bias=1e-6).then_inc(std_ready, 1)

            @block.vector
            def _(ve):
                ve.sem_inc(head_free, 1)
                with ve.Fori(0, M_H) as h:
                    nc.vector.memset(state[:, 0, :], 0.0)
                    for dr in range(2):
                        ve.wait_ge(rel_landed[dr], 16 * h + 16)
                        ve.wait_ge(decay_landed[dr], 16 * h + 16)

                    def argument(u):
                        dr, c = units[u]
                        nc.vector.scalar_tensor_tensor(out=wexp[:, u % 2, :], in0=rel[dr][:, c * P:(c + 1) * P],
                                                       scalar=gate_col(0, c, dr, h), in1=masks[dr],
                                                       op0=ALU.add, op1=ALU.min).then_inc(warg, 1)

                    argument(0)
                    for u in range(NU):
                        dr, c = units[u]
                        if u + 1 < NU:
                            if u >= 1:
                                ve.wait_ge(probs_ready, NU * h + u)
                            argument(u + 1)
                        ve.wait_ge(sc_ready, NU * h + u + 1)
                        ve.wait_ge(wexp_ready, NU * h + u + 1)
                        nc.vector.scalar_tensor_tensor(out=probs[:, u % 2, :], in0=sc[u % 2][:, 0:P], scalar=M_DH ** -0.5,
                                                       in1=wexp[:, u % 2, :], op0=ALU.mult, op1=ALU.mult).then_inc(probs_ready, 1)
                        ve.wait_ge(kv_ready, NU * h + u + 1)
                        if u == DT - 1:
                            nc.vector.memset(state[:, 0, :], 0.0).then_inc(state_done, 1)
                        else:
                            nc.vector.scalar_tensor_tensor(out=state[:, (u + 1) % 2, 0:W], in0=state[:, u % 2, 0:W],
                                                           scalar=decay[:, dr, c:c + 1], in1=kv[:, 0:W],
                                                           op0=ALU.mult, op1=ALU.add).then_inc(state_done, 1)
                        ve.wait_ge(inter_ready, NU * h + u + 1)
                        ve.wait_ge(intra_ready, NU * h + u + 1)
                        i = u % 2
                        nc.vector.tensor_scalar(num[:, 0, 0:W], inter[:, 0:W], gate_col(1, c, dr, h), None, ALU.mult)
                        ve.drain()
                        nc.vector.tensor_tensor(num[:, 1, 0:W], num[:, 0, 0:W], intra[i][:, 0:W], ALU.add).then_inc(num_done, 1)
                        ve.wait_ge(num_done, NU * h + u + 1)
                        nc.vector.tensor_scalar(den[:, 0:1], num[:, 1, M_DH:W], -1.0, None, ALU.mult)
                        ve.drain()
                        nc.vector.tensor_tensor(den[:, 0:1], den[:, 0:1], num[:, 1, M_DH:W], ALU.max)
                        ve.drain()
                        nc.vector.tensor_tensor(den[:, 0:1], den[:, 0:1], gate_col(3, c, dr, h), ALU.max)
                        ve.drain()
                        nc.vector.reciprocal(den[:, 1:2], den[:, 0:1])
                        ve.drain()
                        if dr == 0:
                            nc.vector.tensor_scalar(hsum[:, c, :], num[:, 1, 0:M_DH], den[:, 1:2], None, ALU.mult)
                        else:
                            nc.vector.scalar_tensor_tensor(out=hsum[:, c, :], in0=num[:, 1, 0:M_DH], scalar=den[:, 1:2],
                                                           in1=hsum[:, c, :], op0=ALU.mult, op1=ALU.add)
                    ve.drain()
                    for t in range(DT):
                        nc.vector.bn_stats(stats[:, t, :], hsum[:, t, :])
                    ve.drain()
                    for t in range(DT):
                        last = nc.vector.bn_aggr(mv[:, t, :], stats[:, t, :])
                    last.then_inc(mv_ready, 1)
                    ve.wait_ge(std_ready, h + 1)
                    nc.vector.reciprocal(rstd[:], rstd[:])
                    ve.drain()
                    for t in range(DT):
                        last = nc.vector.tensor_scalar(hsum[:, t, :], hsum[:, t, :], mv[:, t, 0:1], rstd[:, t:t + 1],
                                                       ALU.subtract, ALU.mult)
                    last.then_inc(normed, 1)
                    ve.wait_ge(h_turned, h + 1)
                    nc.vector.scalar_tensor_tensor(out=mix[:, h, :], in0=turned[:], scalar=cols["m_norm_g"][:, bass.ds(h, 1)],
                                                   in1=og[:, h, :], op0=ALU.mult, op1=ALU.mult).then_inc(head_free, 1)


def window_attention(nc, d, consts, cols, aq, ak, av, mix):
    with Phase(nc, "gqa") as ph:
        qs = [ph.sb(f"qs{i}", [P, S]) for i in range(2)]
        bias = ph.sb("bias", [P, 2, 2, 3 * P])
        sink = ph.sb("sink", [P, 8])
        s = ph.sb("s", [P, 2, 3 * P])
        e = ph.sb("e", [P, 2, 3 * P])
        et = ph.sb("et", [P, 2, 3 * P])
        small = ph.sb("small", [P, 2, 4])
        sc = [ph.ps(f"sc{i}", [P, HALF]) for i in range(2)]
        turned = [ph.ps(f"turned{i}", [P, HALF]) for i in range(2)]
        o = [ph.ps(f"o{i}", [P, HALF]) for i in range(2)]
        staged = ph.sem("staged")
        bias_landed = [ph.sem(f"bias_landed{i}") for i in range(2)]
        sink_landed = ph.sem("sink_landed")
        pair_done = ph.sem("pair_done")
        sc_ready = ph.sem("sc_ready")
        max_ready = ph.sem("max_ready")
        exp_ready = ph.sem("exp_ready")
        e_ready = ph.sem("e_ready")
        turned_ready = ph.sem("turned_ready")
        et_ready = ph.sem("et_ready")
        o_ready = ph.sem("o_ready")
        o_taken = ph.sem("o_taken")
        NU = 2 * DT
        units = [(n, j) for n in range(DT) for j in range(2)]

        def window(n):
            lo, hi = max(n - 1, 0), min(n + 2, DT)
            return lo, hi, slice((lo - n + 1) * P, (hi - n + 1) * P)

        with nc.Block() as block:

            @block.sync
            def _(sp):
                sp.dma_start(sink[:], d["a_sink"].broadcast_to([P, 8])).then_inc(sink_landed, 16)
                with sp.Fori(0, 2) as b2:
                    for i in range(2):
                        sp.wait_ge(pair_done, 2 * b2 + i + 1)
                        sp.dma_start(bias[:, i, :, :].rearrange("p j c -> p (j c)"),
                                     d["a_bias"][2 * b2 + i]).then_inc(bias_landed[i], 16)

            @block.gpsimd
            def _(pool):
                with pool.Fori(0, 2) as b2:
                    for i in range(2):
                        pool.wait_ge(pair_done, 2 * b2 + i + 1)
                        nc.gpsimd.tensor_copy(qs[i][:], aq[:, 2 * b2 + i, :]).then_inc(staged, 1)

            @block.tensor
            def _(pe):
                pe.sem_inc(pair_done, 1)
                with pe.Fori(0, 2) as b2:
                    for i in range(2):
                        b = 2 * b2 + i
                        pe.wait_ge(staged, b + 1)
                        for u in range(NU + 2):
                            if u < NU:
                                n, j = units[u]
                                lo, hi, w = window(n)
                                rows = slice(GQ_D * j, GQ_D * (j + 1))
                                if u >= 2:
                                    pe.wait_ge(max_ready, NU * b + u - 1)
                                nc.tensor.matmul(sc[u % 2][:, w], qs[i][rows, n * P:(n + 1) * P], ak[rows, lo * P:hi * P],
                                                 start=True, stop=True).then_inc(sc_ready, 1)
                            if 1 <= u <= NU:
                                n, j = units[u - 1]
                                lo, hi, w = window(n)
                                pe.wait_ge(e_ready, NU * b + u)
                                if u >= 3:
                                    pe.wait_ge(et_ready, NU * b + u - 2)
                                for t in range(hi - lo):
                                    last = nc.tensor.transpose(turned[(u - 1) % 2][:, t * P:(t + 1) * P],
                                                               e[:, (u - 1) % 2, w.start + t * P:w.start + (t + 1) * P], consts["ident"])
                                last.then_inc(turned_ready, 1)
                            if u >= 2:
                                q = u - 2
                                n, j = units[q]
                                lo, hi, w = window(n)
                                rows = slice(GQ_D * j, GQ_D * (j + 1))
                                pe.wait_ge(et_ready, NU * b + q + 1)
                                if j == 0 and n >= 2:
                                    pe.wait_ge(o_taken, DT * b + n - 1)
                                for t in range(hi - lo):
                                    last = nc.tensor.matmul(o[n % 2][rows, 0:P], av[:, lo + t, rows], et[:, q % 2, t * P:(t + 1) * P],
                                                            start=(t == 0), stop=(t == hi - lo - 1))
                                if j == 1:
                                    last.then_inc(o_ready, 1)
                        pe.drain().then_inc(pair_done, 1)

            @block.vector
            def _(ve):
                ve.wait_ge(sink_landed, 16)
                with ve.Fori(0, 2) as b2:
                    for i in range(2):
                        b = 2 * b2 + i
                        ve.wait_ge(bias_landed[i], 16 * b2 + 16)
                        for u in range(NU + 1):
                            if u < NU:
                                n, j = units[u]
                                lo, hi, w = window(n)
                                ve.wait_ge(sc_ready, NU * b + u + 1)
                                if u >= 2:
                                    ve.wait_ge(exp_ready, NU * b + u - 1)
                                sl = u % 2
                                nc.vector.scalar_tensor_tensor(out=s[:, sl, w], in0=sc[sl][:, w], scalar=GQ_D ** -0.5,
                                                               in1=bias[:, i, j, w], op0=ALU.mult, op1=ALU.add)
                                ve.drain()
                                nc.vector.tensor_reduce(small[:, sl, 0:1], s[:, sl, w], AX_X, ALU.max)
                                ve.drain()
                                nc.vector.tensor_scalar(small[:, sl, 0:1], small[:, sl, 0:1], sink[:, bass.ds(b + 4 * j, 1)], -1.0,
                                                        ALU.max, ALU.mult).then_inc(max_ready, 1)
                            if u >= 1:
                                q = u - 1
                                n, j = units[q]
                                lo, hi, w = window(n)
                                sl = q % 2
                                ve.wait_ge(exp_ready, NU * b + q + 1)
                                nc.vector.tensor_tensor(small[:, sl, 1:2], small[:, sl, 1:2], small[:, sl, 2:3], ALU.add)
                                ve.drain()
                                nc.vector.reciprocal(small[:, sl, 3:4], small[:, sl, 1:2])
                                ve.drain()
                                nc.vector.tensor_scalar(e[:, sl, w], e[:, sl, w], small[:, sl, 3:4], None, ALU.mult).then_inc(e_ready, 1)

            @block.scalar
            def _(se):
                se.wait_ge(sink_landed, 16)
                with se.Fori(0, 2) as b2:
                    for i in range(2):
                        b = 2 * b2 + i
                        for u in range(NU + 2):
                            if u < NU:
                                n, j = units[u]
                                lo, hi, w = window(n)
                                sl = u % 2
                                se.wait_ge(max_ready, NU * b + u + 1)
                                if u >= 2:
                                    se.wait_ge(turned_ready, NU * b + u - 1)
                                nc.scalar.activation(e[:, sl, w], s[:, sl, w], ACT.Exp, bias=small[:, sl, 0:1], accum_out=small[:, sl, 1:2])
                                nc.scalar.activation(small[:, sl, 2:3], sink[:, bass.ds(b + 4 * j, 1)], ACT.Exp, bias=small[:, sl, 0:1])
                                se.drain().then_inc(exp_ready, 1)
                            if u >= 1 and u <= NU:
                                q = u - 1
                                n, j = units[q]
                                lo, hi, w = window(n)
                                se.wait_ge(turned_ready, NU * b + q + 1)
                                nc.scalar.activation(et[:, q % 2, 0:(hi - lo) * P], turned[q % 2][:, 0:(hi - lo) * P], ACT.Copy).then_inc(et_ready, 1)
                            if u >= 2 and (u - 2) % 2 == 1:
                                n = (u - 2) // 2
                                se.wait_ge(o_ready, DT * b + n + 1)
                                nc.scalar.activation(mix[:, 4 + b, n * P:(n + 1) * P], o[n % 2][:, 0:P], ACT.Copy).then_inc(o_taken, 1)


def second_block(nc, d, consts, cols, x):
    def x_rows(k):
        return x[:, k, :]

    dram = {"m_rel": nc.dram_tensor("m_rel", (GATE_ROWS, S), F32, kind="Internal").ap(),
            "m_decay": nc.dram_tensor("m_decay", (GATE_ROWS, DT), F32, kind="Internal").ap()}

    with ExitStack() as stack:
        with Phase(nc, "b2m") as ph:
            qk = ph.sb("qk", [P, 8, S])
            og = ph.sb("og", [P, 4, S])
            v = ph.sb("v", [P, DT, M_H, M_DH + 2])
            gate_cols = ph.sb("gate_cols", [P, 4, DT, GATE_ROWS])
            with Phase(nc, "b2g") as pg:
                gi, gf = pg.sb("gi", [GATE_ROWS, S]), pg.sb("gf", [GATE_ROWS, S])
                resets = pg.sb("resets", [P, S])
                load_phase(nc, "b2_resets", [(resets[:], d["reset128"])])
                project_rows(nc, "b2_gi", d["w_mi"], DT, x_rows, 1, m=GATE_ROWS,
                             act=lambda n, acc, tmp, i: nc.scalar.activation(gi[:], acc[:], ACT.Copy))
                project_rows(nc, "b2_gf", d["w_mf"], DT, x_rows, 1, m=GATE_ROWS,
                             act=lambda n, acc, tmp, i: nc.scalar.activation(gf[:], acc[:], ACT.Copy))
                mlstm_rows(nc, d, gi, gf, cols, dict(consts, reset128=resets[:]), dram, gate_cols)
            project_tokens(nc, "b2_v", d["w_mv"], M_H * M_DH, x,
                           act=lambda n, acc: nc.scalar.activation(v[:, n, :, 0:M_DH], acc[:].rearrange("p (h e) -> p h e", h=M_H), ACT.Copy))
            with Phase(nc, "b2one") as po:
                with nc.Block() as block:

                    @block.vector
                    def _(ve):
                        nc.vector.memset(v[:, :, :, M_DH:], 1.0)
            with Phase(nc, "b2x", side="right") as px:
                pair = Pair(px, "x", DT, within=x)
                split_rows(nc, "b2_split", x, pair)
                project_pair(nc, "b2_o", d["w_mo"], DT, pair.rows, 4,
                             act=lambda n, j, i, acc, tmp: nc.scalar.activation(og[:, n, :], acc[:], ACT.Sigmoid))
                conv_pair(nc, "b2_conv", d["w_mqk"], 8, pair.rows, lambda n, tap: cols["m_taps"][:, bass.ds(TAPS * n + tap, 1)], qk,
                          bias_of=lambda n: cols["m_conv_b"][:, bass.ds(n, 1)])
                join_rows(nc, "b2_join", pair, x)
            mix = stack.enter_context(Phase(nc, "b2", side="right")).sb("mix", [P, DT, S])
            mlstm(nc, d, consts, cols, dram, qk, v, og, gate_cols, mix)
        with Phase(nc, "b2a") as ph:
            aq = ph.sb("aq", [P, 4, S])
            ak = ph.sb("ak", [P, S])
            av = ph.sb("av", [P, DT, P])
            project_rows(nc, "b2_ak", d["w_ak"], DT, x_rows, 1,
                         act=lambda n, acc, tmp, i: nc.scalar.activation(ak[:], acc[:], ACT.Copy))
            project_tokens(nc, "b2_av", d["w_av2"], P, x, act=lambda n, acc: nc.scalar.activation(av[:, n, :], acc[:], ACT.Copy))
            project_rows(nc, "b2_aq", d["w_aq"], DT, x_rows, 4, act=lambda n, acc, tmp, i: nc.scalar.activation(aq[:, n, :], acc[:], ACT.Copy))
            window_attention(nc, d, consts, cols, aq, ak, av, mix)
        out_projection(nc, "b2_out", d["w_out2"], mix, x)
    norm_rows(nc, "b2_ln1", x, x, consts["ones"], cols["ln1_g2"], cols["ln1_b2"], centre=True)
    with Phase(nc, "b2f") as ph:
        base = ph.sb("base", [P, DT, S])
        with Phase(nc, "b2p") as pp:
            p_t = pp.sb("p", [P, 2, S])
            load_phase(nc, "b2_p", [(p_t[:], d["pT"].rearrange("p (t s) -> p t s", t=2))])
            project_rows(nc, "b2_plep", d["w_plep"], 2, lambda k: p_t[:, k, :], 8,
                         act=lambda n, acc, tmp, i: nc.scalar.activation(base[:, n, :], acc[:], ACT.Copy))
        pair = Pair(ph, "x", DT, within=x)
        split_rows(nc, "b2_splitf", x, pair)

        def add_gate(n, j, i, acc, tmp, res):
            nc.vector.tensor_tensor(base[:, n, :], base[:, n, :], tmp[:], ALU.mult)
            nc.vector.drain()
            add_residual(nc, base[:, n, :], pair, n, base[:, n, :])

        project_pair(nc, "b2_pleg", d["w_pleg"], DT, pair.rows, 8, dve=add_gate,
                     act=lambda n, j, i, acc, tmp: nc.scalar.activation(tmp[:], acc[:], ACT.Sigmoid))
        hidden = Pair(ph, "hidden", DT)
        at = 0
        for c, KT in enumerate(FFN_CUTS2):

            def gated(n, j, i, acc, tmp, res):
                nc.vector.tensor_tensor(tmp[:], acc[:], tmp[:], ALU.mult)
                nc.vector.drain()
                put_pair(nc, hidden, j, tmp)

            project_pair(nc, f"b2_ffn{c}", d["w_ffn"][2 * at:2 * (at + KT)], DT, pair.rows, 2 * KT, pairs=True, dve=gated,
                         act=lambda n, j, i, acc, tmp: nc.scalar.activation(tmp[:], acc[:], ACT.Silu))
            project_pair(nc, f"b2_ffo{c}", d[f"w_ffo{c}"], KT, hidden.rows, 8,
                         dve=lambda n, j, i, acc, tmp, res: nc.vector.tensor_tensor(base[:, n, :], base[:, n, :], acc[:], ALU.add))
            at += KT
        norm_rows(nc, "b2_ln2", base, x, consts["ones"], cols["ln2_g2"], cols["ln2_b2"], centre=True)


L2_COLUMNS = {"m_bi": 1, "m_bf": 1, "m_taps": 40, "m_conv_b": 8, "m_norm_g": 4, "ln1_g2": 8, "ln1_b2": 8, "ln2_g2": 8, "ln2_b2": 8}
L2_SQUARES = ("m_mask_f", "m_mask_b")


def gate_rows(w):
    import numpy as np
    out = np.zeros((w.shape[0], GATE_ROWS), np.float32)
    out[:, 0:4], out[:, 32:36] = w[:, 0:4], w[:, 4:8]
    return out


def gate_column(b):
    import numpy as np
    out = np.zeros((P, 1), np.float32)
    out[0:4, 0], out[32:36, 0] = b[0:4], b[4:8]
    return out


def second_arrays(a):
    import numpy as np
    w = a["w_in_2"][0]
    mqk, mv, mo, gates, aq, ak, av = np.split(w, np.cumsum([1024, 512, 512, 16, 512, 128]), axis=1)
    order = np.concatenate([np.r_[b * 64:(b + 1) * 64, (b + 4) * 64:(b + 5) * 64] for b in range(4)])
    wo = a["w_out_2"][0]
    ffn = a["w_ffn_in_2"][0]
    pair = rows_weight(ffn).reshape(2, D_FF2 // P, P, 1024).transpose(1, 0, 2, 3).reshape(-1, P, 1024)
    q, k = np.arange(P)[:, None], np.arange(3 * P)[None, :]
    rel = np.abs(k - P - q).astype(np.float32)
    slopes = 2.0 ** (-8.0 * np.arange(1, 9, dtype=np.float32) / 8)
    bias = np.where(rel[None] <= 128, -slopes[:, None, None] * rel[None], -BIG).astype(np.float32)
    bias = np.stack([bias[0:4], bias[4:8]], axis=2)
    tiles = lambda g: gate_rows(g).reshape(DT, P, GATE_ROWS).transpose(1, 0, 2).reshape(1, P, DT * GATE_ROWS)
    out = {"w_mqk": rows_weight(mqk), "w_mv": tokens_weight(mv), "w_mo": rows_weight(mo),
           "w_mi": tiles(gates[:, 0:8]), "w_mf": tiles(gates[:, 8:16]),
           "w_aq": rows_weight(aq[:, order]), "w_ak": rows_weight(ak), "w_av2": tokens_weight(av),
           "a_bias": bias.reshape(4, P, 2 * 3 * P), "a_sink": a["attn_sink_2"],
           "w_out2": rows_weight(np.concatenate([wo[0:512], wo[512:][order]])), "w_ffn": pair,
           "w_pleg": rows_weight(a["w_ple_gate_2"][0]),
           "w_plep": rows_weight(a["w_ple_proj_2"][0]),
           "pT": a["p_2"][0, 0].T.reshape(2, P, S).transpose(1, 0, 2).reshape(P, 2 * S),
           "reset128": np.broadcast_to((np.arange(S) % P != 0).astype(np.float32), (P, S))}
    ends = P * np.cumsum(FFN_CUTS2)
    for c, part in enumerate(np.split(a["w_ffn_out_2"][0], ends[:-1])):
        out[f"w_ffo{c}"] = rows_weight(part)
    bg = a["b_gate_2"][0]
    taps = a["conv_w_2"][0].reshape(TAPS, 8, P).transpose(2, 1, 0).reshape(P, 40)
    columns = {"m_bi": gate_column(bg[0:8]), "m_bf": gate_column(bg[8:16]), "m_taps": taps,
               "m_conv_b": column(a["conv_b_2"]), "m_norm_g": column(a["mlstm_norm_g_2"]),
               "ln1_g2": column(a["ln1_g_2"]), "ln1_b2": column(a["ln1_b_2"]),
               "ln2_g2": column(a["ln2_g_2"]), "ln2_b2": column(a["ln2_b_2"])}
    i = np.arange(P)
    seen = i[:, None] <= i[None, :]
    squares = {"m_mask_f": np.where(seen, 0, -BIG).astype(np.float32), "m_mask_b": np.where(seen.T, 0, -BIG).astype(np.float32)}
    return out, columns, squares

G_H, G_D = 4, 128
LEVELS = 7
GRID, GRID_ROWS = 64, 16
WIN_R, WIN_C = 8, 16
N_D = 64
RPB_R, RPB_C = 2 * WIN_R - 1, 2 * WIN_C - 1
D_FF3 = 4096


def l2_normalise(nc, d, qkv):
    NB = 2 * G_H
    with Phase(nc, "l2n") as ph:
        pick = ph.sb("pick", [P, NB, NB])
        spread = ph.sb("spread", [NB, NB, P])
        sq = [ph.sb(f"sq{i}", [P, S]) for i in range(2)]
        rows = ph.sb("rows", [NB, S])
        total = ph.ps("total", [NB, S])
        every = [ph.ps(f"every{i}", [P, S]) for i in range(2)]
        pick_landed, spread_landed = ph.sem("pick_landed"), ph.sem("spread_landed")
        squared, summed = ph.sem("squared"), ph.sem("summed")
        std_ready, rstd_ready = ph.sem("std_ready"), ph.sem("rstd_ready")
        spread_ready, scaled = ph.sem("spread_ready"), ph.sem("scaled")
        with nc.Block() as block:

            @block.sync
            def _(sp):
                sp.dma_start(pick[:].rearrange("p a b -> p (a b)"), d["l2_pick"]).then_inc(pick_landed, 16)
                sp.dma_start(spread[:].rearrange("p a b -> p (a b)"), d["l2_spread"]).then_inc(spread_landed, 16)

            @block.scalar
            def _(se):
                for k in range(NB):
                    if k >= 2:
                        se.wait_ge(summed, k - 1)
                    nc.scalar.activation(sq[k % 2][:], qkv[:, k, :], ACT.Square).then_inc(squared, 1)
                se.wait_ge(summed, NB)
                nc.scalar.activation(rows[:], total[:], ACT.Sqrt, bias=1e-6).then_inc(std_ready, 1)

            @block.tensor
            def _(pe):
                pe.wait_ge(pick_landed, 16)
                for k in range(NB):
                    pe.wait_ge(squared, k + 1)
                    for half in range(2):
                        c = slice(half * HALF, (half + 1) * HALF)
                        last = nc.tensor.matmul(total[:, c], pick[:, k, :], sq[k % 2][:, c], start=(k == 0), stop=(k == NB - 1))
                    last.then_inc(summed, 1)
                pe.wait_ge(spread_landed, 16)
                pe.wait_ge(rstd_ready, 1)
                for k in range(NB):
                    if k >= 2:
                        pe.wait_ge(scaled, k - 1)
                    for half in range(2):
                        c = slice(half * HALF, (half + 1) * HALF)
                        last = nc.tensor.matmul(every[k % 2][:, c], spread[:, k, :], rows[:, c], start=True, stop=True)
                    last.then_inc(spread_ready, 1)

            @block.vector
            def _(ve):
                ve.wait_ge(std_ready, 1)
                nc.vector.reciprocal(rows[:], rows[:]).then_inc(rstd_ready, 1)
                for k in range(NB):
                    ve.wait_ge(spread_ready, k + 1)
                    nc.vector.scalar_tensor_tensor(out=qkv[:, k, :], in0=qkv[:, k, :], scalar=(G_D ** -0.5 if k < G_H else 1.0),
                                                   in1=every[k % 2][:], op0=ALU.mult, op1=ALU.mult).then_inc(scaled, 1)


def delta_rows(nc, ga, gb, cols, consts, dram, col_out):
    R, NCH = GATE_ROWS, DT
    with Phase(nc, "grow") as ph:
        soft = ph.sb("soft", [R, S])
        g = ph.sb("g", [R, S])
        quant = [ph.sb(f"quant{i}", [R, S]) for i in range(4)]
        ends = ph.sb("ends", [R, NCH])
        rate = ph.sb("rate", [R, 1])
        turned = [ph.ps(f"turned{i}", [P, DT, R]) for i in range(4)]
        soft_ready, rate_ready = ph.sem("soft_ready"), ph.sem("rate_ready")
        args_ready, exps_done = ph.sem("args_ready"), ph.sem("exps_done")
        turned_ready = ph.sem("turned_ready")
        stored = [ph.sem(f"stored{i}") for i in range(3)]
        F, B = slice(0, G_H), slice(32, 32 + G_H)

        def chunks(x):
            return x.rearrange("p (n c) -> p n c", c=P)

        with nc.Block() as block:

            @block.scalar
            def _(se):
                nc.scalar.activation(soft[:], ga[:], ACT.Abs, bias=cols["g_dt"][0:R, :])
                nc.scalar.activation(rate[:], cols["g_alog"][0:R, :], ACT.Exp).then_inc(rate_ready, 1)
                se.drain()
                nc.scalar.activation(soft[:], soft[:], ACT.Exp, scale=-1.0)
                se.drain()
                nc.scalar.activation(soft[:], soft[:], ACT.Ln, bias=1.0).then_inc(soft_ready, 1)
                nc.scalar.activation(quant[1][:], gb[:], ACT.Sigmoid)
                se.wait_ge(args_ready, 1)
                nc.scalar.activation(quant[2][:], quant[0][:], ACT.Exp)
                nc.scalar.activation(quant[3][:], quant[3][:], ACT.Exp)
                nc.scalar.activation(ends[:], ends[:], ACT.Exp)
                se.drain().then_inc(exps_done, 1)
                for i in range(4):
                    se.wait_ge(turned_ready, i + 1)
                    nc.scalar.activation(col_out[:, i, :, :], turned[i][:], ACT.Copy)
                nc.scalar.activation(col_out[:, 4, :, :], turned[2][:], ACT.Copy, scale=-1.0)

            @block.vector
            def _(ve):
                gc = quant[0]
                nc.vector.tensor_scalar(g[:], ga[:], cols["g_dt"][0:R, :], 0.0, ALU.add, ALU.max)
                nc.vector.memset(gc[:], 0.0)
                nc.vector.memset(ends[:], 0.0)
                ve.drain()
                ve.wait_ge(soft_ready, 1)
                nc.vector.tensor_tensor(g[:], g[:], soft[:], ALU.add)
                ve.drain()
                ve.wait_ge(rate_ready, 1)
                nc.vector.tensor_scalar(g[:], g[:], rate[:], -1.0, ALU.mult, ALU.mult)
                ve.drain()
                nc.vector.tensor_tensor_scan(gc[F, :], consts["reset128"][F, :], g[F, :], 0.0, ALU.mult, ALU.add)
                nc.vector.tensor_tensor_scan(gc[B, ::-1], consts["reset128"][B, :], g[B, ::-1], 0.0, ALU.mult, ALU.add)
                ve.drain()
                nc.vector.tensor_copy(ends[F, :], chunks(gc[:])[F, :, P - 1])
                nc.vector.tensor_copy(ends[B, :], chunks(gc[:])[B, :, 0])
                ve.drain()
                nc.vector.tensor_tensor(chunks(quant[3][:]), ends[:, :, None].broadcast_to([R, NCH, P]), chunks(gc[:]),
                                        ALU.subtract)
                ve.drain().then_inc(args_ready, 1)

            @block.tensor
            def _(pe):
                pe.wait_ge(exps_done, 1)
                for i in range(4):
                    for t in range(DT):
                        last = nc.tensor.transpose(turned[i][:, t, :], quant[i][:, t * P:(t + 1) * P], consts["ident"][0:R, 0:R])
                    last.then_inc(turned_ready, 1)

            @block.sync
            def _(sp):
                sp.wait_ge(exps_done, 1)
                for i, (name, src) in enumerate((("g_gc", quant[0]), ("g_beta", quant[1]), ("g_end", ends))):
                    sp.dma_start(dram[name], src[:]).then_inc(stored[i], 16)
                for i in range(3):
                    sp.wait_ge(stored[i], 16)


def delta_rule(nc, d, consts, cols, dram, qkv, z, gate_cols, mix):
    NG = 4
    N_INV = 2 * LEVELS * 2
    N_Z = 2 * (LEVELS - 1) * 2
    NU = 2 * DT
    with Phase(nc, "delta") as ph:
        qs, ks, vf = ph.sb("qs", [P, S]), ph.sb("ks", [P, S]), ph.sb("vf", [P, S])
        kt = ph.sb("kt", [P, DT, P])
        vt = vf[:].rearrange("p (t c) -> p t c", c=P)
        gc_row = [ph.sb(f"gc_row{i}", [P, S]) for i in range(2)]
        beta_row = [ph.sb(f"beta_row{i}", [P, S]) for i in range(2)]
        end_row = ph.sb("end_row", [P, 2, DT])
        level = ph.sb("level", [P, 2 * LEVELS, P])
        gam = [ph.sb(f"gam{i}", [P, NG, P]) for i in range(2)]
        pt = [ph.sb(f"pt{i}", [P, NG, P]) for i in range(4)]
        at = [ph.sb(f"at{i}", [P, NG, P]) for i in range(4)]
        xt = [ph.sb(f"xt{i}", [P, NG, P]) for i in range(4)]
        free = [mix[:, 4 + i, :].rearrange("p (a n c) -> p a n c", a=2, c=P) for i in range(3)]
        bt = [[free[i][:, j] for j in range(2)] for i in range(2)]
        xx = [free[2][:, i] for i in range(2)]
        r, rb, vn, vkd = (mix[:, 7, 2 * i * P:2 * (i + 1) * P].rearrange("p (a c) -> p a c", a=2) for i in range(4))
        ys = gam
        state = ph.sb("state", [P, 2, P])
        t1 = ph.sb("t1", [P, 2, P])
        osum = gc_row[0][:].rearrange("p (t c) -> p t c", c=P)
        ss = ph.sb("ss", [P, DT])
        bank = [ph.ps(f"bank{i}", [P, NG, P]) for i in range(4)]
        turned_k, turned_v = ph.ps("turned_k", [P, S]), ph.ps("turned_v", [P, S])
        zt_bank = [turned_k[:, 0:HALF].rearrange("p (n c) -> p n c", c=P), turned_k[:, HALF:S].rearrange("p (n c) -> p n c", c=P)]
        level_landed = ph.sem("level_landed")
        row_landed = [ph.sem(f"row_landed{i}") for i in range(6)]
        staged = ph.sem("staged")
        head_free = ph.sem("head_free")
        turned_ready = ph.sem("turned_ready")
        kv_ready = ph.sem("kv_ready")
        prod_ready = ph.sem("prod_ready")
        garg = ph.sem("garg")
        gam_ready = ph.sem("gam_ready")
        kk_ready = ph.sem("kk_ready")
        at_ready = ph.sem("at_ready")
        bt_ready = ph.sem("bt_ready")
        y_ready = ph.sem("y_ready")
        y_copied = ph.sem("y_copied")
        z_ready = ph.sem("z_ready")
        x_done = ph.sem("x_done")
        ks_ready = ph.sem("ks_ready")
        r_ready = ph.sem("r_ready")
        rb_ready = ph.sem("rb_ready")
        vn_ready = ph.sem("vn_ready")
        vns_ready = ph.sem("vns_ready")
        vkd_ready = ph.sem("vkd_ready")
        su_ready = ph.sem("su_ready")
        s_done = ph.sem("s_done")
        ss_ready, std_ready = ph.sem("ss_ready"), ph.sem("std_ready")
        normed, o_turned = ph.sem("normed"), ph.sem("o_turned")
        ident = consts["ident"]
        masks = (consts["m_mask_f"], consts["m_mask_b"])

        def gate_col(q, chunk, dr, h):
            return gate_cols[:, q, chunk, bass.ds(32 * dr + h, 1)]

        def tok(c):
            return slice(c * P, (c + 1) * P)

        def chunk_of(step, dr):
            return step if dr == 0 else DT - 1 - step

        inverse_steps = [(pp, l, g) for pp in range(2) for l in range(LEVELS) for g in range(2)]

        with nc.Block() as block:

            @block.sync
            def _(sp):
                sp.dma_start(level[:].rearrange("p l c -> p (l c)"), d["g_levels"]).then_inc(level_landed, 16)
                with sp.Fori(0, G_H) as h:
                    sp.wait_ge(head_free, h + 1)
                    for dr in range(2):
                        row = bass.ds(32 * dr + h, 1)
                        sp.dma_start(gc_row[dr][:], dram["g_gc"][row, :].broadcast_to([P, S])).then_inc(row_landed[3 * dr], 16)
                        sp.dma_start(beta_row[dr][:], dram["g_beta"][row, :].broadcast_to([P, S])).then_inc(row_landed[3 * dr + 1], 16)
                        sp.dma_start(end_row[:, dr, :], dram["g_end"][row, :].broadcast_to([P, DT])).then_inc(row_landed[3 * dr + 2], 16)

            @block.gpsimd
            def _(pool):
                pool.wait_ge(level_landed, 16)
                with pool.Fori(0, G_H) as h:
                    pool.wait_ge(head_free, h + 1)
                    nc.gpsimd.tensor_copy(ks[:], qkv[:, h + G_H, :])
                    nc.gpsimd.tensor_copy(vf[:], qkv[:, h + 2 * G_H, :])
                    nc.gpsimd.tensor_copy(qs[:], qkv[:, h, :])
                    pool.drain().then_inc(staged, 1)
                    for dr in range(2):
                        pool.wait_ge(row_landed[3 * dr + 1], 16 * h + 16)
                    for gi in range(4):
                        pool.wait_ge(kk_ready, 4 * h + gi + 1)
                        c0 = (gi % 2) * HALF
                        nc.gpsimd.tensor_tensor(at[gi][:].rearrange("p n c -> p (n c)"), at[gi][:].rearrange("p n c -> p (n c)"),
                                                beta_row[gi // 2][:, c0:c0 + HALF], ALU.mult).then_inc(at_ready, 1)
                    pool.wait_ge(at_ready, 4 * h + 4)
                    for n, (pp, l, g) in enumerate(inverse_steps):
                        if n >= 4:
                            pool.wait_ge(x_done, N_INV * h + n - 3)
                        mask = level[:, LEVELS * pp + l:LEVELS * pp + l + 1, :].broadcast_to([P, NG, P])
                        nc.gpsimd.tensor_tensor(bt[g][(pp * LEVELS + l) % 2], at[2 * pp + g][:], mask, ALU.mult).then_inc(bt_ready, 1)

            @block.tensor
            def _(pe):
                with pe.Fori(0, G_H) as h:
                    pe.wait_ge(staged, h + 1)
                    for t in range(DT):
                        nc.tensor.transpose(turned_k[:, tok(t)], ks[:, tok(t)], ident)
                    for t in range(DT):
                        last = nc.tensor.transpose(turned_v[:, tok(t)], vf[:, tok(t)], ident)
                    last.then_inc(turned_ready, 1)
                    for half in range(2):
                        for i in range(NG):
                            c = tok(half * NG + i)
                            nc.tensor.matmul(bank[half][:, i, :], ks[:, c], ks[:, c], start=True, stop=True)
                        for i in range(NG):
                            c = tok(half * NG + i)
                            last = nc.tensor.matmul(bank[2 + half][:, i, :], ks[:, c], qs[:, c], start=True, stop=True)
                        last.then_inc(prod_ready, 1)
                    pe.wait_ge(kv_ready, h + 1)
                    pe.wait_ge(kk_ready, 4 * h + 4)
                    zn = 0
                    for pp in range(2):
                        for l in range(LEVELS):
                            n0 = (pp * LEVELS + l) * 2
                            for g in range(2):
                                pe.wait_ge(bt_ready, N_INV * h + n0 + g + 1)
                                if l:
                                    pe.wait_ge(x_done, N_INV * h + n0 + g - 1)
                                elif pp:
                                    pe.wait_ge(y_copied, N_INV * h + n0 + g - 1)
                                for i in range(NG):
                                    last = nc.tensor.matmul(bank[g][:, i, :], bt[g][(pp * LEVELS + l) % 2][:, i, :],
                                                            xx[g][:, i, :] if l else ident, start=True, stop=True)
                                last.then_inc(y_ready, 1)
                            if l:
                                for g in range(2):
                                    pe.wait_ge(y_copied, N_INV * h + n0 + g + 1)
                                    if l < LEVELS - 1:
                                        for i in range(NG):
                                            nc.tensor.matmul(bank[2 + g][:, i, :], xt[2 * pp + g][:, i, :], ys[g][:, i, :],
                                                             start=True, stop=True)
                                    for i in range(NG):
                                        last = nc.tensor.matmul(zt_bank[g][:, i, :], ys[g][:, i, :], xt[2 * pp + g][:, i, :],
                                                                start=True, stop=True)
                                    last.then_inc(z_ready, 1)
                    pe.wait_ge(x_done, N_INV * h + N_INV)
                    for k in range(DT):
                        for dr in range(2):
                            c, m = tok(chunk_of(k, dr)), 2 * k + dr
                            if k:
                                pe.wait_ge(s_done, NU * h + m - 1)
                            nc.tensor.matmul(bank[dr][:, 0, :], ks[:, c], state[:, dr, :], start=True, stop=True)
                            nc.tensor.matmul(bank[dr][:, 1, :], qs[:, c], state[:, dr, :], start=True, stop=True).then_inc(ks_ready, 1)
                        for dr in range(2):
                            ch, m = chunk_of(k, dr), 2 * k + dr
                            pe.wait_ge(rb_ready, NU * h + m + 1)
                            nc.tensor.matmul(bank[2 + dr][:, 0, :], xt[2 * dr + ch // NG][:, ch % NG, :], rb[:, dr, :],
                                             start=True, stop=True).then_inc(vn_ready, 1)
                        for dr in range(2):
                            ch, m = chunk_of(k, dr), 2 * k + dr
                            pe.wait_ge(vns_ready, NU * h + m + 1)
                            nc.tensor.matmul(zt_bank[dr][:, 0, :], pt[2 * dr + ch // NG][:, ch % NG, :], vn[:, dr, :], start=True, stop=True)
                            pe.wait_ge(vkd_ready, NU * h + m + 1)
                            nc.tensor.matmul(zt_bank[dr][:, 1, :], kt[:, ch, :], vkd[:, dr, :], start=True, stop=True).then_inc(su_ready, 1)
                    pe.wait_ge(normed, h + 1)
                    for t in range(DT):
                        last = nc.tensor.transpose(turned_v[:, tok(t)], osum[:, t, :], ident)
                    last.then_inc(o_turned, 1)

            @block.scalar
            def _(se):
                with se.Fori(0, G_H) as h:
                    se.wait_ge(turned_ready, h + 1)
                    nc.scalar.activation(kt[:].rearrange("p t c -> p (t c)"), turned_k[:], ACT.Copy)
                    nc.scalar.activation(vf[:], turned_v[:], ACT.Copy)
                    se.drain().then_inc(kv_ready, 1)
                    for gi in range(4):
                        se.wait_ge(garg, 4 * h + gi + 1)
                        nc.scalar.activation(gam[gi % 2][:], gam[gi % 2][:], ACT.Exp).then_inc(gam_ready, 1)
                    for n in range(N_INV):
                        g = n % 2
                        se.wait_ge(y_ready, N_INV * h + n + 1)
                        if n >= 2:
                            se.wait_ge(x_done, N_INV * h + n - 1)
                        nc.scalar.activation(ys[g][:], bank[g][:], ACT.Copy).then_inc(y_copied, 1)
                    for k in range(DT):
                        for dr in range(2):
                            ch, m = chunk_of(k, dr), 2 * k + dr
                            se.wait_ge(r_ready, NU * h + m + 1)
                            nc.scalar.activation(rb[:, dr, :], r[:, dr, :], ACT.Copy, scale=gate_col(1, ch, dr, h)).then_inc(rb_ready, 1)
                        for dr in range(2):
                            ch, m = chunk_of(k, dr), 2 * k + dr
                            se.wait_ge(vns_ready, NU * h + m + 1)
                            nc.scalar.activation(vkd[:, dr, :], vn[:, dr, :], ACT.Copy, scale=gate_col(3, ch, dr, h)).then_inc(vkd_ready, 1)
                    se.wait_ge(ss_ready, h + 1)
                    nc.scalar.activation(ss[:], ss[:], ACT.Sqrt, scale=1.0 / G_D, bias=1e-6).then_inc(std_ready, 1)

            @block.vector
            def _(ve):
                ve.sem_inc(head_free, 1)
                with ve.Fori(0, G_H) as h:
                    nc.vector.memset(state[:], 0.0)
                    for dr in range(2):
                        ve.wait_ge(row_landed[3 * dr], 16 * h + 16)
                        ve.wait_ge(row_landed[3 * dr + 2], 16 * h + 16)

                    def argument(gi):
                        dr, half = gi // 2, gi % 2
                        for i in range(NG):
                            c = half * NG + i
                            last = nc.vector.scalar_tensor_tensor(out=gam[gi % 2][:, i, :], in0=gc_row[dr][:, tok(c)],
                                                                  scalar=gate_col(0, c, dr, h), in1=masks[dr],
                                                                  op0=ALU.subtract, op1=ALU.min)
                        last.then_inc(garg, 1)

                    argument(0)
                    for gi in range(4):
                        if gi < 3:
                            if gi:
                                ve.wait_ge(kk_ready, 4 * h + gi)
                            argument(gi + 1)
                        ve.wait_ge(gam_ready, 4 * h + gi + 1)
                        ve.wait_ge(prod_ready, 2 * h + gi % 2 + 1)
                        nc.vector.tensor_tensor(pt[gi][:], bank[2 + gi % 2][:], gam[gi % 2][:], ALU.mult)
                        nc.vector.tensor_tensor(at[gi][:], bank[gi % 2][:], gam[gi % 2][:], ALU.mult)
                        ve.drain().then_inc(kk_ready, 1)
                    for n, (pp, l, g) in enumerate(inverse_steps):
                        gi = 2 * pp + g
                        if l == 0:
                            ve.wait_ge(y_copied, N_INV * h + n + 1)
                            ident4 = ident[:, None, :].broadcast_to([P, NG, P])
                            nc.vector.tensor_tensor(xx[g], ident4, ys[g][:], ALU.subtract)
                            nc.vector.tensor_tensor(xt[gi][:], ident4, bt[g][(pp * LEVELS + l) % 2], ALU.subtract)
                        else:
                            ve.wait_ge(z_ready, N_Z * h + (pp * (LEVELS - 1) + l - 1) * 2 + g + 1)
                            if l < LEVELS - 1:
                                nc.vector.tensor_tensor(xx[g], xx[g], bank[2 + g][:], ALU.subtract)
                            nc.vector.tensor_tensor(xt[gi][:], xt[gi][:], zt_bank[g], ALU.subtract)
                        ve.drain().then_inc(x_done, 1)
                    for k in range(DT):
                        for dr in range(2):
                            ch, m = chunk_of(k, dr), 2 * k + dr
                            ve.wait_ge(ks_ready, NU * h + m + 1)
                            nc.vector.scalar_tensor_tensor(out=r[:, dr, :], in0=bank[dr][:, 0, :], scalar=gate_col(4, ch, dr, h),
                                                           in1=vt[:, ch, :], op0=ALU.mult, op1=ALU.add).then_inc(r_ready, 1)
                            if k < DT // 2:
                                nc.vector.tensor_scalar(t1[:, dr, :], bank[dr][:, 1, :], gate_col(2, ch, dr, h), None, ALU.mult)
                            else:
                                nc.vector.scalar_tensor_tensor(out=t1[:, dr, :], in0=bank[dr][:, 1, :], scalar=gate_col(2, ch, dr, h),
                                                               in1=osum[:, ch, :], op0=ALU.mult, op1=ALU.add)
                        for dr in range(2):
                            ve.wait_ge(vn_ready, NU * h + 2 * k + dr + 1)
                            nc.vector.tensor_copy(vn[:, dr, :], bank[2 + dr][:, 0, :]).then_inc(vns_ready, 1)
                        for dr in range(2):
                            ch, m = chunk_of(k, dr), 2 * k + dr
                            ve.wait_ge(su_ready, NU * h + m + 1)
                            nc.vector.scalar_tensor_tensor(out=state[:, dr, :], in0=state[:, dr, :], scalar=end_row[:, dr, ch:ch + 1],
                                                           in1=zt_bank[dr][:, 1, :], op0=ALU.mult, op1=ALU.add).then_inc(s_done, 1)
                            nc.vector.tensor_tensor(osum[:, ch, :], t1[:, dr, :], zt_bank[dr][:, 0, :], ALU.add)
                        ve.drain()
                    nc.vector.tensor_tensor(kt[:], osum, osum, ALU.mult)
                    ve.drain()
                    nc.vector.tensor_reduce(ss[:], kt[:], AX_X, ALU.add).then_inc(ss_ready, 1)
                    ve.wait_ge(std_ready, h + 1)
                    nc.vector.reciprocal(ss[:], ss[:])
                    ve.drain()
                    nc.vector.tensor_tensor(osum, osum, ss[:, :, None].broadcast_to([P, DT, P]), ALU.mult).then_inc(normed, 1)
                    ve.wait_ge(o_turned, h + 1)
                    nc.vector.scalar_tensor_tensor(out=mix[:, h, :], in0=turned_v[:], scalar=cols["g_norm_g"], in1=z[:, h, :],
                                                   op0=ALU.mult, op1=ALU.mult).then_inc(head_free, 1)


def neighbourhood_attention(nc, d, consts, cols, dram, nq, nk, nv, mix):
    NU = 2 * DT
    WK = WIN_R * GRID
    WE = WK + P

    def first_row(r):
        return min(max(r - WIN_R // 2, 0), GRID_ROWS - WIN_R)

    def shifted(pr):
        return first_row(2 * pr) != first_row(2 * pr + 1)

    units = [(pr, j) for pr in range(DT) for j in range(2)]
    with Phase(nc, "na") as ph:
        qs, ks = ph.sb("qs", [P, S]), ph.sb("ks", [P, S])
        vs = ph.sb("vs", [P, DT, P])
        table = ph.sb("table", [P, 2, RPB_R * GRID])
        window = ph.sb("window", [P, RPB_R * GRID])
        s = ph.sb("s", [P, 2, WK])
        e = ph.sb("e", [P, 2, WE])
        et = ph.sb("et", [P, 2, WE])
        small = ph.sb("small", [P, 2, 3])
        ob = ph.sb("ob", [P, S])
        sq = ph.sb("sq", [P, S])
        sc = [ph.ps(f"sc{i}", [P, HALF]) for i in range(2)]
        turned = [ph.ps(f"turned{i}", [P, S]) for i in range(2)]
        o = [ph.ps(f"o{i}", [P, HALF]) for i in range(2)]
        window_landed = ph.sem("window_landed")
        tables_stored = ph.sem("tables_stored")
        table_landed = [ph.sem(f"table_landed{i}") for i in range(4)]
        table_ready = ph.sem("table_ready")
        staged = ph.sem("staged")
        pair_free = ph.sem("pair_free")
        waited = ph.sem("waited")
        sc_ready = ph.sem("sc_ready")
        max_ready = ph.sem("max_ready")
        exp_ready = ph.sem("exp_ready")
        e_ready = ph.sem("e_ready")
        turned_ready = ph.sem("turned_ready")
        et_ready = ph.sem("et_ready")
        o_ready = ph.sem("o_ready")
        o_taken = ph.sem("o_taken")
        squared, summed, std_ready = ph.sem("squared"), ph.sem("summed"), ph.sem("std_ready")
        rpb = d["rpb"]
        toeplitz = bass.AP(rpb.tensor, GRID - 1, [[RPB_R * 2 * GRID, 2 * 4], [2 * GRID, RPB_R], [-1, GRID], [1, GRID]])

        with nc.Block() as block:

            @block.sync
            def _(sp):
                sp.dma_start(window[:], d["na_columns"]).then_inc(window_landed, 16)
                for head in range(8):
                    sp.dma_start(dram["n_tables"][head].rearrange("q (r c) -> r q c", c=GRID), toeplitz[head]).then_inc(tables_stored, 16)
                sp.wait_ge(tables_stored, 8 * 16)
                with sp.Fori(0, 4) as b:
                    sp.wait_ge(pair_free, b + 1)
                    for j in range(2):
                        for i in range(2):
                            sp.dma_start(table[i * GRID:(i + 1) * GRID, j, :], dram["n_tables"][2 * b + j]).then_inc(table_landed[2 * j + i], 16)

            @block.gpsimd
            def _(pool):
                with pool.Fori(0, 4) as b:
                    pool.wait_ge(pair_free, b + 1)
                    nc.gpsimd.tensor_copy(qs[:], nq[:, b, :])
                    nc.gpsimd.tensor_copy(ks[:], nk[:, b, :])
                    nc.gpsimd.tensor_copy(vs[:], nv[:].rearrange("p t (b c) -> p t b c", c=P)[:, :, b, :])
                    pool.drain().then_inc(staged, 1)

            @block.tensor
            def _(pe):
                with pe.Fori(0, 4) as b:
                    pe.wait_ge(staged, b + 1)
                    for u in range(NU + 2):
                        if u < NU:
                            pr, j = units[u]
                            rows = slice(N_D * j, N_D * (j + 1))
                            if u >= 2:
                                pe.wait_ge(max_ready, NU * b + u - 1)
                            pe.sem_inc(waited, 1)
                            for i in range(2):
                                r = 2 * pr + i
                                k0 = first_row(r) * GRID
                                last = nc.tensor.matmul(sc[j][i * GRID:(i + 1) * GRID, :], qs[rows, r * GRID:(r + 1) * GRID],
                                                        ks[rows, k0:k0 + WK], start=True, stop=True)
                            last.then_inc(sc_ready, 1)
                        if 1 <= u <= NU:
                            pr, j = units[u - 1]
                            pe.wait_ge(e_ready, NU * b + u)
                            if u >= 3:
                                pe.wait_ge(et_ready, NU * b + u - 2)
                            for t in range(5 if shifted(pr) else 4):
                                last = nc.tensor.transpose(turned[j][:, t * P:(t + 1) * P], e[:, j, t * P:(t + 1) * P], consts["ident"])
                            last.then_inc(turned_ready, 1)
                        if u >= 2:
                            pr, j = units[u - 2]
                            rows = slice(N_D * j, N_D * (j + 1))
                            tiles = 5 if shifted(pr) else 4
                            pe.wait_ge(et_ready, NU * b + u - 1)
                            if j == 0 and pr >= 2:
                                pe.wait_ge(o_taken, DT * b + pr - 1)
                            for t in range(tiles):
                                last = nc.tensor.matmul(o[pr % 2][rows, 0:P], vs[:, first_row(2 * pr) // 2 + t, rows],
                                                        et[:, j, t * P:(t + 1) * P], start=(t == 0), stop=(t == tiles - 1))
                            if j == 1:
                                last.then_inc(o_ready, 1)
                    pe.wait_ge(squared, b + 1)
                    for half in range(2):
                        c = slice(half * HALF, (half + 1) * HALF)
                        last = nc.tensor.matmul(turned[0][:, c], consts["ones64"], sq[:, c], start=True, stop=True)
                    last.then_inc(summed, 1)

            @block.vector
            def _(ve):
                ve.sem_inc(pair_free, 1)
                ve.wait_ge(window_landed, 16)
                with ve.Fori(0, 4) as b:
                    for i in range(4):
                        ve.wait_ge(table_landed[i], 16 * b + 16)
                    nc.vector.tensor_tensor(table[:], table[:], window[:, None, :].broadcast_to([P, 2, RPB_R * GRID]), ALU.min)
                    ve.drain()
                    for u in range(NU + 1):
                        if u < NU:
                            pr, j = units[u]
                            ve.wait_ge(sc_ready, NU * b + u + 1)
                            if u >= 2:
                                ve.wait_ge(exp_ready, NU * b + u - 1)
                            at = [(first_row(2 * pr + i) - 2 * pr - i + WIN_R - 1) * GRID for i in range(2)]
                            for rows, a in ([(slice(0, P), at[0])] if at[0] == at[1] else
                                            [(slice(i * GRID, (i + 1) * GRID), at[i]) for i in range(2)]):
                                nc.vector.scalar_tensor_tensor(out=s[rows, j, :], in0=sc[j][rows, :], scalar=N_D ** -0.5,
                                                               in1=table[rows, j, a:a + WK], op0=ALU.mult, op1=ALU.add)
                            ve.drain()
                            nc.vector.tensor_reduce(small[:, j, 0:1], s[:, j, :], AX_X, ALU.max, negate=True)
                            if shifted(pr) and not shifted(pr - 1):
                                ve.wait_ge(turned_ready, NU * b + u - 1)
                                nc.vector.memset(e[0:GRID, j, WK:WE], 0.0)
                                nc.vector.memset(e[GRID:P, j, 0:GRID], 0.0)
                                nc.vector.memset(e[GRID:P, j, WK + GRID:WE], 0.0)
                            ve.drain().then_inc(max_ready, 1)
                        if u >= 1:
                            pr, j = units[u - 1]
                            w = WE if shifted(pr) else WK
                            ve.wait_ge(exp_ready, NU * b + u)
                            nc.vector.reciprocal(small[:, j, 2:3], small[:, j, 1:2])
                            ve.drain()
                            nc.vector.tensor_scalar(e[:, j, 0:w], e[:, j, 0:w], small[:, j, 2:3], None, ALU.mult).then_inc(e_ready, 1)
                    ve.wait_ge(std_ready, b + 1)
                    nc.vector.reciprocal(sq[:], sq[:])
                    ve.drain()
                    nc.vector.scalar_tensor_tensor(out=mix[:, 4 + b, :], in0=ob[:], scalar=cols["n_norm_g"], in1=sq[:],
                                                   op0=ALU.mult, op1=ALU.mult).then_inc(pair_free, 1)

            @block.scalar
            def _(se):
                with se.Fori(0, 4) as b:
                    for u in range(NU + 2):
                        if u < NU:
                            pr, j = units[u]
                            se.wait_ge(max_ready, NU * b + u + 1)
                            if u >= 2:
                                se.wait_ge(turned_ready, NU * b + u - 1)
                            for i, rows in enumerate((slice(0, GRID), slice(GRID, P)) if shifted(pr) else (slice(0, P),)):
                                nc.scalar.activation(e[rows, j, i * GRID:i * GRID + WK], s[rows, j, :], ACT.Exp,
                                                     bias=small[rows, j, 0:1], accum_out=small[rows, j, 1:2])
                            se.drain().then_inc(exp_ready, 1)
                        if 1 <= u <= NU:
                            pr, j = units[u - 1]
                            w = WE if shifted(pr) else WK
                            se.wait_ge(turned_ready, NU * b + u)
                            nc.scalar.activation(et[:, j, 0:w], turned[j][:, 0:w], ACT.Copy).then_inc(et_ready, 1)
                        if u >= 2 and units[u - 2][1] == 1:
                            pr = units[u - 2][0]
                            se.wait_ge(o_ready, DT * b + pr + 1)
                            nc.scalar.activation(ob[:, pr * P:(pr + 1) * P], o[pr % 2][:, 0:P], ACT.Copy).then_inc(o_taken, 1)
                    se.drain()
                    nc.scalar.activation(sq[:], ob[:], ACT.Square).then_inc(squared, 1)
                    se.wait_ge(summed, b + 1)
                    nc.scalar.activation(sq[:], turned[0][:], ACT.Sqrt, scale=1.0 / N_D, bias=1e-6).then_inc(std_ready, 1)


def third_block(nc, d, consts, cols, x):
    def x_rows(k):
        return x[:, k, :]

    dram = {"g_gc": nc.dram_tensor("g_gc", (GATE_ROWS, S), F32, kind="Internal").ap(),
            "g_beta": nc.dram_tensor("g_beta", (GATE_ROWS, S), F32, kind="Internal").ap(),
            "g_end": nc.dram_tensor("g_end", (GATE_ROWS, DT), F32, kind="Internal").ap()}
    dram["n_tables"] = nc.dram_tensor("n_tables", (8, GRID, RPB_R * GRID), F32, kind="Internal").ap()
    norm_rows(nc, "b3_in", x, x, consts["ones"], cols["ln_in_g"], cols["ln_in_b"], centre=True)
    with ExitStack() as stack:
        with Phase(nc, "b3g") as ph:
            z = ph.sb("z", [P, 4, S])
            qkv = ph.sb("qkv", [P, 12, S])
            gate_cols = ph.sb("gate_cols", [P, 5, DT, GATE_ROWS])
            with Phase(nc, "b3r") as pg:
                ga, gb = pg.sb("ga", [GATE_ROWS, S]), pg.sb("gb", [GATE_ROWS, S])
                resets = pg.sb("resets", [P, S])
                load_phase(nc, "b3_resets", [(resets[:], d["reset128_3"])])
                project_rows(nc, "b3_ga", d["w_ga"], DT, x_rows, 1, m=GATE_ROWS,
                             act=lambda n, acc, tmp, i: nc.scalar.activation(ga[:], acc[:], ACT.Copy))
                project_rows(nc, "b3_gb", d["w_gb"], DT, x_rows, 1, m=GATE_ROWS,
                             act=lambda n, acc, tmp, i: nc.scalar.activation(gb[:], acc[:], ACT.Copy))
                delta_rows(nc, ga, gb, cols, dict(consts, reset128=resets[:]), dram, gate_cols)
            with Phase(nc, "b3x", side="right") as px:
                pair = Pair(px, "x", DT, within=x)
                split_rows(nc, "b3_split", x, pair)
                project_pair(nc, "b3_z", d["w_gz"], DT, pair.rows, 4,
                             act=lambda n, j, i, acc, tmp: nc.scalar.activation(z[:, n, :], acc[:], ACT.Silu))
                conv_pair(nc, "b3_conv", d["w_gqkv"], 12, pair.rows, lambda n, tap: cols["g_taps"][:, bass.ds(TAPS * n + tap, 1)], qkv)
                join_rows(nc, "b3_join", pair, x)
            mix = stack.enter_context(Phase(nc, "b3", side="right")).sb("mix", [P, DT, S])
            l2_normalise(nc, d, qkv)
            delta_rule(nc, d, consts, cols, dram, qkv, z, gate_cols, mix)
        with Phase(nc, "b3n") as ph:
            nq, nk = ph.sb("nq", [P, 4, S]), ph.sb("nk", [P, 4, S])
            nv = ph.sb("nv", [P, DT, HALF])
            project_tokens(nc, "b3_nv", d["w_nv"], HALF, x, act=lambda n, acc: nc.scalar.activation(nv[:, n, :], acc[:], ACT.Copy))
            with Phase(nc, "b3y") as py:
                pair = Pair(py, "x", DT, within=x)
                split_rows(nc, "b3_splitn", x, pair)
                project_pair(nc, "b3_nq", d["w_nq"], DT, pair.rows, 4,
                             act=lambda n, j, i, acc, tmp: nc.scalar.activation(nq[:, n, :], acc[:], ACT.Copy))
                project_pair(nc, "b3_nk", d["w_nk"], DT, pair.rows, 4,
                             act=lambda n, j, i, acc, tmp: nc.scalar.activation(nk[:, n, :], acc[:], ACT.Copy))
                join_rows(nc, "b3_joinn", pair, x)
            neighbourhood_attention(nc, d, consts, cols, dram, nq, nk, nv, mix)
        out_projection(nc, "b3_out", d["w_out3"], mix, x)
    norm_rows(nc, "b3_ln1", x, x, consts["ones"], cols["ln1_g3"], cols["ln1_b3"], centre=True)
    with Phase(nc, "b3f") as ph:
        y = ph.sb("y", [P, DT, S])
        pair = Pair(ph, "x", DT, within=x)
        hidden = Pair(ph, "hidden", DT)
        split_rows(nc, "b3_splitf", x, pair)
        for c in range(D_FF3 // P // DT):
            b1 = cols["b1_3"][:, c * DT:(c + 1) * DT]

            def squared(n, j, i, acc, tmp, res):
                nc.vector.tensor_tensor(tmp[:], tmp[:], tmp[:], ALU.mult)
                nc.vector.drain()
                put_pair(nc, hidden, n, tmp)

            project_pair(nc, f"b3_w1{c}", d["w1_3"][c * DT:(c + 1) * DT], DT, pair.rows, DT, dve=squared,
                         act=lambda n, j, i, acc, tmp: nc.scalar.activation(tmp[:], acc[:], ACT.Relu, bias=b1[:, bass.ds(n, 1)]))
            if c == 0:
                project_pair(nc, f"b3_w2{c}", d[f"w2_3_{c}"], DT, hidden.rows, 8,
                             act=lambda n, j, i, acc, tmp: nc.scalar.activation(tmp[:], acc[:], ACT.Identity, bias=cols["b2_3"][:, bass.ds(n, 1)]),
                             dve=lambda n, j, i, acc, tmp, res: add_residual(nc, y[:, n, :], pair, n, tmp[:]))
            else:
                project_pair(nc, f"b3_w2{c}", d[f"w2_3_{c}"], DT, hidden.rows, 8,
                             dve=lambda n, j, i, acc, tmp, res: nc.vector.tensor_tensor(y[:, n, :], y[:, n, :], acc[:], ALU.add))
        norm_rows(nc, "b3_ln2", y, x, consts["ones"], cols["ln2_g3"], cols["ln2_b3"], centre=True)


L3_COLUMNS = {"ln_in_g": 8, "ln_in_b": 8, "g_alog": 1, "g_dt": 1, "g_taps": 60, "g_norm_g": 1, "n_norm_g": 1,
              "ln1_g3": 8, "ln1_b3": 8, "b1_3": 32, "b2_3": 8, "ln2_g3": 8, "ln2_b3": 8}
L3_SQUARES = ()


def third_arrays(a):
    import numpy as np
    w = a["w_in_3"][0]
    gqkv, gz, ga, gb, nq, nk, nv = np.split(w, np.cumsum([1536, 512, 8, 8, 512, 512]), axis=1)
    tiles = lambda g: gate_rows(g).reshape(DT, P, GATE_ROWS).transpose(1, 0, 2).reshape(1, P, DT * GATE_ROWS)
    i = np.arange(P)
    forward = np.stack([(i[:, None] >> (l + 1) == i[None, :] >> (l + 1)) & ((i[:, None] >> l) % 2 == 0) & ((i[None, :] >> l) % 2 == 1)
                        for l in range(LEVELS)])
    levels = np.concatenate([forward, forward.transpose(0, 2, 1)]).astype(np.float32).transpose(1, 0, 2).reshape(P, -1)
    eye = np.eye(8, dtype=np.float32)
    rpb = np.zeros((8, RPB_R, 2 * GRID), np.float32)
    rpb[:, :, GRID - WIN_C:GRID - WIN_C + RPB_C] = a["rpb_3"][0]
    q, k = np.arange(GRID)[:, None], np.arange(GRID)[None, :]
    start = np.clip(q - WIN_C // 2, 0, GRID - WIN_C)
    window = np.where((k >= start) & (k < start + WIN_C), BIG, -BIG).astype(np.float32)
    w2 = a["w2_3"][0]
    out = {"w_gqkv": rows_weight(gqkv), "w_gz": rows_weight(gz), "w_ga": tiles(ga), "w_gb": tiles(gb),
           "w_nq": rows_weight(nq), "w_nk": rows_weight(nk), "w_nv": tokens_weight(nv),
           "g_levels": levels, "l2_pick": np.tile(eye.reshape(1, 64), (P, 1)), "l2_spread": np.repeat(eye, P, axis=1),
           "rpb": rpb, "na_columns": np.tile(window, (2, RPB_R)), "w_out3": rows_weight(a["w_out_3"][0]),
           "w1_3": rows_weight(a["w1_3"][0]),
           "reset128_3": np.broadcast_to((np.arange(S) % P != 0).astype(np.float32), (P, S))}
    for c, part in enumerate(np.split(w2, D_FF3 // P // DT)):
        out[f"w2_3_{c}"] = rows_weight(part)
    columns = {"ln_in_g": column(a["ln_in_g_3"]), "ln_in_b": column(a["ln_in_b_3"]),
               "g_alog": gate_column(a["a_log_3"].reshape(8)), "g_dt": gate_column(a["dt_bias_3"].reshape(8)),
               "g_taps": a["conv_w_3"][0].reshape(TAPS, 12, P).transpose(2, 1, 0).reshape(P, 60),
               "g_norm_g": column(a["gdn_norm_g_3"]), "n_norm_g": np.tile(a["na_norm_g_3"].reshape(1, 64), (2, 1)).reshape(P, 1),
               "ln1_g3": column(a["ln1_g_3"]), "ln1_b3": column(a["ln1_b_3"]), "b1_3": column(a["b1_3"]), "b2_3": column(a["b2_3"]),
               "ln2_g3": column(a["ln2_g_3"]), "ln2_b3": column(a["ln2_b_3"])}
    return out, columns, {}

COLUMNS = {"pre_g": 8, "post_g": 8, "b_a2": 4, "b_norm_g": 8, "a_ln_g": 8, "a_ln_b": 8}
COLUMNS |= L2_COLUMNS | L3_COLUMNS
SQUARES = ("ones", "ident", "le", "gla_mask", "ones64") + tuple(L2_SQUARES) + tuple(L3_SQUARES)


def build_program(nc, d, layers=(1, 2, 3)):
    with Phase(nc, "all") as ph:
        x = ph.sb("x", [P, DT, S])
        squares = ph.sb("squares", [P, len(SQUARES), P])
        columns = ph.sb("columns", [P, sum(COLUMNS.values())])
        consts = {name: squares[:, i, :] for i, name in enumerate(SQUARES)}
        cols, at = {}, 0
        for name, n in COLUMNS.items():
            cols[name] = columns[:, at:at + n]
            at += n
        load_phase(nc, "consts", [(squares[:].rearrange("p n c -> p (n c)"), d["squares"]), (columns[:], d["columns"])])
        consts["le3"] = squares[:, SQUARES.index("le"):SQUARES.index("le") + 1, :].broadcast_to([P, 8, P])
        if 1 in layers:
            first_block(nc, d, consts, cols, x)
        else:
            load_phase(nc, "x", [(x[:, :, :], d["xT"].rearrange("p (t s) -> p t s", t=DT))])
        if 2 in layers:
            second_block(nc, d, consts, cols, x)
        if 3 in layers:
            third_block(nc, d, consts, cols, x)
        with Phase(nc, "store") as ps:
            stored = ps.sem("stored")
            with nc.Block() as block:

                @block.sync
                def _(sp):
                    sp.dma_start(d["outT"].rearrange("p (t s) -> p t s", t=DT), x[:, :, :]).then_inc(stored, 16)
                    sp.wait_ge(stored, 16)



def rows_weight(w):
    K, N = w.shape
    return w.reshape(K // P, P, N // P, P).transpose(2, 1, 0, 3).reshape(N // P, P, K)


def tokens_weight(w):
    K, N = w.shape
    return w.reshape(K // P, P, N).transpose(1, 0, 2).reshape(P, (K // P) * N)


def column(v):
    return v.reshape(-1, P).T


def causal_squares():
    import numpy as np
    i = np.arange(P)
    le = (i[:, None] <= i[None, :]).astype(np.float32)
    return {"ones": np.ones((P, P), np.float32), "ident": np.eye(P, dtype=np.float32), "le": le,
            "gla_mask": le * (i[:, None] // 64 == i[None, :] // 64),
            "ones64": (i[:, None] // 64 == i[None, :] // 64).astype(np.float32)}


def first_arrays(a):
    import numpy as np
    w = a["w_in"][0]
    cuts = np.cumsum([1024, 1024, 1024, 512, 512, 1024, 1024])
    au, av, ag, bq, bk, bv, bg, lr = np.split(w, cuts, axis=1)
    out = {"w_au": rows_weight(au), "w_agate": rows_weight(ag), "w_bgate": rows_weight(bg),
           "w_qk": rows_weight(w[:, 3072:4096]), "w_av": tokens_weight(av), "w_bv": tokens_weight(bv),
           "w_lr": lr.reshape(DT, P, 16).transpose(1, 0, 2).reshape(1, P, DT * 16),
           "w_a2": a["w_a2"][0].reshape(16, 4, P).transpose(1, 0, 2),
           "w_sT": a["a_w_s"][0].transpose(2, 0, 1).reshape(P, 8 * P),
           "b_s": a["a_b_s"].reshape(1, 8 * P), "w_out1a": rows_weight(a["w_out"][0][0:1024]), "w_out1b": rows_weight(a["w_out"][0][1024:]),
           "reset64": np.broadcast_to((np.arange(S) % 64 != 0).astype(np.float32), (P, S))}
    columns = {"pre_g": column(a["pre_norm_g"]), "post_g": column(a["post_norm_g"]), "b_a2": column(a["b_a2"]),
               "b_norm_g": column(a["b_norm_g"]), "a_ln_g": column(a["a_ln_g"]), "a_ln_b": column(a["a_ln_b"])}
    return out, columns, {}


def arrays_of(a, layers=(1, 2, 3)):
    import numpy as np
    out = {"xT": a["x"][0].T.reshape(DT, P, S).transpose(1, 0, 2).reshape(P, DT * S)}
    columns, squares = {}, causal_squares()
    for n, arrays in ((1, first_arrays), (2, second_arrays), (3, third_arrays)):
        more, cols, sqs = arrays(a)
        if n in layers:
            out.update(more)
        columns.update(cols)
        squares.update(sqs)
    for name, n in COLUMNS.items():
        assert columns[name].shape == (P, n), (name, columns[name].shape)
    out["columns"] = np.concatenate([columns[name] for name in COLUMNS], axis=1)
    out["squares"] = np.concatenate([squares[name] for name in SQUARES], axis=1)
    return {name: np.ascontiguousarray(v) for name, v in out.items()}


def kernel(**inputs):
    import numpy as _np
    import concourse.bacc as _bacc
    from concourse import mybir as _mybir
    from concourse.bass_utils import run_bass_kernel_spmd as _run

    nc = _bacc.Bacc("TRN2", target_bir_lowering=False, num_devices=1)
    arrays = arrays_of({name: _np.asarray(v) for name, v in inputs.items()})
    d = {name: nc.dram_tensor(name, v.shape, _mybir.dt.from_np(v.dtype), kind="ExternalInput").ap()
         for name, v in arrays.items()}
    d["outT"] = nc.dram_tensor("outT", (P, DT * S), F32, kind="ExternalOutput").ap()
    build_program(nc, d)
    r = _run(nc, [arrays], core_ids=[0])
    got = r.results[0]["outT"].reshape(P, DT, S).transpose(2, 1, 0).reshape(1, S, DT * P)
    return _np.ascontiguousarray(got)
```

```python
import math
from contextlib import ExitStack

import concourse.bass as bass
from concourse import mybir

P = 128
S = 1024
HALF = 512
DT = 8
F32 = mybir.dt.float32
F32R = mybir.dt.float32r
ACT = mybir.ActivationFunctionType
ALU = mybir.AluOpType
AX_X = mybir.AxisListType.X
ROWS = "p (t s) -> p t s"
ALPHA = 2.0 ** 0.25
GATE_ROWS = 36
TAPS = 5
PAD = TAPS // 2
BIG = 1.0e30

PLACES = {}


class Phase:

    def __init__(self, nc, name, side="left"):
        self.nc, self.name, self.side, self.stack, self.sems = nc, name, side, ExitStack(), []

    def __enter__(self):
        self.stack.__enter__()
        return self

    def __exit__(self, *what):
        for sem in self.sems:
            self.nc.sync.sem_clear(sem)
        return self.stack.__exit__(*what)

    def sb(self, name, shape, dt=F32):
        got = self.stack.enter_context(self.nc.sbuf_tensor(f"{self.name}_{name}", shape, dt, side=self.side))
        size = 4 * math.prod(shape[1:])
        PLACES[got.name] = self.nc.sbuf_base - size if self.side == "left" else self.nc.sbuf_top
        return got

    def ps(self, name, shape, dt=F32):
        return self.stack.enter_context(self.nc.psum_tensor(f"{self.name}_{name}", shape, dt))

    def sem(self, name):
        self.sems.append(self.stack.enter_context(self.nc.semaphore(f"{self.name}_{name}")))
        return self.sems[-1]


def load_phase(nc, name, pairs):
    with Phase(nc, name) as ph:
        landed = [ph.sem(f"landed{i}") for i in range(len(pairs))]
        with nc.Block() as block:

            @block.sync
            def _(sp):
                for i, (dst, src) in enumerate(pairs):
                    sp.dma_start(dst, src).then_inc(landed[i], 16)
                for i in range(len(pairs)):
                    sp.wait_ge(landed[i], 16)


def project_rows(nc, name, w, KT, rhs, NB, act=None, dve=None, kp=P, m=P):
    with Phase(nc, name) as ph:
        wt = [ph.sb(f"w{i}", [kp, KT, m]) for i in range(2)]
        tmp = [ph.sb(f"tmp{i}", [m, S]) for i in range(2)]
        acc = [ph.ps(f"acc{i}", [m, S]) for i in range(2)]
        w_landed = [ph.sem(f"w_landed{i}") for i in range(2)]
        acc_ready = ph.sem("acc_ready")
        act_done = ph.sem("act_done")
        taken = ph.sem("taken")
        blocks2, odd = NB // 2, NB % 2
        last_reader_is_dve = dve is not None

        with nc.Block() as block:

            @block.sync
            def _(sp):
                def load(n, i):
                    sp.dma_start(wt[i][:], w[n].rearrange("k (t m) -> k t m", t=KT)).then_inc(w_landed[i], 16)

                load(0, 0)
                if NB > 1:
                    load(1, 1)
                if blocks2 > 1:
                    with sp.Fori(1, blocks2) as j:
                        for i in range(2):
                            sp.wait_ge(acc_ready, 2 * j - 1 + i)
                            load(2 * j + i, i)
                if odd and NB > 1:
                    sp.wait_ge(acc_ready, NB - 2)
                    load(NB - 1, 0)

            @block.tensor
            def _(pe):
                def product(n, i, round_):
                    pe.wait_ge(w_landed[i], 16 * round_ + 16)
                    pe.wait_ge(taken, n + 1)
                    for k in range(KT):
                        for half in range(2):
                            cols = slice(half * HALF, (half + 1) * HALF)
                            last = nc.tensor.matmul(acc[i][:, cols], wt[i][:, k, :], rhs(k)[:, cols],
                                                    start=(k == 0), stop=(k == KT - 1))
                    last.then_inc(acc_ready, 1)

                if blocks2:
                    with pe.Fori(0, blocks2) as j:
                        for i in range(2):
                            product(2 * j + i, i, j)
                if odd:
                    product(NB - 1, 0, blocks2)

            if act is not None:
                @block.scalar
                def _(se):
                    if not last_reader_is_dve:
                        se.sem_inc(taken, 2)

                    def take(n, i):
                        se.wait_ge(acc_ready, n + 1)
                        if last_reader_is_dve:
                            se.wait_ge(taken, n + 1)
                        act(n, acc[i], tmp[i], i).then_inc(act_done if last_reader_is_dve else taken, 1)

                    if blocks2:
                        with se.Fori(0, blocks2) as j:
                            for i in range(2):
                                take(2 * j + i, i)
                    if odd:
                        take(NB - 1, 0)

            if last_reader_is_dve:
                @block.vector
                def _(ve):
                    ve.sem_inc(taken, 2)

                    def take(n, i):
                        ve.wait_ge(act_done if act is not None else acc_ready, n + 1)
                        last = dve(n, acc[i], tmp[i], i)
                        if last is None:
                            ve.drain().then_inc(taken, 1)
                        else:
                            last.then_inc(taken, 1)

                    if blocks2:
                        with ve.Fori(0, blocks2) as j:
                            for i in range(2):
                                take(2 * j + i, i)
                    if odd:
                        take(NB - 1, 0)


def tile_of(src, n):
    return src[:].rearrange("p t (n c) -> p t n c", c=P)[:, :, n, :]


def tile_product(nc, acc, stage, wt, N):
    for k in range(DT):
        for a in range(0, N, HALF):
            cols = slice(a, min(a + HALF, N))
            last = nc.tensor.matmul(acc[:, cols], stage[:, k, :], wt[:, k, cols], start=(k == 0), stop=(k == DT - 1))
    return last


def gate_inputs(nc, name, w, x, first, second):
    R = GATE_ROWS

    def part(n, acc, tmp, i):
        nc.scalar.activation(first[:], acc[0:R, :], ACT.Copy)
        nc.scalar.activation(second[:], acc[64:64 + R, :], ACT.Copy)
        return nc.scalar.drain()

    project_rows(nc, name, w, DT, lambda k: x[:, k, :], 1, m=64 + R, act=part)


def chunk_resets(nc, resets, chunk=P):
    nc.vector.memset(resets[:], 1.0)
    nc.vector.drain()
    nc.vector.memset(resets[:].rearrange("p (n c) -> p n c", c=chunk)[:, :, 0], 0.0)


def norm_rows(nc, name, x, out, consts, g, b=None, centre=False, eps=1e-5, add=None, preload=None, source=None, sink=None, block_sum=None):
    D = DT * P
    with Phase(nc, name) as ph:
        sq = [ph.sb(f"sq{i}", [P, S]) for i in range(4)]
        pick = ph.sb("pick", [P, DT, DT])
        spread = ph.sb("spread", [DT, DT, P])
        rows = ph.sb("rows", [DT, P])
        addt = [ph.sb(f"add{i}", [P, S]) for i in range(2)] if add is not None else None
        total = ph.ps("total", [P, S])
        total_sq = ph.ps("total_sq", [DT, P])
        partial = ph.sem("partial")
        summed = ph.sem("summed")
        centred = ph.sem("centred")
        squared = ph.sem("squared")
        paired = ph.sem("paired")
        sq_used = ph.sem("sq_used")
        std_ready, rstd_ready, spread_ready = ph.sem("std_ready"), ph.sem("rstd_ready"), ph.sem("spread_ready")
        scaled = ph.sem("scaled")
        pick_landed, spread_landed = ph.sem("pick_landed"), ph.sem("spread_landed")
        add_landed = [ph.sem(f"add_landed{i}") for i in range(2)]
        added = ph.sem("added")
        preloaded = ph.sem("preloaded")
        biased, stored = ph.sem("biased"), ph.sem("stored")
        x_landed = [ph.sem(f"x_landed{k}") for k in range(DT)] if source is not None else None
        parts = (slice(0, 5), slice(5, 8))

        def part_sum(engine, eng, i):
            blocks = list(range(DT))[parts[i]]
            engine.tensor_tensor(sq[i][:], x[:, blocks[0], :], x[:, blocks[1], :], ALU.add)
            for k in blocks[2:]:
                eng.drain()
                engine.tensor_tensor(sq[i][:], sq[i][:], x[:, k, :], ALU.add)
            eng.drain().then_inc(partial, 1)

        with nc.Block() as block:

            @block.sync
            def _(sp):
                if source is not None:
                    for k in range(DT):
                        sp.dma_start(x[:, k, :], source.rearrange(ROWS, t=DT)[:, k, :]).then_inc(x_landed[k], 16)
                sp.dma_start(pick[:].rearrange("p a b -> p (a b)"), consts["pick_rows"]).then_inc(pick_landed, 16)
                sp.dma_start(spread[:].rearrange("p a b -> p (a b)"), consts["spread_rows"]).then_inc(spread_landed, 16)
                if preload is not None:
                    sp.dma_start(*preload).then_inc(preloaded, 16)
                if add is not None:
                    for k in range(DT):
                        if k >= 2:
                            sp.wait_ge(added, k - 1)
                        sp.dma_start(addt[k % 2][:], add.rearrange(ROWS, t=DT)[:, k, :]).then_inc(add_landed[k % 2], 16)
                if preload is not None:
                    sp.wait_ge(preloaded, 16)
                if sink is not None:
                    for k in range(DT):
                        sp.wait_ge(biased, k + 1)
                        sp.dma_start(sink.rearrange(ROWS, t=DT)[:, k, :], out[:, k, :]).then_inc(stored, 16)
                    sp.wait_ge(stored, 16 * DT)

            @block.gpsimd
            def _(pool):
                if centre and block_sum is None:
                    part_sum(nc.gpsimd, pool, 1)
                for m in range(DT // 2):
                    pool.wait_ge(squared, 2 * m + 2)
                    even, odd = sq[2 * m % 4], sq[(2 * m + 1) % 4]
                    nc.gpsimd.tensor_tensor(even[:], even[:], odd[:], ALU.add).then_inc(paired, 1)

            @block.tensor
            def _(pe):
                if centre:
                    sums = [block_sum] if block_sum is not None else sq[0:2]
                    if block_sum is None:
                        pe.wait_ge(partial, 2)
                    for i, part in enumerate(sums):
                        for half in range(2):
                            cols = slice(half * HALF, (half + 1) * HALF)
                            last = nc.tensor.matmul(total[:, cols], consts["ones"], part[:, cols],
                                                    start=(i == 0), stop=(i == len(sums) - 1))
                    last.then_inc(summed, 1)
                pe.wait_ge(pick_landed, 16)
                for m in range(DT // 2):
                    pe.wait_ge(paired, m + 1)
                    for t in range(DT):
                        last = nc.tensor.matmul(total_sq[:], pick[:, t, :], sq[2 * m % 4][:, t * P:(t + 1) * P],
                                                start=(m == 0 and t == 0), stop=(m == DT // 2 - 1 and t == DT - 1))
                    last.then_inc(sq_used, 1)
                pe.wait_ge(spread_landed, 16)
                pe.wait_ge(rstd_ready, 1)
                for t in range(DT):
                    last = nc.tensor.matmul(total[:, t * P:(t + 1) * P], spread[:, t, :], rows[:], start=True, stop=True)
                last.then_inc(spread_ready, 1)

            @block.scalar
            def _(se):
                for k in range(DT):
                    if centre:
                        se.wait_ge(centred, k + 1)
                    if source is not None:
                        se.wait_ge(x_landed[k], 16)
                    if k >= 4:
                        se.wait_ge(sq_used, (k - 4) // 2 + 1)
                    nc.scalar.activation(sq[k % 4][:], x[:, k, :], ACT.Square).then_inc(squared, 1)
                se.wait_ge(sq_used, DT // 2)
                nc.scalar.activation(rows[:], total_sq[:], ACT.Sqrt, scale=1.0 / D, bias=eps).then_inc(std_ready, 1)
                if b is not None:
                    for k in range(DT):
                        se.wait_ge(scaled, k + 1)
                        nc.scalar.activation(out[:, k, :], out[:, k, :], ACT.Identity, bias=b[:, k:k + 1]).then_inc(biased, 1)

            @block.vector
            def _(ve):
                if centre:
                    if block_sum is None:
                        part_sum(nc.vector, ve, 0)
                    ve.wait_ge(summed, 1)
                    for k in range(DT):
                        nc.vector.scalar_tensor_tensor(out=x[:, k, :], in0=total[:], scalar=-1.0 / D, in1=x[:, k, :],
                                                       op0=ALU.mult, op1=ALU.add).then_inc(centred, 1)
                ve.wait_ge(std_ready, 1)
                nc.vector.reciprocal(rows[:], rows[:]).then_inc(rstd_ready, 1)
                ve.wait_ge(spread_ready, 1)
                for k in range(DT):
                    nc.vector.scalar_tensor_tensor(out=out[:, k, :], in0=x[:, k, :], scalar=g[:, k:k + 1], in1=total[:],
                                                   op0=ALU.mult, op1=ALU.mult).then_inc(scaled, 1)
                    if add is not None:
                        ve.wait_ge(scaled, k + 1)
                        ve.wait_ge(add_landed[k % 2], 16 * (k // 2) + 16)
                        nc.vector.tensor_tensor(out[:, k, :], out[:, k, :], addt[k % 2][:], ALU.add).then_inc(added, 1)


class Pair:

    def __init__(self, ph, name, KT, within=None):
        self.hi = ph.sb(f"{name}_hi", [P, KT, S], F32R)
        if within is None:
            self.lo = ph.sb(f"{name}_lo", [P, KT, S], F32R)
        else:
            self.lo = ph.nc.alloc_sbuf_tensor_at(f"{ph.name}_{name}_lo", [P, KT, S], F32R, offset=PLACES[within.name])

    def rows(self, k):
        return self.hi[:, k, :], self.lo[:, k, :]


def split_blocks(splits):
    return [(x, pair, k) for x, pair, KT in splits for k in range(KT)]


def split_high(nc, blocks, rounded):
    for x, pair, k in blocks:
        nc.scalar.activation(pair.hi[:, k, :], x[:, k, :], ACT.Copy).then_inc(rounded, 1)


def split_low(nc, ve, blocks, rounded, split_done, done=0):
    for n, (x, pair, k) in enumerate(blocks):
        ve.wait_ge(rounded, done + n + 1)
        nc.vector.tensor_tensor(pair.lo[:, k, :], x[:, k, :], pair.hi[:, k, :], ALU.subtract).then_inc(split_done, 1)


class Stage:

    def __init__(self, w, KT, rhs, NB, act=None, dve=None, late=None, pairs=False, pads=0):
        assert NB % 2 == 0 and NB >= 4
        self.w, self.KT, self.rhs, self.NB, self.J = w, KT, rhs, NB, NB // 2
        self.act, self.dve, self.late, self.pairs, self.pads = act, dve, late, pairs, pads


def project_chain(nc, name, stages, splits=(), join=None, block_sum=None):
    KT_MAX = max(st.KT for st in stages)
    pads = max(st.pads for st in stages)
    split = split_blocks(splits)
    begin, acts, at, acted = [], [], 0, 0
    for st in stages:
        begin.append(at)
        acts.append(acted)
        at += st.NB
        if st.act is not None and st.dve is not None:
            acted += st.J if st.pairs else st.NB
    with Phase(nc, name) as ph:
        raw = [ph.sb(f"raw{i}", [P, KT_MAX * P]) for i in range(2)]
        wh = [ph.sb(f"wh{i}", [P, KT_MAX * P], F32R) for i in range(2)]
        wl = [ph.sb(f"wl{i}", [P, KT_MAX * P], F32R) for i in range(2)]
        tmp = [ph.sb(f"tmp{i}", [P, S + 2 * pads]) for i in range(2)] if acted else [None] * 2
        conv = [ph.sb(f"conv{i}", [P, S]) for i in range(2)] if pads else [None] * 2
        acc = [ph.ps(f"acc{i}", [P, S]) for i in range(2)]
        w_landed = [ph.sem(f"w_landed{i}") for i in range(2)]
        hi_done = ph.sem("hi_done")
        lo_done = ph.sem("lo_done")
        acc_ready = ph.sem("acc_ready")
        act_done = ph.sem("act_done")
        taken = ph.sem("taken")
        late_done = ph.sem("late_done")
        rounded = ph.sem("rounded")
        split_done = ph.sem("split_done")

        with nc.Block() as block:

            @block.sync
            def _(sp):
                for st, b in zip(stages, begin):
                    def load(j, i):
                        sp.dma_start(raw[i][:, 0:st.KT * P], st.w[2 * j + i]).then_inc(w_landed[i], 16)

                    for i in range(2):
                        if b:
                            sp.wait_ge(lo_done, b + i - 1)
                        load(0, i)
                    with sp.Fori(1, st.J) as j:
                        for i in range(2):
                            sp.wait_ge(lo_done, b + 2 * j + i - 1)
                            load(j, i)

            @block.tensor
            def _(pe):
                for st, b in zip(stages, begin):
                    if b:
                        pe.wait_ge(taken, b + 1)
                        if split:
                            pe.wait_ge(split_done, len(split))
                    with pe.Fori(0, st.J) as j:
                        for i in range(2):
                            pe.wait_ge(lo_done, b + 2 * j + i + 1)
                            pe.wait_ge(taken, b + 2 * j + i + 1)
                            for k in range(st.KT):
                                if b and i == 0 and k == st.KT - 1:
                                    pe.wait_ge(taken, b + 2)
                                if split and not b and i == 0:
                                    pe.wait_ge(split_done, k + 1)
                                xh, xl = st.rhs(k)
                                wk = slice(k * P, (k + 1) * P)
                                for half in range(2):
                                    c = slice(half * HALF, (half + 1) * HALF)
                                    nc.tensor.matmul(acc[i][:, c], wh[i][:, wk], xh[:, c], start=(k == 0), stop=False)
                                    nc.tensor.matmul(acc[i][:, c], wh[i][:, wk], xl[:, c], start=False, stop=False)
                                    last = nc.tensor.matmul(acc[i][:, c], wl[i][:, wk], xh[:, c], start=False, stop=(k == st.KT - 1))
                            last.then_inc(acc_ready, 1)

            @block.scalar
            def _(se):
                se.sem_inc(taken, 2)
                se.sem_inc(late_done, 2)
                split_high(nc, split[:2], rounded)

                def high(s, j, i, first=False):
                    st, b = stages[s], begin[s]
                    se.wait_ge(w_landed[i], 8 * b + 16 * j + 16)
                    if not first:
                        se.wait_ge(acc_ready, b + 2 * j + i - 1)
                    nc.scalar.activation(wh[i][:, 0:st.KT * P], raw[i][:, 0:st.KT * P], ACT.Copy).then_inc(hi_done, 1)

                def take(s, j, i):
                    st, n = stages[s], 2 * j + i
                    if st.act is None or (st.pairs and i):
                        return
                    se.wait_ge(acc_ready, begin[s] + n + 1)
                    if st.dve is not None:
                        se.wait_ge(taken, begin[s] + (n + 2 if st.pairs else n + 1))
                    st.act(n, acc[i], tmp[i]).then_inc(act_done if st.dve is not None else taken, 1)

                def end(s, j, i):
                    if stages[s].late is None:
                        return
                    se.wait_ge(taken, begin[s] + 2 * j + i + 3)
                    stages[s].late(2 * j + i, conv[i]).then_inc(late_done, 1)

                high(0, 0, 0, True)
                high(0, 0, 1, True)
                split_high(nc, split[2:], rounded)
                take(0, 0, 0)
                for s, st in enumerate(stages):
                    with se.Fori(0, st.J - 1) as j:
                        high(s, j + 1, 0)
                        take(s, j, 1)
                        end(s, j, 0)
                        high(s, j + 1, 1)
                        take(s, j + 1, 0)
                        end(s, j, 1)
                    more = s + 1 < len(stages)
                    if more:
                        high(s + 1, 0, 0)
                    take(s, st.J - 1, 1)
                    end(s, st.J - 1, 0)
                    if more:
                        high(s + 1, 0, 1)
                        take(s + 1, 0, 0)
                    end(s, st.J - 1, 1)

            @block.vector
            def _(ve):
                def low(s, j, i):
                    cols = slice(0, stages[s].KT * P)
                    ve.wait_ge(hi_done, begin[s] + 2 * j + i + 1)
                    nc.vector.tensor_tensor(wl[i][:, cols], raw[i][:, cols], wh[i][:, cols], ALU.subtract).then_inc(lo_done, 1)

                def take(s, j, i):
                    st, n = stages[s], 2 * j + i
                    if st.dve is None:
                        return
                    if st.act is None or (st.pairs and i):
                        ve.wait_ge(acc_ready, begin[s] + n + 1)
                    else:
                        ve.wait_ge(act_done, acts[s] + (j + 1 if st.pairs else n + 1))
                    if st.late is not None:
                        ve.wait_ge(late_done, n + 1)
                    if st.pairs and i == 0:
                        ve.sem_inc(taken, 1)
                    else:
                        st.dve(j if st.pairs else n, acc[i], tmp[0 if st.pairs else i], conv[i])
                        ve.drain().then_inc(taken, 1)

                split_low(nc, ve, split[:2], rounded, split_done)
                if pads:
                    for t in tmp:
                        nc.vector.memset(t[:, 0:pads], 0.0)
                        nc.vector.memset(t[:, pads + S:], 0.0)
                    ve.drain()
                low(0, 0, 0)
                low(0, 0, 1)
                split_low(nc, ve, split[2:], rounded, split_done, 2)
                take(0, 0, 0)
                for s, st in enumerate(stages):
                    with ve.Fori(0, st.J - 1) as j:
                        low(s, j + 1, 0)
                        take(s, j, 1)
                        low(s, j + 1, 1)
                        take(s, j + 1, 0)
                    more = s + 1 < len(stages)
                    if more:
                        low(s + 1, 0, 0)
                    take(s, st.J - 1, 1)
                    if more:
                        low(s + 1, 0, 1)
                        take(s + 1, 0, 0)
                if join is not None:
                    ve.wait_ge(acc_ready, at)
                    join_blocks(nc.vector, join, range(0, 5))

            if block_sum is not None:
                @block.gpsimd
                def _(pool):
                    tile, out = block_sum
                    for n in range(1, DT):
                        pool.wait_ge(taken, begin[-1] + n + 3)
                        if n > 1:
                            pool.drain()
                        nc.gpsimd.tensor_tensor(tile[:], (out[:, 0, :] if n == 1 else tile[:]), out[:, n, :], ALU.add)

            if join is not None:
                @block.gpsimd
                def _(pool):
                    pool.wait_ge(acc_ready, at)
                    join_blocks(nc.gpsimd, join, range(5, DT))


def join_blocks(engine, join, blocks):
    pair, x = join
    for k in blocks:
        engine.tensor_tensor(x[:, k, :], pair.hi[:, k, :], pair.lo[:, k, :], ALU.add)


def conv_stage(nc, w, NB, rhs, taps_of, out, bias_of=None):
    def copy(n, acc, tmp):
        return nc.scalar.activation(tmp[:, PAD:PAD + S], acc[:], ACT.Copy)

    def convolve(n, acc, tmp, conv):
        nc.vector.tensor_scalar(conv[:], tmp[:, 0:S], taps_of(n, 0), None, ALU.mult)
        for tap in range(1, TAPS):
            nc.vector.drain()
            nc.vector.scalar_tensor_tensor(out=conv[:], in0=tmp[:, tap:tap + S], scalar=taps_of(n, tap), in1=conv[:],
                                           op0=ALU.mult, op1=ALU.add)

    def silu(n, conv):
        if bias_of is None:
            return nc.scalar.activation(out[:, n, :], conv[:], ACT.Silu)
        return nc.scalar.activation(out[:, n, :], conv[:], ACT.Silu, bias=bias_of(n))

    return Stage(w, DT, rhs, NB, act=copy, dve=convolve, late=silu, pads=PAD)


def copy_stage(nc, w, rhs, NB, dst, func=ACT.Copy):
    return Stage(w, DT, rhs, NB, act=lambda n, acc, tmp: nc.scalar.activation(dst[:, n, :], acc[:], func))


def add_stage(nc, w, KT, rhs, NB, dst):
    return Stage(w, KT, rhs, NB, dve=lambda n, acc, tmp, conv: nc.vector.tensor_tensor(dst[:, n, :], dst[:, n, :], acc[:], ALU.add))


class Aside:

    def __init__(self, scalar=(), vector=None, tensor=None, sync=None):
        self.scalar, self.vector, self.tensor, self.sync = scalar, vector, tensor, sync


def tokens_pair(nc, name, w, N, pair, act, splits=(), aside=Aside()):
    split = split_blocks(splits)
    with Phase(nc, name) as ph:
        raw = [ph.sb(f"raw{i}", [P, N]) for i in range(2)]
        wh, wl = ph.sb("wh", [P, DT, N], F32R), ph.sb("wl", [P, DT, N], F32R)
        acc = [ph.ps(f"acc{i}", [P, N]) for i in range(2)]
        w_landed = [ph.sem(f"w_landed{i}") for i in range(2)]
        hi_done, lo_done = ph.sem("hi_done"), ph.sem("lo_done")
        acc_ready = ph.sem("acc_ready")
        taken = ph.sem("taken")
        rounded, split_done = ph.sem("rounded"), ph.sem("split_done")

        with nc.Block() as block:

            @block.sync
            def _(sp):
                for k in range(DT):
                    if k >= 2:
                        sp.wait_ge(lo_done, k - 1)
                    sp.dma_start(raw[k % 2][:], w[:, k, :]).then_inc(w_landed[k % 2], 16)
                if aside.sync:
                    aside.sync(sp)

            @block.tensor
            def _(pe):
                for n in range(DT):
                    if n >= 2:
                        pe.wait_ge(taken, n - 1)
                    tile = slice(n * P, (n + 1) * P)
                    for k in range(DT):
                        if n == 0:
                            pe.wait_ge(lo_done, k + 1)
                            if split:
                                pe.wait_ge(split_done, k + 1)
                        xh, xl = pair.rows(k)
                        nc.tensor.matmul(acc[n % 2][:], xh[:, tile], wh[:, k, :], start=(k == 0), stop=False)
                        nc.tensor.matmul(acc[n % 2][:], xh[:, tile], wl[:, k, :], start=False, stop=False)
                        last = nc.tensor.matmul(acc[n % 2][:], xl[:, tile], wh[:, k, :], start=False, stop=(k == DT - 1))
                    last.then_inc(acc_ready, 1)
                if aside.tensor:
                    aside.tensor(pe)

            @block.scalar
            def _(se):
                for k in range(DT):
                    split_high(nc, split[k:k + 1], rounded)
                    se.wait_ge(w_landed[k % 2], 16 * (k // 2) + 16)
                    nc.scalar.activation(wh[:, k, :], raw[k % 2][:], ACT.Copy).then_inc(hi_done, 1)
                parts = dict(zip((0, 4, DT), aside.scalar))
                for n in range(DT + 1):
                    if n in parts:
                        parts[n](se)
                    if n < DT:
                        se.wait_ge(acc_ready, n + 1)
                        act(n, acc[n % 2]).then_inc(taken, 1)

            @block.vector
            def _(ve):
                for k in range(DT):
                    split_low(nc, ve, split[k:k + 1], rounded, split_done, k)
                    ve.wait_ge(hi_done, k + 1)
                    nc.vector.tensor_tensor(wl[:, k, :], raw[k % 2][:], wh[:, k, :], ALU.subtract).then_inc(lo_done, 1)
                if aside.vector:
                    aside.vector(ve)


def put_pair(nc, pair, k, x):
    nc.vector.tensor_copy(pair.hi[:, k, :], x[:])
    nc.vector.drain()
    nc.vector.tensor_tensor(pair.lo[:, k, :], x[:], pair.hi[:, k, :], ALU.subtract)


def add_residual(nc, out, pair, k, more):
    nc.vector.scalar_tensor_tensor(out=out, in0=pair.lo[:, k, :], scalar=ALPHA, in1=more, op0=ALU.mult, op1=ALU.add)
    nc.vector.drain()
    nc.vector.scalar_tensor_tensor(out=out, in0=pair.hi[:, k, :], scalar=ALPHA, in1=out, op0=ALU.mult, op1=ALU.add)


def out_projection(nc, name, w, mix, x, block_sum, x_pair=None):
    def residual(n, acc, tmp, conv):
        if x_pair is None:
            nc.vector.scalar_tensor_tensor(out=x[:, n, :], in0=x[:, n, :], scalar=ALPHA, in1=acc[:], op0=ALU.mult, op1=ALU.add)
        else:
            nc.vector.tensor_tensor(x[:, n, :], x_pair.hi[:, n, :], x_pair.lo[:, n, :], ALU.add)
            nc.vector.drain()
            nc.vector.scalar_tensor_tensor(out=x[:, n, :], in0=x[:, n, :], scalar=ALPHA, in1=acc[:], op0=ALU.mult, op1=ALU.add)

    with Phase(nc, name + "p") as ph:
        pair = Pair(ph, "mix", DT, within=mix)
        project_chain(nc, name, [Stage(w, DT, pair.rows, 8, dve=residual)], splits=[(mix, pair, DT)],
                      block_sum=(block_sum, x))

GLA_H, GLA_DK, GLA_DV, GLA_C = 4, 128, 256, 64


def decay_sums(nc, cols, logits, beside):
    with Phase(nc, "decays") as ph:
        soft = [ph.sb(f"soft{i}", [P, S]) for i in range(2)]
        resets = ph.sb("resets", [P, S])
        magnitude_read = ph.sem("magnitude_read")
        soft_ready = ph.sem("soft_ready")
        soft_used = ph.sem("soft_used")
        ba = cols["b_a2"]

        def soften(se, heads):
            for h in heads:
                if h >= 2:
                    se.wait_ge(soft_used, h - 1)
                nc.scalar.activation(soft[h % 2][:], logits[:, h, :], ACT.Abs, bias=ba[:, h:h + 1]).then_inc(magnitude_read, 1)
                se.wait_ge(magnitude_read, h + 1)
                nc.scalar.activation(soft[h % 2][:], soft[h % 2][:], ACT.Exp, scale=-1.0)
                se.drain()
                nc.scalar.activation(soft[h % 2][:], soft[h % 2][:], ACT.Ln, bias=1.0).then_inc(soft_ready, 1)

        def sum_up(ve):
            chunk_resets(nc, resets, GLA_C)
            for h in range(GLA_H):
                ve.wait_ge(magnitude_read, h + 1)
                nc.vector.tensor_scalar(logits[:, h, :], logits[:, h, :], ba[:, h:h + 1], 0.0, ALU.add, ALU.min)
                ve.drain()
                ve.wait_ge(soft_ready, h + 1)
                nc.vector.tensor_tensor(soft[h % 2][:], logits[:, h, :], soft[h % 2][:], ALU.subtract)
                ve.drain()
                nc.vector.tensor_tensor_scan(logits[:, h, :], resets[:], soft[h % 2][:], 0.0, ALU.mult, ALU.add).then_inc(soft_used, 1)

        beside(Aside((lambda se: soften(se, (0, 1)), lambda se: soften(se, (2, 3))), sum_up))


def gated_linear_attention(nc, consts, cols, logits, qk, v, out):
    NCH = S // GLA_C
    qscale = GLA_DK ** -0.5
    with Phase(nc, "gla") as ph:
        low = ph.sb("low", [P, S])
        kd = ph.sb("kd", [P, S])
        ke = ph.sb("ke", [P, S])
        qe = ph.sb("qe", [P, S])
        qb = ph.sb("qb", [P, S])
        dref, dlast = ke, kd
        decay = ph.sb("decay", [P, NCH])
        kdt = ph.sb("kdt", [P, DT, P])
        vh = ph.sb("vh", [P, DT, GLA_DV])
        state = ph.sb("state", [P, NCH + 1, GLA_DV])
        probs = ph.sb("probs", [P, 2, P])
        junk = low[:, 0:GLA_DV]
        ss = ph.sb("ss", [P, 2])
        rstd = ph.sb("rstd", [P, 2])
        on = low[:, 2 * GLA_DV:4 * GLA_DV].rearrange("p (a c) -> p a c", a=2)
        turned = ph.ps("turned", [P, S])
        sc = [turned[:, 0:P], turned[:, HALF:HALF + P]]
        kv = [ph.ps(f"kv{i}", [P, HALF]) for i in range(2)]
        o = [ph.ps(f"o{i}", [P, HALF]) for i in range(2)]
        ot = [ph.ps(f"ot{i}", [P, 4, P]) for i in range(2)]
        cum_ready = ph.sem("cum_ready")
        exp_ready = ph.sem("exp_ready")
        derived = ph.sem("derived")
        turned_ready = ph.sem("turned_ready")
        kdt_ready = ph.sem("kdt_ready")
        v_staged = ph.sem("v_staged")
        head_free = ph.sem("head_free")
        kv_ready = ph.sem("kv_ready")
        state_done = ph.sem("state_done")
        sc_ready = ph.sem("sc_ready")
        masked = ph.sem("masked")
        o_ready = ph.sem("o_ready")
        std_ready = ph.sem("std_ready")
        on_done = ph.sem("on_done")
        ot_ready = ph.sem("ot_ready")
        ot_done = ph.sem("ot_done")
        ident, mask = consts["ident"], consts["gla_mask"]
        ba, bg = cols["b_a2"], cols["b_norm_g"]

        def tile(x, p):
            return x[:, p * P:(p + 1) * P]

        with nc.Block() as block:

            @block.scalar
            def _(se):
                with se.Fori(0, GLA_H) as h:
                    se.wait_ge(head_free, h + 1)
                    se.wait_ge(cum_ready, h + 1)
                    for dst, src, scale in ((kd, dlast[:], 1.0), (qe, dref[:], 1.0), (ke, dref[:], -1.0), (qb, logits[:, h, :], 1.0)):
                        nc.scalar.activation(dst[:], src, ACT.Exp, scale=scale / 16.0).then_inc(exp_ready, 1)
                    last_b = logits[:, h, :].rearrange("p (n c) -> p n c", c=GLA_C)[:, :, GLA_C - 1]
                    nc.scalar.activation(decay[:], last_b, ACT.Exp, scale=1.0 / 16.0).then_inc(exp_ready, 1)
                    se.wait_ge(turned_ready, h + 1)
                    nc.scalar.activation(kdt[:].rearrange("p t c -> p (t c)"), turned[:], ACT.Copy).then_inc(kdt_ready, 1)
                    for p in range(DT + 1):
                        if p < DT:
                            se.wait_ge(o_ready, DT * h + p + 1)
                            nc.scalar.activation(junk, o[p % 2][:, 0:GLA_DV], ACT.Square, scale=GLA_DV ** -0.5,
                                                 accum_out=ss[:, p % 2:p % 2 + 1])
                            se.drain()
                            nc.scalar.activation(rstd[:, p % 2:p % 2 + 1], ss[:, p % 2:p % 2 + 1], ACT.Sqrt,
                                                 bias=1e-6).then_inc(std_ready, 1)
                        if p >= 1:
                            q = p - 1
                            se.wait_ge(ot_ready, DT * h + q + 1)
                            for i in range(2):
                                last = nc.scalar.activation(out[:, 2 * h + i, q * P:(q + 1) * P], ot[q % 2][:, i, :],
                                                            ACT.Copy, scale=bg[:, bass.ds(2 * h + i, 1)])
                            last.then_inc(ot_done, 1)

            @block.vector
            def _(ve):
                nc.vector.memset(state[:, 0, :], 0.0)
                with ve.Fori(0, GLA_H) as h:
                    ve.wait_ge(head_free, h + 1)
                    b3 = logits[:, h, :].rearrange("p (n c) -> p n c", c=GLA_C)
                    nc.vector.tensor_tensor(dref[:].rearrange("p (n c) -> p n c", c=GLA_C), b3,
                                            b3[:, :, GLA_C // 2 - 1:GLA_C // 2].broadcast_to([P, NCH, GLA_C]), ALU.subtract)
                    nc.vector.tensor_tensor(dlast[:].rearrange("p (n c) -> p n c", c=GLA_C),
                                            b3[:, :, GLA_C - 1:GLA_C].broadcast_to([P, NCH, GLA_C]), b3,
                                            ALU.subtract).then_inc(cum_ready, 1)
                    for i, (dst, of_q) in enumerate(((kd, 0), (qe, 1), (ke, 0), (qb, 1))):
                        ve.wait_ge(exp_ready, 5 * h + i + 1)
                        nc.vector.scalar_tensor_tensor(out=dst[:], in0=qk[:, (h if of_q else h + GLA_H), :],
                                                       scalar=(qscale if of_q else 1.0), in1=dst[:],
                                                       op0=ALU.mult, op1=ALU.mult).then_inc(derived, 1)
                    ve.wait_ge(exp_ready, 5 * h + 5)
                    for p in range(DT + 1):
                        if p < DT:
                            ve.wait_ge(kv_ready, DT * h + p + 1)
                            for c in (2 * p, 2 * p + 1):
                                if c:
                                    ve.wait_ge(state_done, NCH * h + c)
                                nc.vector.scalar_tensor_tensor(out=state[:, c + 1, :], in0=state[:, c, :],
                                                               scalar=decay[:, c:c + 1], in1=kv[c % 2][:, 0:GLA_DV],
                                                               op0=ALU.mult, op1=ALU.add).then_inc(state_done, 1)
                            ve.wait_ge(sc_ready, DT * h + p + 1)
                            if p >= 2:
                                ve.wait_ge(o_ready, DT * h + p - 1)
                            nc.vector.scalar_tensor_tensor(out=probs[:, p % 2, :], in0=sc[p % 2], scalar=3.0e38,
                                                           in1=mask, op0=ALU.min, op1=ALU.mult).then_inc(masked, 1)
                        if p >= 1:
                            q = p - 1
                            ve.wait_ge(std_ready, DT * h + q + 1)
                            nc.vector.reciprocal(rstd[:, q % 2:q % 2 + 1], rstd[:, q % 2:q % 2 + 1])
                            ve.drain()
                            if q >= 2:
                                ve.wait_ge(ot_ready, DT * h + q - 1)
                            nc.vector.tensor_scalar(on[:, q % 2, :], o[q % 2][:, 0:GLA_DV], rstd[:, q % 2:q % 2 + 1], None,
                                                    ALU.mult).then_inc(on_done, 1)

            @block.gpsimd
            def _(pool):
                with pool.Fori(0, GLA_H) as h:
                    pool.wait_ge(head_free, h + 1)
                    nc.gpsimd.tensor_copy(vh[:], v[:].rearrange("p t (h d) -> p t h d", h=GLA_H)[:, :, h, :]).then_inc(v_staged, 1)

            @block.tensor
            def _(pe):
                pe.sem_inc(head_free, 1)
                with pe.Fori(0, GLA_H) as h:
                    pe.wait_ge(derived, 4 * h + 1)
                    for p in range(DT):
                        last = nc.tensor.transpose(tile(turned, p), tile(kd, p), ident)
                    last.then_inc(turned_ready, 1)
                    pe.wait_ge(kdt_ready, h + 1)
                    pe.wait_ge(v_staged, h + 1)
                    pe.wait_ge(derived, 4 * h + 4)
                    for p in range(DT + 2):
                        if p < DT:
                            if p >= 1:
                                pe.wait_ge(state_done, NCH * h + 2 * p)
                            for c in range(2):
                                rows = slice(c * GLA_C, (c + 1) * GLA_C)
                                last = nc.tensor.matmul(kv[c][:, 0:GLA_DV], kdt[rows, p, :], vh[rows, p, :], start=True, stop=True)
                            last.then_inc(kv_ready, 1)
                            if p >= 2:
                                pe.wait_ge(masked, DT * h + p - 1)
                            nc.tensor.matmul(sc[p % 2], tile(ke, p), tile(qe, p), start=True, stop=True).then_inc(sc_ready, 1)
                        if 1 <= p <= DT:
                            q = p - 1
                            pe.wait_ge(masked, DT * h + q + 1)
                            if q >= 2:
                                pe.wait_ge(on_done, DT * h + q - 1)
                            nc.tensor.matmul(o[q % 2][:, 0:GLA_DV], probs[:, q % 2, :], vh[:, q, :], start=True, stop=False, skip_group_check=True)
                            for c in range(2):
                                if q or c:
                                    pe.wait_ge(state_done, NCH * h + 2 * q + c)
                                rows = slice(c * GLA_C, (c + 1) * GLA_C)
                                at = q * P + c * GLA_C
                                last = nc.tensor.matmul(o[q % 2][rows, 0:GLA_DV], qb[:, at:at + GLA_C], state[:, 2 * q + c, :],
                                                        start=False, stop=(c == 1), skip_group_check=True)
                            last.then_inc(o_ready, 1)
                        if p >= 2:
                            q = p - 2
                            pe.wait_ge(on_done, DT * h + q + 1)
                            if q >= 2:
                                pe.wait_ge(ot_done, DT * h + q - 1)
                            for i in range(2):
                                last = nc.tensor.transpose(ot[q % 2][:, i, :], on[:, q % 2, i * P:(i + 1) * P], ident)
                            last.then_inc(ot_ready, 1)
                    pe.drain().then_inc(head_free, 1)


def spatial_gating(nc, consts, cols, w_v, h, w_s, b_s, out):
    G = 8
    with Phase(nc, "sgu") as ph:
        wt = ph.sb("w", [P, DT, S])
        ws = ph.sb("ws", [P, G, P])
        bs = ph.sb("bs", [P, G, P])
        shift = ph.sb("shift", [P, G, P])
        stage = [ph.sb(f"stage{i}", [P, DT, P]) for i in range(2)]
        gv = [ph.sb(f"gv{i}", [P, S]) for i in range(2)]
        stats = ph.sb("stats", [P, 2, 6])
        mv = ph.sb("mv", [P, 2, 2])
        rstd = ph.sb("rstd", [P, 2])
        acc = [ph.ps(f"acc{i}", [P, S]) for i in range(2)]
        mix = [ph.ps(f"mix{i}", [P, S]) for i in range(2)]
        w_landed = [ph.sem(f"w_landed{k}") for k in range(DT)]
        ws_landed, bs_landed = ph.sem("ws_landed"), ph.sem("bs_landed")
        ws_masked = ph.sem("ws_masked")
        sums_ready = ph.sem("sums_ready")
        staged = ph.sem("staged")
        acc_ready = ph.sem("acc_ready")
        gelu_done = ph.sem("gelu_done")
        mv_ready = ph.sem("mv_ready")
        std_ready = ph.sem("std_ready")
        normed = ph.sem("normed")
        mixed = ph.sem("mixed")
        mix_taken = ph.sem("mix_taken")
        g, b = cols["a_ln_g"], cols["a_ln_b"]
        w3 = w_v.rearrange("p (t n) -> p t n", t=DT)

        with nc.Block() as block:

            @block.sync
            def _(sp):
                sp.dma_start(ws[:].rearrange("p g t -> p (g t)"), w_s).then_inc(ws_landed, 16)
                sp.dma_start(bs[:].rearrange("p g t -> p (g t)"), b_s.broadcast_to([P, G * P])).then_inc(bs_landed, 16)
                for k in range(DT):
                    sp.dma_start(wt[:, k, :], w3[:, k, :]).then_inc(w_landed[k], 16)

            @block.gpsimd
            def _(pool):
                for i in range(2):
                    nc.gpsimd.tensor_copy(stage[i][:], h[:, :, i * P:(i + 1) * P]).then_inc(staged, 1)

                with pool.Fori(1, DT // 2) as j:
                    for i in range(2):
                        pool.wait_ge(acc_ready, 2 * j - 1 + i)
                        nc.gpsimd.tensor_copy(stage[i][:], tile_of(h, 2 * j + i)).then_inc(staged, 1)

            @block.tensor
            def _(pe):
                pe.wait_ge(ws_masked, 1)
                for half in range(2):
                    last = nc.tensor.matmul(mix[0][:, half * HALF:(half + 1) * HALF], consts["ones"],
                                            ws[:].rearrange("p g t -> p (g t)")[:, half * HALF:(half + 1) * HALF],
                                            start=True, stop=True)
                last.then_inc(sums_ready, 1)
                for k in range(DT):
                    pe.wait_ge(w_landed[k], 16)

                def project(n, i, first=False):
                    pe.wait_ge(staged, n + 1)
                    if not first:
                        pe.wait_ge(gelu_done, n - 1)
                    tile_product(nc, acc[i], stage[i], wt, S).then_inc(acc_ready, 1)

                def mixing(n, i, first=False):
                    pe.wait_ge(normed, n + 1)
                    pe.wait_ge(mix_taken, n + 1 if first else n)
                    for gr in range(G):
                        last = nc.tensor.matmul(mix[i][:, gr * P:(gr + 1) * P], gv[i][:, gr * P:(gr + 1) * P], ws[:, gr, :],
                                                start=True, stop=True)
                    last.then_inc(mixed, 1)

                project(0, 0, True)
                project(1, 1, True)
                mixing(0, 0, True)
                with pe.Fori(1, DT // 2) as j:
                    project(2 * j, 0)
                    mixing(2 * j - 1, 1)
                    project(2 * j + 1, 1)
                    mixing(2 * j, 0)
                mixing(DT - 1, 1)

            @block.scalar
            def _(se):
                def gelu(n, i, first=False):
                    se.wait_ge(acc_ready, n + 1)
                    if not first:
                        se.wait_ge(mixed, n - 1)
                    nc.scalar.activation(gv[i][:], acc[i][:], ACT.Gelu).then_inc(gelu_done, 1)

                def std(n, i):
                    se.wait_ge(mv_ready, n + 1)
                    nc.scalar.activation(rstd[:, i:i + 1], mv[:, i, 1:2], ACT.Sqrt, bias=1e-6).then_inc(std_ready, 1)

                gelu(0, 0, True)
                std(0, 0)
                gelu(1, 1, True)
                std(1, 1)
                with se.Fori(1, DT // 2) as j:
                    for i in range(2):
                        gelu(2 * j + i, i)
                        std(2 * j + i, i)

            @block.vector
            def _(ve):
                ve.wait_ge(ws_landed, 16)
                nc.vector.tensor_tensor(ws[:], ws[:], consts["le3"], ALU.mult).then_inc(ws_masked, 1)
                ve.wait_ge(sums_ready, 1)
                ve.wait_ge(bs_landed, 16)
                for gr in range(G):
                    last = nc.vector.scalar_tensor_tensor(out=shift[:, gr, :], in0=mix[0][:, gr * P:(gr + 1) * P],
                                                          scalar=b[:, gr:gr + 1], in1=bs[:, gr, :], op0=ALU.mult, op1=ALU.add)
                last.then_inc(mix_taken, 1)
                ve.drain()

                def norm(n, i):
                    ve.wait_ge(gelu_done, n + 1)
                    for half in range(2):
                        nc.vector.bn_stats(stats[:, half, :], gv[i][:, half * HALF:(half + 1) * HALF])
                    ve.drain()
                    nc.vector.bn_aggr(mv[:, i, :], stats[:].rearrange("p a b -> p (a b)")).then_inc(mv_ready, 1)
                    ve.wait_ge(std_ready, n + 1)
                    nc.vector.reciprocal(rstd[:, i:i + 1], rstd[:, i:i + 1])
                    ve.drain()
                    nc.vector.tensor_scalar(gv[i][:], gv[i][:], mv[:, i, 0:1], rstd[:, i:i + 1],
                                            ALU.subtract, ALU.mult).then_inc(normed, 1)

                def take(n, i):
                    ve.wait_ge(mixed, n + 1)
                    for gr in range(G):
                        last = nc.vector.scalar_tensor_tensor(
                            out=out[:].rearrange("p t (n c) -> p t n c", c=P)[:, gr, n, :], in0=mix[i][:, gr * P:(gr + 1) * P],
                            scalar=g[:, gr:gr + 1], in1=shift[:, gr, :], op0=ALU.mult, op1=ALU.add)
                    last.then_inc(mix_taken, 1)

                norm(0, 0)
                with ve.Fori(0, DT // 2 - 1) as j:
                    norm(2 * j + 1, 1)
                    take(2 * j, 0)
                    norm(2 * j + 2, 0)
                    take(2 * j + 1, 1)
                norm(DT - 1, 1)
                take(DT - 2, 0)
                take(DT - 1, 1)


def first_block(nc, d, consts, cols, x):
    with Phase(nc, "b1") as ph:
        attn = ph.sb("attn", [P, DT, S])
        with Phase(nc, "b1h") as ph2:
            h = ph2.sb("h", [P, DT, S])
            norm_rows(nc, "b1_pre", x, h, consts, cols["pre_g"], eps=1e-6, source=d["xT"])
            with Phase(nc, "b1a") as pa:
                v = x
                logits = pa.sb("logits", [P, 4, S])
                with Phase(nc, "b1lr") as pl:
                    lr = pl.sb("lr", [16, S])
                    project_rows(nc, "b1_lr", d["w_lr"], DT, lambda k: h[:, k, :], 1, m=16,
                                 act=lambda n, acc, tmp, i: nc.scalar.activation(lr[:], acc[:], ACT.Copy))
                    project_rows(nc, "b1_log", d["w_a2"], 1, lambda k: lr[:], 4, kp=16,
                                 act=lambda n, acc, tmp, i: nc.scalar.activation(logits[:, n, :], acc[:], ACT.Copy))
                with Phase(nc, "b1x", side="right") as px:
                    pair = Pair(px, "h", DT, within=h)
                    def value_half(half, **more):
                        columns = slice(half * HALF, (half + 1) * HALF)
                        tokens_pair(nc, f"b1_v{half}", d["w_bv"].rearrange("p (t n) -> p t n", t=DT)[:, :, columns], HALF, pair,
                                    act=lambda n, acc: nc.scalar.activation(v[:, n, columns], acc[:], ACT.Copy), **more)

                    decay_sums(nc, cols, logits, lambda aside: value_half(0, splits=[(h, pair, DT)], aside=aside))
                    value_half(1)
                    qk = pa.sb("qk", [P, 8, S])
                    project_chain(nc, "b1_qk", [copy_stage(nc, d["w_qk"], pair.rows, 8, qk)], join=(pair, h))
                gated_linear_attention(nc, consts, cols, logits, qk, v, attn)
            gate = x
            spatial_gating(nc, consts, cols, d["w_av"], h, d["w_sT"], d["b_s"], gate)
            with Phase(nc, "b1b") as pb:
                pair = Pair(pb, "h", DT)

                def times_stage(w, dst, func):
                    return Stage(w, DT, pair.rows, 8, act=lambda n, acc, tmp: nc.scalar.activation(tmp[:], acc[:], func),
                                 dve=lambda n, acc, tmp, conv: nc.vector.tensor_tensor(dst[:, n, :], dst[:, n, :], tmp[:], ALU.mult))

                project_chain(nc, "b1_gates", [times_stage(d["w_bgate"], attn, ACT.Silu), times_stage(d["w_au"], gate, ACT.Gelu),
                                               times_stage(d["w_agate"], gate, ACT.Silu)], splits=[(h, pair, DT)])
        with Phase(nc, "b1c") as pc:
            y = pc.sb("y", [P, DT, S])
            halves = [Pair(pc, f"mix{i}", DT, within=half) for i, half in enumerate((gate, attn))]
            project_chain(nc, "b1_out", [copy_stage(nc, d["w_out1a"], halves[0].rows, 8, y),
                                         add_stage(nc, d["w_out1b"], DT, halves[1].rows, 8, y)],
                          splits=[(gate, halves[0], DT), (attn, halves[1], DT)])
            norm_rows(nc, "b1_post", y, x, consts, cols["post_g"], eps=1e-6, add=d["xT"])

M_H, M_DH = 4, 128
GQ_D, GQ_KV = 64, 2
D_FF2 = 2816
FFN_CUTS2 = (8, 8, 6)


def mlstm_rows(nc, gi, gf, cols, consts, dram, col_out, beside):
    R = GATE_ROWS
    NCH = DT
    with Phase(nc, "mrow") as ph:
        soft = ph.sb("soft", [R, S])
        lf = ph.sb("lf", [R, S])
        resets = ph.sb("resets", [R, S])
        b = ph.sb("b", [R, S])
        m = ph.sb("m", [R, S])
        rel = ph.sb("rel", [R, S])
        quant = [ph.sb(f"quant{i}", [R, S]) for i in range(4)]
        before = ph.sb("before", [R, NCH])
        ends = ph.sb("ends", [R, 3, NCH])
        decay = ph.sb("decay", [R, NCH])
        turned = [ph.ps(f"turned{i}", [P, DT, R]) for i in range(4)]
        soft_ready, lf_ready = ph.sem("soft_ready"), ph.sem("lf_ready")
        biased = ph.sem("biased")
        args_ready = ph.sem("args_ready")
        exps_done = ph.sem("exps_done")
        turned_ready = ph.sem("turned_ready")
        stored = [ph.sem(f"stored{i}") for i in range(2)]
        bi, bf = cols["m_bi"], cols["m_bf"]
        F, B = slice(0, M_H), slice(32, 32 + M_H)

        def chunks(x):
            return x.rearrange("p (n c) -> p n c", c=P)

        def soften(se):
            nc.scalar.activation(soft[:], gf[:], ACT.Abs, bias=bf[0:R, :])
            se.drain()
            nc.scalar.activation(soft[:], soft[:], ACT.Exp, scale=-1.0)
            se.drain()
            nc.scalar.activation(soft[:], soft[:], ACT.Ln, bias=1.0).then_inc(soft_ready, 1)

        def exponentials(se):
            se.wait_ge(args_ready, 1)
            for i in (1, 2):
                nc.scalar.activation(quant[i][:], quant[i][:], ACT.Exp)
            nc.scalar.activation(quant[3][:], m[:], ACT.Exp, scale=-1.0)
            nc.scalar.activation(decay[:], decay[:], ACT.Exp)
            se.drain().then_inc(exps_done, 1)

        def columns_out(se):
            for i in range(4):
                se.wait_ge(turned_ready, i + 1)
                nc.scalar.activation(col_out[:, i, :, :], turned[i][:], ACT.Copy, scale=(M_DH ** -0.5 if i == 1 else 1.0))

        def arguments(ve):
            nc.vector.tensor_scalar(gi[:], gi[:], bi[0:R, :], None, ALU.add)
            nc.vector.tensor_scalar(lf[:], gf[:], bf[0:R, :], 0.0, ALU.add, ALU.min)
            chunk_resets(nc, resets)
            nc.vector.memset(b[:], 0.0)
            nc.vector.memset(m[:], 0.0)
            nc.vector.memset(before[:], 0.0)
            nc.vector.memset(ends[:], 0.0)
            ve.drain()
            ve.wait_ge(soft_ready, 1)
            nc.vector.tensor_tensor(lf[:], lf[:], soft[:], ALU.subtract)
            ve.drain()
            nc.vector.tensor_tensor_scan(b[F, :], resets[F, :], lf[F, :], 0.0, ALU.mult, ALU.add)
            nc.vector.tensor_tensor_scan(b[B, ::-1], resets[B, :], lf[B, ::-1], 0.0, ALU.mult, ALU.add)
            nc.vector.tensor_tensor_scan(m[F, :], lf[F, :], gi[F, :], 0.0, ALU.add, ALU.max)
            nc.vector.tensor_tensor_scan(m[B, ::-1], lf[B, ::-1], gi[B, ::-1], 0.0, ALU.add, ALU.max)
            ve.drain()
            b3, m3 = chunks(b[:]), chunks(m[:])
            nc.vector.tensor_copy(ends[F, 0, :], b3[F, :, P - 1])
            nc.vector.tensor_copy(ends[B, 0, :], b3[B, :, 0])
            nc.vector.tensor_copy(ends[F, 1, :], m3[F, :, P - 1])
            nc.vector.tensor_copy(ends[B, 1, :], m3[B, :, 0])
            nc.vector.tensor_copy(before[F, 1:NCH], m3[F, 0:NCH - 1, P - 1])
            nc.vector.tensor_copy(before[B, 0:NCH - 1], m3[B, 1:NCH, 0])
            nc.vector.tensor_tensor(rel[:], b[:], m[:], ALU.subtract)
            nc.vector.tensor_tensor(quant[0][:], gi[:], b[:], ALU.subtract)
            ve.drain()
            nc.vector.tensor_tensor(ends[:, 2, :], ends[:, 0, :], ends[:, 1, :], ALU.subtract)
            ve.drain()
            nc.vector.tensor_tensor(decay[:], ends[:, 2, :], before[:], ALU.add)
            nc.vector.tensor_tensor(chunks(quant[1][:]), chunks(rel[:]), before[:, :, None].broadcast_to([R, NCH, P]), ALU.add)
            nc.vector.tensor_tensor(chunks(quant[2][:]), chunks(quant[0][:]), ends[:, 2, :, None].broadcast_to([R, NCH, P]), ALU.add)
            ve.drain().then_inc(args_ready, 1)

        def turn(pe):
            pe.wait_ge(exps_done, 1)
            for i in range(4):
                for t in range(DT):
                    last = nc.tensor.transpose(turned[i][:, t, :], quant[i][:, t * P:(t + 1) * P], consts["ident"][0:R, 0:R])
                last.then_inc(turned_ready, 1)

        def store(sp):
            sp.wait_ge(exps_done, 1)
            sp.dma_start(dram["m_rel"], rel[:]).then_inc(stored[0], 16)
            sp.dma_start(dram["m_decay"], decay[:]).then_inc(stored[1], 16)
            for i in range(2):
                sp.wait_ge(stored[i], 16)

        beside(Aside((soften, exponentials, columns_out), arguments, turn, store))


def mlstm(nc, d, consts, cols, dram, qk, v, og, gate_cols, mix):
    NU = 2 * DT
    with Phase(nc, "mlstm") as ph:
        qs2 = ph.sb("qs", [P, 2, S])
        ks2 = ph.sb("ks", [P, 2, S])
        vs2 = ph.sb("vs", [P, 2, DT, M_DH + 2])
        kt = ph.sb("kt", [P, DT, P])
        rel2 = ph.sb("rel", [P, 2, 2, S])
        decay2 = ph.sb("decay", [P, 2, 2, DT])
        wexp = ph.sb("wexp", [P, 2, P])
        probs = ph.sb("probs", [P, 2, P])
        vw = ph.sb("vw", [P, 2, M_DH + 2])
        state = ph.sb("state", [P, 2, M_DH + 2])
        den = ph.sb("den", [P, 2, DT])
        num = ph.sb("num", [P, 2, DT, M_DH + 2])
        hsum = ph.sb("hsum", [P, DT, P])
        stats = ph.sb("stats", [P, DT, 6])
        mv = ph.sb("mv", [P, DT, 2])
        rstd = ph.sb("rstd", [P, DT])
        sc = [ph.ps(f"sc{i}", [P, HALF]) for i in range(2)]
        kv = [ph.ps(f"kv{i}", [P, HALF]) for i in range(2)]
        both = [ph.ps(f"both{i}", [P, HALF]) for i in range(2)]
        inter, intra = [b[:, 0:M_DH + 1] for b in both], [b[:, HALF // 2:HALF // 2 + M_DH + 1] for b in both]
        turned = ph.ps("turned", [P, S])
        staged = ph.sem("staged")
        rel_landed = [[ph.sem(f"rel_landed{p}{i}") for i in range(2)] for p in range(2)]
        decay_landed = [[ph.sem(f"decay_landed{p}{i}") for i in range(2)] for p in range(2)]
        head_free = ph.sem("head_free")
        kt_ps = ph.sem("kt_ps")
        kt_ready = ph.sem("kt_ready")
        warg = ph.sem("warg")
        wexp_ready = ph.sem("wexp_ready")
        vw_ready = ph.sem("vw_ready")
        sc_ready = ph.sem("sc_ready")
        probs_ready = ph.sem("probs_ready")
        kv_ready = ph.sem("kv_ready")
        inter_ready = ph.sem("inter_ready")
        intra_ready = ph.sem("intra_ready")
        state_done = ph.sem("state_done")
        num_copied = ph.sem("num_copied")
        num_done = ph.sem("num_done")
        mv_ready = ph.sem("mv_ready")
        std_ready = ph.sem("std_ready")
        normed = ph.sem("normed")
        h_turned = ph.sem("h_turned")
        masks = (consts["m_mask_f"], consts["m_mask_b"])
        W = M_DH + 1
        units = [(0, c) for c in range(DT)] + [(1, DT - 1 - c) for c in range(DT)]

        def gate_col(q, chunk, dr, h):
            return gate_cols[:, q, chunk, bass.ds(32 * dr + h, 1)]

        with nc.Block() as block:

            @block.sync
            def _(sp):
                with sp.Fori(0, M_H // 2) as h2:
                    for p in range(2):
                        h = 2 * h2 + p
                        sp.wait_ge(head_free, h + 1)
                        for dr in range(2):
                            sp.dma_start(rel2[:, p, dr, :], dram["m_rel"][bass.ds(32 * dr + h, 1), :].broadcast_to([P, S])).then_inc(rel_landed[p][dr], 16)
                            sp.dma_start(decay2[:, p, dr, :], dram["m_decay"][bass.ds(32 * dr + h, 1), :].broadcast_to([P, DT])).then_inc(decay_landed[p][dr], 16)

            @block.gpsimd
            def _(pool):
                nc.gpsimd.memset(vs2[:, :, :, M_DH:], 1.0)
                with pool.Fori(0, M_H // 2) as h2:
                    for p in range(2):
                        h = 2 * h2 + p
                        pool.wait_ge(head_free, h + 1)
                        nc.gpsimd.tensor_copy(ks2[:, p, :], qk[:, h + M_H, :])
                        nc.gpsimd.tensor_copy(qs2[:, p, :], qk[:, h, :])
                        nc.gpsimd.tensor_copy(vs2[:, p, :, 0:M_DH], v[:, :, h, :])
                        pool.drain().then_inc(staged, 1)

            @block.tensor
            def _(pe):
                with pe.Fori(0, M_H // 2) as h2:
                    for p in range(2):
                        h = 2 * h2 + p
                        qs, ks, vs = qs2[:, p], ks2[:, p], vs2[:, p]
                        pe.wait_ge(staged, h + 1)
                        pe.wait_ge(head_free, h + 2)
                        for t in range(DT):
                            last = nc.tensor.transpose(turned[:, t * P:(t + 1) * P], ks[:, t * P:(t + 1) * P], consts["ident"])
                        last.then_inc(kt_ps, 1)
                        for u in range(NU + 2):
                            if u < NU:
                                dr, c = units[u]
                                tok = slice(c * P, (c + 1) * P)
                                if u >= 2:
                                    pe.wait_ge(probs_ready, NU * h + u - 1)
                                nc.tensor.matmul(sc[u % 2][:, 0:P], ks[:, tok], qs[:, tok], start=True, stop=True).then_inc(sc_ready, 1)
                                if u == 0:
                                    pe.wait_ge(kt_ready, h + 1)
                            if 1 <= u <= NU:
                                q = u - 1
                                pe.wait_ge(vw_ready, NU * h + q + 1)
                                if q >= 2:
                                    pe.wait_ge(state_done, NU * h + q - 1)
                                nc.tensor.matmul(kv[q % 2][:, 0:W], kt[:, units[q][1], :], vw[:, q % 2, 0:W],
                                                 start=True, stop=True).then_inc(kv_ready, 1)
                            if u >= 2:
                                q = u - 2
                                dr, c = units[q]
                                tok = slice(c * P, (c + 1) * P)
                                pe.wait_ge(probs_ready, NU * h + q + 1)
                                if q:
                                    pe.wait_ge(state_done, NU * h + q)
                                if q >= 2:
                                    pe.wait_ge(num_done, NU * h + q - 1)
                                nc.tensor.matmul(inter[q % 2], qs[:, tok], state[:, q % 2, 0:W], start=True, stop=True).then_inc(inter_ready, 1)
                                nc.tensor.matmul(intra[q % 2], probs[:, q % 2, :], vs[:, c, 0:W], start=True, stop=True).then_inc(intra_ready, 1)
                        pe.wait_ge(normed, h + 1)
                        for t in range(DT):
                            last = nc.tensor.transpose(turned[:, t * P:(t + 1) * P], hsum[:, t, :], consts["ident"])
                        last.then_inc(h_turned, 1)

            @block.scalar
            def _(se):
                with se.Fori(0, M_H // 2) as h2:
                    for p in range(2):
                        h = 2 * h2 + p
                        vs = vs2[:, p]
                        se.wait_ge(kt_ps, h + 1)
                        nc.scalar.activation(kt[:].rearrange("p t c -> p (t c)"), turned[:], ACT.Copy).then_inc(kt_ready, 1)
                        for u in range(NU + 3):
                            if u < NU:
                                dr, c = units[u]
                                if u >= 2:
                                    se.wait_ge(kv_ready, NU * h + u - 1)
                                nc.scalar.activation(vw[:, u % 2, 0:W], vs[:, c, 0:W], ACT.Copy, scale=gate_col(2, c, dr, h)).then_inc(vw_ready, 1)
                                se.wait_ge(warg, NU * h + u + 1)
                                nc.scalar.activation(wexp[:, u % 2, :], wexp[:, u % 2, :], ACT.Exp).then_inc(wexp_ready, 1)
                            if u >= 3:
                                dr, c = units[u - 3]
                                se.wait_ge(intra_ready, NU * h + u - 2)
                                nc.scalar.activation(num[:, dr, c, 0:W], intra[(u - 3) % 2], ACT.Copy).then_inc(num_copied, 1)
                        se.wait_ge(mv_ready, h + 1)
                        nc.scalar.activation(rstd[:], mv[:, :, 1], ACT.Sqrt, bias=1e-6).then_inc(std_ready, 1)

            @block.vector
            def _(ve):
                ve.sem_inc(head_free, 2)
                with ve.Fori(0, M_H // 2) as h2:
                    for p in range(2):
                        h = 2 * h2 + p
                        rel, decay = rel2[:, p], decay2[:, p]
                        nc.vector.memset(state[:, 0, :], 0.0)
                        for dr in range(2):
                            ve.wait_ge(rel_landed[p][dr], 16 * h2 + 16)
                            ve.wait_ge(decay_landed[p][dr], 16 * h2 + 16)

                        def argument(u):
                            dr, c = units[u]
                            nc.vector.scalar_tensor_tensor(out=wexp[:, u % 2, :], in0=rel[:, dr, c * P:(c + 1) * P],
                                                           scalar=gate_col(0, c, dr, h), in1=masks[dr],
                                                           op0=ALU.add, op1=ALU.min).then_inc(warg, 1)

                        for u in range(NU + 3):
                            if u < NU:
                                if u >= 2:
                                    ve.wait_ge(probs_ready, NU * h + u - 1)
                                argument(u)
                            if 1 <= u <= NU:
                                q = u - 1
                                ve.wait_ge(sc_ready, NU * h + q + 1)
                                ve.wait_ge(wexp_ready, NU * h + q + 1)
                                if q >= 2:
                                    ve.wait_ge(intra_ready, NU * h + q - 1)
                                nc.vector.scalar_tensor_tensor(out=probs[:, q % 2, :], in0=sc[q % 2][:, 0:P], scalar=M_DH ** -0.5,
                                                               in1=wexp[:, q % 2, :], op0=ALU.mult, op1=ALU.mult).then_inc(probs_ready, 1)
                            if 2 <= u < NU + 2:
                                q = u - 2
                                dr, c = units[q]
                                ve.wait_ge(kv_ready, NU * h + q + 1)
                                if q:
                                    ve.wait_ge(inter_ready, NU * h + q)
                                    ve.wait_ge(state_done, NU * h + q)
                                if q == DT - 1:
                                    nc.vector.memset(state[:, 0, :], 0.0).then_inc(state_done, 1)
                                else:
                                    nc.vector.scalar_tensor_tensor(out=state[:, (q + 1) % 2, 0:W], in0=state[:, q % 2, 0:W],
                                                                   scalar=decay[:, dr, c:c + 1], in1=kv[q % 2][:, 0:W],
                                                                   op0=ALU.mult, op1=ALU.add).then_inc(state_done, 1)
                            if u >= 3:
                                q = u - 3
                                dr, c = units[q]
                                ve.wait_ge(num_copied, NU * h + q + 1)
                                nc.vector.scalar_tensor_tensor(out=num[:, dr, c, 0:W], in0=inter[q % 2], scalar=gate_col(1, c, dr, h),
                                                               in1=num[:, dr, c, 0:W], op0=ALU.mult, op1=ALU.add).then_inc(num_done, 1)
                        ve.wait_ge(num_done, NU * h + NU)
                        last_col = num[:, :, :, M_DH]
                        nc.vector.tensor_scalar(den[:], last_col, -1.0, None, ALU.mult)
                        ve.drain()
                        nc.vector.tensor_tensor(den[:], den[:], last_col, ALU.max)
                        ve.drain()
                        for dr in range(2):
                            nc.vector.tensor_tensor(den[:, dr, :], den[:, dr, :], gate_cols[:, 3, :, bass.ds(32 * dr + h, 1)].rearrange("p t o -> p (t o)"),
                                                    ALU.max)
                        ve.drain()
                        nc.vector.reciprocal(den[:], den[:])
                        ve.drain()
                        nc.vector.tensor_tensor(num[:, :, :, 0:M_DH], num[:, :, :, 0:M_DH], den[:, :, :, None].broadcast_to([P, 2, DT, M_DH]), ALU.mult)
                        ve.drain()
                        nc.vector.tensor_tensor(hsum[:], num[:, 0, :, 0:M_DH], num[:, 1, :, 0:M_DH], ALU.add)
                        ve.drain()
                        for t in range(DT):
                            nc.vector.bn_stats(stats[:, t, :], hsum[:, t, :])
                        ve.drain()
                        for t in range(DT):
                            last = nc.vector.bn_aggr(mv[:, t, :], stats[:, t, :])
                        last.then_inc(mv_ready, 1)
                        ve.wait_ge(std_ready, h + 1)
                        nc.vector.reciprocal(rstd[:], rstd[:])
                        ve.drain()
                        for t in range(DT):
                            last = nc.vector.tensor_scalar(hsum[:, t, :], hsum[:, t, :], mv[:, t, 0:1], rstd[:, t:t + 1],
                                                           ALU.subtract, ALU.mult)
                        last.then_inc(normed, 1)
                        ve.wait_ge(h_turned, h + 1)
                        nc.vector.scalar_tensor_tensor(out=mix[:, h, :], in0=turned[:], scalar=cols["m_norm_g"][:, bass.ds(h, 1)],
                                                       in1=og[:, h, :], op0=ALU.mult, op1=ALU.mult).then_inc(head_free, 1)


def window_attention(nc, d, consts, cols, aq, ak, av_rows, av, mix):
    with Phase(nc, "gqa") as ph:
        qs = [ph.sb(f"qs{i}", [P, S]) for i in range(2)]
        bias = ph.sb("bias", [P, 2, 2, 3 * P])
        sink = ph.sb("sink", [P, 8])
        s = ph.sb("s", [P, 2, 3 * P])
        e = ph.sb("e", [P, 2, 3 * P])
        et = ph.sb("et", [P, 2, 3 * P])
        small = ph.sb("small", [P, 2, 4])
        sc = [ph.ps(f"sc{i}", [P, HALF]) for i in range(2)]
        turned = [ph.ps(f"turned{i}", [P, HALF]) for i in range(2)]
        o = [ph.ps(f"o{i}", [P, HALF]) for i in range(2)]
        staged = ph.sem("staged")
        bias_landed = [ph.sem(f"bias_landed{i}") for i in range(2)]
        sink_landed = ph.sem("sink_landed")
        pair_done = ph.sem("pair_done")
        sc_ready = ph.sem("sc_ready")
        max_ready = ph.sem("max_ready")
        exp_ready = ph.sem("exp_ready")
        e_ready = ph.sem("e_ready")
        turned_ready = ph.sem("turned_ready")
        et_ready = ph.sem("et_ready")
        o_ready = ph.sem("o_ready")
        o_taken = ph.sem("o_taken")
        av_turned, av_ready = ph.sem("av_turned"), ph.sem("av_ready")
        NU = 2 * DT
        units = [(n, j) for n in range(DT) for j in range(2)]

        def window(n):
            lo, hi = max(n - 1, 0), min(n + 2, DT)
            return lo, hi, slice((lo - n + 1) * P, (hi - n + 1) * P)

        with nc.Block() as block:

            @block.sync
            def _(sp):
                sp.dma_start(sink[:], d["a_sink"].broadcast_to([P, 8])).then_inc(sink_landed, 16)
                with sp.Fori(0, 2) as b2:
                    for i in range(2):
                        sp.wait_ge(pair_done, 2 * b2 + i + 1)
                        sp.dma_start(bias[:, i, :, :].rearrange("p j c -> p (j c)"),
                                     d["a_bias"][2 * b2 + i]).then_inc(bias_landed[i], 16)

            @block.gpsimd
            def _(pool):
                with pool.Fori(0, 2) as b2:
                    for i in range(2):
                        pool.wait_ge(pair_done, 2 * b2 + i + 1)
                        nc.gpsimd.tensor_copy(qs[i][:], aq[:, 2 * b2 + i, :]).then_inc(staged, 1)

            @block.tensor
            def _(pe):
                pe.sem_inc(pair_done, 2)
                for n in range(DT):
                    last = nc.tensor.transpose(turned[n // 4][:, n % 4 * P:(n % 4 + 1) * P], av_rows[:, n * P:(n + 1) * P], consts["ident"])
                last.then_inc(av_turned, 1)
                pe.wait_ge(av_ready, 1)
                with pe.Fori(0, 2) as b2:
                    for i in range(2):
                        b = 2 * b2 + i
                        pe.wait_ge(staged, b + 1)
                        for u in range(NU + 3):
                            if u < NU:
                                n, j = units[u]
                                lo, hi, w = window(n)
                                rows = slice(GQ_D * j, GQ_D * (j + 1))
                                if u >= 2:
                                    pe.wait_ge(max_ready, NU * b + u - 1)
                                nc.tensor.matmul(sc[u % 2][:, w], qs[i][rows, n * P:(n + 1) * P], ak[rows, lo * P:hi * P],
                                                 start=True, stop=True).then_inc(sc_ready, 1)
                            if 2 <= u < NU + 2:
                                q = u - 2
                                n, j = units[q]
                                lo, hi, w = window(n)
                                pe.wait_ge(e_ready, NU * b + q + 1)
                                if q >= 2:
                                    pe.wait_ge(et_ready, NU * b + q - 1)
                                for t in range(hi - lo):
                                    last = nc.tensor.transpose(turned[q % 2][:, t * P:(t + 1) * P],
                                                               e[:, q % 2, w.start + t * P:w.start + (t + 1) * P], consts["ident"])
                                last.then_inc(turned_ready, 1)
                            if u >= 3:
                                q = u - 3
                                n, j = units[q]
                                lo, hi, w = window(n)
                                rows = slice(GQ_D * j, GQ_D * (j + 1))
                                pe.wait_ge(et_ready, NU * b + q + 1)
                                if j == 0 and n >= 2:
                                    pe.wait_ge(o_taken, DT * b + n - 1)
                                for t in range(hi - lo):
                                    last = nc.tensor.matmul(o[n % 2][rows, 0:P], av[:, lo + t, rows], et[:, q % 2, t * P:(t + 1) * P],
                                                            start=(t == 0), stop=(t == hi - lo - 1))
                                if j == 1:
                                    last.then_inc(o_ready, 1)
                        pe.drain().then_inc(pair_done, 1)

            @block.vector
            def _(ve):
                ve.wait_ge(sink_landed, 16)
                with ve.Fori(0, 2) as b2:
                    for i in range(2):
                        b = 2 * b2 + i
                        ve.wait_ge(bias_landed[i], 16 * b2 + 16)
                        for u in range(NU + 1):
                            if u < NU:
                                n, j = units[u]
                                lo, hi, w = window(n)
                                ve.wait_ge(sc_ready, NU * b + u + 1)
                                if u >= 2:
                                    ve.wait_ge(exp_ready, NU * b + u - 1)
                                sl = u % 2
                                nc.vector.scalar_tensor_tensor(out=s[:, sl, w], in0=sc[sl][:, w], scalar=GQ_D ** -0.5,
                                                               in1=bias[:, i, j, w], op0=ALU.mult, op1=ALU.add)
                                ve.drain()
                                nc.vector.tensor_reduce(small[:, sl, 0:1], s[:, sl, w], AX_X, ALU.max)
                                ve.drain()
                                nc.vector.tensor_scalar(small[:, sl, 0:1], small[:, sl, 0:1], sink[:, bass.ds(b + 4 * j, 1)], -1.0,
                                                        ALU.max, ALU.mult).then_inc(max_ready, 1)
                            if u >= 1:
                                q = u - 1
                                n, j = units[q]
                                lo, hi, w = window(n)
                                sl = q % 2
                                ve.wait_ge(exp_ready, NU * b + q + 1)
                                nc.vector.tensor_tensor(small[:, sl, 1:2], small[:, sl, 1:2], small[:, sl, 2:3], ALU.add)
                                ve.drain()
                                nc.vector.reciprocal(small[:, sl, 3:4], small[:, sl, 1:2])
                                ve.drain()
                                nc.vector.tensor_scalar(e[:, sl, w], e[:, sl, w], small[:, sl, 3:4], None, ALU.mult).then_inc(e_ready, 1)

            @block.scalar
            def _(se):
                se.wait_ge(av_turned, 1)
                for half in range(2):
                    nc.scalar.activation(av[:, 4 * half:4 * half + 4, :].rearrange("p t c -> p (t c)"), turned[half][:], ACT.Copy)
                se.drain().then_inc(av_ready, 1)
                se.wait_ge(sink_landed, 16)
                with se.Fori(0, 2) as b2:
                    for i in range(2):
                        b = 2 * b2 + i
                        for u in range(NU + 4):
                            if u < NU:
                                n, j = units[u]
                                lo, hi, w = window(n)
                                sl = u % 2
                                se.wait_ge(max_ready, NU * b + u + 1)
                                if u >= 2:
                                    se.wait_ge(turned_ready, NU * b + u - 1)
                                nc.scalar.activation(e[:, sl, w], s[:, sl, w], ACT.Exp, bias=small[:, sl, 0:1], accum_out=small[:, sl, 1:2])
                                nc.scalar.activation(small[:, sl, 2:3], sink[:, bass.ds(b + 4 * j, 1)], ACT.Exp, bias=small[:, sl, 0:1])
                                se.drain().then_inc(exp_ready, 1)
                            if 2 <= u < NU + 2:
                                q = u - 2
                                n, j = units[q]
                                lo, hi, w = window(n)
                                se.wait_ge(turned_ready, NU * b + q + 1)
                                nc.scalar.activation(et[:, q % 2, 0:(hi - lo) * P], turned[q % 2][:, 0:(hi - lo) * P], ACT.Copy).then_inc(et_ready, 1)
                            if u >= 4 and (u - 4) % 2 == 1:
                                n = (u - 4) // 2
                                se.wait_ge(o_ready, DT * b + n + 1)
                                nc.scalar.activation(mix[:, 4 + b, n * P:(n + 1) * P], o[n % 2][:, 0:P], ACT.Copy).then_inc(o_taken, 1)


def second_block(nc, d, consts, cols, x):
    dram = {"m_rel": nc.dram_tensor("m_rel", (GATE_ROWS, S), F32, kind="Internal").ap(),
            "m_decay": nc.dram_tensor("m_decay", (GATE_ROWS, DT), F32, kind="Internal").ap()}

    with ExitStack() as tail:
        with ExitStack() as stack:
            with Phase(nc, "b2m") as ph:
                og = ph.sb("og", [P, 4, S])
                v = ph.sb("v", [P, DT, M_H, M_DH])
                gate_cols = ph.sb("gate_cols", [P, 4, DT, GATE_ROWS])
                with Phase(nc, "b2x", side="right") as px:
                    with Phase(nc, "b2g") as pg:
                        gi, gf = pg.sb("gi", [GATE_ROWS, S]), pg.sb("gf", [GATE_ROWS, S])
                        gate_inputs(nc, "b2_gates", d["w_mif"], x, gi, gf)
                        pair = Pair(px, "x", DT, within=x)
                        mlstm_rows(nc, gi, gf, cols, consts, dram, gate_cols, lambda aside: tokens_pair(
                            nc, "b2_v", d["w_mv"].rearrange("p (t n) -> p t n", t=DT), M_H * M_DH, pair, splits=[(x, pair, DT)], aside=aside,
                            act=lambda n, acc: nc.scalar.activation(v[:, n, :, :].rearrange("p h e -> p (h e)"), acc[:], ACT.Copy)))
                    qk = ph.sb("qk", [P, 8, S])
                    project_chain(nc, "b2_conv", [
                        copy_stage(nc, d["w_mo"], pair.rows, 4, og, ACT.Sigmoid),
                        conv_stage(nc, d["w_mqk"], 8, pair.rows, lambda n, tap: cols["m_taps"][:, bass.ds(TAPS * n + tap, 1)], qk,
                                   bias_of=lambda n: cols["m_conv_b"][:, bass.ds(n, 1)])], join=(pair, x))
                mix = stack.enter_context(Phase(nc, "b2", side="right")).sb("mix", [P, DT, S])
                mlstm(nc, d, consts, cols, dram, qk, v, og, gate_cols, mix)
            block_sum = tail.enter_context(Phase(nc, "b2s")).sb("block_sum", [P, S])
            with Phase(nc, "b2y") as py:
                pair = Pair(py, "x", DT, within=x)
                with Phase(nc, "b2a") as ph:
                    aqkv = ph.sb("aqkv", [P, 6, S])
                    av = ph.sb("av", [P, DT, P])
                    project_chain(nc, "b2_aqkv", [copy_stage(nc, d["w_aqkv"], pair.rows, 6, aqkv)], splits=[(x, pair, DT)])
                    window_attention(nc, d, consts, cols, aqkv[:, 0:4, :], aqkv[:, 4, :], aqkv[:, 5, :], av, mix)
                out_projection(nc, "b2_out", d["w_out2"], mix, x, block_sum, pair)
        with Phase(nc, "b2f") as ph:
            base = ph.sb("base", [P, DT, S])
            norm_rows(nc, "b2_ln1", x, x, consts, cols["ln1_g2"], cols["ln1_b2"], centre=True, block_sum=block_sum,
                      preload=(base[:, 0:2, :], d["pT"].rearrange(ROWS, t=2)))
            pair, hidden = Pair(ph, "x", DT, within=x), Pair(ph, "hidden", DT)

            def add_gate(n, acc, tmp, conv):
                nc.vector.tensor_tensor(base[:, n, :], base[:, n, :], tmp[:], ALU.mult)
                nc.vector.drain()
                add_residual(nc, base[:, n, :], pair, n, base[:, n, :])

            stages = [Stage(d["w_plep"], 2, hidden.rows, 8, act=lambda n, acc, tmp: nc.scalar.activation(base[:, n, :], acc[:], ACT.Copy)),
                      Stage(d["w_pleg"], DT, pair.rows, 8, dve=add_gate,
                            act=lambda n, acc, tmp: nc.scalar.activation(tmp[:], acc[:], ACT.Sigmoid))]

            def gated(j, acc, tmp, conv):
                nc.vector.tensor_tensor(tmp[:], acc[:], tmp[:], ALU.mult)
                nc.vector.drain()
                put_pair(nc, hidden, j, tmp)

            at = 0
            for c, KT in enumerate(FFN_CUTS2):
                stages.append(Stage(d["w_ffn"][2 * at:2 * (at + KT)], DT, pair.rows, 2 * KT, pairs=True, dve=gated,
                                    act=lambda n, acc, tmp: nc.scalar.activation(tmp[:], acc[:], ACT.Silu)))
                stages.append(add_stage(nc, d[f"w_ffo{c}"], KT, hidden.rows, 8, base))
                at += KT
            project_chain(nc, "b2_ffn", stages, splits=[(base, hidden, 2), (x, pair, DT)], block_sum=(block_sum, base))
            norm_rows(nc, "b2_ln2", base, x, consts, cols["ln2_g2"], cols["ln2_b2"], centre=True, block_sum=block_sum)


L2_COLUMNS = {"m_bi": 1, "m_bf": 1, "m_taps": 40, "m_conv_b": 8, "m_norm_g": 4, "ln1_g2": 8, "ln1_b2": 8, "ln2_g2": 8, "ln2_b2": 8}
L2_SQUARES = ("m_mask_f", "m_mask_b")


def gate_rows(w):
    import numpy as np
    out = np.zeros((w.shape[0], GATE_ROWS), np.float32)
    out[:, 0:4], out[:, 32:36] = w[:, 0:4], w[:, 4:8]
    return out


def gate_weight(first, second):
    import numpy as np
    out = np.zeros((first.shape[0], 64 + GATE_ROWS), np.float32)
    out[:, 0:GATE_ROWS], out[:, 64:] = gate_rows(first), gate_rows(second)
    return out.reshape(DT, P, -1).transpose(1, 0, 2).reshape(1, P, -1)


def gate_column(b):
    import numpy as np
    out = np.zeros((P, 1), np.float32)
    out[0:4, 0], out[32:36, 0] = b[0:4], b[4:8]
    return out


def second_arrays(a):
    import numpy as np
    w = a["w_in_2"][0]
    mqk, mv, mo, gates, aq, ak, av = np.split(w, np.cumsum([1024, 512, 512, 16, 512, 128]), axis=1)
    order = np.concatenate([np.r_[b * 64:(b + 1) * 64, (b + 4) * 64:(b + 5) * 64] for b in range(4)])
    wo = a["w_out_2"][0]
    ffn = a["w_ffn_in_2"][0]
    pair = rows_weight(ffn).reshape(2, D_FF2 // P, P, 1024).transpose(1, 0, 2, 3).reshape(-1, P, 1024)
    q, k = np.arange(P)[:, None], np.arange(3 * P)[None, :]
    rel = np.abs(k - P - q).astype(np.float32)
    slopes = 2.0 ** (-8.0 * np.arange(1, 9, dtype=np.float32) / 8)
    bias = np.where(rel[None] <= 128, -slopes[:, None, None] * rel[None], -BIG).astype(np.float32)
    bias = np.stack([bias[0:4], bias[4:8]], axis=2)
    out = {"w_mqk": rows_weight(mqk), "w_mv": tokens_weight(mv), "w_mo": rows_weight(mo),
           "w_mif": gate_weight(gates[:, 0:8], gates[:, 8:16]),
           "w_aqkv": rows_weight(np.concatenate([aq[:, order], ak, av], axis=1)),
           "a_bias": bias.reshape(4, P, 2 * 3 * P), "a_sink": a["attn_sink_2"],
           "w_out2": rows_weight(np.concatenate([wo[0:512], wo[512:][order]])), "w_ffn": pair,
           "w_pleg": rows_weight(a["w_ple_gate_2"][0]),
           "w_plep": rows_weight(a["w_ple_proj_2"][0]),
           "pT": a["p_2"][0, 0].T.reshape(2, P, S).transpose(1, 0, 2).reshape(P, 2 * S)}
    ends = P * np.cumsum(FFN_CUTS2)
    for c, part in enumerate(np.split(a["w_ffn_out_2"][0], ends[:-1])):
        out[f"w_ffo{c}"] = rows_weight(part)
    bg = a["b_gate_2"][0]
    taps = a["conv_w_2"][0].reshape(TAPS, 8, P).transpose(2, 1, 0).reshape(P, 40)
    columns = {"m_bi": gate_column(bg[0:8]), "m_bf": gate_column(bg[8:16]), "m_taps": taps,
               "m_conv_b": column(a["conv_b_2"]), "m_norm_g": column(a["mlstm_norm_g_2"]),
               "ln1_g2": column(a["ln1_g_2"]), "ln1_b2": column(a["ln1_b_2"]),
               "ln2_g2": column(a["ln2_g_2"]), "ln2_b2": column(a["ln2_b_2"])}
    i = np.arange(P)
    seen = i[:, None] <= i[None, :]
    squares = {"m_mask_f": np.where(seen, 0, -BIG).astype(np.float32), "m_mask_b": np.where(seen.T, 0, -BIG).astype(np.float32)}
    return out, columns, squares

G_H, G_D = 4, 128
LEVELS = 7
GRID, GRID_ROWS = 64, 16
WIN_R, WIN_C = 8, 16
N_D = 64
RPB_R, RPB_C = 2 * WIN_R - 1, 2 * WIN_C - 1
D_FF3 = 4096


def normalise_heads(nc, name, x, first, NB, picks, spreads, var_scale, scale_of):
    NH = 8
    with Phase(nc, name) as ph:
        pick = ph.sb("pick", [P, NB, NH])
        spread = ph.sb("spread", [NH, NB, P])
        sq = [ph.sb(f"sq{i}", [P, S]) for i in range(2)]
        rows = ph.sb("rows", [NH, S])
        total = ph.ps("total", [NH, S])
        every = [ph.ps(f"every{i}", [P, S]) for i in range(2)]
        pick_landed, spread_landed = ph.sem("pick_landed"), ph.sem("spread_landed")
        squared, summed = ph.sem("squared"), ph.sem("summed")
        std_ready, rstd_ready = ph.sem("std_ready"), ph.sem("rstd_ready")
        spread_ready, scaled = ph.sem("spread_ready"), ph.sem("scaled")
        with nc.Block() as block:

            @block.sync
            def _(sp):
                sp.dma_start(pick[:].rearrange("p a b -> p (a b)"), picks).then_inc(pick_landed, 16)
                sp.dma_start(spread[:].rearrange("p a b -> p (a b)"), spreads).then_inc(spread_landed, 16)

            @block.scalar
            def _(se):
                for k in range(NB):
                    if k >= 2:
                        se.wait_ge(summed, k - 1)
                    nc.scalar.activation(sq[k % 2][:], x[:, first + k, :], ACT.Square).then_inc(squared, 1)
                se.wait_ge(summed, NB)
                nc.scalar.activation(rows[:], total[:], ACT.Sqrt, scale=var_scale, bias=1e-6).then_inc(std_ready, 1)

            @block.tensor
            def _(pe):
                pe.wait_ge(pick_landed, 16)
                for k in range(NB):
                    pe.wait_ge(squared, k + 1)
                    for half in range(2):
                        c = slice(half * HALF, (half + 1) * HALF)
                        last = nc.tensor.matmul(total[:, c], pick[:, k, :], sq[k % 2][:, c], start=(k == 0), stop=(k == NB - 1))
                    last.then_inc(summed, 1)
                pe.wait_ge(spread_landed, 16)
                pe.wait_ge(rstd_ready, 1)
                for k in range(NB):
                    if k >= 2:
                        pe.wait_ge(scaled, k - 1)
                    for half in range(2):
                        c = slice(half * HALF, (half + 1) * HALF)
                        last = nc.tensor.matmul(every[k % 2][:, c], spread[:, k, :], rows[:, c], start=True, stop=True)
                    last.then_inc(spread_ready, 1)

            @block.vector
            def _(ve):
                ve.wait_ge(std_ready, 1)
                nc.vector.reciprocal(rows[:], rows[:]).then_inc(rstd_ready, 1)
                for k in range(NB):
                    ve.wait_ge(spread_ready, k + 1)
                    nc.vector.scalar_tensor_tensor(out=x[:, first + k, :], in0=x[:, first + k, :], scalar=scale_of(k),
                                                   in1=every[k % 2][:], op0=ALU.mult, op1=ALU.mult).then_inc(scaled, 1)


def delta_rows(nc, ga, gb, cols, consts, dram, col_out):
    R, NCH = GATE_ROWS, DT
    with Phase(nc, "grow") as ph:
        soft = ph.sb("soft", [R, S])
        g = ph.sb("g", [R, S])
        resets = ph.sb("resets", [R, S])
        quant = [ph.sb(f"quant{i}", [R, S]) for i in range(4)]
        ends = ph.sb("ends", [R, NCH])
        rate = ph.sb("rate", [R, 1])
        turned = [ph.ps(f"turned{i}", [P, DT, R]) for i in range(4)]
        soft_ready, rate_ready = ph.sem("soft_ready"), ph.sem("rate_ready")
        args_ready, exps_done = ph.sem("args_ready"), ph.sem("exps_done")
        turned_ready = ph.sem("turned_ready")
        stored = [ph.sem(f"stored{i}") for i in range(3)]
        F, B = slice(0, G_H), slice(32, 32 + G_H)

        def chunks(x):
            return x.rearrange("p (n c) -> p n c", c=P)

        with nc.Block() as block:

            @block.scalar
            def _(se):
                nc.scalar.activation(soft[:], ga[:], ACT.Abs, bias=cols["g_dt"][0:R, :])
                nc.scalar.activation(rate[:], cols["g_alog"][0:R, :], ACT.Exp).then_inc(rate_ready, 1)
                se.drain()
                nc.scalar.activation(soft[:], soft[:], ACT.Exp, scale=-1.0)
                se.drain()
                nc.scalar.activation(soft[:], soft[:], ACT.Ln, bias=1.0).then_inc(soft_ready, 1)
                nc.scalar.activation(quant[1][:], gb[:], ACT.Sigmoid)
                se.wait_ge(args_ready, 1)
                nc.scalar.activation(quant[2][:], quant[0][:], ACT.Exp)
                nc.scalar.activation(quant[3][:], quant[3][:], ACT.Exp)
                nc.scalar.activation(ends[:], ends[:], ACT.Exp)
                se.drain().then_inc(exps_done, 1)
                for i in range(4):
                    se.wait_ge(turned_ready, i + 1)
                    nc.scalar.activation(col_out[:, i, :, :], turned[i][:], ACT.Copy)
                nc.scalar.activation(col_out[:, 4, :, :], turned[2][:], ACT.Copy, scale=-1.0)

            @block.vector
            def _(ve):
                gc = quant[0]
                nc.vector.tensor_scalar(g[:], ga[:], cols["g_dt"][0:R, :], 0.0, ALU.add, ALU.max)
                chunk_resets(nc, resets)
                nc.vector.memset(gc[:], 0.0)
                nc.vector.memset(ends[:], 0.0)
                ve.drain()
                ve.wait_ge(soft_ready, 1)
                nc.vector.tensor_tensor(g[:], g[:], soft[:], ALU.add)
                ve.drain()
                ve.wait_ge(rate_ready, 1)
                nc.vector.tensor_scalar(g[:], g[:], rate[:], -1.0, ALU.mult, ALU.mult)
                ve.drain()
                nc.vector.tensor_tensor_scan(gc[F, :], resets[F, :], g[F, :], 0.0, ALU.mult, ALU.add)
                nc.vector.tensor_tensor_scan(gc[B, ::-1], resets[B, :], g[B, ::-1], 0.0, ALU.mult, ALU.add)
                ve.drain()
                nc.vector.tensor_copy(ends[F, :], chunks(gc[:])[F, :, P - 1])
                nc.vector.tensor_copy(ends[B, :], chunks(gc[:])[B, :, 0])
                ve.drain()
                nc.vector.tensor_tensor(chunks(quant[3][:]), ends[:, :, None].broadcast_to([R, NCH, P]), chunks(gc[:]),
                                        ALU.subtract)
                ve.drain().then_inc(args_ready, 1)

            @block.tensor
            def _(pe):
                pe.wait_ge(exps_done, 1)
                for i in range(4):
                    for t in range(DT):
                        last = nc.tensor.transpose(turned[i][:, t, :], quant[i][:, t * P:(t + 1) * P], consts["ident"][0:R, 0:R])
                    last.then_inc(turned_ready, 1)

            @block.sync
            def _(sp):
                sp.wait_ge(exps_done, 1)
                for i, (name, src) in enumerate((("g_gc", quant[0]), ("g_beta", quant[1]), ("g_end", ends))):
                    sp.dma_start(dram[name], src[:]).then_inc(stored[i], 16)
                for i in range(3):
                    sp.wait_ge(stored[i], 16)


def delta_rule(nc, d, consts, cols, dram, qkv, z, gate_cols, mix):
    NG = 4
    N_INV = 2 * LEVELS * 2
    N_Z = 2 * (LEVELS - 1) * 2
    NU = 2 * DT
    with Phase(nc, "delta") as ph:
        qs, ks, vf = ph.sb("qs", [P, S]), ph.sb("ks", [P, S]), ph.sb("vf", [P, S])
        kt = ph.sb("kt", [P, DT, P])
        vt = vf[:].rearrange("p (t c) -> p t c", c=P)
        gc_row = [ph.sb(f"gc_row{i}", [P, S]) for i in range(2)]
        beta_row = [ph.sb(f"beta_row{i}", [P, S]) for i in range(2)]
        end_row = ph.sb("end_row", [P, 2, G_H, DT])
        level = ph.sb("level", [P, 2 * LEVELS, P])
        gam = [ph.sb(f"gam{i}", [P, NG, P]) for i in range(2)]
        pt = [ph.sb(f"pt{i}", [P, NG, P]) for i in range(4)]
        at_all = ph.sb("at", [P, 4 * NG, P])
        at = [at_all[:, i * NG:(i + 1) * NG, :] for i in range(4)]
        xt = [ph.sb(f"xt{i}", [P, NG, P]) for i in range(4)]
        free = [mix[:, 4 + i, :].rearrange("p (a n c) -> p a n c", a=2, c=P) for i in range(3)]
        bt = [[free[i][:, j] for j in range(2)] for i in range(2)]
        xx = [free[2][:, i] for i in range(2)]
        r, rb, vn, vkd = (mix[:, 7, 2 * i * P:2 * (i + 1) * P].rearrange("p (a c) -> p a c", a=2) for i in range(4))
        ys = gam
        state = ph.sb("state", [P, 2, P])
        t1 = ph.sb("t1", [P, 2, P])
        osum = at_all[:, 0:DT, :]
        ss = ph.sb("ss", [P, DT])
        bank = [ph.ps(f"bank{i}", [P, NG, P]) for i in range(4)]
        turned_k, turned_v = ph.ps("turned_k", [P, S]), ph.ps("turned_v", [P, S])
        zt_bank = [turned_k[:, 0:HALF].rearrange("p (n c) -> p n c", c=P), turned_k[:, HALF:S].rearrange("p (n c) -> p n c", c=P)]
        level_landed = ph.sem("level_landed")
        row_landed = [ph.sem(f"row_landed{i}") for i in range(4)]
        end_landed = [ph.sem(f"end_landed{i}") for i in range(2)]
        staged = ph.sem("staged")
        head_free = ph.sem("head_free")
        turned_ready = ph.sem("turned_ready")
        kv_ready = ph.sem("kv_ready")
        prod_ready = ph.sem("prod_ready")
        garg = ph.sem("garg")
        gam_ready = ph.sem("gam_ready")
        kk_ready = ph.sem("kk_ready")
        at_ready = ph.sem("at_ready")
        bt_ready = ph.sem("bt_ready")
        y_ready = ph.sem("y_ready")
        y_copied = ph.sem("y_copied")
        z_ready = ph.sem("z_ready")
        x_done = ph.sem("x_done")
        ks_ready = ph.sem("ks_ready")
        r_ready = ph.sem("r_ready")
        rb_ready = ph.sem("rb_ready")
        vn_ready = ph.sem("vn_ready")
        vns_ready = ph.sem("vns_ready")
        vkd_ready = ph.sem("vkd_ready")
        su_ready = ph.sem("su_ready")
        s_done = ph.sem("s_done")
        ss_ready, std_ready = ph.sem("ss_ready"), ph.sem("std_ready")
        normed, o_turned = ph.sem("normed"), ph.sem("o_turned")
        ident = consts["ident"]
        masks = (consts["m_mask_f"], consts["m_mask_b"])

        def gate_col(q, chunk, dr, h):
            return gate_cols[:, q, chunk, bass.ds(32 * dr + h, 1)]

        def tok(c):
            return slice(c * P, (c + 1) * P)

        def chunk_of(step, dr):
            return step if dr == 0 else DT - 1 - step

        inverse_steps = [(pp, l, g) for pp in range(2) for l in range(LEVELS) for g in range(2)]

        with nc.Block() as block:

            @block.sync
            def _(sp):
                sp.dma_start(level[:].rearrange("p l c -> p (l c)"), d["g_levels"]).then_inc(level_landed, 16)
                for dr in range(2):
                    sp.dma_start(end_row[:, dr].rearrange("p h t -> p (h t)"), dram["g_end"][32 * dr:32 * dr + G_H, :].rearrange(
                        "(o h) t -> o (h t)", o=1).broadcast_to([P, G_H * DT])).then_inc(end_landed[dr], 16)

                def load_rows(h):
                    for dr in range(2):
                        row = bass.ds(32 * dr + h, 1)
                        sp.dma_start(gc_row[dr][:], dram["g_gc"][row, :].broadcast_to([P, S])).then_inc(row_landed[2 * dr], 16)
                        sp.dma_start(beta_row[dr][:], dram["g_beta"][row, :].broadcast_to([P, S])).then_inc(row_landed[2 * dr + 1], 16)

                load_rows(0)
                with sp.Fori(1, G_H) as h:
                    sp.wait_ge(garg, 4 * h)
                    sp.wait_ge(at_ready, 4 * h)
                    load_rows(h)

            @block.gpsimd
            def _(pool):
                pool.wait_ge(level_landed, 16)
                with pool.Fori(0, G_H) as h:
                    pool.wait_ge(head_free, h + 1)
                    nc.gpsimd.tensor_copy(vf[:], qkv[:, h + 2 * G_H, :]).then_inc(staged, 1)
                    for dr in range(2):
                        pool.wait_ge(row_landed[2 * dr + 1], 16 * h + 16)
                    for gi in range(4):
                        pool.wait_ge(kk_ready, 4 * h + gi + 1)
                        c0 = (gi % 2) * HALF
                        nc.gpsimd.tensor_tensor(at[gi].rearrange("p n c -> p (n c)"), at[gi].rearrange("p n c -> p (n c)"),
                                                beta_row[gi // 2][:, c0:c0 + HALF], ALU.mult).then_inc(at_ready, 1)
                    pool.wait_ge(at_ready, 4 * h + 4)
                    for n, (pp, l, g) in enumerate(inverse_steps):
                        if n >= 4:
                            pool.wait_ge(x_done, N_INV * h + n - 3)
                        mask = level[:, LEVELS * pp + l:LEVELS * pp + l + 1, :].broadcast_to([P, NG, P])
                        nc.gpsimd.tensor_tensor(bt[g][(pp * LEVELS + l) % 2], at[2 * pp + g], mask, ALU.mult).then_inc(bt_ready, 1)

            @block.tensor
            def _(pe):
                with pe.Fori(0, G_H) as h:
                    pe.wait_ge(staged, 3 * h + 3)
                    for t in range(DT):
                        nc.tensor.transpose(turned_k[:, tok(t)], ks[:, tok(t)], ident)
                    for t in range(DT):
                        last = nc.tensor.transpose(turned_v[:, tok(t)], vf[:, tok(t)], ident)
                    last.then_inc(turned_ready, 1)
                    for half in range(2):
                        for i in range(NG):
                            c = tok(half * NG + i)
                            nc.tensor.matmul(bank[half][:, i, :], ks[:, c], ks[:, c], start=True, stop=True)
                        for i in range(NG):
                            c = tok(half * NG + i)
                            last = nc.tensor.matmul(bank[2 + half][:, i, :], ks[:, c], qs[:, c], start=True, stop=True)
                        last.then_inc(prod_ready, 1)
                    pe.wait_ge(kv_ready, h + 1)
                    pe.wait_ge(kk_ready, 4 * h + 4)
                    zn = 0
                    for pp in range(2):
                        for l in range(LEVELS):
                            n0 = (pp * LEVELS + l) * 2
                            for g in range(2):
                                pe.wait_ge(bt_ready, N_INV * h + n0 + g + 1)
                                if l:
                                    pe.wait_ge(x_done, N_INV * h + n0 + g - 1)
                                elif pp:
                                    pe.wait_ge(y_copied, N_INV * h + n0 + g - 1)
                                for i in range(NG):
                                    last = nc.tensor.matmul(bank[g][:, i, :], bt[g][(pp * LEVELS + l) % 2][:, i, :],
                                                            xx[g][:, i, :] if l else ident, start=True, stop=True)
                                last.then_inc(y_ready, 1)
                            if l:
                                for g in range(2):
                                    pe.wait_ge(y_copied, N_INV * h + n0 + g + 1)
                                    if l < LEVELS - 1:
                                        for i in range(NG):
                                            nc.tensor.matmul(bank[2 + g][:, i, :], xt[2 * pp + g][:, i, :], ys[g][:, i, :],
                                                             start=True, stop=True)
                                    for i in range(NG):
                                        last = nc.tensor.matmul(zt_bank[g][:, i, :], ys[g][:, i, :], xt[2 * pp + g][:, i, :],
                                                                start=True, stop=True)
                                    last.then_inc(z_ready, 1)
                    pe.wait_ge(x_done, N_INV * h + N_INV)
                    for k in range(DT):
                        for dr in range(2):
                            c, m = tok(chunk_of(k, dr)), 2 * k + dr
                            if k:
                                pe.wait_ge(s_done, NU * h + m - 1)
                            nc.tensor.matmul(bank[dr][:, 0, :], ks[:, c], state[:, dr, :], start=True, stop=True)
                            nc.tensor.matmul(bank[dr][:, 1, :], qs[:, c], state[:, dr, :], start=True, stop=True).then_inc(ks_ready, 1)
                        for dr in range(2):
                            ch, m = chunk_of(k, dr), 2 * k + dr
                            pe.wait_ge(rb_ready, NU * h + m + 1)
                            nc.tensor.matmul(bank[2 + dr][:, 0, :], xt[2 * dr + ch // NG][:, ch % NG, :], rb[:, dr, :],
                                             start=True, stop=True).then_inc(vn_ready, 1)
                        for dr in range(2):
                            ch, m = chunk_of(k, dr), 2 * k + dr
                            pe.wait_ge(vns_ready, NU * h + m + 1)
                            nc.tensor.matmul(zt_bank[dr][:, 0, :], pt[2 * dr + ch // NG][:, ch % NG, :], vn[:, dr, :], start=True, stop=True)
                            pe.wait_ge(vkd_ready, NU * h + m + 1)
                            nc.tensor.matmul(zt_bank[dr][:, 1, :], kt[:, ch, :], vkd[:, dr, :], start=True, stop=True).then_inc(su_ready, 1)
                    pe.wait_ge(normed, h + 1)
                    for t in range(DT):
                        last = nc.tensor.transpose(turned_v[:, tok(t)], osum[:, t, :], ident)
                    last.then_inc(o_turned, 1)

            @block.scalar
            def _(se):
                with se.Fori(0, G_H) as h:
                    se.wait_ge(head_free, h + 1)
                    nc.scalar.activation(qs[:], qkv[:, h, :], ACT.Copy).then_inc(staged, 1)
                    se.wait_ge(turned_ready, h + 1)
                    nc.scalar.activation(kt[:].rearrange("p t c -> p (t c)"), turned_k[:], ACT.Copy)
                    nc.scalar.activation(vf[:], turned_v[:], ACT.Copy)
                    se.drain().then_inc(kv_ready, 1)
                    for gi in range(4):
                        se.wait_ge(garg, 4 * h + gi + 1)
                        nc.scalar.activation(gam[gi % 2][:], gam[gi % 2][:], ACT.Exp).then_inc(gam_ready, 1)
                    for n in range(N_INV):
                        g = n % 2
                        se.wait_ge(y_ready, N_INV * h + n + 1)
                        if n >= 2:
                            se.wait_ge(x_done, N_INV * h + n - 1)
                        nc.scalar.activation(ys[g][:], bank[g][:], ACT.Copy).then_inc(y_copied, 1)
                    for k in range(DT):
                        for dr in range(2):
                            ch, m = chunk_of(k, dr), 2 * k + dr
                            se.wait_ge(r_ready, NU * h + m + 1)
                            nc.scalar.activation(rb[:, dr, :], r[:, dr, :], ACT.Copy, scale=gate_col(1, ch, dr, h)).then_inc(rb_ready, 1)
                        for dr in range(2):
                            ch, m = chunk_of(k, dr), 2 * k + dr
                            se.wait_ge(vns_ready, NU * h + m + 1)
                            nc.scalar.activation(vkd[:, dr, :], vn[:, dr, :], ACT.Copy, scale=gate_col(3, ch, dr, h)).then_inc(vkd_ready, 1)
                    se.wait_ge(ss_ready, h + 1)
                    nc.scalar.activation(ss[:], ss[:], ACT.Sqrt, scale=1.0 / G_D, bias=1e-6).then_inc(std_ready, 1)

            @block.vector
            def _(ve):
                ve.sem_inc(head_free, 1)
                for dr in range(2):
                    ve.wait_ge(end_landed[dr], 16)
                with ve.Fori(0, G_H) as h:
                    nc.vector.tensor_copy(ks[:], qkv[:, h + G_H, :]).then_inc(staged, 1)
                    nc.vector.memset(state[:], 0.0)
                    for dr in range(2):
                        ve.wait_ge(row_landed[2 * dr], 16 * h + 16)

                    def argument(gi):
                        dr, half = gi // 2, gi % 2
                        for i in range(NG):
                            c = half * NG + i
                            last = nc.vector.scalar_tensor_tensor(out=gam[gi % 2][:, i, :], in0=gc_row[dr][:, tok(c)],
                                                                  scalar=gate_col(0, c, dr, h), in1=masks[dr],
                                                                  op0=ALU.subtract, op1=ALU.min)
                        last.then_inc(garg, 1)

                    argument(0)
                    for gi in range(4):
                        if gi < 3:
                            if gi:
                                ve.wait_ge(kk_ready, 4 * h + gi)
                            argument(gi + 1)
                        ve.wait_ge(gam_ready, 4 * h + gi + 1)
                        ve.wait_ge(prod_ready, 2 * h + gi % 2 + 1)
                        nc.vector.tensor_tensor(pt[gi][:], bank[2 + gi % 2][:], gam[gi % 2][:], ALU.mult)
                        nc.vector.tensor_tensor(at[gi], bank[gi % 2][:], gam[gi % 2][:], ALU.mult)
                        ve.drain().then_inc(kk_ready, 1)
                    for n, (pp, l, g) in enumerate(inverse_steps):
                        gi = 2 * pp + g
                        if l == 0:
                            ve.wait_ge(y_copied, N_INV * h + n + 1)
                            ident4 = ident[:, None, :].broadcast_to([P, NG, P])
                            nc.vector.tensor_tensor(xx[g], ident4, ys[g][:], ALU.subtract)
                            nc.vector.tensor_tensor(xt[gi][:], ident4, bt[g][(pp * LEVELS + l) % 2], ALU.subtract)
                        else:
                            ve.wait_ge(z_ready, N_Z * h + (pp * (LEVELS - 1) + l - 1) * 2 + g + 1)
                            if l < LEVELS - 1:
                                nc.vector.tensor_tensor(xx[g], xx[g], bank[2 + g][:], ALU.subtract)
                            nc.vector.tensor_tensor(xt[gi][:], xt[gi][:], zt_bank[g], ALU.subtract)
                        ve.drain().then_inc(x_done, 1)
                    for k in range(DT):
                        for dr in range(2):
                            ch, m = chunk_of(k, dr), 2 * k + dr
                            ve.wait_ge(ks_ready, NU * h + m + 1)
                            nc.vector.scalar_tensor_tensor(out=r[:, dr, :], in0=bank[dr][:, 0, :], scalar=gate_col(4, ch, dr, h),
                                                           in1=vt[:, ch, :], op0=ALU.mult, op1=ALU.add).then_inc(r_ready, 1)
                            if k < DT // 2:
                                nc.vector.tensor_scalar(t1[:, dr, :], bank[dr][:, 1, :], gate_col(2, ch, dr, h), None, ALU.mult)
                            else:
                                nc.vector.scalar_tensor_tensor(out=t1[:, dr, :], in0=bank[dr][:, 1, :], scalar=gate_col(2, ch, dr, h),
                                                               in1=osum[:, ch, :], op0=ALU.mult, op1=ALU.add)
                        for dr in range(2):
                            ve.wait_ge(vn_ready, NU * h + 2 * k + dr + 1)
                            nc.vector.tensor_copy(vn[:, dr, :], bank[2 + dr][:, 0, :]).then_inc(vns_ready, 1)
                        for dr in range(2):
                            ch, m = chunk_of(k, dr), 2 * k + dr
                            ve.wait_ge(su_ready, NU * h + m + 1)
                            nc.vector.scalar_tensor_tensor(out=state[:, dr, :], in0=state[:, dr, :], scalar=end_row[:, dr].rearrange("p h t -> p (h t)")[:, bass.ds(DT * h + ch, 1)],
                                                           in1=zt_bank[dr][:, 1, :], op0=ALU.mult, op1=ALU.add).then_inc(s_done, 1)
                            nc.vector.tensor_tensor(osum[:, ch, :], t1[:, dr, :], zt_bank[dr][:, 0, :], ALU.add)
                        ve.drain()
                    nc.vector.tensor_tensor(kt[:], osum, osum, ALU.mult)
                    ve.drain()
                    nc.vector.tensor_reduce(ss[:], kt[:], AX_X, ALU.add).then_inc(ss_ready, 1)
                    ve.wait_ge(std_ready, h + 1)
                    nc.vector.reciprocal(ss[:], ss[:])
                    ve.drain()
                    nc.vector.tensor_tensor(osum, osum, ss[:, :, None].broadcast_to([P, DT, P]), ALU.mult).then_inc(normed, 1)
                    ve.wait_ge(o_turned, h + 1)
                    nc.vector.scalar_tensor_tensor(out=mix[:, h, :], in0=turned_v[:], scalar=cols["g_norm_g"], in1=z[:, h, :],
                                                   op0=ALU.mult, op1=ALU.mult).then_inc(head_free, 1)


def neighbourhood_attention(nc, d, consts, cols, dram, nq, nk, nv, mix):
    NU = 2 * DT
    WK = WIN_R * GRID
    WE = WK + P

    def first_row(r):
        return min(max(r - WIN_R // 2, 0), GRID_ROWS - WIN_R)

    def shifted(pr):
        return first_row(2 * pr) != first_row(2 * pr + 1)

    units = [(pr, j) for pr in range(DT) for j in range(2)]
    with Phase(nc, "na") as ph:
        qs2, ks2 = ph.sb("qs", [P, 2, S]), ph.sb("ks", [P, 2, S])
        vs2 = ph.sb("vs", [P, 2, DT, P])
        table2 = ph.sb("table", [P, 2, 2, RPB_R * GRID])
        window = ph.sb("window", [P, RPB_R * GRID])
        s = ph.sb("s", [P, 2, WK])
        e = ph.sb("e", [P, 2, WE])
        et = ph.sb("et", [P, 2, WE])
        small = ph.sb("small", [P, 2, 3])
        sc = [ph.ps(f"sc{i}", [P, HALF]) for i in range(2)]
        turned = [ph.ps(f"turned{i}", [P, S]) for i in range(2)]
        o = [ph.ps(f"o{i}", [P, HALF]) for i in range(2)]
        window_landed = ph.sem("window_landed")
        tables_stored = ph.sem("tables_stored")
        table_landed = [[ph.sem(f"table_landed{p}{i}") for i in range(4)] for p in range(2)]
        staged = ph.sem("staged")
        pair_free = ph.sem("pair_free")
        waited = ph.sem("waited")
        sc_ready = ph.sem("sc_ready")
        max_ready = ph.sem("max_ready")
        exp_ready = ph.sem("exp_ready")
        e_ready = ph.sem("e_ready")
        turned_ready = ph.sem("turned_ready")
        et_ready = ph.sem("et_ready")
        o_ready = ph.sem("o_ready")
        o_taken = ph.sem("o_taken")
        rpb = d["rpb"]
        toeplitz = bass.AP(rpb.tensor, GRID - 1, [[RPB_R * 2 * GRID, 2 * 4], [2 * GRID, RPB_R], [-1, GRID], [1, GRID]])

        with nc.Block() as block:

            @block.sync
            def _(sp):
                sp.dma_start(window[:], d["na_columns"]).then_inc(window_landed, 16)
                for head in range(8):
                    sp.dma_start(dram["n_tables"][head].rearrange("q (r c) -> r q c", c=GRID), toeplitz[head]).then_inc(tables_stored, 16)
                sp.wait_ge(tables_stored, 8 * 16)
                with sp.Fori(0, 2) as b2:
                    for p in range(2):
                        b = 2 * b2 + p
                        sp.wait_ge(pair_free, b + 1)
                        for j in range(2):
                            for i in range(2):
                                sp.dma_start(table2[i * GRID:(i + 1) * GRID, p, j, :], dram["n_tables"][2 * b + j]).then_inc(table_landed[p][2 * j + i], 16)

            @block.gpsimd
            def _(pool):
                with pool.Fori(0, 2) as b2:
                    for p in range(2):
                        b = 2 * b2 + p
                        pool.wait_ge(pair_free, b + 1)
                        nc.gpsimd.tensor_copy(qs2[:, p, :], nq[:, b, :])
                        nc.gpsimd.tensor_copy(ks2[:, p, :], nk[:, b, :])
                        nc.gpsimd.tensor_copy(vs2[:, p], nv[:].rearrange("p t (b c) -> p t b c", c=P)[:, :, b, :])
                        pool.drain().then_inc(staged, 1)

            @block.tensor
            def _(pe):
                pe.sem_inc(pair_free, 2)
                with pe.Fori(0, 2) as b2:
                    for p in range(2):
                        b = 2 * b2 + p
                        qs, ks, vs = qs2[:, p], ks2[:, p], vs2[:, p]
                        pe.wait_ge(staged, b + 1)
                        for u in range(NU + 3):
                            if u < NU:
                                pr, j = units[u]
                                rows = slice(N_D * j, N_D * (j + 1))
                                if u >= 2:
                                    pe.wait_ge(max_ready, NU * b + u - 1)
                                pe.sem_inc(waited, 1)
                                for i in range(2):
                                    r = 2 * pr + i
                                    k0 = first_row(r) * GRID
                                    last = nc.tensor.matmul(sc[j][i * GRID:(i + 1) * GRID, :], qs[rows, r * GRID:(r + 1) * GRID],
                                                            ks[rows, k0:k0 + WK], start=True, stop=True)
                                last.then_inc(sc_ready, 1)
                            if 2 <= u < NU + 2:
                                q = u - 2
                                pr, j = units[q]
                                pe.wait_ge(e_ready, NU * b + q + 1)
                                if q >= 2:
                                    pe.wait_ge(et_ready, NU * b + q - 1)
                                for t in range(5 if shifted(pr) else 4):
                                    last = nc.tensor.transpose(turned[j][:, t * P:(t + 1) * P], e[:, j, t * P:(t + 1) * P], consts["ident"])
                                last.then_inc(turned_ready, 1)
                            if u >= 3:
                                q = u - 3
                                pr, j = units[q]
                                rows = slice(N_D * j, N_D * (j + 1))
                                tiles = 5 if shifted(pr) else 4
                                pe.wait_ge(et_ready, NU * b + q + 1)
                                if j == 0 and pr >= 2:
                                    pe.wait_ge(o_taken, DT * b + pr - 1)
                                for t in range(tiles):
                                    last = nc.tensor.matmul(o[pr % 2][rows, 0:P], vs[:, first_row(2 * pr) // 2 + t, rows],
                                                            et[:, j, t * P:(t + 1) * P], start=(t == 0), stop=(t == tiles - 1))
                                if j == 1:
                                    last.then_inc(o_ready, 1)
                        pe.drain().then_inc(pair_free, 1)

            @block.vector
            def _(ve):
                ve.wait_ge(window_landed, 16)
                with ve.Fori(0, 2) as b2:
                    for p in range(2):
                        b = 2 * b2 + p
                        table = table2[:, p]
                        for i in range(4):
                            ve.wait_ge(table_landed[p][i], 16 * b2 + 16)
                        nc.vector.tensor_tensor(table, table, window[:, None, :].broadcast_to([P, 2, RPB_R * GRID]), ALU.min)
                        ve.drain()
                        for u in range(NU + 1):
                            if u < NU:
                                pr, j = units[u]
                                ve.wait_ge(sc_ready, NU * b + u + 1)
                                if u >= 2:
                                    ve.wait_ge(exp_ready, NU * b + u - 1)
                                at = [(first_row(2 * pr + i) - 2 * pr - i + WIN_R - 1) * GRID for i in range(2)]
                                for rows, a in ([(slice(0, P), at[0])] if at[0] == at[1] else
                                                [(slice(i * GRID, (i + 1) * GRID), at[i]) for i in range(2)]):
                                    nc.vector.scalar_tensor_tensor(out=s[rows, j, :], in0=sc[j][rows, :], scalar=N_D ** -0.5,
                                                                   in1=table[rows, j, a:a + WK], op0=ALU.mult, op1=ALU.add)
                                ve.drain()
                                nc.vector.tensor_reduce(small[:, j, 0:1], s[:, j, :], AX_X, ALU.max, negate=True)
                                if shifted(pr) and not shifted(pr - 1):
                                    ve.wait_ge(turned_ready, NU * b + u - 1)
                                    nc.vector.memset(e[0:GRID, j, WK:WE], 0.0)
                                    nc.vector.memset(e[GRID:P, j, 0:GRID], 0.0)
                                    nc.vector.memset(e[GRID:P, j, WK + GRID:WE], 0.0)
                                ve.drain().then_inc(max_ready, 1)
                            if u >= 1:
                                pr, j = units[u - 1]
                                w = WE if shifted(pr) else WK
                                ve.wait_ge(exp_ready, NU * b + u)
                                nc.vector.reciprocal(small[:, j, 2:3], small[:, j, 1:2])
                                ve.drain()
                                nc.vector.tensor_scalar(e[:, j, 0:w], e[:, j, 0:w], small[:, j, 2:3], None, ALU.mult).then_inc(e_ready, 1)

            @block.scalar
            def _(se):
                with se.Fori(0, 2) as b2:
                    for p in range(2):
                        b = 2 * b2 + p
                        for u in range(NU + 4):
                            if u < NU:
                                pr, j = units[u]
                                se.wait_ge(max_ready, NU * b + u + 1)
                                if u >= 2:
                                    se.wait_ge(turned_ready, NU * b + u - 1)
                                for i, rows in enumerate((slice(0, GRID), slice(GRID, P)) if shifted(pr) else (slice(0, P),)):
                                    nc.scalar.activation(e[rows, j, i * GRID:i * GRID + WK], s[rows, j, :], ACT.Exp,
                                                         bias=small[rows, j, 0:1], accum_out=small[rows, j, 1:2])
                                se.drain().then_inc(exp_ready, 1)
                            if 2 <= u < NU + 2:
                                pr, j = units[u - 2]
                                w = WE if shifted(pr) else WK
                                se.wait_ge(turned_ready, NU * b + u - 1)
                                nc.scalar.activation(et[:, j, 0:w], turned[j][:, 0:w], ACT.Copy).then_inc(et_ready, 1)
                            if u >= 4 and units[u - 4][1] == 1:
                                pr = units[u - 4][0]
                                se.wait_ge(o_ready, DT * b + pr + 1)
                                nc.scalar.activation(mix[:, 4 + b, pr * P:(pr + 1) * P], o[pr % 2][:, 0:P], ACT.Copy).then_inc(o_taken, 1)


def third_block(nc, d, consts, cols, x, sink):
    dram = {"g_gc": nc.dram_tensor("g_gc", (GATE_ROWS, S), F32, kind="Internal").ap(),
            "g_beta": nc.dram_tensor("g_beta", (GATE_ROWS, S), F32, kind="Internal").ap(),
            "g_end": nc.dram_tensor("g_end", (GATE_ROWS, DT), F32, kind="Internal").ap()}
    dram["n_tables"] = nc.dram_tensor("n_tables", (8, GRID, RPB_R * GRID), F32, kind="Internal").ap()
    norm_rows(nc, "b3_in", x, x, consts, cols["ln_in_g"], cols["ln_in_b"], centre=True)
    with ExitStack() as tail:
        with ExitStack() as stack:
            with Phase(nc, "b3g") as ph:
                z = ph.sb("z", [P, 4, S])
                qkv = ph.sb("qkv", [P, 12, S])
                gate_cols = ph.sb("gate_cols", [P, 5, DT, GATE_ROWS])
                with Phase(nc, "b3r") as pg:
                    ga, gb = pg.sb("ga", [GATE_ROWS, S]), pg.sb("gb", [GATE_ROWS, S])
                    gate_inputs(nc, "b3_gates", d["w_gab"], x, ga, gb)
                    delta_rows(nc, ga, gb, cols, consts, dram, gate_cols)
                with Phase(nc, "b3x", side="right") as px:
                    pair = Pair(px, "x", DT, within=x)
                    project_chain(nc, "b3_conv", [
                        copy_stage(nc, d["w_gz"], pair.rows, 4, z, ACT.Silu),
                        conv_stage(nc, d["w_gqkv"], 12, pair.rows, lambda n, tap: cols["g_taps"][:, bass.ds(TAPS * n + tap, 1)], qkv)],
                        splits=[(x, pair, DT)], join=(pair, x))
                mix = stack.enter_context(Phase(nc, "b3", side="right")).sb("mix", [P, DT, S])
                normalise_heads(nc, "l2n", qkv, 0, 2 * G_H, d["pick_rows"], d["spread_rows"], 1.0, lambda k: G_D ** -0.5 if k < G_H else 1.0)
                delta_rule(nc, d, consts, cols, dram, qkv, z, gate_cols, mix)
            with Phase(nc, "b3n") as ph:
                nq, nk = ph.sb("nq", [P, 4, S]), ph.sb("nk", [P, 4, S])
                nv = ph.sb("nv", [P, DT, HALF])
                with Phase(nc, "b3y") as py:
                    pair = Pair(py, "x", DT, within=x)
                    tokens_pair(nc, "b3_nv", d["w_nv"].rearrange("p (t n) -> p t n", t=DT), HALF, pair, splits=[(x, pair, DT)],
                                act=lambda n, acc: nc.scalar.activation(nv[:, n, :], acc[:], ACT.Copy))
                    project_chain(nc, "b3_nqk", [copy_stage(nc, d["w_nq"], pair.rows, 4, nq), copy_stage(nc, d["w_nk"], pair.rows, 4, nk)], join=(pair, x))
                neighbourhood_attention(nc, d, consts, cols, dram, nq, nk, nv, mix)
                normalise_heads(nc, "nan", mix, 4, 4, d["na_pick"], d["na_spread"], 1.0 / N_D, lambda k: cols["n_norm_g"])
            block_sum = tail.enter_context(Phase(nc, "b3s")).sb("block_sum", [P, S])
            out_projection(nc, "b3_out", d["w_out3"], mix, x, block_sum)
        norm_rows(nc, "b3_ln1", x, x, consts, cols["ln1_g3"], cols["ln1_b3"], centre=True, block_sum=block_sum)
        with Phase(nc, "b3f") as ph:
            y = ph.sb("y", [P, DT, S])
            pair = Pair(ph, "x", DT, within=x)
            hidden = Pair(ph, "hidden", DT)

            def squared(n, acc, tmp, conv):
                nc.vector.tensor_tensor(tmp[:], tmp[:], tmp[:], ALU.mult)
                nc.vector.drain()
                put_pair(nc, hidden, n, tmp)

            def relu(b1):
                return lambda n, acc, tmp: nc.scalar.activation(tmp[:], acc[:], ACT.Relu, bias=b1[:, bass.ds(n, 1)])

            stages = []
            for c in range(D_FF3 // P // DT):
                blocks = slice(c * DT, (c + 1) * DT)
                stages.append(Stage(d["w1_3"][blocks], DT, pair.rows, DT, dve=squared, act=relu(cols["b1_3"][:, blocks])))
                if c == 0:
                    stages.append(Stage(d["w2_3_0"], DT, hidden.rows, 8,
                                        act=lambda n, acc, tmp: nc.scalar.activation(tmp[:], acc[:], ACT.Identity, bias=cols["b2_3"][:, bass.ds(n, 1)]),
                                        dve=lambda n, acc, tmp, conv: add_residual(nc, y[:, n, :], pair, n, tmp[:])))
                else:
                    stages.append(add_stage(nc, d[f"w2_3_{c}"], DT, hidden.rows, 8, y))
            project_chain(nc, "b3_ffn", stages, splits=[(x, pair, DT)], block_sum=(block_sum, y))
            norm_rows(nc, "b3_ln2", y, x, consts, cols["ln2_g3"], cols["ln2_b3"], centre=True, sink=sink, block_sum=block_sum)


L3_COLUMNS = {"ln_in_g": 8, "ln_in_b": 8, "g_alog": 1, "g_dt": 1, "g_taps": 60, "g_norm_g": 1, "n_norm_g": 1,
              "ln1_g3": 8, "ln1_b3": 8, "b1_3": 32, "b2_3": 8, "ln2_g3": 8, "ln2_b3": 8}
L3_SQUARES = ()


def third_arrays(a):
    import numpy as np
    w = a["w_in_3"][0]
    gqkv, gz, ga, gb, nq, nk, nv = np.split(w, np.cumsum([1536, 512, 8, 8, 512, 512]), axis=1)
    i = np.arange(P)
    forward = np.stack([(i[:, None] >> (l + 1) == i[None, :] >> (l + 1)) & ((i[:, None] >> l) % 2 == 0) & ((i[None, :] >> l) % 2 == 1)
                        for l in range(LEVELS)])
    levels = np.concatenate([forward, forward.transpose(0, 2, 1)]).astype(np.float32).transpose(1, 0, 2).reshape(P, -1)
    eye = np.eye(8, dtype=np.float32)
    rpb = np.zeros((8, RPB_R, 2 * GRID), np.float32)
    rpb[:, :, GRID - WIN_C:GRID - WIN_C + RPB_C] = a["rpb_3"][0]
    q, k = np.arange(GRID)[:, None], np.arange(GRID)[None, :]
    start = np.clip(q - WIN_C // 2, 0, GRID - WIN_C)
    window = np.where((k >= start) & (k < start + WIN_C), BIG, -BIG).astype(np.float32)
    w2 = a["w2_3"][0]
    half_heads = np.repeat(eye, N_D, axis=0)
    out = {"w_gqkv": rows_weight(gqkv), "w_gz": rows_weight(gz), "w_gab": gate_weight(ga, gb),
           "w_nq": rows_weight(nq), "w_nk": rows_weight(nk), "w_nv": tokens_weight(nv),
           "g_levels": levels, 
           "na_pick": half_heads.reshape(4, P, 8).transpose(1, 0, 2).reshape(P, 32), "na_spread": half_heads.T,
           "rpb": rpb, "na_columns": np.tile(window, (2, RPB_R)), "w_out3": rows_weight(a["w_out_3"][0]),
           "w1_3": rows_weight(a["w1_3"][0])}
    for c, part in enumerate(np.split(w2, D_FF3 // P // DT)):
        out[f"w2_3_{c}"] = rows_weight(part)
    columns = {"ln_in_g": column(a["ln_in_g_3"]), "ln_in_b": column(a["ln_in_b_3"]),
               "g_alog": gate_column(a["a_log_3"].reshape(8)), "g_dt": gate_column(a["dt_bias_3"].reshape(8)),
               "g_taps": a["conv_w_3"][0].reshape(TAPS, 12, P).transpose(2, 1, 0).reshape(P, 60),
               "g_norm_g": column(a["gdn_norm_g_3"]), "n_norm_g": np.tile(a["na_norm_g_3"].reshape(1, 64), (2, 1)).reshape(P, 1),
               "ln1_g3": column(a["ln1_g_3"]), "ln1_b3": column(a["ln1_b_3"]), "b1_3": column(a["b1_3"]), "b2_3": column(a["b2_3"]),
               "ln2_g3": column(a["ln2_g_3"]), "ln2_b3": column(a["ln2_b_3"])}
    return out, columns, {}

COLUMNS = {"pre_g": 8, "post_g": 8, "b_a2": 4, "b_norm_g": 8, "a_ln_g": 8, "a_ln_b": 8}
COLUMNS |= L2_COLUMNS | L3_COLUMNS
SQUARES = ("ones", "ident", "le", "gla_mask", "ones64") + tuple(L2_SQUARES) + tuple(L3_SQUARES)


def build_program(nc, d, layers=(1, 2, 3)):
    with Phase(nc, "all") as ph:
        x = ph.sb("x", [P, DT, S])
        squares = ph.sb("squares", [P, len(SQUARES), P])
        columns = ph.sb("columns", [P, sum(COLUMNS.values())])
        consts = {name: squares[:, i, :] for i, name in enumerate(SQUARES)}
        cols, at = {}, 0
        for name, n in COLUMNS.items():
            cols[name] = columns[:, at:at + n]
            at += n
        load_phase(nc, "consts", [(squares[:].rearrange("p n c -> p (n c)"), d["squares"]), (columns[:], d["columns"])])
        consts["pick_rows"], consts["spread_rows"] = d["pick_rows"], d["spread_rows"]
        consts["le3"] = squares[:, SQUARES.index("le"):SQUARES.index("le") + 1, :].broadcast_to([P, 8, P])
        if 1 in layers:
            first_block(nc, d, consts, cols, x)
        else:
            load_phase(nc, "x", [(x[:, :, :], d["xT"].rearrange("p (t s) -> p t s", t=DT))])
        if 2 in layers:
            second_block(nc, d, consts, cols, x)
        if 3 in layers:
            third_block(nc, d, consts, cols, x, sink=d["outT"])



def rows_weight(w):
    K, N = w.shape
    return w.reshape(K // P, P, N // P, P).transpose(2, 1, 0, 3).reshape(N // P, P, K)


def tokens_weight(w):
    K, N = w.shape
    return w.reshape(K // P, P, N).transpose(1, 0, 2).reshape(P, (K // P) * N)


def column(v):
    return v.reshape(-1, P).T


def causal_squares():
    import numpy as np
    i = np.arange(P)
    le = (i[:, None] <= i[None, :]).astype(np.float32)
    return {"ones": np.ones((P, P), np.float32), "ident": np.eye(P, dtype=np.float32), "le": le,
            "gla_mask": le * (i[:, None] // 64 == i[None, :] // 64),
            "ones64": (i[:, None] // 64 == i[None, :] // 64).astype(np.float32)}


def first_arrays(a):
    import numpy as np
    w = a["w_in"][0]
    cuts = np.cumsum([1024, 1024, 1024, 512, 512, 1024, 1024])
    au, av, ag, bq, bk, bv, bg, lr = np.split(w, cuts, axis=1)
    out = {"w_au": rows_weight(au), "w_agate": rows_weight(ag), "w_bgate": rows_weight(bg),
           "w_qk": rows_weight(w[:, 3072:4096]), "w_av": tokens_weight(av), "w_bv": tokens_weight(bv),
           "w_lr": lr.reshape(DT, P, 16).transpose(1, 0, 2).reshape(1, P, DT * 16),
           "w_a2": a["w_a2"][0].reshape(16, 4, P).transpose(1, 0, 2),
           "w_sT": a["a_w_s"][0].transpose(2, 0, 1).reshape(P, 8 * P),
           "b_s": a["a_b_s"].reshape(1, 8 * P), "w_out1a": rows_weight(a["w_out"][0][0:1024]), "w_out1b": rows_weight(a["w_out"][0][1024:])}
    columns = {"pre_g": column(a["pre_norm_g"]), "post_g": column(a["post_norm_g"]), "b_a2": column(a["b_a2"]),
               "b_norm_g": column(a["b_norm_g"]), "a_ln_g": column(a["a_ln_g"]), "a_ln_b": column(a["a_ln_b"])}
    return out, columns, {}


def arrays_of(a, layers=(1, 2, 3)):
    import numpy as np
    out = {"xT": a["x"][0].T.reshape(DT, P, S).transpose(1, 0, 2).reshape(P, DT * S)}
    eye = np.eye(DT, dtype=np.float32)
    out["pick_rows"], out["spread_rows"] = np.tile(eye.reshape(1, DT * DT), (P, 1)), np.repeat(eye, P, axis=1)
    columns, squares = {}, causal_squares()
    for n, arrays in ((1, first_arrays), (2, second_arrays), (3, third_arrays)):
        more, cols, sqs = arrays(a)
        if n in layers:
            out.update(more)
        columns.update(cols)
        squares.update(sqs)
    for name, n in COLUMNS.items():
        assert columns[name].shape == (P, n), (name, columns[name].shape)
    out["columns"] = np.concatenate([columns[name] for name in COLUMNS], axis=1)
    out["squares"] = np.concatenate([squares[name] for name in SQUARES], axis=1)
    return {name: np.ascontiguousarray(v) for name, v in out.items()}


def kernel(**inputs):
    import numpy as _np
    import concourse.bacc as _bacc
    from concourse import mybir as _mybir
    from concourse.bass_utils import run_bass_kernel_spmd as _run

    nc = _bacc.Bacc("TRN2", target_bir_lowering=False, num_devices=1)
    arrays = arrays_of({name: _np.asarray(v) for name, v in inputs.items()})
    d = {name: nc.dram_tensor(name, v.shape, _mybir.dt.from_np(v.dtype), kind="ExternalInput").ap()
         for name, v in arrays.items()}
    d["outT"] = nc.dram_tensor("outT", (P, DT * S), F32, kind="ExternalOutput").ap()
    build_program(nc, d)
    r = _run(nc, [arrays], core_ids=[0])
    got = r.results[0]["outT"].reshape(P, DT, S).transpose(2, 1, 0).reshape(1, S, DT * P)
    return _np.ascontiguousarray(got)
```
